# Optimizing a Trainium2 kernel written in Bass

```python
import jax, jax.numpy as jnp
from jax import lax
import numpy as np
import jax
import jax.numpy as jnp

D_MODEL = 1024
BATCH = 1
SEQ = 256
DEPTH = 2

CHUNK = 64
Q_BLOCK = 128

MLA_HEADS = 8
Q_LORA = 384
KV_LORA = 256
QK_NOPE = 64
QK_ROPE = 32
V_HEAD = 64
ROPE_THETA = 10000.0

MLSTM_HEADS = 8
MLSTM_HEAD_DIM = 64
MLSTM_W = MLSTM_HEADS * MLSTM_HEAD_DIM
MLSTM_CONV = 4

D_FF = 2816
FFN_CONV = 3

MLA_W = MLA_HEADS * V_HEAD
IN_SIZES = (Q_LORA, KV_LORA, QK_ROPE,
            MLSTM_W, MLSTM_W, MLSTM_W, MLSTM_W,
            MLSTM_HEADS, MLSTM_HEADS,
            D_MODEL, D_MODEL)
IN_COLS = sum(IN_SIZES)


def _rmsnorm(x, w, eps=1e-6):
    x32 = x.astype(jnp.float32)
    y = x32 * lax.rsqrt(jnp.mean(x32 * x32, axis=-1, keepdims=True) + eps)
    return y.astype(x.dtype) * w

def _rope(x, positions):
    half = x.shape[-1] // 2
    inv = ROPE_THETA ** (-jnp.arange(half, dtype=jnp.float32) / half)
    ang = positions.astype(jnp.float32)[..., None] * inv
    if x.ndim == 4:
        ang = ang[:, :, None, :]
    cos = jnp.cos(ang).astype(x.dtype)
    sin = jnp.sin(ang).astype(x.dtype)
    x1, x2 = x[..., :half], x[..., half:]
    return jnp.concatenate([x1 * cos - x2 * sin, x2 * cos + x1 * sin], axis=-1)

def _causal_dwconv(x, w, b):
    k_w, ch = w.shape
    y = lax.conv_general_dilated(
        x, w[:, None, :].astype(x.dtype), window_strides=(1,),
        padding=[(k_w - 1, 0)], dimension_numbers=("NWC", "WIO", "NWC"),
        feature_group_count=ch)
    return y + b

def _mla_attention(q_nope, q_rope, k_nope, k_rope, v):
    s_len = q_nope.shape[1]
    scale = (QK_NOPE + QK_ROPE) ** -0.5
    outs = []
    for qb in range(s_len // Q_BLOCK):
        s0, e = qb * Q_BLOCK, (qb + 1) * Q_BLOCK
        sc = (jnp.einsum("bqhd,bkhd->bhqk", q_nope[:, s0:e], k_nope[:, :e])
              + jnp.einsum("bqhr,bkr->bhqk", q_rope[:, s0:e], k_rope[:, :e]))
        sc = sc.astype(jnp.float32) * scale
        q_chunk = (s0 + jnp.arange(Q_BLOCK)) // CHUNK
        k_chunk = jnp.arange(e) // CHUNK
        sc = jnp.where(k_chunk[None, :] <= q_chunk[:, None], sc, -jnp.inf)
        p = jax.nn.softmax(sc, axis=-1).astype(v.dtype)
        outs.append(jnp.einsum("bhqk,bkhd->bqhd", p, v[:, :e]))
    return jnp.concatenate(outs, axis=1)

def _mlstm_chunkwise(q, k, v, i_pre, log_f):
    bsz, s_len, nh, dk = q.shape
    dv = v.shape[-1]
    L = CHUNK
    nc = s_len // L
    f32 = jnp.float32

    def to_chunks(a):
        return jnp.moveaxis(a.astype(f32).reshape((bsz, nc, L) + a.shape[2:]), 1, 0)

    xs = tuple(to_chunks(a) for a in (q, k, v, i_pre, log_f))
    causal = jnp.tril(jnp.ones((L, L), dtype=bool))

    def step(carry, inp):
        C, n, m = carry
        qc, kc, vc, ic, fc = inp
        b = jnp.cumsum(fc, axis=1).transpose(0, 2, 1)
        ih = ic.transpose(0, 2, 1)
        log_d = jnp.where(causal, b[..., :, None] - b[..., None, :] + ih[..., None, :], -jnp.inf)
        log_inter = b + m[..., None]
        m_t = jnp.maximum(log_inter, jnp.max(log_d, axis=-1))
        w_intra = jnp.exp(log_d - m_t[..., None])
        w_inter = jnp.exp(log_inter - m_t)
        s = jnp.einsum("bthd,bshd->bhts", qc, kc) * w_intra
        num = (jnp.einsum("bhts,bshv->bhtv", s, vc)
               + w_inter[..., None] * jnp.einsum("bhvk,bthk->bhtv", C, qc))
        den = s.sum(-1) + w_inter * jnp.einsum("bhk,bthk->bht", n, qc)
        h = num / jnp.maximum(jnp.abs(den), jnp.exp(-m_t))[..., None]
        b_last = b[..., -1]
        log_w = b_last[..., None] - b + ih
        m_new = jnp.maximum(b_last + m, jnp.max(log_w, axis=-1))
        w_s = jnp.exp(log_w - m_new[..., None])
        decay = jnp.exp(b_last + m - m_new)
        C = decay[..., None, None] * C + jnp.einsum("bhs,bshv,bshk->bhvk", w_s, vc, kc)
        n = decay[..., None] * n + jnp.einsum("bhs,bshk->bhk", w_s, kc)
        return (C, n, m_new), h.transpose(0, 2, 1, 3)

    init = (jnp.zeros((bsz, nh, dv, dk), f32), jnp.zeros((bsz, nh, dk), f32),
            jnp.zeros((bsz, nh), f32))
    _, hs = lax.scan(step, init, xs)
    return jnp.moveaxis(hs, 0, 1).reshape(bsz, s_len, nh, dv).astype(v.dtype)

def _mixer(h, positions, w_in, q_norm_w, kv_norm_w, w_uq, w_ukv, conv_w, conv_b,
           gate_b, head_norm_w, w_br_mla, w_br_mlstm, w_out):
    bsz, s_len, _ = h.shape
    split_at = [int(s) for s in np.cumsum(IN_SIZES)[:-1]]
    proj = h @ w_in
    c_q, c_kv, k_rope, q_m, k_m, v_m, o_m, i_m, f_m, g_mla, g_mlstm = jnp.split(proj, split_at, axis=-1)

    q = (_rmsnorm(c_q, q_norm_w) @ w_uq).reshape(bsz, s_len, MLA_HEADS, QK_NOPE + QK_ROPE)
    q_nope, q_rope = q[..., :QK_NOPE], _rope(q[..., QK_NOPE:], positions)
    kv = (_rmsnorm(c_kv, kv_norm_w) @ w_ukv).reshape(bsz, s_len, MLA_HEADS, QK_NOPE + V_HEAD)
    k_nope, v = kv[..., :QK_NOPE], kv[..., QK_NOPE:]
    k_rope = _rope(k_rope, positions)
    y_mla = _mla_attention(q_nope, q_rope, k_nope, k_rope, v).reshape(bsz, s_len, MLA_W)

    qk = jax.nn.silu(_causal_dwconv(jnp.concatenate([q_m, k_m], axis=-1), conv_w, conv_b))
    q_m, k_m = jnp.split(qk, 2, axis=-1)
    i_pre, f_pre = jnp.split(jnp.concatenate([i_m, f_m], axis=-1) + gate_b, 2, axis=-1)
    hd = (bsz, s_len, MLSTM_HEADS, MLSTM_HEAD_DIM)
    hm = _mlstm_chunkwise(q_m.reshape(hd), k_m.reshape(hd) * (MLSTM_HEAD_DIM ** -0.5),
                          v_m.reshape(hd), i_pre.astype(jnp.float32),
                          jax.nn.log_sigmoid(f_pre.astype(jnp.float32)))
    hm = _rmsnorm(hm, head_norm_w.reshape(MLSTM_HEADS, MLSTM_HEAD_DIM))
    y_mlstm = jax.nn.sigmoid(o_m) * hm.reshape(bsz, s_len, MLSTM_W)

    merged = (jax.nn.sigmoid(g_mla) * (y_mla @ w_br_mla)
              + jax.nn.sigmoid(g_mlstm) * (y_mlstm @ w_br_mlstm))
    return merged @ w_out

def _conv_ffn(h, w_up, conv_w, conv_b, w_down):
    u = _causal_dwconv(h @ w_up, conv_w, conv_b)
    a, val = jnp.split(u, 2, axis=-1)
    return (jax.nn.gelu(a) * val) @ w_down

def first_inputs(seed: int = 0) -> dict:
    key = jax.random.key(seed)
    ks = jax.random.split(key, 32)
    f32 = jnp.float32

    def nrm(k, shape, scale):
        return jax.random.normal(k, shape, f32) * scale

    def gain(k, shape):
        return 1.0 + 0.02 * jax.random.normal(k, shape, f32)

    offsets = jax.random.randint(ks[2], (BATCH, 1), 0, 4096, dtype=jnp.int32)
    positions = offsets + jnp.arange(SEQ, dtype=jnp.int32)[None, :]
    gate_b = jnp.concatenate([
        0.1 * jax.random.normal(ks[12], (DEPTH, MLSTM_HEADS), f32),
        3.0 + 3.0 * jax.random.uniform(ks[13], (DEPTH, MLSTM_HEADS), f32)], axis=-1)
    return {
        "x": nrm(ks[0], (BATCH, SEQ, D_MODEL), 1.0),
        "c": nrm(ks[1], (BATCH, D_MODEL), 1.0),
        "positions": positions,
        "ada_w": nrm(ks[3], (DEPTH, D_MODEL, 6 * D_MODEL), 0.5 * D_MODEL ** -0.5),
        "ada_b": nrm(ks[4], (DEPTH, 6 * D_MODEL), 0.02),
        "norm_mix_w": gain(ks[5], (DEPTH, D_MODEL)),
        "w_in": nrm(ks[6], (DEPTH, D_MODEL, IN_COLS), D_MODEL ** -0.5),
        "q_norm_w": gain(ks[7], (DEPTH, Q_LORA)),
        "kv_norm_w": gain(ks[8], (DEPTH, KV_LORA)),
        "w_uq": nrm(ks[9], (DEPTH, Q_LORA, MLA_HEADS * (QK_NOPE + QK_ROPE)), Q_LORA ** -0.5),
        "w_ukv": nrm(ks[10], (DEPTH, KV_LORA, MLA_HEADS * (QK_NOPE + V_HEAD)), KV_LORA ** -0.5),
        "mlstm_conv_w": nrm(ks[11], (DEPTH, MLSTM_CONV, 2 * MLSTM_W), MLSTM_CONV ** -0.5),
        "mlstm_conv_b": nrm(ks[14], (DEPTH, 2 * MLSTM_W), 0.02),
        "mlstm_gate_b": gate_b,
        "mlstm_head_norm_w": gain(ks[15], (DEPTH, MLSTM_W)),
        "w_br_mla": nrm(ks[16], (DEPTH, MLA_W, D_MODEL), MLA_W ** -0.5),
        "w_br_mlstm": nrm(ks[17], (DEPTH, MLSTM_W, D_MODEL), MLSTM_W ** -0.5),
        "w_out": nrm(ks[18], (DEPTH, D_MODEL, D_MODEL), D_MODEL ** -0.5),
        "norm_ffn_w": gain(ks[19], (DEPTH, D_MODEL)),
        "ffn_w_up": nrm(ks[20], (DEPTH, D_MODEL, 2 * D_FF), D_MODEL ** -0.5),
        "ffn_conv_w": nrm(ks[21], (DEPTH, FFN_CONV, 2 * D_FF), FFN_CONV ** -0.5),
        "ffn_conv_b": nrm(ks[22], (DEPTH, 2 * D_FF), 0.02),
        "ffn_w_down": nrm(ks[23], (DEPTH, D_FF, D_MODEL), D_FF ** -0.5),
        "final_norm_w": gain(ks[24], (D_MODEL,)),
    }

def first_block(x, c, positions, ada_w, ada_b, norm_mix_w, w_in, q_norm_w, kv_norm_w,
              w_uq, w_ukv, mlstm_conv_w, mlstm_conv_b, mlstm_gate_b, mlstm_head_norm_w,
              w_br_mla, w_br_mlstm, w_out, norm_ffn_w, ffn_w_up, ffn_conv_w, ffn_conv_b,
              ffn_w_down, final_norm_w):
    c_act = jax.nn.silu(c)
    for l in range(DEPTH):
        mod = (c_act @ ada_w[l] + ada_b[l])[:, None, :]
        sh1, sc1, g1, sh2, sc2, g2 = jnp.split(mod, 6, axis=-1)
        h = _rmsnorm(x, norm_mix_w[l]) * (1 + sc1) + sh1
        x = x + g1 * _mixer(h, positions, w_in[l], q_norm_w[l], kv_norm_w[l], w_uq[l], w_ukv[l],
                            mlstm_conv_w[l], mlstm_conv_b[l], mlstm_gate_b[l],
                            mlstm_head_norm_w[l], w_br_mla[l], w_br_mlstm[l], w_out[l])
        h = _rmsnorm(x, norm_ffn_w[l]) * (1 + sc2) + sh2
        x = x + g2 * _conv_ffn(h, ffn_w_up[l], ffn_conv_w[l], ffn_conv_b[l], ffn_w_down[l])
    return _rmsnorm(x, final_norm_w)


DEPTH_2 = 1

GRID_W = 64
CTX_LEN = 256
HEAD_DIM = D_MODEL // 16
A_HEADS = 4
B_HEADS = 4
C_HEADS = 8
A_WIDTH = A_HEADS * HEAD_DIM
B_WIDTH = B_HEADS * HEAD_DIM
C_WIDTH = C_HEADS * HEAD_DIM
MIX_WIDTH = A_WIDTH + B_WIDTH + C_WIDTH
HGRN_CHUNK = 16
HGRN_F_FLOOR = 1e-20
RWKV_W_RANK = 64
RWKV_A_RANK = 64
RWKV_G_RANK = 128
RWKV_LN_EPS = 64e-5
NA_WIN_ROWS = 8
NA_WIN_COLS = 16
NA_COL_BLOCK = 16
NA_KEY_COLS = NA_COL_BLOCK + NA_WIN_COLS
N_GROUPS = 4
EXPERTS_PER_GROUP = 8
TOP_K_IN_GROUP = 2
D_EXPERT = 512
EPS = 1e-6
NEG_INF = -1e30
A_PROJ = 5 * A_WIDTH
B_PROJ = 3 * B_WIDTH + 2 * RWKV_W_RANK + 2 * RWKV_A_RANK + RWKV_G_RANK
C_PROJ = 3 * C_WIDTH
P_TOTAL = A_PROJ + B_PROJ + C_PROJ
RWKV_SPLITS = (B_WIDTH, 2 * B_WIDTH, 3 * B_WIDTH, 3 * B_WIDTH + RWKV_W_RANK, 3 * B_WIDTH + 2 * RWKV_W_RANK,
               3 * B_WIDTH + 2 * RWKV_W_RANK + RWKV_A_RANK, 3 * B_WIDTH + 2 * RWKV_W_RANK + 2 * RWKV_A_RANK)


def rms_norm(x, gain):
    xf = x.astype(jnp.float32)
    return xf * lax.rsqrt(jnp.mean(xf * xf, axis=-1, keepdims=True) + EPS) * gain.astype(jnp.float32)

def to_heads(t, n_heads):
    b, t_len, _ = t.shape
    return t.reshape(b, t_len, n_heads, HEAD_DIM).transpose(0, 2, 1, 3)

def chunk_gla(q, k, v, log_f, s0):
    b, h, t_len, _ = q.shape
    n = t_len // HGRN_CHUNK

    def blocks(u):
        return u.reshape(b, h, n, HGRN_CHUNK, u.shape[-1])

    q, k, v, log_f = blocks(q), blocks(k), blocks(v), blocks(log_f)
    cum = jnp.cumsum(log_f, axis=3)
    tri = jnp.tril(jnp.ones((HGRN_CHUNK, HGRN_CHUNK), dtype=bool))[:, :, None]
    diff = cum[:, :, :, :, None, :] - cum[:, :, :, None, :, :]
    decay = jnp.where(tri, jnp.exp(jnp.where(tri, diff, 0.0)), 0.0)
    scores = jnp.einsum('bhntd,bhnsd,bhntsd->bhnts', q, k, decay)
    o_intra = jnp.einsum('bhnts,bhnsv->bhntv', scores, v)
    q_in = q * jnp.exp(cum)
    k_out = k * jnp.exp(cum[:, :, :, -1:, :] - cum)
    kv = jnp.einsum('bhnsd,bhnsv->bhndv', k_out, v)
    chunk_decay = jnp.exp(cum[:, :, :, -1, :])

    def step(s, inp):
        q_c, dec_c, kv_c = inp
        o_c = jnp.einsum('bhtd,bhdv->bhtv', q_c, s)
        return s * dec_c[..., None] + kv_c, o_c

    s_fin, o_inter = lax.scan(step, s0, (jnp.moveaxis(q_in, 2, 0), jnp.moveaxis(chunk_decay, 2, 0),
                                         jnp.moveaxis(kv, 2, 0)))
    o = o_intra + jnp.moveaxis(o_inter, 0, 2)
    return o.reshape(b, h, t_len, v.shape[-1]), s_fin

def hgrn2_forget(f_pre, lb):
    f = lb + (1.0 - lb) * jax.nn.sigmoid(f_pre)
    log_f = jnp.log(jnp.maximum(f, HGRN_F_FLOOR))
    k = (1.0 - lb) * jax.nn.sigmoid(-f_pre)
    return to_heads(log_f, A_HEADS), to_heads(k, A_HEADS)

def hgrn2_mixer(p_ctx, p_lat, lb_fwd, lb_bwd, gn_gain):
    qc, ffc, fbc, ic, gc = jnp.split(p_ctx, 5, axis=-1)
    ql, ffl, fbl, il, gl = jnp.split(p_lat, 5, axis=-1)
    qc, ic, ql, il = (to_heads(t, A_HEADS) for t in (qc, ic, ql, il))
    s0 = jnp.zeros((p_lat.shape[0], A_HEADS, HEAD_DIM, HEAD_DIM), jnp.float32)

    def flip(t):
        return t[:, :, ::-1]

    lf, kf = hgrn2_forget(ffc, lb_fwd)
    oc_f, s_f = chunk_gla(qc, kf, ic, lf, s0)
    lf, kf = hgrn2_forget(ffl, lb_fwd)
    ol_f, _ = chunk_gla(ql, kf, il, lf, s_f)
    lbk, kb = hgrn2_forget(fbc, lb_bwd)
    oc_b, s_b = chunk_gla(flip(qc), flip(kb), flip(ic), flip(lbk), s0)
    lbk, kb = hgrn2_forget(fbl, lb_bwd)
    ol_b, _ = chunk_gla(flip(ql), flip(kb), flip(il), flip(lbk), s_b)

    def readout(o, g):
        o = rms_norm(o.transpose(0, 2, 1, 3), gn_gain)
        return o.reshape(g.shape) * jax.nn.silu(g)

    return readout(ol_f + flip(ol_b), gl), readout(oc_f + flip(oc_b), gc)

def centred_shift(u):
    pad = jnp.pad(u, ((0, 0), (1, 1), (0, 0)))
    return 0.5 * (pad[:, :-2] + pad[:, 2:])

def rwkv7_scan(r, w, k, v, kk, ak, s0):
    def step(s, inp):
        r_t, w_t, k_t, v_t, kk_t, ak_t = inp
        sa = jnp.einsum('bhvk,bhk->bhv', s, kk_t)
        s = s * w_t[:, :, None, :] - sa[..., None] * ak_t[:, :, None, :] + v_t[..., None] * k_t[:, :, None, :]
        return s, jnp.einsum('bhvk,bhk->bhv', s, r_t)

    xs = tuple(jnp.moveaxis(u, 1, 0) for u in (r, w, k, v, kk, ak))
    s_fin, ys = lax.scan(step, s0, xs)
    return jnp.moveaxis(ys, 0, 1), s_fin

def rwkv7_mixer(p_ctx, p_lat, mu, w0, w_up, a0, a_up, g_up, kk_scale, k_a, r_k, ln_gain, ln_bias):
    def hd(t):
        return t.reshape(t.shape[0], t.shape[1], B_HEADS, HEAD_DIM)

    def prep(p):
        p = p + (centred_shift(p) - p) * mu
        r, k, v, wdf, wdb, adf, adb, gd = jnp.split(p, list(RWKV_SPLITS), axis=-1)
        kk = hd(k * kk_scale)
        kk = kk / jnp.maximum(jnp.sqrt(jnp.sum(kk * kk, axis=-1, keepdims=True)), 1e-12)
        dirs = []
        for d, (wd, ad) in enumerate(((wdf, adf), (wdb, adb))):
            w = -jax.nn.softplus(-(w0[d] + jnp.tanh(wd) @ w_up[d])) - 0.5
            decay = jnp.exp(-jnp.exp(w))
            a = jax.nn.sigmoid(a0[d] + ad @ a_up[d])
            k_d = k * (1.0 + (a - 1.0) * k_a)
            dirs.append((hd(decay), hd(k_d), hd(a) * kk))
        g = jax.nn.sigmoid(gd) @ g_up
        return hd(r), hd(v), kk, dirs, g

    rc, vc, kkc, dc, gc = prep(p_ctx)
    rl, vl, kkl, dl, gl = prep(p_lat)
    s0 = jnp.zeros((p_lat.shape[0], B_HEADS, HEAD_DIM, HEAD_DIM), jnp.float32)

    def flip(t):
        return t[:, ::-1]

    (wcf, kcf, akcf), (wcb, kcb, akcb) = dc
    (wlf, klf, aklf), (wlb, klb, aklb) = dl
    yc_f, s_f = rwkv7_scan(rc, wcf, kcf, vc, kkc, akcf, s0)
    yl_f, _ = rwkv7_scan(rl, wlf, klf, vl, kkl, aklf, s_f)
    yc_b, s_b = rwkv7_scan(flip(rc), flip(wcb), flip(kcb), flip(vc), flip(kkc), flip(akcb), s0)
    yl_b, _ = rwkv7_scan(flip(rl), flip(wlb), flip(klb), flip(vl), flip(kkl), flip(aklb), s_b)

    def readout(y, r, v, k_f, k_b, g):
        mean = jnp.mean(y, axis=-1, keepdims=True)
        var = jnp.mean(jnp.square(y - mean), axis=-1, keepdims=True)
        y = ((y - mean) * lax.rsqrt(var + RWKV_LN_EPS)).reshape(g.shape) * ln_gain + ln_bias
        bonus = (jnp.sum(r * (k_f + k_b) * r_k, axis=-1, keepdims=True) * v).reshape(g.shape)
        return (y + bonus) * g

    out_lat = readout(yl_f + flip(yl_b), rl, vl, klf, klb, gl)
    out_ctx = readout(yc_f + flip(yc_b), rc, vc, kcf, kcb, gc)
    return out_lat, out_ctx

def axial_rope(t, pos_r, pos_c):
    quarter = HEAD_DIM // 4
    inv = ROPE_THETA ** (-jnp.arange(quarter, dtype=jnp.float32) / quarter)
    ang = jnp.concatenate([pos_r[:, None] * inv, pos_c[:, None] * inv], axis=-1)
    cos = jnp.cos(ang)[None, :, None, :]
    sin = jnp.sin(ang)[None, :, None, :]
    t1, t2 = jnp.split(t, 2, axis=-1)
    return jnp.concatenate([t1 * cos - t2 * sin, t2 * cos + t1 * sin], axis=-1)

def neighbourhood_attention(p_ctx, p_lat, q_gain, k_gain, rpb, pos_r, pos_c, need_ctx):
    bsz, t_lat, _ = p_lat.shape
    n_ctx = p_ctx.shape[1]
    rows = t_lat // GRID_W
    win_r = min(NA_WIN_ROWS, rows)
    scale = HEAD_DIM ** -0.5

    def qkv(p):
        q, k, v = jnp.split(p, 3, axis=-1)
        hd = lambda t: t.reshape(t.shape[0], t.shape[1], C_HEADS, HEAD_DIM)
        return rms_norm(hd(q), q_gain), rms_norm(hd(k), k_gain), hd(v)

    qc, kc, vc = qkv(p_ctx)
    ql, kl, vl = qkv(p_lat)
    ql, kl = axial_rope(ql, pos_r, pos_c), axial_rope(kl, pos_r, pos_c)
    kc_h, vc_h = kc.transpose(0, 2, 1, 3), vc.transpose(0, 2, 1, 3)

    def grid(t):
        return t.transpose(0, 2, 1, 3).reshape(bsz, C_HEADS, rows, GRID_W, HEAD_DIM)

    qg, kg, vg = grid(ql), grid(kl), grid(vl)
    n_cb = GRID_W // NA_COL_BLOCK
    q_col = jnp.arange(GRID_W).reshape(n_cb, NA_COL_BLOCK)
    k_start = jnp.clip(jnp.arange(n_cb) * NA_COL_BLOCK - NA_WIN_COLS // 2, 0, GRID_W - NA_KEY_COLS)
    k_col = k_start[:, None] + jnp.arange(NA_KEY_COLS)
    w_start = jnp.clip(q_col - NA_WIN_COLS // 2, 0, GRID_W - NA_WIN_COLS)
    kc3 = k_col[:, None, :]
    in_win = (kc3 >= w_start[..., None]) & (kc3 < w_start[..., None] + NA_WIN_COLS)
    col_idx = jnp.clip(kc3 - q_col[..., None] + NA_WIN_COLS - 1, 0, 2 * NA_WIN_COLS - 2)
    n_win = win_r * NA_KEY_COLS

    def one_row(r):
        r_start = jnp.clip(r - win_r // 2, 0, rows - win_r)
        k_blk = lax.dynamic_slice_in_dim(kg, r_start, win_r, axis=2)[:, :, :, k_col]
        v_blk = lax.dynamic_slice_in_dim(vg, r_start, win_r, axis=2)[:, :, :, k_col]
        q_row = lax.dynamic_index_in_dim(qg, r, axis=2, keepdims=False).reshape(
            bsz, C_HEADS, n_cb, NA_COL_BLOCK, HEAD_DIM)
        s_win = jnp.einsum('bhjqd,bhrjkd->bhjqrk', q_row, k_blk) * scale
        row_idx = r_start + jnp.arange(win_r) - r + NA_WIN_ROWS - 1
        bias = rpb[:, row_idx[None, None, :, None], col_idx[:, :, None, :]]
        s_win = jnp.where(in_win[:, :, None, :], s_win + bias, NEG_INF)
        s_ctx = jnp.einsum('bhjqd,bhld->bhjql', q_row, kc_h) * scale
        s_all = jnp.concatenate([s_win.reshape(s_win.shape[:4] + (n_win,)), s_ctx], axis=-1)
        prob = jax.nn.softmax(s_all, axis=-1)
        p_win = prob[..., :n_win].reshape(s_win.shape)
        p_ctx = prob[..., n_win:]
        o = (jnp.einsum('bhjqrk,bhrjkd->bhjqd', p_win, v_blk)
             + jnp.einsum('bhjql,bhld->bhjqd', p_ctx, vc_h))
        return o.reshape(bsz, C_HEADS, GRID_W, HEAD_DIM)

    o = lax.map(one_row, jnp.arange(rows))
    out_lat = o.transpose(1, 0, 3, 2, 4).reshape(bsz, t_lat, C_WIDTH)
    out_ctx = None
    if need_ctx:
        qc_h = qc.transpose(0, 2, 1, 3)
        pc = jax.nn.softmax(jnp.einsum('bhqd,bhkd->bhqk', qc_h, kc_h) * scale, axis=-1)
        out_ctx = jnp.einsum('bhqk,bhkd->bhqd', pc, vc_h).transpose(0, 2, 1, 3).reshape(bsz, n_ctx, C_WIDTH)
    return out_lat, out_ctx

def hierarchical_moe(h, w_rg, b_rg, w_re, b_re, w_gate, w_up, w_down):
    g_logits = h @ w_rg + b_rg
    g_prob = jax.nn.softmax(g_logits, axis=-1)
    g_sel = jnp.argmax(g_logits, axis=-1)
    g_w = jnp.take_along_axis(g_prob, g_sel[:, None], axis=-1)
    e_logits = (h @ w_re + b_re).reshape(-1, N_GROUPS, EXPERTS_PER_GROUP)
    e_logits = jnp.take_along_axis(e_logits, g_sel[:, None, None], axis=1)[:, 0]
    e_prob = jax.nn.softmax(e_logits, axis=-1)
    top_w, top_i = lax.top_k(e_prob, TOP_K_IN_GROUP)
    top_w = top_w / jnp.sum(top_w, axis=-1, keepdims=True) * g_w
    e_w = jnp.sum(jax.nn.one_hot(top_i, EXPERTS_PER_GROUP, dtype=jnp.float32) * top_w[..., None], axis=1)
    comb = jax.nn.one_hot(g_sel, N_GROUPS, dtype=jnp.float32)[:, :, None] * e_w[:, None, :]
    y = jnp.zeros(h.shape, jnp.float32)
    for gi in range(N_GROUPS):
        hid = jax.nn.silu(jnp.einsum('nd,edf->nef', h, w_gate[gi])) * jnp.einsum('nd,edf->nef', h, w_up[gi])
        y = y + jnp.einsum('nef,efd->nd', hid * comb[:, gi, :, None], w_down[gi])
    return y

def second_inputs(seed: int = 0) -> dict:
    key = jax.random.key(seed)
    ks = iter(jax.random.split(key, 40))
    D, G, E, F = D_MODEL, N_GROUPS, EXPERTS_PER_GROUP, D_EXPERT

    def nrm(shape, s):
        return s * jax.random.normal(next(ks), shape, jnp.float32)

    return {
        'x': nrm((BATCH, SEQ, D), 1.0),
        'c': nrm((BATCH, D), 1.0),
        'ctx': nrm((BATCH, CTX_LEN, D), 1.0),
        'c_ctx': nrm((D,), 1.0),
        'norm1_gain': 1.0 + nrm((DEPTH_2, D), 0.02),
        'norm2_gain': 1.0 + nrm((DEPTH_2, D), 0.02),
        'w_ada': nrm((DEPTH_2, D, 6 * D), 0.5 * D ** -0.5),
        'b_ada': nrm((DEPTH_2, 6 * D), 0.02),
        'w_in': nrm((DEPTH_2, D, P_TOTAL), D ** -0.5),
        'w_out': nrm((DEPTH_2, MIX_WIDTH, D), MIX_WIDTH ** -0.5),
        'hgrn_lb_logits': nrm((2, DEPTH_2, A_WIDTH), 0.5),
        'hgrn_gn_gain': 1.0 + nrm((DEPTH_2, A_HEADS, HEAD_DIM), 0.02),
        'rwkv_mu': jax.random.uniform(next(ks), (DEPTH_2, B_PROJ), jnp.float32, 0.0, 1.0),
        'rwkv_w0': -1.5 + nrm((DEPTH_2, 2, B_WIDTH), 0.5),
        'rwkv_w_up': nrm((DEPTH_2, 2, RWKV_W_RANK, B_WIDTH), RWKV_W_RANK ** -0.5),
        'rwkv_a0': nrm((DEPTH_2, 2, B_WIDTH), 0.1),
        'rwkv_a_up': nrm((DEPTH_2, 2, RWKV_A_RANK, B_WIDTH), RWKV_A_RANK ** -0.5),
        'rwkv_g_up': nrm((DEPTH_2, RWKV_G_RANK, B_WIDTH), RWKV_G_RANK ** -0.5),
        'rwkv_kk_scale': 0.85 + nrm((DEPTH_2, B_WIDTH), 0.02),
        'rwkv_k_a': 1.0 + nrm((DEPTH_2, B_WIDTH), 0.02),
        'rwkv_r_k': nrm((DEPTH_2, B_HEADS, HEAD_DIM), 0.1),
        'rwkv_ln_gain': 1.0 + nrm((DEPTH_2, B_WIDTH), 0.02),
        'rwkv_ln_bias': nrm((DEPTH_2, B_WIDTH), 0.02),
        'na_q_gain': 1.0 + nrm((DEPTH_2, HEAD_DIM), 0.02),
        'na_k_gain': 1.0 + nrm((DEPTH_2, HEAD_DIM), 0.02),
        'na_rpb': nrm((DEPTH_2, C_HEADS, 2 * NA_WIN_ROWS - 1, 2 * NA_WIN_COLS - 1), 0.1),
        'w_router_group': nrm((DEPTH_2, D, G), D ** -0.5),
        'b_router_group': nrm((DEPTH_2, G), 0.01),
        'w_router_expert': nrm((DEPTH_2, D, G * E), D ** -0.5),
        'b_router_expert': nrm((DEPTH_2, G * E), 0.01),
        'w_exp_gate': nrm((DEPTH_2, G, E, D, F), D ** -0.5),
        'w_exp_up': nrm((DEPTH_2, G, E, D, F), D ** -0.5),
        'w_exp_down': nrm((DEPTH_2, G, E, F, D), F ** -0.5),
    }

def second_block(x, c, ctx, c_ctx, norm1_gain, norm2_gain, w_ada, b_ada, w_in, w_out,
              hgrn_lb_logits, hgrn_gn_gain, rwkv_mu, rwkv_w0, rwkv_w_up, rwkv_a0, rwkv_a_up,
              rwkv_g_up, rwkv_kk_scale, rwkv_k_a, rwkv_r_k, rwkv_ln_gain, rwkv_ln_bias,
              na_q_gain, na_k_gain, na_rpb, w_router_group, b_router_group,
              w_router_expert, b_router_expert, w_exp_gate, w_exp_up, w_exp_down):
    f32 = jnp.float32
    bsz, t_lat, _ = x.shape
    n_ctx = ctx.shape[1]
    pos = jnp.arange(t_lat)
    pos_r = (pos // GRID_W).astype(f32)
    pos_c = (pos % GRID_W).astype(f32)
    lb_p = jax.nn.softmax(hgrn_lb_logits.astype(f32), axis=1)
    lower_bounds = jnp.cumsum(lb_p, axis=1) - lb_p[:, :1]
    silu_c = jax.nn.silu(c.astype(f32))
    silu_cc = jax.nn.silu(c_ctx.astype(f32))
    xl = x.astype(f32)
    xc = ctx.astype(f32)
    for layer in range(DEPTH_2):
        last = layer == DEPTH_2 - 1
        mod_l = (silu_c @ w_ada[layer] + b_ada[layer])[:, None, :]
        mod_c = (silu_cc @ w_ada[layer] + b_ada[layer])[None, None, :]
        sh1l, sc1l, g1l, sh2l, sc2l, g2l = jnp.split(mod_l, 6, axis=-1)
        sh1c, sc1c, g1c, sh2c, sc2c, g2c = jnp.split(mod_c, 6, axis=-1)
        hl = rms_norm(xl, norm1_gain[layer]) * (1.0 + sc1l) + sh1l
        hc = rms_norm(xc, norm1_gain[layer]) * (1.0 + sc1c) + sh1c
        pl = hl @ w_in[layer]
        pc = hc @ w_in[layer]
        al, bl, cl = jnp.split(pl, [A_PROJ, A_PROJ + B_PROJ], axis=-1)
        ac, bc, cc = jnp.split(pc, [A_PROJ, A_PROJ + B_PROJ], axis=-1)
        a_lat, a_ctx = hgrn2_mixer(ac, al, lower_bounds[0, layer], lower_bounds[1, layer], hgrn_gn_gain[layer])
        b_lat, b_ctx = rwkv7_mixer(bc, bl, rwkv_mu[layer], rwkv_w0[layer], rwkv_w_up[layer], rwkv_a0[layer],
                                   rwkv_a_up[layer], rwkv_g_up[layer], rwkv_kk_scale[layer], rwkv_k_a[layer],
                                   rwkv_r_k[layer], rwkv_ln_gain[layer], rwkv_ln_bias[layer])
        c_lat, c_ctxo = neighbourhood_attention(cc, cl, na_q_gain[layer], na_k_gain[layer], na_rpb[layer],
                                                pos_r, pos_c, not last)
        xl = xl + g1l * (jnp.concatenate([a_lat, b_lat, c_lat], axis=-1) @ w_out[layer])
        h2l = (rms_norm(xl, norm2_gain[layer]) * (1.0 + sc2l) + sh2l).reshape(-1, D_MODEL)
        moe_w = (w_router_group[layer], b_router_group[layer], w_router_expert[layer], b_router_expert[layer],
                 w_exp_gate[layer], w_exp_up[layer], w_exp_down[layer])
        if last:
            xl = xl + g2l * hierarchical_moe(h2l, *moe_w).reshape(xl.shape)
        else:
            xc = xc + g1c * (jnp.concatenate([a_ctx, b_ctx, c_ctxo], axis=-1) @ w_out[layer])
            h2c = (rms_norm(xc, norm2_gain[layer]) * (1.0 + sc2c) + sh2c).reshape(-1, D_MODEL)
            y = hierarchical_moe(jnp.concatenate([h2c, h2l], axis=0), *moe_w)
            xc = xc + g2c * y[:bsz * n_ctx].reshape(xc.shape)
            xl = xl + g2l * y[bsz * n_ctx:].reshape(xl.shape)
    return xl.astype(x.dtype)


def setup_inputs(seed=0):
    out = dict(first_inputs(seed))
    for name, value in second_inputs(seed + 1).items():
        if name != "x":
            out[name + "_2"] = value
    return out


def reference(
    x, c, positions, ada_w, ada_b, norm_mix_w, w_in, q_norm_w, kv_norm_w, w_uq, w_ukv,
    mlstm_conv_w, mlstm_conv_b, mlstm_gate_b, mlstm_head_norm_w, w_br_mla, w_br_mlstm, w_out,
    norm_ffn_w, ffn_w_up, ffn_conv_w, ffn_conv_b, ffn_w_down, final_norm_w, c_2, ctx_2, c_ctx_2,
    norm1_gain_2, norm2_gain_2, w_ada_2, b_ada_2, w_in_2, w_out_2, hgrn_lb_logits_2,
    hgrn_gn_gain_2, rwkv_mu_2, rwkv_w0_2, rwkv_w_up_2, rwkv_a0_2, rwkv_a_up_2, rwkv_g_up_2,
    rwkv_kk_scale_2, rwkv_k_a_2, rwkv_r_k_2, rwkv_ln_gain_2, rwkv_ln_bias_2, na_q_gain_2,
    na_k_gain_2, na_rpb_2, w_router_group_2, b_router_group_2, w_router_expert_2,
    b_router_expert_2, w_exp_gate_2, w_exp_up_2, w_exp_down_2,
):
    x = first_block(
        x, c, positions, ada_w, ada_b, norm_mix_w, w_in, q_norm_w, kv_norm_w, w_uq, w_ukv,
        mlstm_conv_w, mlstm_conv_b, mlstm_gate_b, mlstm_head_norm_w, w_br_mla, w_br_mlstm,
        w_out, norm_ffn_w, ffn_w_up, ffn_conv_w, ffn_conv_b, ffn_w_down, final_norm_w,
    )
    return second_block(
        x, c_2, ctx_2, c_ctx_2, norm1_gain_2, norm2_gain_2, w_ada_2, b_ada_2, w_in_2, w_out_2,
        hgrn_lb_logits_2, hgrn_gn_gain_2, rwkv_mu_2, rwkv_w0_2, rwkv_w_up_2, rwkv_a0_2,
        rwkv_a_up_2, rwkv_g_up_2, rwkv_kk_scale_2, rwkv_k_a_2, rwkv_r_k_2, rwkv_ln_gain_2,
        rwkv_ln_bias_2, na_q_gain_2, na_k_gain_2, na_rpb_2, w_router_group_2, b_router_group_2,
        w_router_expert_2, b_router_expert_2, w_exp_gate_2, w_exp_up_2, w_exp_down_2,
    )


_drawn_inputs = setup_inputs


def setup_inputs(seed=0):
    import zlib

    import numpy as np

    out = dict(_drawn_inputs(seed))
    spreads = {}
    factors = {'norm_mix_w': 7.831,
     'q_norm_w': 8.0,
     'kv_norm_w': 8.0,
     'mlstm_conv_b': 23.409,
     'mlstm_head_norm_w': 8.0,
     'norm_ffn_w': 5.479,
     'ffn_conv_b': 5.765,
     'norm1_gain_2': 8.0,
     'norm2_gain_2': 40.008,
     'b_ada_2': 3.024,
     'hgrn_gn_gain_2': 64.0,
     'rwkv_w_up_2': 28.832,
     'rwkv_a0_2': 8.0,
     'rwkv_kk_scale_2': 200.0,
     'rwkv_k_a_2': 8.0,
     'rwkv_ln_gain_2': 200.0,
     'rwkv_ln_bias_2': 200.0,
     'na_q_gain_2': 64.0,
     'na_k_gain_2': 64.0,
     'na_rpb_2': 200.0,
     'b_router_group_2': 64.0,
     'b_router_expert_2': 64.0,
     'ctx_2': 4.313,
     'c_ctx_2': 6.004,
     'rwkv_w0_2': 8.0}
    for name, (base, spread) in spreads.items():
        noise = np.random.default_rng([zlib.crc32(name.encode()), seed]).standard_normal(out[name].shape)
        drawn = base * np.exp(spread * noise) if base else spread * noise
        out[name] = jnp.asarray(drawn.astype(out[name].dtype))
    for name, factor in factors.items():
        out[name] = (out[name] * factor).astype(out[name].dtype)
    return out
```

```python
from contextlib import ExitStack, contextmanager

import numpy as np

import concourse.bass as bass
from concourse import mybir

F32 = mybir.dt.float32
I32 = mybir.dt.int32
ALU = mybir.AluOpType
ACT = mybir.ActivationFunctionType
AX_X = mybir.AxisListType.X

P = 128
DM = 1024
KD = DM // P
SEQ = 256
TT = SEQ // P
DEPTH = 2
EPS = 1e-6
MASKED = -1e30

Q_LORA, KV_LORA, ROPE = 384, 256, 32
NOPE, VH = 64, 64
HEADS = 8
QK = NOPE + ROPE
ML_W = 512
LATENT = Q_LORA + KV_LORA + ROPE
ML_AT = LATENT
GATE_AT = ML_AT + 4 * ML_W
BR_AT = GATE_AT + 2 * HEADS
D_FF = 2816
FF_TILES = D_FF // P

GRID_W = 64
A_HEADS = B_HEADS = 4
HD = 64
A_W = A_HEADS * HD
B_AT = 5 * A_W
B_PROJ = 3 * A_W + 4 * 64 + 128
B_TILES = B_PROJ // P
C_AT = B_AT + B_PROJ
C_HEADS = 8
C_W = C_HEADS * HD
GROUPS, PER_GROUP = 4, 8
EXPERTS = GROUPS * PER_GROUP
D_EXP = 512
RW_CHUNK = 64
NTOK = 2 * SEQ
NT4 = NTOK // P

L_COLS = dict(c=8, ada_b=48, norm_mix=8, q_norm=3, kv_norm=2, conv_w=32, conv_b=8, head_norm=4,
              norm_ffn=8, ffn_conv_w=3 * 2 * FF_TILES, ffn_conv_b=2 * FF_TILES, gate_b=2)
S_COLS = dict(c=16, ada_b=48, norm1=8, norm2=8, lb=4, out_gain=8, mu=B_TILES, w0=4, a0=4,
              kk_scale=2, k_a=2, r_k=2)
R_COLS = dict(final=DM, ln_gain=A_W, ln_bias=A_W, q_gain=HD, k_gain=HD, b_rg=GROUPS, b_re=EXPERTS)
LEVELS = (1, 2, 4, 8, 16, 32, 64)
C_COLS = dict(ident=P, head_ones=P, head_pick=2, inv_freq=ROPE // 2, sel=HEADS * P, ml_mask=2 * P,
              mla_mask=2 * SEQ, na_cos=2 * 32, na_sin=2 * 32, chunk_start=NTOK)
M_COLS = dict(ident=P, lv=len(LEVELS) * P, strict=P, incl=P)


def offsets(cols):
    out, at = {}, 0
    for name, n in cols.items():
        out[name] = (at, at + n)
        at += n
    return out, at


class Order:

    def __init__(self, eng, sem):
        self.eng, self.sem, self.n = eng, sem, 0

    def __call__(self, ins):
        self.n += 1
        ins.then_inc(self.sem, 1)
        self.eng.wait_ge(self.sem, self.n)


class Core:

    def __init__(self, nc, ctx):
        self.nc, self.ctx = nc, ctx
        self.spent, self.number, self.tensors = [], 0, 0
        self.ps = ctx.enter_context(nc.psum_tensor("ps", [P, 8, 512], F32))

    def sb(self, mem, name, shape, dt=F32):
        self.tensors += 1
        return mem.enter_context(self.nc.sbuf_tensor(f"{name}_{self.tensors}", shape, dt))

    def clear_spent(self):
        for s in self.spent:
            self.nc.gpsimd.sem_clear(s)

    @contextmanager
    def stage(self, *names):
        before = self.spent
        self.clear_spent()
        self.number += 1
        sems = [self.nc.alloc_semaphore(f"{n}_{self.number}") for n in names]
        with self.nc.Block(no_gpsimd_drain=True) as block:
            yield (block, *sems)
        self.nc.extend_free_semaphores([s.num for s in before])
        self.spent = sems

    def settle(self):
        with self.stage():
            pass


def products(core, what, n, multiply, evacuate, on_scalar=None, banks=8):
    nc = core.nc
    on_scalar = on_scalar or (lambda i: False)
    by_scalar = [on_scalar(i) for i in range(n)]
    with core.stage(f"{what}_multiplied", f"{what}_read_v", f"{what}_read_s", f"{what}_order_v",
                    f"{what}_order_s") as (block, multiplied, read_v, read_s, order_v, order_s):
        def bank(i):
            return core.ps[:, i % banks, :]

        @block.tensor
        def _(pe):
            for i in range(n):
                if i >= banks:
                    j = i - banks
                    if by_scalar[j]:
                        pe.wait_ge(read_s, sum(by_scalar[:j + 1]))
                    else:
                        pe.wait_ge(read_v, j + 1 - sum(by_scalar[:j + 1]))
                multiply(i, bank(i)).then_inc(multiplied, 1)

        @block.vector
        def _(dve):
            order = Order(dve, order_v)
            for i in range(n):
                if not by_scalar[i]:
                    dve.wait_ge(multiplied, i + 1)
                    evacuate(i, bank(i), nc.vector, order).then_inc(read_v, 1)

        @block.scalar
        def _(act):
            order = Order(act, order_s)
            for i in range(n):
                if by_scalar[i]:
                    act.wait_ge(multiplied, i + 1)
                    evacuate(i, bank(i), nc.scalar, order).then_inc(read_s, 1)


def odd(i):
    return i % 2 == 1


def copy(nc, eng, out, in_, scale=None, bias=None):
    if eng is nc.scalar:
        return eng.activation(out, in_, ACT.Identity if bias is not None else ACT.Copy,
                              bias=0.0 if bias is None else bias, scale=1.0 if scale is None else scale)
    if scale is None:
        return eng.tensor_copy(out, in_)
    if bias is None:
        return eng.tensor_scalar(out, in_, scale, None, ALU.mult)
    return eng.tensor_scalar(out, in_, scale, bias, ALU.mult, ALU.add)


SLOT = KD * 512
RING = 6
STREAM = 4


def linear(core, what, ring, xT, w, chunks, evacuate, on_scalar=None, banks=8):
    nc = core.nc
    kt = w.shape[0] // P
    wv = w.rearrange("(k p) n -> p k n", p=P)
    slots = STREAM
    units = []
    for j, (c0, width, tiles) in enumerate(chunks):
        units += [(j, t) for t in (range(width // P) if tiles is None else tiles)]
    last_unit = [max(i for i, u in enumerate(units) if u[0] == j) for j in range(len(chunks))]
    by_scalar = [bool(on_scalar and on_scalar(i)) for i in range(len(units))]

    def slot(j):
        at = (j % slots) * SLOT
        return ring[:, at:at + kt * chunks[j][1]].rearrange("p (k n) -> p k n", k=kt)

    def bank(i):
        return core.ps[:, i % banks, :]

    with core.stage(f"{what}_multiplied", f"{what}_read_v", f"{what}_read_s", f"{what}_order_v",
                    f"{what}_order_s", *[f"{what}_landed{s}" for s in range(slots)]) as (
            block, multiplied, read_v, read_s, order_v, order_s, *landed):

        @block.sync
        def _(sp):
            for j, (c0, width, _) in enumerate(chunks):
                if j >= slots:
                    sp.wait_ge(multiplied, last_unit[j - slots] + 1)
                sp.dma_start(slot(j), wv[:, :, c0:c0 + width]).then_inc(landed[j % slots], 16)

        @block.tensor
        def _(pe):
            for i, (j, t) in enumerate(units):
                if i == 0 or units[i - 1][0] != j:
                    pe.wait_ge(landed[j % slots], 16 * (j // slots + 1))
                if i >= banks:
                    r = i - banks
                    if by_scalar[r]:
                        pe.wait_ge(read_s, sum(by_scalar[:r + 1]))
                    else:
                        pe.wait_ge(read_v, r + 1 - sum(by_scalar[:r + 1]))
                _, width, tiles = chunks[j]
                for k in range(kt):
                    if tiles is None:
                        mm = nc.tensor.matmul(bank(i)[:, 0:xT.shape[2]], slot(j)[:, k, t * P:(t + 1) * P],
                                              xT[:, k, :], start=(k == 0), stop=(k == kt - 1))
                    else:
                        mm = nc.tensor.matmul(bank(i)[:, 0:width], xT[:, k, t * P:(t + 1) * P],
                                              slot(j)[:, k, :], start=(k == 0), stop=(k == kt - 1))
                mm.then_inc(multiplied, 1)

        @block.vector
        def _(dve):
            order = Order(dve, order_v)
            for i, (j, t) in enumerate(units):
                if not by_scalar[i]:
                    dve.wait_ge(multiplied, i + 1)
                    evacuate(j, t, bank(i), nc.vector, order).then_inc(read_v, 1)

        @block.scalar
        def _(act):
            order = Order(act, order_s)
            for i, (j, t) in enumerate(units):
                if by_scalar[i]:
                    act.wait_ge(multiplied, i + 1)
                    evacuate(j, t, bank(i), nc.scalar, order).then_inc(read_s, 1)


def load(core, what, pairs):
    with core.stage(f"{what}_landed") as (block, landed):
        @block.sync
        def _(sp):
            for dst, src in pairs:
                sp.dma_start(dst, src).then_inc(landed, 16)
            sp.wait_ge(landed, 16 * len(pairs))


def inverse_rms(core, what, parts, out, junk, width, eps=EPS):
    nc = core.nc
    n = len(parts)
    with core.stage(f"{what}_squared", f"{what}_meaned", f"{what}_rooted", f"{what}_done") as (
            block, squared, meaned, rooted, done):
        @block.scalar
        def _(act):
            order = Order(act, squared)
            for i, part in enumerate(parts):
                order(nc.scalar.activation(junk[:, 0:width], part, ACT.Square, accum_out=out[:, i:i + 1]))
            act.wait_ge(meaned, 1)
            nc.scalar.activation(out[:, 0:n], out[:, 0:n], ACT.Sqrt).then_inc(rooted, 1)

        @block.vector
        def _(dve):
            dve.wait_ge(squared, n)
            nc.vector.tensor_scalar(out[:, 0:n], out[:, 0:n], 1.0 / width, eps, ALU.mult, ALU.add)\
                .then_inc(meaned, 1)
            dve.wait_ge(rooted, 1)
            nc.vector.reciprocal(out[:, 0:n], out[:, 0:n]).then_inc(done, 1)


def head_inverse_rms(core, what, x, sq, out, tiles, heads, eps=EPS):
    nc = core.nc
    flat = out.rearrange("p t h -> p (t h)")
    with core.stage(f"{what}_order", f"{what}_meaned", f"{what}_rooted") as (block, own, meaned, rooted):
        @block.vector
        def _(dve):
            order = Order(dve, own)
            for t in range(tiles):
                order(nc.vector.tensor_tensor(sq[:, t], x[:, t], x[:, t], ALU.mult))
                order(nc.vector.tensor_reduce(out[:, t, :], sq[:, t], AX_X, ALU.add))
            nc.vector.tensor_scalar(flat, flat, 1.0 / HD, eps, ALU.mult, ALU.add).then_inc(meaned, 1)
            dve.wait_ge(rooted, 1)
            order(nc.vector.reciprocal(flat, flat))

        @block.scalar
        def _(act):
            act.wait_ge(meaned, 1)
            nc.scalar.activation(flat, flat, ACT.Sqrt).then_inc(rooted, 1)


def norm_transposed(core, what, ident, x, hT, at, gain, shift, mem_junk):
    nc = core.nc
    rstd, xn = mem_junk
    inverse_rms(core, f"{what}_rms", [x[:, t, :] for t in range(TT)], rstd, xn[:, 0, :], DM)
    with core.stage(f"{what}_scaled") as (block, scaled):
        @block.vector
        def _(dve):
            nc.vector.tensor_scalar(xn[:, 0, :], x[:, 0, :], rstd[:, 0:1], None, ALU.mult).then_inc(scaled, 1)

        @block.scalar
        def _(act):
            nc.scalar.activation(xn[:, 1, :], x[:, 1, :], ACT.Copy, scale=rstd[:, 1:2]).then_inc(scaled, 1)

    def turn(i, bank):
        for t in range(TT):
            ins = nc.tensor.transpose(bank[:, t * P:(t + 1) * P], xn[:, t, i * P:(i + 1) * P], ident)
        return ins

    def out(i, bank, eng, order):
        return copy(nc, eng, hT[:, i, at:at + SEQ], bank[:, 0:SEQ], gain[:, i:i + 1], shift[:, i:i + 1])

    products(core, f"{what}_turn", KD, turn, out, odd)


def modulation(core, what, ring, w, cT, vectors, bias, mod):
    nc = core.nc
    n_chunks = 6 * DM // 512
    wv = w.rearrange("(k p) n -> p k n", p=P)

    def slot(j):
        return ring[:, (j % RING) * SLOT:(j % RING + 1) * SLOT].rearrange("p (k n) -> p k n", k=KD)

    with core.stage(f"{what}_silu", f"{what}_multiplied", f"{what}_added",
                    *[f"{what}_landed{s}" for s in range(RING)]) as (block, silu, multiplied, added, *landed):
        @block.scalar
        def _(act):
            nc.scalar.activation(cT, cT, ACT.Silu).then_inc(silu, 1)

        @block.sync
        def _(sp):
            for j in range(n_chunks):
                if j >= RING:
                    sp.wait_ge(multiplied, j - RING + 1)
                sp.dma_start(slot(j), wv[:, :, j * 512:(j + 1) * 512]).then_inc(landed[j % RING], 16)

        @block.tensor
        def _(pe):
            pe.wait_ge(silu, 1)
            for j in range(n_chunks):
                pe.wait_ge(landed[j % RING], 16 * (j // RING + 1))
                for m in range(4):
                    col = (4 * j + m) * vectors
                    for k in range(KD):
                        mm = nc.tensor.matmul(core.ps[:, 0, col:col + vectors], slot(j)[:, k, m * P:(m + 1) * P],
                                              cT[:, :, k], start=(k == 0), stop=(k == KD - 1))
                mm.then_inc(multiplied, 1)

        @block.vector
        def _(dve):
            dve.wait_ge(multiplied, n_chunks)
            nc.vector.tensor_tensor(mod, core.ps[:, 0, 0:48 * vectors].rearrange("p (m v) -> p m v", v=vectors),
                                    bias.unsqueeze(2).to_broadcast([P, 48, vectors]), ALU.add).then_inc(added, 1)


def spread_rows(core, what, ident, ones, cols, diag, out):
    nc = core.nc
    with core.stage(f"{what}_diag") as (block, made):
        @block.vector
        def _(dve):
            nc.vector.tensor_tensor(diag, ident.unsqueeze(1).to_broadcast([P, KD, P]),
                                    cols.unsqueeze(2).to_broadcast([P, KD, P]), ALU.mult).then_inc(made, 1)

    def mult(i, bank):
        for k in range(4):
            mm = nc.tensor.matmul(bank[:, k * P:(k + 1) * P], ones, diag[:, 4 * i + k, :], start=True, stop=True)
        return mm

    def out_(i, bank, eng, order):
        return copy(nc, eng, out[:, i * 512:(i + 1) * 512], bank)

    products(core, f"{what}_spread", 2, mult, out_, odd)


def gains(core, what, mod, v, norm, out, at_scale):
    nc = core.nc
    with core.stage(f"{what}_made") as (block, made):
        @block.vector
        def _(dve):
            nc.vector.scalar_tensor_tensor(out=out, in0=mod[:, at_scale:at_scale + KD, v], scalar=1.0, in1=norm,
                                           op0=ALU.add, op1=ALU.mult).then_inc(made, 1)


def attention(core, what, mem, ident, heads, keys, d, qT, kT, scale, mask, masked_keys, value, out, scratch):
    nc = core.nc
    n = heads * TT
    kt = keys // P
    s, pT = (a.rearrange("p (n k) -> p n k", n=n) for a in scratch)
    top = core.sb(mem, f"{what}_top", [P, n])
    total = core.sb(mem, f"{what}_total", [P, n])

    def score(i, bank):
        t, h = divmod(i, heads)
        return nc.tensor.matmul(bank[:, 0:keys], qT(h, t), kT(h), start=True, stop=True)

    def masked(i, bank, eng, order):
        t, h = divmod(i, heads)
        ins = nc.vector.scalar_tensor_tensor(out=s[:, i, 0:masked_keys], in0=bank[:, 0:masked_keys], scalar=scale,
                                             in1=mask(h, t), op0=ALU.mult, op1=ALU.add)
        if masked_keys < keys:
            order(ins)
            ins = nc.vector.tensor_scalar(s[:, i, masked_keys:keys], bank[:, masked_keys:keys], scale, None, ALU.mult)
        return ins

    products(core, f"{what}_score", n, score, masked)

    with core.stage(f"{what}_topped", f"{what}_exped", f"{what}_summed") as (block, topped, exped, summed):
        @block.vector
        def _(dve):
            for i in range(n):
                nc.vector.tensor_reduce(top[:, i:i + 1], s[:, i, :], AX_X, ALU.max, negate=True).then_inc(topped, 1)
            dve.wait_ge(exped, n)
            nc.vector.reciprocal(total[:, :], total[:, :]).then_inc(summed, 1)

        @block.scalar
        def _(act):
            for i in range(n):
                act.wait_ge(topped, i + 1)
                nc.scalar.activation(s[:, i, :], s[:, i, :], ACT.Exp, bias=top[:, i:i + 1],
                                     accum_out=total[:, i:i + 1]).then_inc(exped, 1)

    def turn(i, bank):
        for k in range(kt):
            ins = nc.tensor.transpose(bank[:, k * P:(k + 1) * P], s[:, i, k * P:(k + 1) * P], ident)
        return ins

    def turned(i, bank, eng, order):
        return copy(nc, eng, pT[:, i, :], bank[:, 0:keys])

    products(core, f"{what}_turn", n, turn, turned, odd)

    def weigh(i, bank):
        for h in range(heads):
            for k in range(kt):
                mm = nc.tensor.matmul(bank[:, h * HD:(h + 1) * HD], pT[:, i * heads + h, k * P:(k + 1) * P],
                                      value(h, k), start=(k == 0), stop=(k == kt - 1))
        return mm

    def normed(i, bank, eng, order):
        return nc.vector.tensor_tensor(out(i), bank.rearrange("p (h d) -> p h d", d=HD),
                                       total[:, i * heads:(i + 1) * heads].unsqueeze(2)
                                       .to_broadcast([P, heads, HD]), ALU.mult)

    products(core, f"{what}_weigh", TT, weigh, normed)


def turn_features(core, what, ident, src, tiles, yT, scale=None):
    nc = core.nc

    def turn(i, bank):
        for t in range(TT):
            ins = nc.tensor.transpose(bank[:, t * P:(t + 1) * P], src[:, t, i * P:(i + 1) * P], ident)
        return ins

    def out(i, bank, eng, order):
        return copy(nc, eng, yT[:, i, :], bank[:, 0:SEQ], None if scale is None else scale[:, i:i + 1])

    products(core, what, tiles, turn, out, odd)


def rotary_tables(core, mem, pos, inv, cos, sin):
    nc = core.nc
    n = ROPE // 2
    posf = core.sb(mem, "posf", [P, TT])
    ang = core.sb(mem, "ang", [P, TT, n])
    turns = core.sb(mem, "turns", [P, TT, n])
    over = core.sb(mem, "over", [P, TT, n])
    two_pi = 2 * np.pi
    c1 = 6.28125
    c2 = float(np.float32(np.round((two_pi - c1) * 2 ** 21) / 2 ** 21))
    c3 = float(two_pi - c1 - c2)
    pi = 3.1415925
    magic = 12582912.0
    with core.stage("rotary_order", "rotary_reduced", "rotary_done") as (block, own, reduced, done):
        @block.vector
        def _(dve):
            order = Order(dve, own)
            order(nc.vector.tensor_copy(posf[:, :], pos))
            order(nc.vector.tensor_tensor(ang[:, :, :], posf[:, :].unsqueeze(2).to_broadcast([P, TT, n]),
                                          inv.unsqueeze(1).to_broadcast([P, TT, n]), ALU.mult))
            order(nc.vector.tensor_scalar(turns[:, :, :], ang[:, :, :], 1.0 / two_pi, None, ALU.mult))
            order(nc.vector.tensor_scalar(turns[:, :, :], turns[:, :, :], magic, None, ALU.add))
            order(nc.vector.tensor_scalar(turns[:, :, :], turns[:, :, :], magic, None, ALU.subtract))
            for c in (c1, c2, c3):
                order(nc.vector.scalar_tensor_tensor(out=ang[:, :, :], in0=turns[:, :, :], scalar=-c,
                                                     in1=ang[:, :, :], op0=ALU.mult, op1=ALU.add))
            order(nc.vector.tensor_scalar(sin, ang[:, :, :], pi, -pi, ALU.min, ALU.max))
            order(nc.vector.tensor_scalar(ang[:, :, :], ang[:, :, :], np.pi / 2, None, ALU.add))
            order(nc.vector.tensor_scalar(over[:, :, :], ang[:, :, :], np.pi, two_pi, ALU.is_gt, ALU.mult))
            order(nc.vector.tensor_tensor(ang[:, :, :], ang[:, :, :], over[:, :, :], ALU.subtract))
            nc.vector.tensor_scalar(cos, ang[:, :, :], pi, -pi, ALU.min, ALU.max).then_inc(reduced, 1)

        @block.scalar
        def _(act):
            act.wait_ge(reduced, 1)
            nc.scalar.activation(sin, sin, ACT.Sin).then_inc(done, 1)
            nc.scalar.activation(cos, cos, ACT.Sin).then_inc(done, 1)


def rotate(nc, order, x1, x2, cos, sin, tmp):
    a, b, c = tmp
    order(nc.vector.tensor_tensor(a, x2, sin, ALU.mult))
    order(nc.vector.tensor_tensor(b, x1, sin, ALU.mult))
    order(nc.vector.tensor_tensor(c, x1, cos, ALU.mult))
    order(nc.vector.tensor_tensor(x1, c, a, ALU.subtract))
    order(nc.vector.tensor_tensor(c, x2, cos, ALU.mult))
    order(nc.vector.tensor_tensor(x2, c, b, ALU.add))


def mla(core, layer_in, k, lat, yT):
    nc, ident = core.nc, k["ident"]
    with ExitStack() as mem:
        rs = core.sb(mem, "lat_rs", [P, 4])
        latT = core.sb(mem, "latT", [P, 5, SEQ])
        q_space = core.sb(mem, "q", [P, TT * HEADS * QK])
        q = q_space[:, :].rearrange("p (t h d) -> p t h d", t=TT, h=HEADS)
        kk = core.sb(mem, "kk", [P, TT, HEADS, QK])
        v = core.sb(mem, "v", [P, TT, HEADS, VH])
        qkT = core.sb(mem, "qkT", [QK, HEADS, 4 * P])
        tmp = core.sb(mem, "rot", [P, 3, HEADS, ROPE // 2])
        junk = q_space[:, 0:Q_LORA]
        y = q_space[:, 0:TT * HEADS * VH].rearrange("p (t h d) -> p t h d", t=TT, h=HEADS)
        inverse_rms(core, "cq_rms", [lat[:, t, 0:Q_LORA] for t in range(TT)], rs[:, 0:2], junk, Q_LORA)
        inverse_rms(core, "ckv_rms", [lat[:, t, Q_LORA:Q_LORA + KV_LORA] for t in range(TT)], rs[:, 2:4],
                    junk, KV_LORA)
        with core.stage("lat_scaled") as (block, scaled):
            @block.vector
            def _(dve):
                for t in range(TT):
                    for j, (a, b) in enumerate(((0, Q_LORA), (Q_LORA, Q_LORA + KV_LORA))):
                        nc.vector.tensor_scalar(lat[:, t, a:b], lat[:, t, a:b], rs[:, 2 * j + t:2 * j + t + 1],
                                                None, ALU.mult).then_inc(scaled, 1)
        turn_features(core, "lat_turn", ident, lat, 5, latT, k["lat_gain"])

        def q_out(j, t, bank, eng, order):
            return copy(nc, eng, q[:, t, 4 * j:4 * j + 4, :], bank[:, 0:4 * QK].rearrange("p (h d) -> p h d", d=QK))
        linear(core, "uq", core.ring, latT[:, 0:3, :], layer_in("w_uq"),
               [(0, 4 * QK, range(TT)), (4 * QK, 4 * QK, range(TT))], q_out, odd)

        def kv_out(j, t, bank, eng, order):
            kv = bank.rearrange("p (h d) -> p h d", d=NOPE + VH)
            order(copy(nc, eng, kk[:, t, 4 * j:4 * j + 4, 0:NOPE], kv[:, :, 0:NOPE]))
            return copy(nc, eng, v[:, t, 4 * j:4 * j + 4, :], kv[:, :, NOPE:])
        linear(core, "ukv", core.ring, latT[:, 3:5, :], layer_in("w_ukv"),
               [(0, 512, range(TT)), (512, 512, range(TT))], kv_out, odd)

        with core.stage("rope_order") as (block, own):
            @block.vector
            def _(dve):
                order = Order(dve, own)
                half = ROPE // 2
                for t in range(TT):
                    cos = k["cos"][:, t, :].unsqueeze(1).to_broadcast([P, HEADS, half])
                    sin = k["sin"][:, t, :].unsqueeze(1).to_broadcast([P, HEADS, half])
                    rotate(nc, order, q[:, t, :, NOPE:NOPE + half], q[:, t, :, NOPE + half:QK], cos, sin,
                           [tmp[:, i] for i in range(3)])
                    kr = lat[:, t, Q_LORA + KV_LORA:LATENT]
                    rotate(nc, order, kr[:, 0:half], kr[:, half:ROPE], k["cos"][:, t, :], k["sin"][:, t, :],
                           [tmp[:, i, 0] for i in range(3)])
                    order(nc.vector.tensor_copy(kk[:, t, :, NOPE:QK],
                                                kr.unsqueeze(1).to_broadcast([P, HEADS, ROPE])))

        def turn(h, bank):
            for t in range(TT):
                nc.tensor.transpose(bank[0:QK, t * P:(t + 1) * P], q[:, t, h, :], ident)
                ins = nc.tensor.transpose(bank[0:QK, (2 + t) * P:(3 + t) * P], kk[:, t, h, :], ident)
            return ins

        def turned(h, bank, eng, order):
            return copy(nc, eng, qkT[:, h, :], bank[0:QK, :])
        products(core, "qk_turn", HEADS, turn, turned, odd)

        attention(core, "mla", mem, ident, HEADS, SEQ, QK,
                  lambda h, t: qkT[:, h, t * P:(t + 1) * P], lambda h: qkT[:, h, SEQ:2 * SEQ], QK ** -0.5,
                  lambda h, t: k["mla_mask"][:, t * SEQ:(t + 1) * SEQ], SEQ,
                  lambda h, j: v[:, j, h, :], lambda t: y[:, t],
                  [core.ring[:, a * SLOT:(a + 1) * SLOT] for a in (STREAM, STREAM + 1)])
        turn_features(core, "mla_y_turn", ident, y.rearrange("p t h d -> p t (h d)"), 4, yT)


def running(nc, order, x, other, op):
    step = 1
    while step < SEQ:
        order(nc.vector.tensor_copy(other[:, 0:step], x[:, 0:step]))
        order(nc.vector.tensor_tensor(other[:, step:SEQ], x[:, step:SEQ], x[:, 0:SEQ - step], op))
        x, other = other, x
        step *= 2
    return x


def mlstm(core, k, qk, gates, vx, og, yT, fv):
    nc, ident = core.nc, k["ident"]
    with ExitStack() as mem:
        conv = core.sb(mem, "conv", [P, KD, SEQ])
        g = [core.sb(mem, f"gate{i}", [HEADS, SEQ]) for i in range(6)]
        aT = core.sb(mem, "aT", [P, TT, HEADS])
        floor = core.sb(mem, "floor", [P, TT, HEADS])
        wT = core.sb(mem, "wT", [P, 2, 384])
        pT = core.sb(mem, "pT", [P, HEADS, 384])
        hn = core.sb(mem, "hn", [P, TT, HEADS, HD + 1])
        den = core.sb(mem, "den", [P, TT, HEADS])
        h = core.sb(mem, "h", [P, TT, HEADS, HD])
        sq = conv[:, 0:4, :].rearrange("p a b -> p (a b)").rearrange("p (t h d) -> p t h d", t=TT, h=HEADS)
        rs = core.sb(mem, "h_rs", [P, TT, HEADS])
        with core.stage("conv_order", "conv_tile", "conv_silu") as (block, own, tile_done, silu):
            @block.vector
            def _(dve):
                order = Order(dve, own)
                for j in range(KD):
                    w = fv["conv_w"]
                    order(nc.vector.tensor_scalar(conv[:, j, :], qk[:, j, 0:SEQ], w[:, j:j + 1],
                                                  fv["conv_b"][:, j:j + 1], ALU.mult, ALU.add))
                    for i in range(1, 4):
                        ins = nc.vector.scalar_tensor_tensor(out=conv[:, j, :], in0=qk[:, j, i:i + SEQ],
                                                             scalar=w[:, 8 * i + j:8 * i + j + 1],
                                                             in1=conv[:, j, :], op0=ALU.mult, op1=ALU.add)
                        if i < 3:
                            order(ins)
                    ins.then_inc(tile_done, 1)

            @block.scalar
            def _(act):
                for j in range(KD):
                    act.wait_ge(tile_done, j + 1)
                    nc.scalar.activation(conv[:, j, :], conv[:, j, :], ACT.Silu).then_inc(silu, 1)
        i_, f_ = gates
        with core.stage("gate_order", "gate_abs", "gate_ln", "gate_exp") as (block, own, absed, lned, exped):
            @block.vector
            def _(dve):
                order = Order(dve, own)
                order(nc.vector.tensor_scalar(i_[:, :], i_[:, :], fv["gate_b"][0:HEADS, 0:1], None, ALU.add))
                order(nc.vector.tensor_scalar(f_[:, :], f_[:, :], fv["gate_b"][0:HEADS, 1:2], None, ALU.add))
                order(nc.vector.tensor_scalar(g[0][:, :], f_[:, :], -1.0, None, ALU.mult))
                nc.vector.tensor_tensor(g[0][:, :], g[0][:, :], f_[:, :], ALU.min).then_inc(absed, 1)
                dve.wait_ge(lned, 2)
                order(nc.vector.scalar_tensor_tensor(out=g[1][:, :], in0=f_[:, :], scalar=0.0, in1=g[0][:, :],
                                                     op0=ALU.min, op1=ALU.subtract))
                F = running(nc, order, g[1], g[2], ALU.add)
                order(nc.vector.tensor_tensor(g[3][:, :], i_[:, :], F[:, :], ALU.subtract))
                order(nc.vector.tensor_scalar(g[4][:, :], g[3][:, :], 0.0, None, ALU.max))
                M = running(nc, order, g[4], g[5], ALU.max)
                order(nc.vector.tensor_tensor(F[:, :], F[:, :], M[:, :], ALU.add))
                order(nc.vector.tensor_scalar(F[:, :], F[:, :], -1.0, 88.0, ALU.mult, ALU.min))
                order(nc.vector.tensor_scalar(M[:, :], M[:, :], -1.0, None, ALU.mult))
                ins = nc.vector.tensor_copy(g[0][:, :], F[:, :])
                ins.then_inc(absed, 1)

            @block.scalar
            def _(act):
                act.wait_ge(absed, 1)
                nc.scalar.activation(g[0][:, :], g[0][:, :], ACT.Exp).then_inc(lned, 1)
                act.wait_ge(lned, 1)
                nc.scalar.activation(g[0][:, :], g[0][:, :], ACT.Ln, bias=k["ones"][0:HEADS, 0:1]).then_inc(lned, 1)
                act.wait_ge(absed, 2)
                nc.scalar.activation(g[0][:, :], g[0][:, :], ACT.Exp).then_inc(exped, 1)
        a, minus_m = g[3], g[4]

        def turn(i, bank):
            src = (a, g[0])[i]
            for t in range(TT):
                ins = nc.tensor.transpose(bank[:, t * HEADS:(t + 1) * HEADS], src[:, t * P:(t + 1) * P],
                                          ident[0:HEADS, 0:HEADS])
            return ins

        def turned(i, bank, eng, order):
            return copy(nc, eng, (aT, floor)[i][:, :, :], bank[:, 0:2 * HEADS].rearrange("p (t h) -> p t h", t=TT))
        products(core, "gate_turn", 2, turn, turned)

        with core.stage("mw_spread", "mw_masked", "mw_exped", "mw_scored", "mw_weighed") as (
                block, spread, maskd, exped, scored, weighed):
            @block.tensor
            def _(pe):
                for hh in range(HEADS):
                    rows = slice(64 * (hh % 2), 64 * (hh % 2) + 64)
                    if hh >= 2:
                        pe.wait_ge(weighed, hh - 1)
                    nc.tensor.matmul(core.ps[:, hh % 2, 0:SEQ], k["sel"][0:HEADS, hh * P:(hh + 1) * P],
                                     minus_m[:, :], start=True, stop=True).then_inc(spread, 1)
                    q_, k_ = conv[rows, hh // 2, :], conv[rows, 4 + hh // 2, :]
                    nc.tensor.matmul(core.ps[:, 2 + hh % 2, 0:256], k_[:, 0:P], q_, start=True, stop=True)
                    nc.tensor.matmul(core.ps[:, 2 + hh % 2, 256:384], k_[:, P:SEQ], q_[:, P:SEQ],
                                     start=True, stop=True).then_inc(scored, 1)

            @block.vector
            def _(dve):
                def weigh(hh):
                    dve.wait_ge(exped, 2 * hh + 2)
                    dve.wait_ge(scored, hh + 1)
                    nc.vector.scalar_tensor_tensor(out=pT[:, hh, :], in0=core.ps[:, 2 + hh % 2, 0:384],
                                                   scalar=HD ** -0.5, in1=wT[:, hh % 2, :],
                                                   op0=ALU.mult, op1=ALU.mult).then_inc(weighed, 1)
                for hh in range(HEADS):
                    dve.wait_ge(spread, hh + 1)
                    if hh >= 2:
                        dve.wait_ge(weighed, hh - 1)
                    b = core.ps[:, hh % 2, :]
                    nc.vector.tensor_tensor(wT[:, hh % 2, 0:256], b[:, 0:256], k["ml_mask"], ALU.add)\
                        .then_inc(maskd, 1)
                    nc.vector.tensor_tensor(wT[:, hh % 2, 256:384], b[:, P:SEQ], k["ml_mask"][:, 0:P], ALU.add)\
                        .then_inc(maskd, 1)
                    if hh >= 1:
                        weigh(hh - 1)
                weigh(HEADS - 1)

            @block.scalar
            def _(act):
                for hh in range(HEADS):
                    act.wait_ge(maskd, 2 * hh + 2)
                    for t, (c0, c1) in enumerate(((0, 256), (256, 384))):
                        nc.scalar.activation(wT[:, hh % 2, c0:c1], wT[:, hh % 2, c0:c1], ACT.Exp,
                                             bias=aT[:, t, hh:hh + 1]).then_inc(exped, 1)

        def total(i, bank):
            t, half = divmod(i, 2)
            for j in range(4):
                hh = 4 * half + j
                o = bank[:, j * (HD + 1):(j + 1) * (HD + 1)]
                if t == 0:
                    mm = nc.tensor.matmul(o, pT[:, hh, 0:P], vx[:, 0, hh, :], start=True, stop=True)
                else:
                    nc.tensor.matmul(o, pT[:, hh, P:2 * P], vx[:, 0, hh, :], start=True, stop=False)
                    mm = nc.tensor.matmul(o, pT[:, hh, 2 * P:3 * P], vx[:, 1, hh, :], start=False, stop=True)
            return mm

        def totalled(i, bank, eng, order):
            t, half = divmod(i, 2)
            return copy(nc, eng, hn[:, t, 4 * half:4 * half + 4, :],
                        bank[:, 0:4 * (HD + 1)].rearrange("p (h d) -> p h d", d=HD + 1))
        products(core, "ml_total", 4, total, totalled, odd)

        with core.stage("hdiv_order", "og_done") as (block, own, og_done):
            @block.vector
            def _(dve):
                order = Order(dve, own)
                order(nc.vector.tensor_scalar(den[:, :, :], hn[:, :, :, HD], -1.0, None, ALU.mult))
                order(nc.vector.tensor_tensor(den[:, :, :], den[:, :, :], hn[:, :, :, HD], ALU.max))
                order(nc.vector.tensor_tensor(den[:, :, :], den[:, :, :], floor[:, :, :], ALU.max))
                order(nc.vector.reciprocal(den[:, :, :], den[:, :, :]))
                for t in range(TT):
                    order(nc.vector.tensor_tensor(h[:, t], hn[:, t, :, 0:HD],
                                                  den[:, t, :].unsqueeze(2).to_broadcast([P, HEADS, HD]), ALU.mult))

            @block.scalar
            def _(act):
                nc.scalar.activation(og, og, ACT.Sigmoid).then_inc(og_done, 1)
        head_inverse_rms(core, "h_rms", h, sq, rs[:, :, :], TT, HEADS)
        with core.stage("hnorm_order") as (block, own):
            @block.vector
            def _(dve):
                order = Order(dve, own)
                for t in range(TT):
                    order(nc.vector.tensor_tensor(h[:, t], h[:, t],
                                                  rs[:, t, :].unsqueeze(2).to_broadcast([P, HEADS, HD]), ALU.mult))
                    order(nc.vector.tensor_tensor(h[:, t], h[:, t],
                                                  og[:, t, :].rearrange("p (h d) -> p h d", d=HD), ALU.mult))
        turn_features(core, "ml_y_turn", ident, h[:, :, :, :].rearrange("p t h d -> p t (h d)"), 4, yT,
                      fv["head_norm"])


def mixer(core, layer_in, k, fv, hT, g_row, x):
    nc = core.nc
    with ExitStack() as mem:
        og = core.sb(mem, "og", [P, TT, ML_W])
        yT = [core.sb(mem, f"yT{i}", [P, 4, SEQ]) for i in range(2)]
        with ExitStack() as inner:
            lat = core.sb(inner, "lat", [P, TT, LATENT])
            qk = core.sb(inner, "qk", [P, KD, SEQ + 3])
            vx = core.sb(inner, "vx", [P, TT, HEADS, HD + 1])
            gi, gf = (core.sb(inner, n, [HEADS, SEQ]) for n in ("gi", "gf"))
            wg = core.sb(inner, "wg", [P, KD, 2 * HEADS])
            with core.stage("pad_set", "gate_w") as (block, pad_set, gate_w):
                @block.gpsimd
                def _(pool):
                    nc.gpsimd.memset(qk[:, :, 0:3], 0.0).then_inc(pad_set, 1)
                    nc.gpsimd.memset(vx[:, :, :, HD:HD + 1], 1.0).then_inc(pad_set, 1)
                    pool.wait_ge(pad_set, 2)

                @block.sync
                def _(sp):
                    sp.dma_start(wg[:, :, :], layer_in("w_in").rearrange("(k p) n -> p k n", p=P)[
                        :, :, GATE_AT:BR_AT]).then_inc(gate_w, 16)
                    sp.wait_ge(gate_w, 16)
            both = range(TT)
            spans = [(0, 512, both), (512, LATENT - 512, both), (ML_AT, 512, None), (ML_AT + 512, 512, None),
                     (ML_AT + 1024, 512, both), (ML_AT + 1536, 512, both)]

            def out(j, t, bank, eng, order):
                c0, width, _ = spans[j]
                if j < 2:
                    return copy(nc, eng, lat[:, t, c0:c0 + width], bank[:, 0:width])
                if j < 4:
                    return copy(nc, eng, qk[:, 4 * (j - 2) + t, 3:], bank[:, 0:SEQ])
                if j == 4:
                    return copy(nc, eng, vx[:, t, :, 0:HD], bank.rearrange("p (h d) -> p h d", d=HD))
                return copy(nc, eng, og[:, t, :], bank)
            linear(core, "proj", core.ring, hT, layer_in("w_in"), spans, out, odd)

            def gate(i, bank):
                for kt in range(KD):
                    mm = nc.tensor.matmul(bank[0:HEADS, 0:SEQ], wg[:, kt, i * HEADS:(i + 1) * HEADS], hT[:, kt, :],
                                          start=(kt == 0), stop=(kt == KD - 1))
                return mm

            def gated(i, bank, eng, order):
                return copy(nc, eng, (gi, gf)[i][:, :], bank[0:HEADS, 0:SEQ])
            products(core, "gates", 2, gate, gated)
            mla(core, layer_in, k, lat, yT[0])
            mlstm(core, k, qk, (gi, gf), vx, og[:, :, :], yT[1], fv)
        with ExitStack() as inner:
            m = core.sb(inner, "merged", [P, TT, DM])
            tmp = core.sb(inner, "merge_tmp", [P, TT, 512])
            mT = core.sb(inner, "mergedT", [P, KD, SEQ])
            br = core.sb(inner, "br", [P, TT, 2 * DM])

            def gate_out(j, t, bank, eng, order):
                return nc.scalar.activation(br[:, t, j * 512:(j + 1) * 512], bank, ACT.Sigmoid)
            linear(core, "branch_gates", core.ring, hT, layer_in("w_in"),
                   [(BR_AT + 512 * j, 512, both) for j in range(4)], gate_out, lambda i: True)
            for b, name in enumerate(("w_br_mla", "w_br_mlstm")):
                def out(j, t, bank, eng, order, b=b):
                    dst = m[:, t, j * 512:(j + 1) * 512]
                    gate = br[:, t, b * DM + j * 512:b * DM + (j + 1) * 512]
                    if b == 0:
                        return nc.vector.tensor_tensor(dst, bank, gate, ALU.mult)
                    order(nc.vector.tensor_tensor(tmp[:, t, :], bank, gate, ALU.mult))
                    return nc.vector.tensor_tensor(dst, dst, tmp[:, t, :], ALU.add)
                linear(core, f"branch{b}", core.ring, yT[b], layer_in(name),
                       [(0, 512, both), (512, 512, both)], out)
            turn_features(core, "merge_turn", k["ident"], m, KD, mT)
            residual(core, "w_out", mT, layer_in("w_out"), g_row, tmp, x)


def residual(core, what, yT, w, g_row, tmp, x):
    nc = core.nc

    def out(j, t, bank, eng, order):
        dst = x[:, t, j * 512:(j + 1) * 512]
        order(nc.vector.tensor_tensor(tmp[:, t, :], bank, g_row[:, j * 512:(j + 1) * 512], ALU.mult))
        return nc.vector.tensor_tensor(dst, dst, tmp[:, t, :], ALU.add)
    linear(core, what, core.ring, yT, w, [(0, 512, range(TT)), (512, 512, range(TT))], out)


def ffn(core, layer_in, k, fv, hT, g_row, x):
    nc = core.nc
    pairs = 2
    n_chunks = FF_TILES // pairs
    w = layer_in("ffn_w_up").rearrange("(k p) n -> p k n", p=P)
    with ExitStack() as mem:
        hid = core.sb(mem, "hid", [P, FF_TILES, SEQ])
        with ExitStack() as inner:
            u = core.sb(inner, "u", [P, 4, 2 + SEQ])
            cv = core.sb(inner, "cv", [P, 4, SEQ])
            slots = 3
            width = 2 * pairs * P

            def slot(j):
                at = (j % slots) * KD * width
                return core.ring[:, at:at + KD * width].rearrange("p (k n) -> p k n", k=KD)

            with core.stage("up_pad", "up_multiplied", "up_copied", "up_conv", "up_gelu", "up_order", "up_hid",
                            *[f"up_landed{s}" for s in range(slots)]) as (
                    block, padded, multiplied, copied, convolved, gelued, own, hid_done, *landed):
                @block.sync
                def _(sp):
                    for j in range(n_chunks):
                        if j >= slots:
                            sp.wait_ge(multiplied, 2 * pairs * (j - slots + 1))
                        for s in range(2):
                            c0 = s * D_FF + j * pairs * P
                            sp.dma_start(slot(j)[:, :, s * pairs * P:(s + 1) * pairs * P], w[:, :, c0:c0 + pairs * P])\
                                .then_inc(landed[j % slots], 16)

                @block.gpsimd
                def _(pool):
                    nc.gpsimd.memset(u[:, :, 0:2], 0.0).then_inc(padded, 1)

                @block.tensor
                def _(pe):
                    for n in range(2 * FF_TILES):
                        tile, side = divmod(n, 2)
                        j, i = divmod(tile, pairs)
                        if n % (2 * pairs) == 0:
                            pe.wait_ge(landed[j % slots], 32 * (j // slots + 1))
                        if n >= 8:
                            pe.wait_ge(copied, n - 7)
                        col = side * pairs * P + i * P
                        for kt in range(KD):
                            mm = nc.tensor.matmul(core.ps[:, n % 8, 0:SEQ], slot(j)[:, kt, col:col + P], hT[:, kt, :],
                                                  start=(kt == 0), stop=(kt == KD - 1))
                        mm.then_inc(multiplied, 1)

                @block.scalar
                def _(act):
                    act.wait_ge(padded, 1)

                    def gelu(tile):
                        act.wait_ge(convolved, 2 * tile + 1)
                        nc.scalar.activation(cv[:, (2 * tile) % 4, :], cv[:, (2 * tile) % 4, :],
                                             ACT.Gelu_apprx_tanh).then_inc(gelued, 1)
                    for n in range(2 * FF_TILES):
                        act.wait_ge(multiplied, n + 1)
                        if n >= 4:
                            act.wait_ge(convolved, n - 3)
                        nc.scalar.activation(u[:, n % 4, 2:], core.ps[:, n % 8, 0:SEQ], ACT.Copy).then_inc(copied, 1)
                        if n % 2 and n >= 3:
                            gelu(n // 2 - 1)
                    gelu(FF_TILES - 1)

                @block.vector
                def _(dve):
                    order = Order(dve, own)

                    def product(tile):
                        dve.wait_ge(gelued, tile + 1)
                        nc.vector.tensor_tensor(hid[:, tile, :], cv[:, (2 * tile) % 4, :], cv[:, (2 * tile + 1) % 4, :],
                                                ALU.mult).then_inc(hid_done, 1)
                    for n in range(2 * FF_TILES):
                        tile, side = divmod(n, 2)
                        f = side * FF_TILES + tile
                        cw, cb = fv["ffn_conv_w"], fv["ffn_conv_b"]
                        dve.wait_ge(copied, n + 1)
                        if n >= 4:
                            dve.wait_ge(hid_done, (n - 4) // 2 + 1)
                        order(nc.vector.tensor_scalar(cv[:, n % 4, :], u[:, n % 4, 0:SEQ], cw[:, f:f + 1],
                                                      cb[:, f:f + 1], ALU.mult, ALU.add))
                        for i in (1, 2):
                            col = i * 2 * FF_TILES + f
                            ins = nc.vector.scalar_tensor_tensor(out=cv[:, n % 4, :], in0=u[:, n % 4, i:i + SEQ],
                                                                 scalar=cw[:, col:col + 1], in1=cv[:, n % 4, :],
                                                                 op0=ALU.mult, op1=ALU.add)
                            if i == 1:
                                order(ins)
                        ins.then_inc(convolved, 1)
                        if side == 1:
                            dve.wait_ge(convolved, n + 1)
                            if tile >= 1:
                                product(tile - 1)
                    product(FF_TILES - 1)
        with ExitStack() as inner:
            tmp = core.sb(inner, "down_tmp", [P, 512])
            half = DM // 2
            wd = layer_in("ffn_w_down").rearrange("(k p) n -> p k n", p=P)
            kts = 8
            parts = [(c, k0, min(kts, FF_TILES - k0)) for c in range(2) for k0 in range(0, FF_TILES, kts)]

            def slot(n):
                at = (n % 6) * kts * half
                return core.ring[:, at:at + parts[n][2] * half].rearrange("p (k n) -> p k n", n=half)

            with core.stage("down_multiplied", "down_order", *[f"down_landed{n}" for n in range(6)]) as (
                    block, multiplied, own, *landed):
                @block.sync
                def _(sp):
                    for n, (c, k0, kn) in enumerate(parts):
                        sp.dma_start(slot(n), wd[:, k0:k0 + kn, c * half:(c + 1) * half]).then_inc(landed[n], 16)

                @block.tensor
                def _(pe):
                    for n, (c, k0, kn) in enumerate(parts):
                        pe.wait_ge(landed[n], 16)
                        for t in range(TT):
                            for i in range(kn):
                                mm = nc.tensor.matmul(core.ps[:, 2 * c + t, :], hid[:, k0 + i, t * P:(t + 1) * P],
                                                      slot(n)[:, i, :], start=(k0 + i == 0),
                                                      stop=(k0 + i == FF_TILES - 1))
                            if k0 + kn == FF_TILES:
                                mm.then_inc(multiplied, 1)

                @block.vector
                def _(dve):
                    order = Order(dve, own)
                    for n in range(4):
                        c, t = divmod(n, 2)
                        dst = x[:, t, c * half:(c + 1) * half]
                        dve.wait_ge(multiplied, n + 1)
                        order(nc.vector.tensor_tensor(tmp[:, :], core.ps[:, n, :],
                                                      g_row[:, c * half:(c + 1) * half], ALU.mult))
                        order(nc.vector.tensor_tensor(dst, dst, tmp[:, :], ALU.add))


def first_block(core, I, k, x):
    nc = core.nc
    L_OFF, n_cols = offsets(L_COLS)
    with ExitStack() as mem:
        fvt = core.sb(mem, "layer_vectors", [P, n_cols])
        fv = {n: fvt[:, a:b] for n, (a, b) in L_OFF.items()}
        core.settle()
        with nc.Fori(0, DEPTH, 1) as layer:
            def layer_in(name):
                return I[name][layer]
            load(core, "layer_vectors", [(fvt[:, :], I["layer_vectors"][layer])])
            mod = core.sb(mem, "mod", [P, 48, 1])
            gain = core.sb(mem, "gain", [P, KD])
            g_row = core.sb(mem, "g_row", [P, DM])
            hT = core.sb(mem, "hT", [P, KD, SEQ])
            kk = dict(k, lat_gain=fvt[:, L_OFF["q_norm"][0]:L_OFF["kv_norm"][1]])
            modulation(core, "ada", core.ring, layer_in("ada_w"), fv["c"].unsqueeze(1), 1, fv["ada_b"],
                       mod[:, :, :])
            for part in range(2):
                with ExitStack() as inner:
                    rstd = core.sb(inner, "rstd", [P, TT])
                    xn = core.sb(inner, "xn", [P, TT, DM])
                    gains(core, f"gain{part}", mod, 0, fv[("norm_mix", "norm_ffn")[part]], gain[:, :],
                          (3 * part + 1) * KD)
                    norm_transposed(core, f"norm{part}", k["ident"], x, hT, 0, gain,
                                    mod[:, 3 * part * KD:(3 * part + 1) * KD, 0], (rstd, xn))
                    spread_rows(core, f"gate{part}", k["ident"], k["ones"],
                                mod[:, (3 * part + 2) * KD:(3 * part + 3) * KD, 0],
                                xn[:, 0, :].rearrange("p (k f) -> p k f", k=KD), g_row)
                (mixer, ffn)[part](core, layer_in, kk, fv, hT[:, :, :], g_row, x)
            core.settle()
        with ExitStack() as inner:
            rstd = core.sb(inner, "rstd", [P, TT])
            junk = core.sb(inner, "junk", [P, DM])
            inverse_rms(core, "final_rms", [x[:, t, :] for t in range(TT)], rstd, junk, DM)
            with core.stage("final") as (block, own):
                @block.vector
                def _(dve):
                    for t in range(TT):
                        nc.vector.scalar_tensor_tensor(out=x[:, t, :], in0=x[:, t, :], scalar=rstd[:, t:t + 1],
                                                       in1=k["final"], op0=ALU.mult, op1=ALU.mult).then_inc(own, 1)


class Carver:

    def __init__(self, space, at=0):
        self.space, self.at = space, at

    def __call__(self, *shape):
        n = int(np.prod(shape))
        assert self.at + n <= self.space.shape[1], (self.at, shape)
        part = self.space[:, self.at:self.at + n]
        self.at += n
        names = "abcde"[:len(shape)]
        if len(shape) == 1:
            return part
        return part.rearrange(f"p ({' '.join(names)}) -> p {' '.join(names)}", **dict(zip(names[1:], shape[1:])))


LAT = slice(SEQ, NTOK)


def flat(a):
    names = "abcde"[:len(a.shape) - 1]
    return a.rearrange(f"p {' '.join(names)} -> p ({' '.join(names)})")


def rows_of(head):
    return slice(HD * (head % 2), HD * (head % 2) + HD)


def hgrn(core, I, k, fv, masks, hT, ycat):
    nc, ident = core.nc, k["ident"]
    with ExitStack() as mem:
        f = core.sb(mem, "hg_f", [P, 6, NTOK])
        v = core.sb(mem, "hg_v", [P, NT4, A_W])
        g = core.sb(mem, "hg_g", [P, TT, A_W])
        lb = core.sb(mem, "hg_lb", [P, 4, 4])
        spans = [(0, 512, None), (512, 256, None), (3 * A_W, A_W, range(NT4)), (4 * A_W, A_W, (2, 3))]

        def out(j, t, bank, eng, order):
            if j < 2:
                return copy(nc, eng, f[:, 4 * j + t, :], bank)
            if j == 2:
                return copy(nc, eng, v[:, t, :], bank[:, 0:A_W])
            return copy(nc, eng, g[:, t - 2, :], bank[:, 0:A_W])
        linear(core, "hg_proj", core.ring, hT, I["w_in_2"], spans, out, odd)
        carve = Carver(core.ring)
        inc, exc, kd = (carve(2, 2, NTOK) for _ in range(3))
        sg, sn = (carve(2, 2, NTOK) for _ in range(2))
        qs, ks = (carve(2, 2, SEQ) for _ in range(2))
        near = carve(TT, 2, 2, P)
        cross = carve(2, 2, 2, P)
        far = carve(TT, 2, 2, SEQ)
        tmp = carve(TT, 2, 2, P)
        sq = carve(TT, A_HEADS, HD)
        o = carve(TT, A_HEADS, HD)
        rs = carve(TT, A_HEADS)

        with core.stage("lb_order", "lb_exp") as (block, own, exped):
            @block.vector
            def _(dve):
                order = Order(dve, own)
                order(nc.vector.tensor_tensor(lb[:, 0, :], fv["lb"], fv["lb"], ALU.subtract))
                dve.wait_ge(exped, 1)
                order(nc.vector.reciprocal(lb[:, 2, :], lb[:, 1, :]))
                order(nc.vector.tensor_tensor(lb[:, 1, :], lb[:, 1, :], lb[:, 2, :], ALU.mult))
                order(nc.vector.tensor_tensor(lb[:, 0, :], lb[:, 1, :], lb[:, 1, :], ALU.subtract))
                order(nc.vector.tensor_scalar(lb[:, 3, :], lb[:, 0, :], -1.0, 1.0, ALU.mult, ALU.add))

            @block.scalar
            def _(act):
                act.wait_ge(own, 1)
                nc.scalar.activation(lb[:, 1, :], lb[:, 0, :], ACT.Exp).then_inc(exped, 1)

        with core.stage("fg_order", "fg_sigmoid", "fg_bounded", "fg_order_s", "fg_logged", "fg_silu") as (
                block, own, sigmoid, bounded, own_s, logged, silu):
            @block.scalar
            def _(act):
                order = Order(act, own_s)
                for d in range(2):
                    nc.scalar.activation(sg[:, d], f[:, 2 + 2 * d:4 + 2 * d, :], ACT.Sigmoid).then_inc(sigmoid, 1)
                    nc.scalar.activation(sn[:, d], f[:, 2 + 2 * d:4 + 2 * d, :], ACT.Sigmoid, scale=-1.0)\
                        .then_inc(sigmoid, 1)
                nc.scalar.activation(g[:, :, :], g[:, :, :], ACT.Silu).then_inc(silu, 1)
                act.wait_ge(bounded, 4)
                order(nc.scalar.activation(flat(sg), flat(sg), ACT.Sqrt))
                nc.scalar.activation(flat(inc), flat(sg), ACT.Ln).then_inc(logged, 1)

            @block.vector
            def _(dve):
                order = Order(dve, own)
                for d in range(2):
                    dve.wait_ge(sigmoid, 2 * d + 2)
                    for i in range(2):
                        c = 2 * d + i
                        order(nc.vector.tensor_scalar(kd[:, d, i], sn[:, d, i], lb[:, 3, c:c + 1], None, ALU.mult))
                        order(nc.vector.tensor_scalar(sg[:, d, i], sg[:, d, i], lb[:, 3, c:c + 1], lb[:, 0, c:c + 1],
                                                      ALU.mult, ALU.add))
                        nc.vector.tensor_scalar(sg[:, d, i], sg[:, d, i], 1e-20, None, ALU.max).then_inc(bounded, 1)
                order(nc.vector.memset(flat(exc), 0.0))
                order(nc.vector.memset(flat(near), 0.0))
                dve.wait_ge(logged, 1)
                order(nc.vector.tensor_scalar(flat(inc), flat(inc), 2.0, None, ALU.mult))

        def decayed(order, dve, exped, n, q_cols, k_cols, b):
            for d in range(2):
                if b:
                    dve.wait_ge(exped, n + 2 * d + 2)
                    order(nc.vector.tensor_tensor(qs[:, d], qs[:, d], f[:, 0:2, q_cols], ALU.mult))
                    ins = nc.vector.tensor_tensor(ks[:, d], ks[:, d], kd[:, d, :, k_cols], ALU.mult)
                else:
                    order(nc.vector.tensor_copy(qs[:, d], f[:, 0:2, q_cols]))
                    ins = nc.vector.tensor_copy(ks[:, d], kd[:, d, :, k_cols])
                yield ins

        def double(order, b):
            for d in range(2):
                a, z, edge = ((0, 1, b - 1), (1, 0, 0))[d]
                i_ = inc[:, d].rearrange("p h t -> p (h t)").rearrange("p (n s b) -> p n s b", s=2, b=b)
                e_ = exc[:, d].rearrange("p h t -> p (h t)").rearrange("p (n s b) -> p n s b", s=2, b=b)
                shape = [P, 2 * NTOK // (2 * b), b]
                order(nc.vector.tensor_tensor(e_[:, :, a, :], e_[:, :, a, :],
                                              i_[:, :, z, edge:edge + 1].to_broadcast(shape), ALU.add))
                order(nc.vector.tensor_tensor(i_[:, :, z, :], i_[:, :, z, :],
                                              i_[:, :, a, edge:edge + 1].to_broadcast(shape), ALU.add))

        for b in (0,) + LEVELS:
            with core.stage(f"hg{b}_exp", f"hg{b}_decayed", f"hg{b}_multiplied", f"hg{b}_order") as (
                    block, exped, decays, multiplied, own):
                @block.scalar
                def _(act):
                    if b:
                        for d in range(2):
                            nc.scalar.activation(qs[:, d], inc[:, d, :, LAT], ACT.Exp).then_inc(exped, 1)
                            nc.scalar.activation(ks[:, d], exc[:, d, :, LAT], ACT.Exp).then_inc(exped, 1)

                @block.tensor
                def _(pe):
                    for d in range(2):
                        pe.wait_ge(decays, d + 1)
                        for t in range(TT):
                            cols = slice(t * P, (t + 1) * P)
                            for par in range(2):
                                for hp in range(2):
                                    r = rows_of(par)
                                    mm = nc.tensor.matmul(core.ps[:, 4 * d + 2 * t + par, hp * P:(hp + 1) * P],
                                                          ks[r, d, hp, cols], qs[r, d, hp, cols],
                                                          start=True, stop=True)
                        mm.then_inc(multiplied, 1)

                @block.vector
                def _(dve):
                    order = Order(dve, own)
                    for ins in decayed(order, dve, exped, 0, LAT, LAT, b):
                        ins.then_inc(decays, 1)
                    if b:
                        dve.wait_ge(exped, 4)
                        double(order, b)
                    for d in range(2):
                        dve.wait_ge(multiplied, d + 1)
                        at = M_OFF["ident"][0] if b == 0 else M_OFF["lv"][0] + LEVELS.index(b) * P
                        mask = masks[:, d, at:at + P]
                        order(nc.vector.tensor_tensor(
                            tmp.rearrange("p a b c t -> p (a b) c t"),
                            core.ps[:, 4 * d:4 * d + 4, 0:2 * P].rearrange("p b (c t) -> p b c t", c=2),
                            mask.unsqueeze(1).unsqueeze(1).to_broadcast([P, 4, 2, P]), ALU.mult))
                        order(nc.vector.tensor_tensor(flat(near), flat(near), flat(tmp), ALU.add))

        with core.stage("hgx_exp", "hgx_decayed", "hgx_multiplied", "hgx_order", "hgx_doubled", "hgx_read") as (
                block, exped, decays, multiplied, own, doubled, read):
            @block.scalar
            def _(act):
                for stage in range(2):
                    if stage:
                        act.wait_ge(doubled, 1)
                        act.wait_ge(multiplied, 1)
                    for d in range(2):
                        nc.scalar.activation(qs[:, d], inc[:, d, :, LAT], ACT.Exp).then_inc(exped, 1)
                        nc.scalar.activation(ks[:, d], exc[:, d, :, (LAT, slice(0, SEQ))[stage]], ACT.Exp)\
                            .then_inc(exped, 1)

            @block.tensor
            def _(pe):
                pe.wait_ge(decays, 2)
                for d in range(2):
                    t, s = (1, 0) if d == 0 else (0, 1)
                    for par in range(2):
                        for hp in range(2):
                            r = rows_of(par)
                            mm = nc.tensor.matmul(core.ps[:, 2 * d + par, hp * P:(hp + 1) * P],
                                                  ks[r, d, hp, s * P:(s + 1) * P], qs[r, d, hp, t * P:(t + 1) * P],
                                                  start=True, stop=True)
                mm.then_inc(multiplied, 1)
                pe.wait_ge(decays, 4)
                for s in range(TT):
                    for par in range(2):
                        for hp in range(2):
                            r = rows_of(par)
                            for d in range(2):
                                mm = nc.tensor.matmul(core.ps[:, 4 + 2 * s + par, hp * SEQ:(hp + 1) * SEQ],
                                                      ks[r, d, hp, s * P:(s + 1) * P], qs[r, d, hp, :],
                                                      start=(d == 0), stop=(d == 1))
                mm.then_inc(multiplied, 1)

            @block.vector
            def _(dve):
                order = Order(dve, own)
                for ins in decayed(order, dve, exped, 0, LAT, LAT, 128):
                    ins.then_inc(decays, 1)
                dve.wait_ge(exped, 4)
                double(order, P)
                nc.vector.tensor_copy(tmp[:, 0, 0, 0, 0:1], tmp[:, 0, 0, 0, 0:1]).then_inc(doubled, 1)
                dve.wait_ge(multiplied, 1)
                order(nc.vector.tensor_copy(cross.rearrange("p a b c t -> p (a b) (c t)"), core.ps[:, 0:4, 0:2 * P]))
                for ins in decayed(order, dve, exped, 4, LAT, slice(0, SEQ), 256):
                    ins.then_inc(decays, 1)
                dve.wait_ge(multiplied, 2)
                nc.vector.tensor_copy(far.rearrange("p a b c t -> p (a b) (c t)"), core.ps[:, 4:8, :]).then_inc(read, 1)

        def weigh(t, bank):
            for h in range(A_HEADS):
                hp, par = divmod(h, 2)
                cols = slice(t * P, (t + 1) * P)
                lefts = [far[:, 0, par, hp, cols], far[:, 1, par, hp, cols], near[:, t, par, hp, :],
                         cross[:, 1 - t, par, hp, :]]
                for j, (left, tile) in enumerate(zip(lefts, (0, 1, 2 + t, 3 - t))):
                    mm = nc.tensor.matmul(bank[:, h * HD:(h + 1) * HD], left, v[:, tile, h * HD:(h + 1) * HD],
                                          start=(j == 0), stop=(j == 3))
            return mm

        def weighed(t, bank, eng, order):
            return copy(nc, eng, o[:, t], bank[:, 0:A_W].rearrange("p (h d) -> p h d", d=HD))
        products(core, "hg_weigh", TT, weigh, weighed, odd)
        head_inverse_rms(core, "hg_rms", o, sq, rs, TT, A_HEADS)
        with core.stage("hg_out") as (block, own):
            @block.vector
            def _(dve):
                order = Order(dve, own)
                for t in range(TT):
                    order(nc.vector.tensor_tensor(o[:, t], o[:, t],
                                                  rs[:, t, :].unsqueeze(2).to_broadcast([P, A_HEADS, HD]), ALU.mult))
                    order(nc.vector.tensor_tensor(ycat[:, t, 0:A_W], o[:, t].rearrange("p h d -> p (h d)"),
                                                  g[:, t, :], ALU.mult))


def rwkv(core, I, k, fv, masks, consts, hT, ycat):
    nc, ident = core.nc, k["ident"]
    with ExitStack() as mem:
        X = core.sb(mem, "rw_x", [P, B_TILES, NTOK])
        up = core.sb(mem, "rw_up", [P, 3 * A_W])
        vt = core.sb(mem, "rw_v", [P, NT4, A_W])
        gt = core.sb(mem, "rw_g", [P, TT, A_W])
        bon = core.sb(mem, "rw_bonus", [P, TT, B_HEADS])
        S = core.sb(mem, "rw_state", [P, 2, 2, HD])
        tot = core.sb(mem, "rw_total", [P, 2, 2, 8])
        y = core.sb(mem, "rw_y", [P, 2, TT, A_W])
        k2t, a2t = (core.sb(mem, n, [P, 2, NT4, A_W]) for n in ("rw_k2t", "rw_a2t"))
        raw = core.ring[:, STREAM * SLOT:STREAM * SLOT + B_TILES * 2 * (SEQ + 2)].rearrange(
            "p (j s n) -> p j s n", j=B_TILES, s=2)
        load(core, "rw_up", [(up[:, :], I["rwkv_up"])])
        with core.stage("rw_pad") as (block, pad):
            @block.vector
            def _(dve):
                nc.vector.memset(raw[:, :, :, 0:1], 0.0).then_inc(pad, 1)
                nc.vector.memset(raw[:, :, :, SEQ + 1:SEQ + 2], 0.0).then_inc(pad, 1)

        def out(j, t, bank, eng, order):
            return copy(nc, eng, raw[:, 4 * j + t, :, 1:SEQ + 1], bank.rearrange("p (s n) -> p s n", s=2))
        linear(core, "rw_proj", core.ring, hT, I["w_in_2"],
               [(B_AT, 512, None), (B_AT + 512, 512, None), (B_AT + 1024, P, None)], out, odd)

        with core.stage("mix_order", "mix_done", "mix_act") as (block, own, mixed, acted):
            @block.vector
            def _(dve):
                order = Order(dve, own)
                for j in (6, 8, 7, 0, 1, 2, 3, 4, 5):
                    xj = X[:, j, :].rearrange("p (s n) -> p s n", s=2)
                    mid = raw[:, j, :, 1:SEQ + 1]
                    order(nc.vector.tensor_tensor(xj, raw[:, j, :, 0:SEQ], raw[:, j, :, 2:SEQ + 2], ALU.add))
                    order(nc.vector.scalar_tensor_tensor(out=xj, in0=xj, scalar=0.5, in1=mid, op0=ALU.mult,
                                                         op1=ALU.subtract))
                    nc.vector.scalar_tensor_tensor(out=xj, in0=xj, scalar=fv["mu"][:, j:j + 1], in1=mid,
                                                   op0=ALU.mult, op1=ALU.add).then_inc(mixed, 1)

            @block.scalar
            def _(act):
                act.wait_ge(mixed, 1)
                nc.scalar.activation(X[:, 6, :], X[:, 6, :], ACT.Tanh).then_inc(acted, 1)
                act.wait_ge(mixed, 2)
                nc.scalar.activation(X[:, 8, :], X[:, 8, :], ACT.Sigmoid).then_inc(acted, 1)

        carve = Carver(core.ring)
        sw, sa = (carve(2, 2, NTOK) for _ in range(2))
        kk, kn = (carve(2, NTOK) for _ in range(2))
        kt, rt, kh, ah, k2, a2 = (carve(2, 2, NTOK) for _ in range(6))
        pi = carve(2, 2, NTOK)
        def low_rank(i, bank):
            which, d, hp = i // 4, (i // 2) % 2, i % 2
            r = rows_of(d)
            return nc.tensor.matmul(bank, up[r, which * A_W + hp * P:which * A_W + (hp + 1) * P],
                                    X[r, 6 + which, :], start=True, stop=True)

        def low_rank_out(i, bank, eng, order):
            which, d, hp = i // 4, (i // 2) % 2, i % 2
            return nc.scalar.activation((sw, sa)[which][:, d, hp], bank, ACT.Sigmoid,
                                        bias=fv[("w0", "a0")[which]][:, 2 * d + hp:2 * d + hp + 1])
        products(core, "rw_low", 8, low_rank, low_rank_out, lambda i: True)

        def gate(t, bank):
            return nc.tensor.matmul(bank[:, 0:A_W], X[:, 8, (2 + t) * P:(3 + t) * P], up[:, 2 * A_W:], start=True,
                                    stop=True)

        def gated(t, bank, eng, order):
            return copy(nc, eng, gt[:, t, :], bank[:, 0:A_W])
        products(core, "rw_gate", TT, gate, gated, odd)

        with core.stage("kk_order") as (block, own):
            @block.vector
            def _(dve):
                order = Order(dve, own)
                for hp in range(2):
                    order(nc.vector.tensor_scalar(kk[:, hp], X[:, 2 + hp, :], fv["kk_scale"][:, hp:hp + 1], None,
                                                  ALU.mult))
                    order(nc.vector.tensor_tensor(kn[:, hp], kk[:, hp], kk[:, hp], ALU.mult))

        def norm(hp, bank):
            return nc.tensor.matmul(bank, consts["head_ones"], kn[:, hp], start=True, stop=True)

        def normed(hp, bank, eng, order):
            return nc.scalar.activation(kn[:, hp], bank, ACT.Sqrt)
        products(core, "kk_norm", 2, norm, normed, lambda i: True)
        with core.stage("prep_order", "prep_ready", "prep_exp") as (block, own, ready, exped):
            @block.vector
            def _(dve):
                order = Order(dve, own)
                order(nc.vector.tensor_scalar(kn, kn, 1e-12, None, ALU.max))
                order(nc.vector.reciprocal(kn, kn))
                order(nc.vector.tensor_tensor(kk, kk, kn, ALU.mult))
                order(nc.vector.tensor_scalar(flat(sw), flat(sw), -float(np.exp(np.float32(-0.5))), None, ALU.mult))
                for d in range(2):
                    for hp in range(2):
                        order(nc.vector.tensor_tensor_scan(pi[:, d, hp], consts["chunk_start"], sw[:, d, hp], 0.0,
                                                           ALU.mult, ALU.add))
                for d in range(2):
                    c = [a[:, d].rearrange("p h t -> p (h t)").rearrange("p (c n) -> p c n", n=RW_CHUNK)
                         for a in (pi, sw, kt, k2, rt)]
                    p_, l_, before, after, here = c
                    last = p_[:, :, RW_CHUNK - 1:RW_CHUNK]
                    if d == 1:
                        before, after = after, before
                    order(nc.vector.tensor_tensor(before, p_, l_, ALU.subtract))
                    order(nc.vector.tensor_tensor(after, last.to_broadcast([P, 16, RW_CHUNK]), p_, ALU.subtract))
                    order(nc.vector.tensor_copy(tot[:, d].rearrange("p h c -> p (h c)"), last.squeeze(2)))
                    if d == 0:
                        ins = nc.vector.tensor_copy(here, p_)
                    else:
                        ins = nc.vector.tensor_tensor(here, after, l_, ALU.add)
                    ins.then_inc(ready, 1)
                for d in range(2):
                    for hp in range(2):
                        order(nc.vector.tensor_tensor(a2[:, d, hp], sa[:, d, hp], kk[:, hp], ALU.mult))
                        order(nc.vector.tensor_scalar(sa[:, d, hp], sa[:, d, hp], 1.0, fv["k_a"][:, hp:hp + 1],
                                                      ALU.subtract, ALU.mult))
                        order(nc.vector.scalar_tensor_tensor(out=sa[:, d, hp], in0=sa[:, d, hp], scalar=1.0,
                                                             in1=X[:, 2 + hp, :], op0=ALU.add, op1=ALU.mult))
                dve.wait_ge(exped, 10)
                for d in range(2):
                    order(nc.vector.tensor_tensor(kh[:, d], ah[:, d], sa[:, d], ALU.mult))
                    order(nc.vector.tensor_tensor(ah[:, d], ah[:, d], a2[:, d], ALU.mult))
                    order(nc.vector.tensor_tensor(kt[:, d], kt[:, d], kk, ALU.mult))
                    order(nc.vector.tensor_tensor(rt[:, d], rt[:, d], X[:, 0:2, :], ALU.mult))
                    order(nc.vector.tensor_tensor(a2[:, d], a2[:, d], k2[:, d], ALU.mult))
                    order(nc.vector.tensor_tensor(k2[:, d], k2[:, d], sa[:, d], ALU.mult))
                order(nc.vector.tensor_tensor(kn[:, :, LAT], sa[:, 0, :, LAT], sa[:, 1, :, LAT], ALU.add))
                order(nc.vector.tensor_tensor(kn[:, :, LAT], kn[:, :, LAT], X[:, 0:2, LAT], ALU.mult))
                for hp in range(2):
                    order(nc.vector.tensor_scalar(kn[:, hp, LAT], kn[:, hp, LAT], fv["r_k"][:, hp:hp + 1], None,
                                                  ALU.mult))
                order(nc.vector.memset(S[:, :, :, :], 0.0))

            @block.scalar
            def _(act):
                for d in range(2):
                    act.wait_ge(ready, d + 1)
                    nc.scalar.activation(ah[:, d], rt[:, d], ACT.Exp, scale=-1.0).then_inc(exped, 1)
                    act.wait_ge(exped, 5 * d + 1)
                    for a in (kt, k2, rt):
                        nc.scalar.activation(a[:, d], a[:, d], ACT.Exp).then_inc(exped, 1)
                    nc.scalar.activation(tot[:, d], tot[:, d], ACT.Exp).then_inc(exped, 1)

        def bonus(t, bank):
            for hp in range(2):
                mm = nc.tensor.matmul(bank[:, 2 * hp:2 * hp + 2], kn[:, hp, (2 + t) * P:(3 + t) * P],
                                      consts["head_pick"], start=True, stop=True)
            return mm

        def bonus_out(t, bank, eng, order):
            return copy(nc, eng, bon[:, t, :], bank[:, 0:B_HEADS])
        products(core, "rw_bonus", TT, bonus, bonus_out, odd)

        sources = [(X[:, 4:6, :], vt), (k2[:, 0], k2t[:, 0]), (a2[:, 0], a2t[:, 0]), (k2[:, 1], k2t[:, 1]),
                   (a2[:, 1], a2t[:, 1])]

        def turn(i, bank):
            src, t = sources[i // NT4][0], i % NT4
            for hp in range(2):
                ins = nc.tensor.transpose(bank[:, hp * P:(hp + 1) * P], src[:, hp, t * P:(t + 1) * P], ident)
            return ins

        def turned(i, bank, eng, order):
            return copy(nc, eng, sources[i // NT4][1][:, i % NT4, :], bank[:, 0:A_W])
        products(core, "rw_turn", 5 * NT4, turn, turned, odd)

        low = Carver(core.ring)
        M1 = low(2, NT4, 4, P)
        N_ = [low(NT4, 4, P)]
        low.at = (8 + 4 + 8) * NTOK
        T_ = low(2, NT4, 4, P)
        Rk, Ra = (low(2, TT, 4, P) for _ in range(2))
        P_ = low(2, NT4, 4, P)
        N_.append(low(NT4, 4, P))
        G = Carver(flat(X[:, :, :]))(2, NT4, 4, P)
        NM = Carver(flat(hT))(2, NT4, 4, P)
        kinds = [(d, t, kind, par) for d in range(2) for t in range(NT4) for kind in range(4) for par in range(2)
                 if kind < 2 or t >= 2]

        def matrix(i, bank):
            d, t, kind, par = kinds[i]
            left = (ah, kh, kh, ah)[kind]
            right = (kt, kt, rt, rt)[kind]
            r, cols = rows_of(par), slice(t * P, (t + 1) * P)
            for hp in range(2):
                mm = nc.tensor.matmul(bank[:, hp * P:(hp + 1) * P], left[r, d, hp, cols], right[r, d, hp, cols],
                                      start=True, stop=True)
            return mm

        def matrix_out(i, bank, eng, order):
            d, t, kind, par = kinds[i]
            dst = (N_[d], M1[:, d], Rk[:, d], Ra[:, d])[kind][:, t if kind < 2 else t - 2]
            a, b = M_OFF["strict" if kind < 2 else "incl"]
            dst = dst.rearrange("p (hp par) t -> p par hp t", par=2)[:, par]
            return nc.vector.tensor_tensor(dst, bank[:, 0:2 * P].rearrange("p (h t) -> p h t", h=2),
                                           masks[:, d, a:b].unsqueeze(1).to_broadcast([P, 2, P]), ALU.mult)
        products(core, "rw_matrix", len(kinds), matrix, matrix_out)

        with core.stage("unit") as (block, unit):
            @block.vector
            def _(dve):
                for a in (G, T_):
                    nc.vector.tensor_copy(a.rearrange("p d t h c -> p (d t h) c"),
                                          ident.unsqueeze(1).to_broadcast([P, 32, P])).then_inc(unit, 1)
        for b in LEVELS[:-1]:
            with core.stage(f"nm{b}_order") as (block, own):
                @block.vector
                def _(dve):
                    at = M_OFF["lv"][0] + LEVELS.index(b) * P
                    for d in range(2):
                        nc.vector.tensor_tensor(NM[:, d].rearrange("p t h c -> p (t h) c"),
                                                N_[d].rearrange("p t h c -> p (t h) c"),
                                                masks[:, d, at:at + P].unsqueeze(1).to_broadcast([P, 16, P]),
                                                ALU.mult).then_inc(own, 1)

            def first(i, bank):
                d, t = divmod(i, NT4)
                for h in range(B_HEADS):
                    mm = nc.tensor.matmul(bank[:, h * P:(h + 1) * P], NM[:, d, t, h], T_[:, d, t, h], start=True,
                                          stop=True)
                return mm

            def first_out(i, bank, eng, order):
                d, t = divmod(i, NT4)
                return copy(nc, eng, P_[:, d, t].rearrange("p h c -> p (h c)"), bank)
            products(core, f"inv{b}_first", 8, first, first_out, odd)
            last = b == LEVELS[-2]
            units = [(d, t, x) for d in range(2) for t in range(NT4) for x in range(2) if x or not last]

            def second(i, bank):
                d, t, x = units[i]
                for h in range(B_HEADS):
                    left, right = ((G, P_), (P_, G))[x]
                    mm = nc.tensor.matmul(bank[:, h * P:(h + 1) * P], left[:, d, t, h], right[:, d, t, h],
                                          start=True, stop=True)
                return mm

            def second_out(i, bank, eng, order):
                d, t, x = units[i]
                dst = (T_, G)[x][:, d, t].rearrange("p h c -> p (h c)")
                return nc.vector.tensor_tensor(dst, dst, bank, ALU.subtract)
            products(core, f"inv{b}_second", len(units), second, second_out)
        rw_sequence(core, S, kt, rt, M1, G, Rk, Ra, vt, k2t, a2t, tot, y)
        with ExitStack() as inner:
            st = core.sb(inner, "rw_stat", [P, 2, TT, B_HEADS])
            yy = y[:, 0].rearrange("p t (h d) -> p t h d", d=HD)
            y1 = y[:, 1].rearrange("p t (h d) -> p t h d", d=HD)

            def wide(a, t):
                return a[:, t, :].unsqueeze(2).to_broadcast([P, B_HEADS, HD])
            with core.stage("ln_order", "ln_rooted", "ln_meaned") as (block, own, rooted, meaned):
                @block.vector
                def _(dve):
                    order = Order(dve, own)
                    order(nc.vector.tensor_tensor(y[:, 0], y[:, 0], y[:, 1], ALU.add))
                    for t in range(TT):
                        order(nc.vector.tensor_reduce(st[:, 0, t, :], yy[:, t], AX_X, ALU.add))
                    order(nc.vector.tensor_scalar(st[:, 0], st[:, 0], 1.0 / HD, None, ALU.mult))
                    for t in range(TT):
                        order(nc.vector.tensor_tensor(yy[:, t], yy[:, t], wide(st[:, 0], t), ALU.subtract))
                        order(nc.vector.tensor_tensor(y1[:, t], yy[:, t], yy[:, t], ALU.mult))
                        order(nc.vector.tensor_reduce(st[:, 1, t, :], y1[:, t], AX_X, ALU.add))
                    nc.vector.tensor_scalar(st[:, 1], st[:, 1], 1.0 / HD, 64e-5, ALU.mult, ALU.add)\
                        .then_inc(meaned, 1)
                    dve.wait_ge(rooted, 1)
                    order(nc.vector.reciprocal(st[:, 1], st[:, 1]))
                    for t in range(TT):
                        order(nc.vector.tensor_tensor(yy[:, t], yy[:, t], wide(st[:, 1], t), ALU.mult))
                        order(nc.vector.tensor_tensor(y[:, 0, t], y[:, 0, t], k["ln_gain"], ALU.mult))
                        order(nc.vector.tensor_tensor(y[:, 0, t], y[:, 0, t], k["ln_bias"], ALU.add))
                        order(nc.vector.tensor_tensor(y1[:, t],
                                                      vt[:, 2 + t, :].rearrange("p (h d) -> p h d", d=HD),
                                                      wide(bon, t), ALU.mult))
                        order(nc.vector.tensor_tensor(y[:, 0, t], y[:, 0, t], y[:, 1, t], ALU.add))
                        order(nc.vector.tensor_tensor(ycat[:, t, A_W:2 * A_W], y[:, 0, t], gt[:, t, :], ALU.mult))

                @block.scalar
                def _(act):
                    act.wait_ge(meaned, 1)
                    nc.scalar.activation(st[:, 1], st[:, 1], ACT.Sqrt).then_inc(rooted, 1)


def rw_sequence(core, S, kt, rt, M1, G, Rk, Ra, vt, k2t, a2t, tot, y):
    nc = core.nc
    chunks = [[0, 1, 2, 3, 4, 5, 6, 7], [3, 2, 1, 0, 7, 6, 5, 4]]
    steps = 8
    with ExitStack() as mem:
        rhs = core.sb(mem, "rw_rhs", [P, 2, 2, 2, HD])
        nu = core.sb(mem, "rw_nu", [P, 2, A_W])
        names = ("rhs_ready", "rhs_copied", "u_ready", "u_copied", "state_added", "state_ready", "y_ready", "y_copied")
        with core.stage(*[f"{n}{d}" for d in range(2) for n in names]) as (block, *sems):
            (rhs_ready, rhs_copied, u_ready, u_copied, state_added, state_ready, y_ready, y_copied) = [
                (sems[i], sems[8 + i]) for i in range(8)]

            def place(n, d):
                c = chunks[d][n]
                return c, c // 2, slice(HD * (c % 2), HD * (c % 2) + HD)

            @block.tensor
            def _(pe):
                for n in range(steps):
                    for d in range(2):
                        c, tile, half = place(n, d)
                        cols = slice(tile * P, (tile + 1) * P)
                        if n:
                            pe.wait_ge(state_ready[d], 4 * n)
                        if n > 4:
                            pe.wait_ge(y_copied[d], n - 4)
                        for par in range(2):
                            r = rows_of(par)
                            for hp in range(2):
                                o = core.ps[:, 4 * d + par, hp * HD:(hp + 1) * HD]
                                h = 2 * hp + par
                                nc.tensor.matmul(o, kt[r, d, hp, cols], S[r, d, hp, :], start=True, stop=False)
                                mm = nc.tensor.matmul(o, M1[:, d, tile, h], vt[:, tile, h * HD:(h + 1) * HD],
                                                      start=False, stop=True)
                        mm.then_inc(rhs_ready[d], 1)
                    for d in range(2):
                        c, tile, half = place(n, d)
                        pe.wait_ge(rhs_copied[d], n + 1)
                        for h in range(B_HEADS):
                            mm = nc.tensor.matmul(core.ps[:, 4 * d + 2, h * HD:(h + 1) * HD], G[:, d, tile, h],
                                                  rhs[:, d, h % 2, h // 2, :], start=True, stop=True)
                        mm.then_inc(u_ready[d], 1)
                    for d in range(2):
                        c, tile, half = place(n, d)
                        pe.wait_ge(u_copied[d], n + 1)
                        for hp in range(2):
                            o = core.ps[:, 4 * d + 3, hp * P:(hp + 1) * P]
                            cols = slice(hp * P, (hp + 1) * P)
                            nc.tensor.matmul(o, k2t[half, d, tile, cols], vt[half, tile, cols], start=True, stop=False)
                            mm = nc.tensor.matmul(o, a2t[half, d, tile, cols], nu[half, d, cols], start=False,
                                                  stop=True)
                        mm.then_inc(state_added[d], 1)
                        if n < 4:
                            continue
                        for par in range(2):
                            r = rows_of(par)
                            for hp in range(2):
                                h = 2 * hp + par
                                o = core.ps[:, 4 * d + par, 2 * P + hp * HD:2 * P + (hp + 1) * HD]
                                nc.tensor.matmul(o, rt[r, d, hp, tile * P:(tile + 1) * P], S[r, d, hp, :], start=True,
                                                 stop=False)
                                nc.tensor.matmul(o, Rk[:, d, tile - 2, h], vt[:, tile, h * HD:(h + 1) * HD],
                                                 start=False, stop=False)
                                mm = nc.tensor.matmul(o, Ra[:, d, tile - 2, h], nu[:, d, h * HD:(h + 1) * HD],
                                                      start=False, stop=True)
                        mm.then_inc(y_ready[d], 1)

            @block.scalar
            def _(act):
                for n in range(steps):
                    for d in range(2):
                        act.wait_ge(rhs_ready[d], n + 1)
                        nc.scalar.activation(rhs[:, d].rearrange("p a b v -> p a (b v)"),
                                             core.ps[:, 4 * d:4 * d + 2, 0:P], ACT.Copy).then_inc(rhs_copied[d], 1)
                    for d in range(2):
                        act.wait_ge(u_ready[d], n + 1)
                        if n > 4:
                            act.wait_ge(y_ready[d], n - 4)
                        nc.scalar.activation(nu[:, d, :], core.ps[:, 4 * d + 2, 0:A_W], ACT.Copy, scale=-1.0)\
                            .then_inc(u_copied[d], 1)

            @block.vector
            def _(dve):
                for n in range(steps):
                    for d in range(2):
                        c, tile, half = place(n, d)
                        dve.wait_ge(state_added[d], n + 1)
                        if n >= 4:
                            dve.wait_ge(y_ready[d], n - 3)
                        for par in range(2):
                            r = rows_of(par)
                            for hp in range(2):
                                nc.vector.scalar_tensor_tensor(
                                    out=S[r, d, hp, :], in0=S[r, d, hp, :], scalar=tot[r, d, hp, c:c + 1],
                                    in1=core.ps[r, 4 * d + 3, hp * P + par * HD:hp * P + (par + 1) * HD],
                                    op0=ALU.mult, op1=ALU.add).then_inc(state_ready[d], 1)
                        if n >= 4:
                            dst = y[half, d, tile - 2, :].rearrange("p (hp par v) -> p par hp v", par=2, v=HD)
                            for par in range(2):
                                ins = nc.vector.tensor_copy(
                                    dst[:, par], core.ps[half, 4 * d + par, 2 * P:3 * P]
                                    .rearrange("p (hp v) -> p hp v", v=HD))
                            ins.then_inc(y_copied[d], 1)


def neighbourhood(core, I, k, consts, hT, ycat):
    nc, ident = core.nc, k["ident"]
    with ExitStack() as mem:
        q = core.sb(mem, "na_q", [P, TT, C_W])
        kx = core.sb(mem, "na_k", [P, NT4, C_W])
        v = core.sb(mem, "na_v", [P, NT4, C_W])
        kT = core.sb(mem, "na_kT", [P, 4, NTOK])
        qT = core.sb(mem, "na_qT", [P, 4, SEQ])
        rs = core.sb(mem, "na_rs", [P, TT + NT4, C_HEADS])
        spans = [(C_AT, 512, (2, 3)), (C_AT + 512, 512, range(NT4)), (C_AT + 1024, 512, range(NT4))]

        def out(j, t, bank, eng, order):
            return copy(nc, eng, (q[:, t - 2] if j == 0 else (kx, v)[j - 1][:, t]), bank)
        linear(core, "na_proj", core.ring, hT, I["w_in_2"], spans, out, odd)
        carve = Carver(core.ring)
        s, pT = carve(2 * C_HEADS * NTOK), carve(2 * C_HEADS * NTOK)
        bias = carve(TT, C_HEADS, SEQ)
        tmp = carve(3, C_HEADS, HD // 2)
        sq = s[:, 0:NT4 * C_W].rearrange("p (t h d) -> p t h d", t=NT4, h=C_HEADS)
        load(core, "na_bias", [(bias[:, t], I["bias"][t]) for t in range(TT)])
        qh = q[:, :, :].rearrange("p t (h d) -> p t h d", d=HD)
        kh = kx[:, :, :].rearrange("p t (h d) -> p t h d", d=HD)
        head_inverse_rms(core, "naq_rms", qh, sq, rs[:, 0:TT, :], TT, C_HEADS)
        head_inverse_rms(core, "nak_rms", kh, sq, rs[:, TT:, :], NT4, C_HEADS)
        with core.stage("na_order") as (block, own):
            @block.vector
            def _(dve):
                order = Order(dve, own)
                for x, tiles, at, gain in ((qh, TT, 0, k["q_gain"]), (kh, NT4, TT, k["k_gain"])):
                    for t in range(tiles):
                        order(nc.vector.tensor_tensor(
                            x[:, t], x[:, t], rs[:, at + t, :].unsqueeze(2).to_broadcast([P, C_HEADS, HD]), ALU.mult))
                        order(nc.vector.tensor_tensor(x[:, t], x[:, t],
                                                      gain.unsqueeze(1).to_broadcast([P, C_HEADS, HD]), ALU.mult))
                    for t in range(TT):
                        xl = x[:, tiles - 2 + t]
                        cos, sin = (consts[n][:, 32 * t:32 * t + 32].unsqueeze(1).to_broadcast([P, C_HEADS, 32])
                                    for n in ("na_cos", "na_sin"))
                        rotate(nc, order, xl[:, :, 0:32], xl[:, :, 32:64], cos, sin, [tmp[:, i] for i in range(3)])

        key_tiles = (2, 3, 0, 1)

        def turn(i, bank):
            src, tiles = (q, (0, 1)) if i < 4 else (kx, key_tiles)
            for j, t in enumerate(tiles):
                ins = nc.tensor.transpose(bank[:, j * P:(j + 1) * P], src[:, t, (i % 4) * P:(i % 4 + 1) * P], ident)
            return ins

        def turned(i, bank, eng, order):
            return copy(nc, eng, qT[:, i, :] if i < 4 else kT[:, i - 4, :], bank[:, 0:SEQ if i < 4 else NTOK])
        products(core, "na_turn", 8, turn, turned, odd)
        attention(core, "na", mem, ident, C_HEADS, NTOK, HD,
                  lambda h, t: qT[rows_of(h), h // 2, t * P:(t + 1) * P], lambda h: kT[rows_of(h), h // 2, :],
                  HD ** -0.5, lambda h, t: bias[:, t, h, :], SEQ,
                  lambda h, j: v[:, key_tiles[j], h * HD:(h + 1) * HD],
                  lambda t: ycat[:, t, 2 * A_W:].rearrange("p (h d) -> p h d", d=HD), (s, pT))


def router(core, I, k, hT, comb_d):
    nc = core.nc
    n = GROUPS + EXPERTS
    with ExitStack() as mem:
        w = core.sb(mem, "rt_w", [P, KD, n])
        lg = core.sb(mem, "rt_logits", [P, TT, n])
        place = core.sb(mem, "rt_place", [P, PER_GROUP])
        a, b, c, e, pr = (core.sb(mem, f"rt_{i}", [P, TT, PER_GROUP]) for i in "abcde")
        pick = [core.sb(mem, f"rt_pick{i}", [P, TT, PER_GROUP]) for i in range(2)]
        group = core.sb(mem, "rt_group", [P, TT, GROUPS])
        col = core.sb(mem, "rt_col", [P, 8, TT])
        comb = core.sb(mem, "rt_comb", [P, GROUPS, PER_GROUP, TT])
        load(core, "router", [(w[:, :, :], I["router"].rearrange("(k p) n -> p k n", p=P))])

        def logit(t, bank):
            for kt in range(KD):
                mm = nc.tensor.matmul(bank[:, 0:n], hT[:, kt, t * P:(t + 1) * P], w[:, kt, :], start=(kt == 0),
                                      stop=(kt == KD - 1))
            return mm

        def logit_out(t, bank, eng, order):
            return nc.vector.tensor_tensor(lg[:, t, :], bank[:, 0:n], k["b_r"], ALU.add)
        products(core, "rt_logit", TT, logit, logit_out)

        def wide(x, m):
            return x.unsqueeze(2).to_broadcast([P, TT, m])

        def first_of_max(order, x, top, out, m, s1, s2):
            order(nc.vector.tensor_tensor(s1, x, wide(top, m), ALU.is_equal))
            order(nc.vector.tensor_scalar(s1, s1, -64.0, 64.0, ALU.mult, ALU.add))
            order(nc.vector.tensor_tensor(s1, s1, place[:, 0:m].unsqueeze(1).to_broadcast([P, TT, m]), ALU.add))
            order(nc.vector.tensor_reduce(s2, s1, AX_X, ALU.min))
            order(nc.vector.tensor_tensor(out, s1, wide(s2, m), ALU.is_equal))

        with core.stage("rt_order", "rt_shift", "rt_exp", "rt_place", "rt_comb", "rt_stored") as (
                block, own, shifted, exped, placed, combed, stored):
            @block.gpsimd
            def _(pool):
                for i in range(PER_GROUP):
                    nc.gpsimd.memset(place[:, i:i + 1], float(i)).then_inc(placed, 1)
                pool.wait_ge(placed, PER_GROUP)

            @block.scalar
            def _(act):
                act.wait_ge(shifted, 1)
                nc.scalar.activation(a[:, :, 0:GROUPS], a[:, :, 0:GROUPS], ACT.Exp).then_inc(exped, 1)
                act.wait_ge(shifted, 2)
                nc.scalar.activation(pr[:, :, :], pr[:, :, :], ACT.Exp).then_inc(exped, 1)

            @block.vector
            def _(dve):
                order = Order(dve, own)
                V = nc.vector
                g = lg[:, :, 0:GROUPS]
                dve.wait_ge(placed, PER_GROUP)
                order(V.tensor_reduce(col[:, 0], g, AX_X, ALU.max))
                V.tensor_tensor(a[:, :, 0:GROUPS], g, wide(col[:, 0], GROUPS), ALU.subtract).then_inc(shifted, 1)
                first_of_max(order, g, col[:, 0], group[:, :, :], GROUPS, b[:, :, 0:GROUPS], col[:, 1])
                dve.wait_ge(exped, 1)
                order(V.tensor_reduce(col[:, 2], a[:, :, 0:GROUPS], AX_X, ALU.add))
                order(V.reciprocal(col[:, 2], col[:, 2]))
                order(V.tensor_tensor(a[:, :, 0:GROUPS], a[:, :, 0:GROUPS], group[:, :, :], ALU.mult))
                order(V.tensor_reduce(col[:, 3], a[:, :, 0:GROUPS], AX_X, ALU.add))
                order(V.tensor_tensor(col[:, 2], col[:, 2], col[:, 3], ALU.mult))
                for gi in range(GROUPS):
                    src = lg[:, :, GROUPS + gi * PER_GROUP:GROUPS + (gi + 1) * PER_GROUP]
                    weight = group[:, :, gi:gi + 1].to_broadcast([P, TT, PER_GROUP])
                    order(V.tensor_tensor(c[:, :, :], src, weight, ALU.mult))
                    if gi == 0:
                        order(V.tensor_copy(e[:, :, :], c[:, :, :]))
                    else:
                        order(V.tensor_tensor(e[:, :, :], e[:, :, :], c[:, :, :], ALU.add))
                order(V.tensor_reduce(col[:, 4], e[:, :, :], AX_X, ALU.max))
                V.tensor_tensor(pr[:, :, :], e[:, :, :], wide(col[:, 4], PER_GROUP), ALU.subtract).then_inc(shifted, 1)
                dve.wait_ge(exped, 2)
                order(V.tensor_reduce(col[:, 5], pr[:, :, :], AX_X, ALU.add))
                order(V.reciprocal(col[:, 5], col[:, 5]))
                order(V.tensor_tensor(pr[:, :, :], pr[:, :, :], wide(col[:, 5], PER_GROUP), ALU.mult))
                order(V.tensor_copy(e[:, :, :], pr[:, :, :]))
                for i in range(2):
                    order(V.tensor_reduce(col[:, 4], e[:, :, :], AX_X, ALU.max))
                    first_of_max(order, e[:, :, :], col[:, 4], pick[i][:, :, :], PER_GROUP, b[:, :, :], col[:, 1])
                    order(V.scalar_tensor_tensor(out=e[:, :, :], in0=pick[i][:, :, :], scalar=-4.0, in1=e[:, :, :],
                                                 op0=ALU.mult, op1=ALU.add))
                order(V.tensor_tensor(b[:, :, :], pick[0][:, :, :], pick[1][:, :, :], ALU.add))
                order(V.tensor_tensor(pr[:, :, :], pr[:, :, :], b[:, :, :], ALU.mult))
                order(V.tensor_reduce(col[:, 5], pr[:, :, :], AX_X, ALU.add))
                order(V.reciprocal(col[:, 5], col[:, 5]))
                order(V.tensor_tensor(pr[:, :, :], pr[:, :, :], wide(col[:, 5], PER_GROUP), ALU.mult))
                order(V.tensor_tensor(pr[:, :, :], pr[:, :, :], wide(col[:, 2], PER_GROUP), ALU.mult))
                for gi in range(GROUPS):
                    V.tensor_tensor(comb[:, gi].rearrange("p e t -> p t e"), pr[:, :, :],
                                    group[:, :, gi:gi + 1].to_broadcast([P, TT, PER_GROUP]), ALU.mult)\
                        .then_inc(combed, 1)

            @block.sync
            def _(sp):
                sp.wait_ge(combed, GROUPS)
                sp.dma_start(comb_d.rearrange("e p t -> p e t"), comb[:, :, :, :].rearrange("p g e t -> p (g e) t"))\
                    .then_inc(stored, 16)
                sp.wait_ge(stored, 16)


TURN = 4


def experts(core, I, hT, comb_d, y):
    nc = core.nc
    half = RING * SLOT // 2
    wg, wu, wd = (I[f"w_exp_{n}_2"].rearrange("(g e) a b -> g e a b", e=TURN) for n in ("gate", "up", "down"))
    FT = D_EXP // P
    with ExitStack() as mem:
        hid = core.sb(mem, "me_hid", [P, 2, FT, SEQ])
        act_ = core.sb(mem, "me_act", [P, 2, SEQ])
        cw = core.sb(mem, "me_comb", [P, TURN, TT])
        landed = [mem.enter_context(nc.semaphore(f"expert_landed{i}")) for i in range(2)]

        def slot(e):
            at = (e % 2) * half
            return (core.ring[:, at:at + SLOT].rearrange("p (k f) -> p k f", k=KD),
                    core.ring[:, at + SLOT:at + 2 * SLOT].rearrange("p (k f) -> p k f", k=KD),
                    core.ring[:, at + 2 * SLOT:at + 3 * SLOT].rearrange("p (k n) -> p k n", k=FT))

        def fetch(sp, e, base):
            g, u, d = slot(e)
            group, e_ = base + e // TURN, e % TURN
            sp.dma_start(g, wg[group, e_].rearrange("(k p) f -> p k f", p=P)).then_inc(landed[e % 2], 16)
            sp.dma_start(u, wu[group, e_].rearrange("(k p) f -> p k f", p=P)).then_inc(landed[e % 2], 16)
            sp.dma_start(d, wd[group, e_].rearrange("(k p) n -> p k n", p=P)).then_inc(landed[e % 2], 16)

        with core.stage("me_zero") as (block, zeroed):
            @block.vector
            def _(dve):
                nc.vector.memset(y, 0.0).then_inc(zeroed, 1)

            @block.sync
            def _(sp):
                for e in range(2):
                    sp.sem_clear(landed[e])
                    fetch(sp, e, 0)
        core.settle()

        def turn(base, ahead):
            with core.stage("me_multiplied", "me_silu", "me_hid", "me_down", "me_added", "me_comb",
                            "me_order") as (block, multiplied, silu, hidden, down, added, comb_here, own):
                @block.sync
                def _(sp):
                    sp.dma_start(cw[:, :, :], comb_d.rearrange("(g e) p t -> g p e t", e=TURN)[base])\
                        .then_inc(comb_here, 16)
                    for e in range(2, TURN + 2 if ahead else TURN):
                        sp.wait_ge(down, 4 * (e - 1))
                        if e >= TURN:
                            sp.sem_clear(landed[e % 2])
                        fetch(sp, e, base)

                @block.tensor
                def _(pe):
                    def rise(e):
                        g, u, _ = slot(e)
                        pe.wait_ge(landed[e % 2], 48 * (e // 2 + 1))
                        for f in range(FT):
                            n = FT * e + f
                            if n >= 4:
                                pe.wait_ge(hidden, n - 3)
                            for w, at in ((g, 0), (u, SEQ)):
                                for kt in range(KD):
                                    mm = nc.tensor.matmul(core.ps[:, n % 4, at:at + SEQ], w[:, kt, f * P:(f + 1) * P],
                                                          hT[:, kt, :], start=(kt == 0), stop=(kt == KD - 1))
                            mm.then_inc(multiplied, 1)

                    def fall(e):
                        _, _, d = slot(e)
                        pe.wait_ge(hidden, FT * (e + 1))
                        for i in range(4):
                            t, c = divmod(i, 2)
                            n = 4 * e + i
                            if n >= 4:
                                pe.wait_ge(added, n - 3)
                            for f in range(FT):
                                mm = nc.tensor.matmul(core.ps[:, 4 + i, :], hid[:, e % 2, f, t * P:(t + 1) * P],
                                                      d[:, f, c * 512:(c + 1) * 512], start=(f == 0), stop=(f == FT - 1))
                            mm.then_inc(down, 1)

                    for e in range(TURN):
                        rise(e)
                        if e:
                            fall(e - 1)
                    fall(TURN - 1)

                @block.scalar
                def _(act):
                    for n in range(FT * TURN):
                        act.wait_ge(multiplied, n + 1)
                        if n >= 2:
                            act.wait_ge(hidden, n - 1)
                        nc.scalar.activation(act_[:, n % 2, :], core.ps[:, n % 4, 0:SEQ], ACT.Silu).then_inc(silu, 1)

                @block.vector
                def _(dve):
                    def add(e):
                        if e == 0:
                            dve.wait_ge(comb_here, 16)
                        for i in range(4):
                            t, c = divmod(i, 2)
                            n = 4 * e + i
                            dst = y[:, t, c * 512:(c + 1) * 512]
                            dve.wait_ge(down, n + 1)
                            if n >= 4:
                                dve.wait_ge(added, n - 3)
                            nc.vector.scalar_tensor_tensor(out=dst, in0=core.ps[:, 4 + i, :], scalar=cw[:, e, t:t + 1],
                                                           in1=dst, op0=ALU.mult, op1=ALU.add).then_inc(added, 1)
                    for e in range(TURN):
                        for f in range(FT):
                            n = FT * e + f
                            dve.wait_ge(silu, n + 1)
                            if e >= 2:
                                dve.wait_ge(down, 4 * (e - 1))
                            nc.vector.tensor_tensor(hid[:, e % 2, f, :], act_[:, n % 2, :], core.ps[:, n % 4, SEQ:],
                                                    ALU.mult).then_inc(hidden, 1)
                        if e:
                            add(e - 1)
                    add(TURN - 1)

        with nc.Fori(0, EXPERTS // TURN - 1, 1) as base:
            turn(base, True)
            core.settle()
        turn(EXPERTS // TURN - 1, False)


def second_block(core, I, k, x):
    nc = core.nc
    S_OFF, n_cols = offsets(S_COLS)
    with ExitStack() as mem:
        fvt = core.sb(mem, "second_vectors", [P, n_cols])
        fv = {n: fvt[:, a:b] for n, (a, b) in S_OFF.items()}
        mod = core.sb(mem, "mod2", [P, 48, 2])
        gain = core.sb(mem, "gain2", [P, KD])
        g_row = core.sb(mem, "g_row2", [P, DM])
        rstd = core.sb(mem, "rstd2", [P, TT])
        k = dict(k)
        comb_d = nc.dram_tensor("comb", [EXPERTS, P, TT], F32).ap()
        load(core, "second", [(fvt[:, :], I["second_vectors"])])
        modulation(core, "ada2", core.ring, I["w_ada_2"], fv["c"].rearrange("p (v k) -> p v k", v=2), 2, fv["ada_b"],
                   mod[:, :, :])
        with ExitStack() as mix:
            ycat = core.sb(mix, "ycat", [P, TT, DM])
            with ExitStack() as inner:
                hT = core.sb(inner, "hT2", [P, KD, NTOK])
                masks = core.sb(inner, "masks", [P, 2, M_WIDTH])
                c_off, n_consts = offsets(C_COLS)
                names = ("head_ones", "head_pick", "na_cos", "na_sin", "chunk_start")
                widths = [c_off[n][1] - c_off[n][0] for n in names]
                ct = core.sb(inner, "consts2", [P, sum(widths)])
                consts = {n: ct[:, sum(widths[:i]):sum(widths[:i + 1])] for i, n in enumerate(names)}
                carve = Carver(core.ring)
                xc, xn = carve(TT, DM), carve(TT, DM)
                load(core, "masks", [(masks[:, d, :], I["masks"][d]) for d in range(2)]
                     + [(consts[n], I["consts"][:, c_off[n][0]:c_off[n][1]]) for n in names]
                     + [(xc, I["ctx"].rearrange("b (t p) d -> p (b t) d", p=P))])
                for v, src in ((1, xc), (0, x)):
                    gains(core, f"gain_v{v}", mod, v, fv["norm1"], gain[:, :], KD)
                    norm_transposed(core, f"norm_v{v}", k["ident"], src, hT, SEQ * (1 - v), gain, mod[:, 0:KD, v],
                                    (rstd, xn))
                hgrn(core, I, k, fv, masks, hT[:, :, :], ycat)
                neighbourhood(core, I, k, consts, hT[:, :, :], ycat)
                rwkv(core, I, k, fv, masks, consts, hT[:, :, :], ycat)
            with ExitStack() as inner:
                yT = core.sb(inner, "yT2", [P, KD, SEQ])
                tmp = core.sb(inner, "res_tmp", [P, TT, 512])
                diag = core.sb(inner, "diag2", [P, KD, P])
                spread_rows(core, "g1", k["ident"], k["ones"], mod[:, 2 * KD:3 * KD, 0], diag[:, :, :], g_row)
                turn_features(core, "ycat_turn", k["ident"], ycat, KD, yT, fv["out_gain"])
                residual(core, "w_out2", yT, I["w_out_2"], g_row, tmp, x)
        hT = core.sb(mem, "h2T", [P, KD, SEQ])
        y = core.sb(mem, "moe_y", [P, TT, DM])
        gains(core, "gain_ffn", mod, 0, fv["norm2"], gain[:, :], 4 * KD)
        norm_transposed(core, "norm_ffn", k["ident"], x, hT, 0, gain, mod[:, 3 * KD:4 * KD, 0], (rstd, y))
        spread_rows(core, "g2", k["ident"], k["ones"], mod[:, 5 * KD:6 * KD, 0],
                    y[:, 0, :].rearrange("p (k f) -> p k f", k=KD), g_row)
        router(core, I, k, hT, comb_d)
        experts(core, I, hT, comb_d, y[:, :, :])
        with core.stage("last_order") as (block, own):
            @block.vector
            def _(dve):
                order = Order(dve, own)
                for t in range(TT):
                    order(nc.vector.tensor_tensor(y[:, t, :], y[:, t, :], g_row[:, :], ALU.mult))
                    order(nc.vector.tensor_tensor(x[:, t, :], x[:, t, :], y[:, t, :], ALU.add))


M_OFF, M_WIDTH = offsets(M_COLS)


def build(nc, I, out, second=True):
    with ExitStack() as ctx:
        core = Core(nc, ctx)
        core.ring = core.sb(ctx, "ring", [P, RING * SLOT])
        x = core.sb(ctx, "x", [P, TT, DM])
        C_OFF, n_consts = offsets(C_COLS)
        R_OFF, n_rows = offsets(R_COLS)
        rows = core.sb(ctx, "rows", [P, n_rows])
        ones = core.sb(ctx, "ones", [P, P])
        ident = core.sb(ctx, "ident", [P, P])
        cv = I["consts"]
        pairs = [(x[:, :, :], I["x"].rearrange("b (t p) d -> p (b t) d", p=P)),
                 (rows[:, :], I["rows"].to_broadcast([P, n_rows])), (ident[:, :], cv[:, 0:P])]
        with ExitStack() as first:
            consts = core.sb(first, "consts", [P, n_consts])
            pos = core.sb(first, "pos", [P, TT], I32)
            k = {n: consts[:, a:b] for n, (a, b) in C_OFF.items()}
            k["ones"] = ones[:, :]
            k["ident"] = ident[:, :]
            k["final"] = rows[:, R_OFF["final"][0]:R_OFF["final"][1]]
            k["cos"] = core.sb(first, "cos", [P, TT, ROPE // 2])
            k["sin"] = core.sb(first, "sin", [P, TT, ROPE // 2])
            load(core, "inputs", pairs + [(consts[:, :], cv[:, 0:n_consts]),
                                          (pos[:, :], I["positions"])])
            with core.stage("ones_set") as (block, ones_set):
                @block.gpsimd
                def _(pool):
                    nc.gpsimd.memset(ones[:, :], 1.0).then_inc(ones_set, 1)
                    pool.wait_ge(ones_set, 1)
            with ExitStack() as mem:
                rotary_tables(core, mem, pos[:, :], k["inv_freq"], k["cos"][:, :, :], k["sin"][:, :, :])
            first_block(core, I, k, x)
        if second:
            second_block(core, I, dict(ident=ident[:, :], ones=ones[:, :],
                                       b_r=rows[:, R_OFF["b_rg"][0]:R_OFF["b_re"][1]],
                                       **{n: rows[:, a:b] for n, (a, b) in R_OFF.items()}), x)
        with core.stage("stored") as (block, stored):
            @block.sync
            def _(sp):
                sp.dma_start(out.rearrange("b (t p) d -> p (b t) d", p=P), x[:, :, :]).then_inc(stored, 16)
                sp.wait_ge(stored, 16)
        core.settle()


def columns(n, *arrays):
    return np.concatenate([a.reshape(-1, P).T for a in arrays], axis=1)


def head_rows(a):
    out = np.zeros((P, a.shape[1]), np.float32)
    out[:a.shape[0]] = a
    return out


def constants():
    p, q = np.arange(P)[:, None], np.arange(P)[None, :]
    ident = (p == q).astype(np.float32)
    sel = np.zeros((P, HEADS, P), np.float32)
    for h in range(HEADS):
        sel[h, h] = 1.0
    diag = np.where(p <= q, 0.0, MASKED)
    mla = np.zeros((P, TT, SEQ))
    for t in range(TT):
        mla[:, t] = np.where(np.arange(SEQ)[None, :] // 64 <= (t * P + p) // 64, 0.0, MASKED)
    quarter = HD // 4
    inv = (10000.0 ** (-np.arange(quarter, dtype=np.float32) / quarter)).astype(np.float32)
    pos = np.arange(SEQ)
    ang = np.concatenate([(pos // GRID_W).astype(np.float32)[:, None] * inv,
                          (pos % GRID_W).astype(np.float32)[:, None] * inv], axis=1)
    turn = lambda a: a.reshape(TT, P, 32).transpose(1, 0, 2).reshape(P, -1)
    half = ROPE // 2
    inv_freq = np.float32(10000.0) ** (-np.arange(half, dtype=np.float32) / np.float32(half))
    start = np.tile((np.arange(NTOK) % RW_CHUNK != 0).astype(np.float32), (P, 1))
    parts = dict(ident=ident, head_ones=(p // HD == q // HD), head_pick=(p // HD == np.arange(2)[None, :]),
                 inv_freq=np.tile(inv_freq, (P, 1)), sel=sel.reshape(P, -1),
                 ml_mask=np.concatenate([diag, 0 * diag], axis=1), mla_mask=mla.reshape(P, -1),
                 na_cos=turn(np.cos(ang)), na_sin=turn(np.sin(ang)), chunk_start=start)
    consts = np.concatenate([parts[n].astype(np.float32) for n in C_COLS], axis=1)
    levels = [(q // b == p // b + 1) & ((q // b) % 2 == 1) for b in LEVELS]
    chunk = p // RW_CHUNK == q // RW_CHUNK
    masks = []
    for forward in (True, False):
        cols = [ident] + levels + [chunk & (p < q), chunk & (p <= q)]
        masks.append(np.concatenate([(m if forward else m.T).astype(np.float32) for m in cols], axis=1))
    return consts, np.stack(masks)


def window_bias(rpb):
    q = np.arange(SEQ)
    qr, qc = q[:, None] // GRID_W, q[:, None] % GRID_W
    kr, kc = q[None, :] // GRID_W, q[None, :] % GRID_W
    start = np.clip(qc - 8, 0, GRID_W - 16)
    inside = (kc >= start) & (kc < start + 16)
    cols = np.clip(kc - qc + 15, 0, 30)
    b = np.where(inside[None], rpb[:, kr - qr + 7, cols], np.float32(MASKED))
    return np.ascontiguousarray(b.reshape(C_HEADS, TT, P, SEQ).transpose(1, 2, 0, 3))


def layouts(a):
    d = {n: a[n] for n in ("x", "positions", "ada_w", "w_in", "w_uq", "w_ukv", "w_br_mla", "w_br_mlstm", "w_out",
                           "ffn_w_up", "ffn_w_down")}
    d["positions"] = a["positions"].reshape(TT, P).T
    layers = []
    for l in range(DEPTH):
        parts = dict(c=columns(8, a["c"][0]), ada_b=columns(48, a["ada_b"][l]), norm_mix=columns(8, a["norm_mix_w"][l]),
                     q_norm=columns(3, a["q_norm_w"][l]), kv_norm=columns(2, a["kv_norm_w"][l]),
                     conv_w=columns(32, *a["mlstm_conv_w"][l]), conv_b=columns(8, a["mlstm_conv_b"][l]),
                     head_norm=columns(4, a["mlstm_head_norm_w"][l]), norm_ffn=columns(8, a["norm_ffn_w"][l]),
                     ffn_conv_w=columns(3, *a["ffn_conv_w"][l]), ffn_conv_b=columns(44, a["ffn_conv_b"][l]),
                     gate_b=head_rows(a["mlstm_gate_b"][l].reshape(2, HEADS).T))
        layers.append(np.concatenate([parts[n] for n in L_COLS], axis=1))
    d["layer_vectors"] = np.stack(layers)
    s = {n[:-2]: v[0] for n, v in a.items() if n.endswith("_2") and n != "c_ctx_2"}
    gn = np.concatenate([s["hgrn_gn_gain"].reshape(-1), np.ones(DM - A_W, np.float32)])
    parts = dict(c=np.stack([columns(8, s["c"]), columns(8, a["c_ctx_2"])], axis=1).reshape(P, -1),
                 ada_b=columns(48, s["b_ada"]), norm1=columns(8, s["norm1_gain"]), norm2=columns(8, s["norm2_gain"]),
                 lb=columns(4, a["hgrn_lb_logits_2"][:, 0]), out_gain=columns(8, gn), mu=columns(9, s["rwkv_mu"]),
                 w0=columns(4, s["rwkv_w0"]), a0=columns(4, s["rwkv_a0"]), kk_scale=columns(2, s["rwkv_kk_scale"]),
                 k_a=columns(2, s["rwkv_k_a"]), r_k=columns(2, s["rwkv_r_k"]))
    d["second_vectors"] = np.concatenate([parts[n] for n in S_COLS], axis=1)
    rows = dict(final=a["final_norm_w"], ln_gain=s["rwkv_ln_gain"], ln_bias=s["rwkv_ln_bias"], q_gain=s["na_q_gain"],
                k_gain=s["na_k_gain"], b_rg=s["b_router_group"], b_re=s["b_router_expert"])
    d["rows"] = np.concatenate([rows[n] for n in R_COLS])[None, :]
    d["ctx"] = s["ctx"][None]
    for n in ("w_ada", "w_in", "w_out", "w_exp_gate", "w_exp_up", "w_exp_down"):
        d[n + "_2"] = s[n].reshape((EXPERTS,) + s[n].shape[2:]) if s[n].ndim == 4 else s[n]
    d["rwkv_up"] = np.concatenate([s["rwkv_w_up"].reshape(P, A_W), s["rwkv_a_up"].reshape(P, A_W),
                                   s["rwkv_g_up"]], axis=1)
    d["router"] = np.concatenate([s["w_router_group"], s["w_router_expert"]], axis=1)
    d["bias"] = window_bias(s["na_rpb"])
    d["consts"], d["masks"] = constants()
    return {n: np.ascontiguousarray(v) for n, v in d.items()}


def kernel(**inputs):
    import concourse.bacc as bacc
    from concourse.bass_utils import run_bass_kernel_spmd

    nc = bacc.Bacc("TRN2", target_bir_lowering=False, num_devices=1)
    arrays = layouts({n: np.asarray(v) for n, v in inputs.items()})
    I = {n: nc.dram_tensor(n, v.shape, mybir.dt.from_np(v.dtype), kind="ExternalInput").ap()
         for n, v in arrays.items()}
    out = nc.dram_tensor("out", (1, SEQ, DM), F32, kind="ExternalOutput").ap()
    build(nc, I, out)
    r = run_bass_kernel_spmd(nc, [arrays], core_ids=[0])
    return r.results[0]["out"]
```

```python
from contextlib import ExitStack, contextmanager

import numpy as np

import concourse.bass as bass
from concourse import mybir

F32 = mybir.dt.float32
F32R = mybir.dt.float32r
I32 = mybir.dt.int32
ALU = mybir.AluOpType
ACT = mybir.ActivationFunctionType
AX_X = mybir.AxisListType.X

P = 128
DM = 1024
KD = DM // P
SEQ = 256
TT = SEQ // P
DEPTH = 2
EPS = 1e-6
MASKED = -1e30

Q_LORA, KV_LORA, ROPE = 384, 256, 32
NOPE, VH = 64, 64
HEADS = 8
QK = NOPE + ROPE
ML_W = 512
LATENT = Q_LORA + KV_LORA + ROPE
ML_AT = LATENT
GATE_AT = ML_AT + 4 * ML_W
BR_AT = GATE_AT + 2 * HEADS
D_FF = 2816
FF_TILES = D_FF // P

GRID_W = 64
A_HEADS = B_HEADS = 4
HD = 64
A_W = A_HEADS * HD
B_AT = 5 * A_W
B_PROJ = 3 * A_W + 4 * 64 + 128
B_TILES = B_PROJ // P
C_AT = B_AT + B_PROJ
C_HEADS = 8
C_W = C_HEADS * HD
GROUPS, PER_GROUP = 4, 8
EXPERTS = GROUPS * PER_GROUP
D_EXP = 512
RW_CHUNK = 64
NTOK = 2 * SEQ
NT4 = NTOK // P

L_COLS = dict(c=8, ada_b=48, norm_mix=8, q_norm=3, kv_norm=2, conv_w=32, conv_b=8, head_norm=4,
              norm_ffn=8, ffn_conv_w=3 * 2 * FF_TILES, ffn_conv_b=2 * FF_TILES, gate_b=2)
S_COLS = dict(c=16, ada_b=48, norm1=8, norm2=8, lb=4, out_gain=8, mu=B_TILES, w0=4, a0=4,
              kk_scale=2, k_a=2, r_k=2)
R_COLS = dict(final=DM, ln_gain=A_W, ln_bias=A_W, q_gain=HD, k_gain=HD, b_rg=GROUPS, b_re=EXPERTS)
LEVELS = (1, 2, 4, 8, 16, 32, 64)
C_COLS = dict(ident=P, head_ones=P, head_pick=2, inv_freq=ROPE // 2, sel=HEADS * P, ml_mask=2 * P,
              mla_mask=2 * SEQ, na_cos=2 * 32, na_sin=2 * 32, chunk_start=NTOK, ones_row=SEQ)
M_COLS = dict(ident=P, lv=len(LEVELS) * P, strict=P, incl=P)


def offsets(cols):
    out, at = {}, 0
    for name, n in cols.items():
        out[name] = (at, at + n)
        at += n
    return out, at


class Order:

    def __init__(self, eng, sem):
        self.eng, self.sem, self.n = eng, sem, 0

    def __call__(self, ins):
        self.n += 1
        ins.then_inc(self.sem, 1)
        self.eng.wait_ge(self.sem, self.n)


class Core:

    def __init__(self, nc, ctx):
        self.nc, self.ctx = nc, ctx
        self.spent, self.number, self.tensors = [], 0, 0
        self.ps = ctx.enter_context(nc.psum_tensor("ps", [P, 8, 512], F32))

    def sb(self, mem, name, shape, dt=F32):
        self.tensors += 1
        return mem.enter_context(self.nc.sbuf_tensor(f"{name}_{self.tensors}", shape, dt))

    def clear_spent(self):
        for s in self.spent:
            self.nc.gpsimd.sem_clear(s)

    @contextmanager
    def stage(self, *names):
        before = self.spent
        self.clear_spent()
        self.number += 1
        sems = [self.nc.alloc_semaphore(f"{n}_{self.number}") for n in names]
        with self.nc.Block(no_gpsimd_drain=True) as block:
            yield (block, *sems)
        self.nc.extend_free_semaphores([s.num for s in before])
        self.spent = sems

    def settle(self):
        with self.stage():
            pass


def products(core, what, n, multiply, evacuate, on_scalar=None, banks=8):
    nc = core.nc
    on_scalar = on_scalar or (lambda i: False)
    by_scalar = [on_scalar(i) for i in range(n)]
    with core.stage(f"{what}_multiplied", f"{what}_read_v", f"{what}_read_s", f"{what}_order_v",
                    f"{what}_order_s") as (block, multiplied, read_v, read_s, order_v, order_s):
        def bank(i):
            return core.ps[:, i % banks, :]

        @block.tensor
        def _(pe):
            for i in range(n):
                if i >= banks:
                    j = i - banks
                    if by_scalar[j]:
                        pe.wait_ge(read_s, sum(by_scalar[:j + 1]))
                    else:
                        pe.wait_ge(read_v, j + 1 - sum(by_scalar[:j + 1]))
                multiply(i, bank(i)).then_inc(multiplied, 1)

        @block.vector
        def _(dve):
            order = Order(dve, order_v)
            for i in range(n):
                if not by_scalar[i]:
                    dve.wait_ge(multiplied, i + 1)
                    evacuate(i, bank(i), nc.vector, order).then_inc(read_v, 1)

        @block.scalar
        def _(act):
            order = Order(act, order_s)
            for i in range(n):
                if by_scalar[i]:
                    act.wait_ge(multiplied, i + 1)
                    evacuate(i, bank(i), nc.scalar, order).then_inc(read_s, 1)


def odd(i):
    return i % 2 == 1


def copy(nc, eng, out, in_, scale=None, bias=None):
    if eng is nc.scalar:
        return eng.activation(out, in_, ACT.Identity if bias is not None else ACT.Copy,
                              bias=0.0 if bias is None else bias, scale=1.0 if scale is None else scale)
    if scale is None:
        return eng.tensor_copy(out, in_)
    if bias is None:
        return eng.tensor_scalar(out, in_, scale, None, ALU.mult)
    return eng.tensor_scalar(out, in_, scale, bias, ALU.mult, ALU.add)


SLOT = KD * 512
STAGES = 2


def split_high(nc, high, x):
    return nc.scalar.activation(high, x, ACT.Copy)


def split_low(nc, low, x, high):
    return nc.vector.tensor_tensor(low, x, high.bitcast(F32), ALU.subtract)


def split_product(nc, out, left, right, start, stop):
    (lh, ll), (rh, rl) = left, right
    nc.tensor.matmul(out, lh, rh, start=start, stop=False)
    nc.tensor.matmul(out, lh, rl, start=False, stop=False)
    return nc.tensor.matmul(out, ll, rh, start=False, stop=stop)


def linear(core, what, xT, w, chunks, evacuate, on_scalar=None, banks=8):
    nc = core.nc
    xT = xT[:, :, :]
    kt = w.shape[0] // P
    kh = (kt + 1) // 2
    halves = (slice(0, kh), slice(kh, kt))
    tokens = xT.shape[2]
    wv = w.rearrange("(k p) n -> p k n", p=P)
    units = []
    for j, (c0, width, tiles) in enumerate(chunks):
        units += [(j, t) for t in (range(width // P) if tiles is None else tiles)]
    last_unit = [max(i for i, u in enumerate(units) if u[0] == j) for j in range(len(chunks))]
    by_scalar = [bool(on_scalar and on_scalar(i)) for i in range(len(units))]
    size = kt * max(width for _, width, _ in chunks)

    def bank(i):
        return core.ps[:, i % banks, :]

    with ExitStack() as mem:
        xs = [core.sb(mem, f"{what}_x{n}", [P, kt, tokens], F32R) for n in ("high", "low")]
        raw = core.sb(mem, f"{what}_w", [P, STAGES, size])
        parts = [core.sb(mem, f"{what}_w{n}", [P, STAGES, size], F32R) for n in ("high", "low")]

        def slot(buffer, j):
            return buffer[:, j % STAGES, 0:kt * chunks[j][1]].rearrange("p (k n) -> p k n", k=kt)

        with core.stage(f"{what}_multiplied", f"{what}_read_v", f"{what}_read_s", f"{what}_order_v",
                        f"{what}_order_s", f"{what}_x_high", f"{what}_x_low", f"{what}_high", f"{what}_low",
                        *[f"{what}_landed{s}" for s in range(STAGES)]) as (
                block, multiplied, read_v, read_s, order_v, order_s, x_high, x_low, high, low, *landed):

            @block.sync
            def _(sp):
                for j, (c0, width, _) in enumerate(chunks):
                    if j >= STAGES:
                        sp.wait_ge(low, 2 * (j - STAGES + 1))
                    sp.dma_start(slot(raw, j), wv[:, :, c0:c0 + width]).then_inc(landed[j % STAGES], 16)

            @block.tensor
            def _(pe):
                pe.wait_ge(x_low, 1)
                for i, (j, t) in enumerate(units):
                    fresh = i == 0 or units[i - 1][0] != j
                    if i >= banks:
                        r = i - banks
                        if by_scalar[r]:
                            pe.wait_ge(read_s, sum(by_scalar[:r + 1]))
                        else:
                            pe.wait_ge(read_v, r + 1 - sum(by_scalar[:r + 1]))
                    _, width, tiles = chunks[j]
                    for k in range(kt):
                        if fresh and k in (0, kh):
                            pe.wait_ge(low, 2 * j + 1 + (k > 0))
                        if tiles is None:
                            mm = split_product(nc, bank(i)[:, 0:tokens],
                                               [slot(a, j)[:, k, t * P:(t + 1) * P] for a in parts],
                                               [a[:, k, :] for a in xs], k == 0, k == kt - 1)
                        else:
                            mm = split_product(nc, bank(i)[:, 0:width], [a[:, k, t * P:(t + 1) * P] for a in xs],
                                               [slot(a, j)[:, k, :] for a in parts], k == 0, k == kt - 1)
                    mm.then_inc(multiplied, 1)

            @block.vector
            def _(dve):
                order = Order(dve, order_v)
                dve.wait_ge(x_high, 1)
                split_low(nc, xs[1][:, :, :], xT, xs[0][:, :, :]).then_inc(x_low, 1)

                def split(j):
                    for n, ks in enumerate(halves):
                        dve.wait_ge(high, 2 * j + n + 1)
                        if j >= STAGES and n == 0:
                            dve.wait_ge(multiplied, last_unit[j - STAGES] + 1)
                        split_low(nc, slot(parts[1], j)[:, ks, :], slot(raw, j)[:, ks, :],
                                  slot(parts[0], j)[:, ks, :]).then_inc(low, 1)

                def read(j):
                    for i, (jj, t) in enumerate(units):
                        if jj == j and not by_scalar[i]:
                            dve.wait_ge(multiplied, i + 1)
                            evacuate(j, t, bank(i), nc.vector, order).then_inc(read_v, 1)

                for j in range(len(chunks)):
                    if j >= STAGES:
                        read(j - STAGES)
                    split(j)
                for j in range(max(0, len(chunks) - STAGES), len(chunks)):
                    read(j)

            @block.scalar
            def _(act):
                order = Order(act, order_s)
                split_high(nc, xs[0][:, :, :], xT).then_inc(x_high, 1)

                def split(j):
                    act.wait_ge(landed[j % STAGES], 16 * (j // STAGES + 1))
                    for n, ks in enumerate(halves):
                        if j >= STAGES and n == 0:
                            act.wait_ge(multiplied, last_unit[j - STAGES] + 1)
                        split_high(nc, slot(parts[0], j)[:, ks, :], slot(raw, j)[:, ks, :]).then_inc(high, 1)

                def read(j):
                    for i, (jj, t) in enumerate(units):
                        if jj == j and by_scalar[i]:
                            act.wait_ge(multiplied, i + 1)
                            evacuate(j, t, bank(i), nc.scalar, order).then_inc(read_s, 1)

                for j in range(len(chunks)):
                    if j >= STAGES:
                        read(j - STAGES)
                    split(j)
                for j in range(max(0, len(chunks) - STAGES), len(chunks)):
                    read(j)


def load(core, what, pairs):
    with core.stage(f"{what}_landed") as (block, landed):
        @block.sync
        def _(sp):
            for dst, src in pairs:
                sp.dma_start(dst, src).then_inc(landed, 16)
            sp.wait_ge(landed, 16 * len(pairs))


def inverse_rms(core, what, parts, out, junk, width, eps=EPS):
    nc = core.nc
    n = len(parts)
    with core.stage(f"{what}_squared", f"{what}_meaned", f"{what}_rooted", f"{what}_done") as (
            block, squared, meaned, rooted, done):
        @block.scalar
        def _(act):
            order = Order(act, squared)
            for i, part in enumerate(parts):
                order(nc.scalar.activation(junk[:, 0:width], part, ACT.Square, accum_out=out[:, i:i + 1]))
            act.wait_ge(meaned, 1)
            nc.scalar.activation(out[:, 0:n], out[:, 0:n], ACT.Sqrt).then_inc(rooted, 1)

        @block.vector
        def _(dve):
            dve.wait_ge(squared, n)
            nc.vector.tensor_scalar(out[:, 0:n], out[:, 0:n], 1.0 / width, eps, ALU.mult, ALU.add)\
                .then_inc(meaned, 1)
            dve.wait_ge(rooted, 1)
            nc.vector.reciprocal(out[:, 0:n], out[:, 0:n]).then_inc(done, 1)


def head_inverse_rms(core, what, x, sq, out, tiles, heads, eps=EPS):
    nc = core.nc
    flat = out.rearrange("p t h -> p (t h)")
    with core.stage(f"{what}_order", f"{what}_meaned", f"{what}_rooted") as (block, own, meaned, rooted):
        @block.vector
        def _(dve):
            order = Order(dve, own)
            for t in range(tiles):
                order(nc.vector.tensor_tensor(sq[:, t], x[:, t], x[:, t], ALU.mult))
                order(nc.vector.tensor_reduce(out[:, t, :], sq[:, t], AX_X, ALU.add))
            nc.vector.tensor_scalar(flat, flat, 1.0 / HD, eps, ALU.mult, ALU.add).then_inc(meaned, 1)
            dve.wait_ge(rooted, 1)
            order(nc.vector.reciprocal(flat, flat))

        @block.scalar
        def _(act):
            act.wait_ge(meaned, 1)
            nc.scalar.activation(flat, flat, ACT.Sqrt).then_inc(rooted, 1)


def norm_transposed(core, what, ident, x, hT, at, gain, shift, mem_junk):
    nc = core.nc
    rstd, xn = mem_junk
    inverse_rms(core, f"{what}_rms", [x[:, t, :] for t in range(TT)], rstd, xn[:, 0, :], DM)
    with core.stage(f"{what}_scaled") as (block, scaled):
        @block.vector
        def _(dve):
            nc.vector.tensor_scalar(xn[:, 0, :], x[:, 0, :], rstd[:, 0:1], None, ALU.mult).then_inc(scaled, 1)

        @block.scalar
        def _(act):
            nc.scalar.activation(xn[:, 1, :], x[:, 1, :], ACT.Copy, scale=rstd[:, 1:2]).then_inc(scaled, 1)

    def turn(i, bank):
        for t in range(TT):
            ins = nc.tensor.transpose(bank[:, t * P:(t + 1) * P], xn[:, t, i * P:(i + 1) * P], ident)
        return ins

    def out(i, bank, eng, order):
        return copy(nc, eng, hT[:, i, at:at + SEQ], bank[:, 0:SEQ], gain[:, i:i + 1], shift[:, i:i + 1])

    products(core, f"{what}_turn", KD, turn, out, odd)


def modulation(core, what, w, c, bias, mod, ones, widths):
    nc = core.nc
    n = 6 * DM // 512
    slots = 4
    wv = w.rearrange("(k p) n -> p k n", p=P)
    jobs = [(j, v) for j in range(n) for v in range(len(widths)) if 512 * j < widths[v]]
    with ExitStack() as mem:
        raw = core.sb(mem, f"{what}_w", [P, slots, KD, 512])
        acc = core.sb(mem, f"{what}_acc", [P, len(widths), 6 * DM])
        with core.stage(f"{what}_silu", f"{what}_order", f"{what}_summed", f"{what}_multiplied", f"{what}_added",
                        *[f"{what}_landed{s}" for s in range(slots)]) as (
                block, silu, own, summed, multiplied, added, *landed):
            @block.scalar
            def _(act):
                nc.scalar.activation(c, c, ACT.Silu).then_inc(silu, 1)

            @block.sync
            def _(sp):
                for j in range(n):
                    if j >= slots:
                        sp.wait_ge(summed, 1 + max(i for i, job in enumerate(jobs) if job[0] == j - slots))
                    sp.dma_start(raw[:, j % slots], wv[:, :, j * 512:(j + 1) * 512]).then_inc(landed[j % slots], 16)

            @block.vector
            def _(dve):
                order = Order(dve, own)
                dve.wait_ge(silu, 1)
                for j, v in jobs:
                    dve.wait_ge(landed[j % slots], 16 * (j // slots + 1))
                    a = acc[:, v, j * 512:(j + 1) * 512]
                    order(nc.vector.tensor_scalar(a, raw[:, j % slots, 0, :], c[:, v, 0:1], None, ALU.mult))
                    for k in range(1, KD):
                        ins = nc.vector.scalar_tensor_tensor(out=a, in0=raw[:, j % slots, k, :],
                                                             scalar=c[:, v, k:k + 1], in1=a, op0=ALU.mult,
                                                             op1=ALU.add)
                        if k < KD - 1:
                            order(ins)
                    ins.then_inc(summed, 1)
                dve.wait_ge(multiplied, len(jobs))
                for v, width in enumerate(widths):
                    m = width // P
                    nc.vector.tensor_tensor(mod[:, 0:m, v], core.ps[:, v, 0:m], bias[:, 0:m], ALU.add)\
                        .then_inc(added, 1)

            @block.tensor
            def _(pe):
                for i, (j, v) in enumerate(jobs):
                    pe.wait_ge(summed, i + 1)
                    for m in range(4 * j, 4 * j + 4):
                        mm = nc.tensor.matmul(core.ps[:, v, m:m + 1], acc[:, v, m * P:(m + 1) * P], ones[:, 0:1],
                                              start=True, stop=True)
                    mm.then_inc(multiplied, 1)


def spread_rows(core, what, ident, ones, cols, diag, out):
    nc = core.nc
    with core.stage(f"{what}_diag") as (block, made):
        @block.vector
        def _(dve):
            nc.vector.tensor_tensor(diag, ident.unsqueeze(1).to_broadcast([P, KD, P]),
                                    cols.unsqueeze(2).to_broadcast([P, KD, P]), ALU.mult).then_inc(made, 1)

    def mult(i, bank):
        for k in range(4):
            mm = nc.tensor.matmul(bank[:, k * P:(k + 1) * P], ones, diag[:, 4 * i + k, :], start=True, stop=True)
        return mm

    def out_(i, bank, eng, order):
        return copy(nc, eng, out[:, i * 512:(i + 1) * 512], bank)

    products(core, f"{what}_spread", 2, mult, out_, odd)


def gains(core, what, mod, v, norm, out, at_scale):
    nc = core.nc
    with core.stage(f"{what}_made") as (block, made):
        @block.vector
        def _(dve):
            nc.vector.scalar_tensor_tensor(out=out, in0=mod[:, at_scale:at_scale + KD, v], scalar=1.0, in1=norm,
                                           op0=ALU.add, op1=ALU.mult).then_inc(made, 1)


def attention(core, what, mem, ident, heads, keys, d, qT, kT, scale, mask, masked_keys, value, out, scratch):
    nc = core.nc
    n = heads * TT
    kt = keys // P
    s, pT = (a.rearrange("p (n k) -> p n k", n=n) for a in scratch)
    top = core.sb(mem, f"{what}_top", [P, n])
    total = core.sb(mem, f"{what}_total", [P, n])

    def score(i, bank):
        t, h = divmod(i, heads)
        return nc.tensor.matmul(bank[:, 0:keys], qT(h, t), kT(h), start=True, stop=True)

    def masked(i, bank, eng, order):
        t, h = divmod(i, heads)
        ins = nc.vector.scalar_tensor_tensor(out=s[:, i, 0:masked_keys], in0=bank[:, 0:masked_keys], scalar=scale,
                                             in1=mask(h, t), op0=ALU.mult, op1=ALU.add)
        if masked_keys < keys:
            order(ins)
            ins = nc.vector.tensor_scalar(s[:, i, masked_keys:keys], bank[:, masked_keys:keys], scale, None, ALU.mult)
        return ins

    products(core, f"{what}_score", n, score, masked)

    with core.stage(f"{what}_topped", f"{what}_exped", f"{what}_summed") as (block, topped, exped, summed):
        @block.vector
        def _(dve):
            for i in range(n):
                nc.vector.tensor_reduce(top[:, i:i + 1], s[:, i, :], AX_X, ALU.max, negate=True).then_inc(topped, 1)
            dve.wait_ge(exped, n)
            nc.vector.reciprocal(total[:, :], total[:, :]).then_inc(summed, 1)

        @block.scalar
        def _(act):
            for i in range(n):
                act.wait_ge(topped, i + 1)
                nc.scalar.activation(s[:, i, :], s[:, i, :], ACT.Exp, bias=top[:, i:i + 1],
                                     accum_out=total[:, i:i + 1]).then_inc(exped, 1)

    def turn(i, bank):
        for k in range(kt):
            ins = nc.tensor.transpose(bank[:, k * P:(k + 1) * P], s[:, i, k * P:(k + 1) * P], ident)
        return ins

    def turned(i, bank, eng, order):
        return copy(nc, eng, pT[:, i, :], bank[:, 0:keys])

    products(core, f"{what}_turn", n, turn, turned, odd)

    def weigh(i, bank):
        for h in range(heads):
            for k in range(kt):
                mm = nc.tensor.matmul(bank[:, h * HD:(h + 1) * HD], pT[:, i * heads + h, k * P:(k + 1) * P],
                                      value(h, k), start=(k == 0), stop=(k == kt - 1))
        return mm

    def normed(i, bank, eng, order):
        return nc.vector.tensor_tensor(out(i), bank.rearrange("p (h d) -> p h d", d=HD),
                                       total[:, i * heads:(i + 1) * heads].unsqueeze(2)
                                       .to_broadcast([P, heads, HD]), ALU.mult)

    products(core, f"{what}_weigh", TT, weigh, normed)


def turn_features(core, what, ident, src, tiles, yT, scale=None):
    nc = core.nc

    def turn(i, bank):
        for t in range(TT):
            ins = nc.tensor.transpose(bank[:, t * P:(t + 1) * P], src[:, t, i * P:(i + 1) * P], ident)
        return ins

    def out(i, bank, eng, order):
        return copy(nc, eng, yT[:, i, :], bank[:, 0:SEQ], None if scale is None else scale[:, i:i + 1])

    products(core, what, tiles, turn, out, odd)


def rotary_tables(core, mem, pos, inv, cos, sin):
    nc = core.nc
    n = ROPE // 2
    posf = core.sb(mem, "posf", [P, TT])
    ang = core.sb(mem, "ang", [P, TT, n])
    turns = core.sb(mem, "turns", [P, TT, n])
    over = core.sb(mem, "over", [P, TT, n])
    two_pi = 2 * np.pi
    c1 = 6.28125
    c2 = float(np.float32(np.round((two_pi - c1) * 2 ** 21) / 2 ** 21))
    c3 = float(two_pi - c1 - c2)
    pi = 3.1415925
    magic = 12582912.0
    with core.stage("rotary_order", "rotary_reduced", "rotary_done") as (block, own, reduced, done):
        @block.vector
        def _(dve):
            order = Order(dve, own)
            order(nc.vector.tensor_copy(posf[:, :], pos))
            order(nc.vector.tensor_tensor(ang[:, :, :], posf[:, :].unsqueeze(2).to_broadcast([P, TT, n]),
                                          inv.unsqueeze(1).to_broadcast([P, TT, n]), ALU.mult))
            order(nc.vector.tensor_scalar(turns[:, :, :], ang[:, :, :], 1.0 / two_pi, None, ALU.mult))
            order(nc.vector.tensor_scalar(turns[:, :, :], turns[:, :, :], magic, None, ALU.add))
            order(nc.vector.tensor_scalar(turns[:, :, :], turns[:, :, :], magic, None, ALU.subtract))
            for c in (c1, c2, c3):
                order(nc.vector.scalar_tensor_tensor(out=ang[:, :, :], in0=turns[:, :, :], scalar=-c,
                                                     in1=ang[:, :, :], op0=ALU.mult, op1=ALU.add))
            order(nc.vector.tensor_scalar(sin, ang[:, :, :], pi, -pi, ALU.min, ALU.max))
            order(nc.vector.tensor_scalar(ang[:, :, :], ang[:, :, :], np.pi / 2, None, ALU.add))
            order(nc.vector.tensor_scalar(over[:, :, :], ang[:, :, :], np.pi, two_pi, ALU.is_gt, ALU.mult))
            order(nc.vector.tensor_tensor(ang[:, :, :], ang[:, :, :], over[:, :, :], ALU.subtract))
            nc.vector.tensor_scalar(cos, ang[:, :, :], pi, -pi, ALU.min, ALU.max).then_inc(reduced, 1)

        @block.scalar
        def _(act):
            act.wait_ge(reduced, 1)
            nc.scalar.activation(sin, sin, ACT.Sin).then_inc(done, 1)
            nc.scalar.activation(cos, cos, ACT.Sin).then_inc(done, 1)


def rotate(nc, order, x1, x2, cos, sin, tmp):
    a, b, c = tmp
    order(nc.vector.tensor_tensor(a, x2, sin, ALU.mult))
    order(nc.vector.tensor_tensor(b, x1, sin, ALU.mult))
    order(nc.vector.tensor_tensor(c, x1, cos, ALU.mult))
    order(nc.vector.tensor_tensor(x1, c, a, ALU.subtract))
    order(nc.vector.tensor_tensor(c, x2, cos, ALU.mult))
    order(nc.vector.tensor_tensor(x2, c, b, ALU.add))


def mla(core, layer_in, k, lat, yT):
    nc, ident = core.nc, k["ident"]
    with ExitStack() as mem:
        rs = core.sb(mem, "lat_rs", [P, 4])
        latT = core.sb(mem, "latT", [P, 5, SEQ])
        q_space = core.sb(mem, "q", [P, TT * HEADS * QK])
        q = q_space[:, :].rearrange("p (t h d) -> p t h d", t=TT, h=HEADS)
        kk = core.sb(mem, "kk", [P, TT, HEADS, QK])
        v = core.sb(mem, "v", [P, TT, HEADS, VH])
        qkT = core.sb(mem, "qkT", [QK, HEADS, 4 * P])
        tmp = core.sb(mem, "rot", [P, 3, HEADS, ROPE // 2])
        junk = q_space[:, 0:Q_LORA]
        y = q_space[:, 0:TT * HEADS * VH].rearrange("p (t h d) -> p t h d", t=TT, h=HEADS)
        inverse_rms(core, "cq_rms", [lat[:, t, 0:Q_LORA] for t in range(TT)], rs[:, 0:2], junk, Q_LORA)
        inverse_rms(core, "ckv_rms", [lat[:, t, Q_LORA:Q_LORA + KV_LORA] for t in range(TT)], rs[:, 2:4],
                    junk, KV_LORA)
        with core.stage("lat_scaled") as (block, scaled):
            @block.vector
            def _(dve):
                for t in range(TT):
                    for j, (a, b) in enumerate(((0, Q_LORA), (Q_LORA, Q_LORA + KV_LORA))):
                        nc.vector.tensor_scalar(lat[:, t, a:b], lat[:, t, a:b], rs[:, 2 * j + t:2 * j + t + 1],
                                                None, ALU.mult).then_inc(scaled, 1)
        turn_features(core, "lat_turn", ident, lat, 5, latT, k["lat_gain"])

        def q_out(j, t, bank, eng, order):
            return copy(nc, eng, q[:, t, 4 * j:4 * j + 4, :], bank[:, 0:4 * QK].rearrange("p (h d) -> p h d", d=QK))
        linear(core, "uq", latT[:, 0:3, :], layer_in("w_uq"),
               [(0, 4 * QK, range(TT)), (4 * QK, 4 * QK, range(TT))], q_out, odd)

        def kv_out(j, t, bank, eng, order):
            kv = bank.rearrange("p (h d) -> p h d", d=NOPE + VH)
            order(copy(nc, eng, kk[:, t, 4 * j:4 * j + 4, 0:NOPE], kv[:, :, 0:NOPE]))
            return copy(nc, eng, v[:, t, 4 * j:4 * j + 4, :], kv[:, :, NOPE:])
        linear(core, "ukv", latT[:, 3:5, :], layer_in("w_ukv"),
               [(0, 512, range(TT)), (512, 512, range(TT))], kv_out, odd)

        with core.stage("rope_order") as (block, own):
            @block.vector
            def _(dve):
                order = Order(dve, own)
                half = ROPE // 2
                for t in range(TT):
                    cos = k["cos"][:, t, :].unsqueeze(1).to_broadcast([P, HEADS, half])
                    sin = k["sin"][:, t, :].unsqueeze(1).to_broadcast([P, HEADS, half])
                    rotate(nc, order, q[:, t, :, NOPE:NOPE + half], q[:, t, :, NOPE + half:QK], cos, sin,
                           [tmp[:, i] for i in range(3)])
                    kr = lat[:, t, Q_LORA + KV_LORA:LATENT]
                    rotate(nc, order, kr[:, 0:half], kr[:, half:ROPE], k["cos"][:, t, :], k["sin"][:, t, :],
                           [tmp[:, i, 0] for i in range(3)])
                    order(nc.vector.tensor_copy(kk[:, t, :, NOPE:QK],
                                                kr.unsqueeze(1).to_broadcast([P, HEADS, ROPE])))

        def turn(h, bank):
            for t in range(TT):
                nc.tensor.transpose(bank[0:QK, t * P:(t + 1) * P], q[:, t, h, :], ident)
                ins = nc.tensor.transpose(bank[0:QK, (2 + t) * P:(3 + t) * P], kk[:, t, h, :], ident)
            return ins

        def turned(h, bank, eng, order):
            return copy(nc, eng, qkT[:, h, :], bank[0:QK, :])
        products(core, "qk_turn", HEADS, turn, turned, odd)

        attention(core, "mla", mem, ident, HEADS, SEQ, QK,
                  lambda h, t: qkT[:, h, t * P:(t + 1) * P], lambda h: qkT[:, h, SEQ:2 * SEQ], QK ** -0.5,
                  lambda h, t: k["mla_mask"][:, t * SEQ:(t + 1) * SEQ], SEQ,
                  lambda h, j: v[:, j, h, :], lambda t: y[:, t],
                  [core.sb(mem, n, [P, HEADS * TT * SEQ])[:, :] for n in ("mla_s", "mla_pT")])
        turn_features(core, "mla_y_turn", ident, y.rearrange("p t h d -> p t (h d)"), 4, yT)


def mlstm(core, k, qk, gates, vx, og, yT, fv):
    nc, ident = core.nc, k["ident"]
    with ExitStack() as mem:
        conv = core.sb(mem, "conv", [P, KD, SEQ])
        g = [core.sb(mem, f"gate{i}", [HEADS, SEQ]) for i in range(5)]
        aT = core.sb(mem, "aT", [P, TT, HEADS])
        floor = core.sb(mem, "floor", [P, TT, HEADS])
        wT = core.sb(mem, "wT", [P, 2, 384])
        pT = core.sb(mem, "pT", [P, HEADS, 384])
        hn = core.sb(mem, "hn", [P, TT, HEADS, HD + 1])
        den = core.sb(mem, "den", [P, TT, HEADS])
        h = core.sb(mem, "h", [P, TT, HEADS, HD])
        sq = conv[:, 0:4, :].rearrange("p a b -> p (a b)").rearrange("p (t h d) -> p t h d", t=TT, h=HEADS)
        rs = core.sb(mem, "h_rs", [P, TT, HEADS])
        with core.stage("conv_order", "conv_tile", "conv_silu") as (block, own, tile_done, silu):
            @block.vector
            def _(dve):
                order = Order(dve, own)
                for j in range(KD):
                    w = fv["conv_w"]
                    order(nc.vector.tensor_scalar(conv[:, j, :], qk[:, j, 0:SEQ], w[:, j:j + 1],
                                                  fv["conv_b"][:, j:j + 1], ALU.mult, ALU.add))
                    for i in range(1, 4):
                        ins = nc.vector.scalar_tensor_tensor(out=conv[:, j, :], in0=qk[:, j, i:i + SEQ],
                                                             scalar=w[:, 8 * i + j:8 * i + j + 1],
                                                             in1=conv[:, j, :], op0=ALU.mult, op1=ALU.add)
                        if i < 3:
                            order(ins)
                    ins.then_inc(tile_done, 1)

            @block.scalar
            def _(act):
                for j in range(KD):
                    act.wait_ge(tile_done, j + 1)
                    nc.scalar.activation(conv[:, j, :], conv[:, j, :], ACT.Silu).then_inc(silu, 1)
        i_, f_ = gates
        with core.stage("gate_order", "gate_abs", "gate_ln", "gate_exp") as (block, own, absed, lned, exped):
            @block.vector
            def _(dve):
                order = Order(dve, own)
                order(nc.vector.tensor_scalar(i_[:, :], i_[:, :], fv["gate_b"][0:HEADS, 0:1], None, ALU.add))
                order(nc.vector.tensor_scalar(f_[:, :], f_[:, :], fv["gate_b"][0:HEADS, 1:2], None, ALU.add))
                order(nc.vector.tensor_scalar(g[0][:, :], f_[:, :], -1.0, None, ALU.mult))
                nc.vector.tensor_tensor(g[0][:, :], g[0][:, :], f_[:, :], ALU.min).then_inc(absed, 1)
                dve.wait_ge(lned, 2)
                order(nc.vector.scalar_tensor_tensor(out=g[1][:, :], in0=f_[:, :], scalar=0.0, in1=g[0][:, :],
                                                     op0=ALU.min, op1=ALU.subtract))
                F, M = g[2], g[4]
                order(nc.vector.tensor_tensor_scan(F[:, :], k["ones_row"][0:HEADS, :], g[1][:, :], 0.0,
                                                   ALU.mult, ALU.add))
                order(nc.vector.tensor_tensor(g[3][:, :], i_[:, :], F[:, :], ALU.subtract))
                order(nc.vector.tensor_tensor_scan(M[:, :], k["ones_row"][0:HEADS, :], g[3][:, :], 0.0,
                                                   ALU.mult, ALU.max))
                order(nc.vector.tensor_tensor(F[:, :], F[:, :], M[:, :], ALU.add))
                order(nc.vector.tensor_scalar(F[:, :], F[:, :], -1.0, 88.0, ALU.mult, ALU.min))
                order(nc.vector.tensor_scalar(M[:, :], M[:, :], -1.0, None, ALU.mult))
                ins = nc.vector.tensor_copy(g[0][:, :], F[:, :])
                ins.then_inc(absed, 1)

            @block.scalar
            def _(act):
                act.wait_ge(absed, 1)
                nc.scalar.activation(g[0][:, :], g[0][:, :], ACT.Exp).then_inc(lned, 1)
                act.wait_ge(lned, 1)
                nc.scalar.activation(g[0][:, :], g[0][:, :], ACT.Ln, bias=k["ones"][0:HEADS, 0:1]).then_inc(lned, 1)
                act.wait_ge(absed, 2)
                nc.scalar.activation(g[0][:, :], g[0][:, :], ACT.Exp).then_inc(exped, 1)
        a, minus_m = g[3], g[4]

        def turn(i, bank):
            src = (a, g[0])[i]
            for t in range(TT):
                ins = nc.tensor.transpose(bank[:, t * HEADS:(t + 1) * HEADS], src[:, t * P:(t + 1) * P],
                                          ident[0:HEADS, 0:HEADS])
            return ins

        def turned(i, bank, eng, order):
            return copy(nc, eng, (aT, floor)[i][:, :, :], bank[:, 0:2 * HEADS].rearrange("p (t h) -> p t h", t=TT))
        products(core, "gate_turn", 2, turn, turned)

        with core.stage("mw_spread", "mw_masked", "mw_exped", "mw_scored", "mw_weighed") as (
                block, spread, maskd, exped, scored, weighed):
            @block.tensor
            def _(pe):
                for hh in range(HEADS):
                    rows = slice(64 * (hh % 2), 64 * (hh % 2) + 64)
                    if hh >= 2:
                        pe.wait_ge(weighed, hh - 1)
                    nc.tensor.matmul(core.ps[:, hh % 2, 0:SEQ], k["sel"][0:HEADS, hh * P:(hh + 1) * P],
                                     minus_m[:, :], start=True, stop=True).then_inc(spread, 1)
                    q_, k_ = conv[rows, hh // 2, :], conv[rows, 4 + hh // 2, :]
                    nc.tensor.matmul(core.ps[:, 2 + hh % 2, 0:256], k_[:, 0:P], q_, start=True, stop=True)
                    nc.tensor.matmul(core.ps[:, 2 + hh % 2, 256:384], k_[:, P:SEQ], q_[:, P:SEQ],
                                     start=True, stop=True).then_inc(scored, 1)

            @block.vector
            def _(dve):
                def weigh(hh):
                    dve.wait_ge(exped, 2 * hh + 2)
                    dve.wait_ge(scored, hh + 1)
                    nc.vector.scalar_tensor_tensor(out=pT[:, hh, :], in0=core.ps[:, 2 + hh % 2, 0:384],
                                                   scalar=HD ** -0.5, in1=wT[:, hh % 2, :],
                                                   op0=ALU.mult, op1=ALU.mult).then_inc(weighed, 1)
                for hh in range(HEADS):
                    dve.wait_ge(spread, hh + 1)
                    if hh >= 2:
                        dve.wait_ge(weighed, hh - 1)
                    b = core.ps[:, hh % 2, :]
                    nc.vector.tensor_tensor(wT[:, hh % 2, 0:256], b[:, 0:256], k["ml_mask"], ALU.add)\
                        .then_inc(maskd, 1)
                    nc.vector.tensor_tensor(wT[:, hh % 2, 256:384], b[:, P:SEQ], k["ml_mask"][:, 0:P], ALU.add)\
                        .then_inc(maskd, 1)
                    if hh >= 1:
                        weigh(hh - 1)
                weigh(HEADS - 1)

            @block.scalar
            def _(act):
                for hh in range(HEADS):
                    act.wait_ge(maskd, 2 * hh + 2)
                    for t, (c0, c1) in enumerate(((0, 256), (256, 384))):
                        nc.scalar.activation(wT[:, hh % 2, c0:c1], wT[:, hh % 2, c0:c1], ACT.Exp,
                                             bias=aT[:, t, hh:hh + 1]).then_inc(exped, 1)

        def total(i, bank):
            t, half = divmod(i, 2)
            for j in range(4):
                hh = 4 * half + j
                o = bank[:, j * (HD + 1):(j + 1) * (HD + 1)]
                if t == 0:
                    mm = nc.tensor.matmul(o, pT[:, hh, 0:P], vx[:, 0, hh, :], start=True, stop=True)
                else:
                    nc.tensor.matmul(o, pT[:, hh, P:2 * P], vx[:, 0, hh, :], start=True, stop=False)
                    mm = nc.tensor.matmul(o, pT[:, hh, 2 * P:3 * P], vx[:, 1, hh, :], start=False, stop=True)
            return mm

        def totalled(i, bank, eng, order):
            t, half = divmod(i, 2)
            return copy(nc, eng, hn[:, t, 4 * half:4 * half + 4, :],
                        bank[:, 0:4 * (HD + 1)].rearrange("p (h d) -> p h d", d=HD + 1))
        products(core, "ml_total", 4, total, totalled, odd)

        with core.stage("hdiv_order", "og_done") as (block, own, og_done):
            @block.vector
            def _(dve):
                order = Order(dve, own)
                order(nc.vector.tensor_scalar(den[:, :, :], hn[:, :, :, HD], -1.0, None, ALU.mult))
                order(nc.vector.tensor_tensor(den[:, :, :], den[:, :, :], hn[:, :, :, HD], ALU.max))
                order(nc.vector.tensor_tensor(den[:, :, :], den[:, :, :], floor[:, :, :], ALU.max))
                order(nc.vector.reciprocal(den[:, :, :], den[:, :, :]))
                for t in range(TT):
                    order(nc.vector.tensor_tensor(h[:, t], hn[:, t, :, 0:HD],
                                                  den[:, t, :].unsqueeze(2).to_broadcast([P, HEADS, HD]), ALU.mult))

            @block.scalar
            def _(act):
                nc.scalar.activation(og, og, ACT.Sigmoid).then_inc(og_done, 1)
        head_inverse_rms(core, "h_rms", h, sq, rs[:, :, :], TT, HEADS)
        with core.stage("hnorm_order") as (block, own):
            @block.vector
            def _(dve):
                order = Order(dve, own)
                for t in range(TT):
                    order(nc.vector.tensor_tensor(h[:, t], h[:, t],
                                                  rs[:, t, :].unsqueeze(2).to_broadcast([P, HEADS, HD]), ALU.mult))
                    order(nc.vector.tensor_tensor(h[:, t], h[:, t],
                                                  og[:, t, :].rearrange("p (h d) -> p h d", d=HD), ALU.mult))
        turn_features(core, "ml_y_turn", ident, h[:, :, :, :].rearrange("p t h d -> p t (h d)"), 4, yT,
                      fv["head_norm"])


def mixer(core, layer_in, k, fv, hT, g_row, x):
    nc = core.nc
    with ExitStack() as mem:
        og = core.sb(mem, "og", [P, TT, ML_W])
        yT = [core.sb(mem, f"yT{i}", [P, 4, SEQ]) for i in range(2)]
        with ExitStack() as inner:
            lat = core.sb(inner, "lat", [P, TT, LATENT])
            qk = core.sb(inner, "qk", [P, KD, SEQ + 3])
            vx = core.sb(inner, "vx", [P, TT, HEADS, HD + 1])
            gi, gf = (core.sb(inner, n, [HEADS, SEQ]) for n in ("gi", "gf"))
            wg = core.sb(inner, "wg", [P, KD, 2 * HEADS])
            with core.stage("pad_set", "gate_w") as (block, pad_set, gate_w):
                @block.gpsimd
                def _(pool):
                    nc.gpsimd.memset(qk[:, :, 0:3], 0.0).then_inc(pad_set, 1)
                    nc.gpsimd.memset(vx[:, :, :, HD:HD + 1], 1.0).then_inc(pad_set, 1)
                    pool.wait_ge(pad_set, 2)

                @block.sync
                def _(sp):
                    sp.dma_start(wg[:, :, :], layer_in("w_in").rearrange("(k p) n -> p k n", p=P)[
                        :, :, GATE_AT:BR_AT]).then_inc(gate_w, 16)
                    sp.wait_ge(gate_w, 16)
            both = range(TT)
            spans = [(0, 512, both), (512, LATENT - 512, both), (ML_AT, 512, None), (ML_AT + 512, 512, None),
                     (ML_AT + 1024, 512, both), (ML_AT + 1536, 512, both)]

            def out(j, t, bank, eng, order):
                c0, width, _ = spans[j]
                if j < 2:
                    return copy(nc, eng, lat[:, t, c0:c0 + width], bank[:, 0:width])
                if j < 4:
                    return copy(nc, eng, qk[:, 4 * (j - 2) + t, 3:], bank[:, 0:SEQ])
                if j == 4:
                    return copy(nc, eng, vx[:, t, :, 0:HD], bank.rearrange("p (h d) -> p h d", d=HD))
                return copy(nc, eng, og[:, t, :], bank)
            linear(core, "proj", hT, layer_in("w_in"), spans, out, odd)

            def gate(i, bank):
                for kt in range(KD):
                    mm = nc.tensor.matmul(bank[0:HEADS, 0:SEQ], wg[:, kt, i * HEADS:(i + 1) * HEADS], hT[:, kt, :],
                                          start=(kt == 0), stop=(kt == KD - 1))
                return mm

            def gated(i, bank, eng, order):
                return copy(nc, eng, (gi, gf)[i][:, :], bank[0:HEADS, 0:SEQ])
            products(core, "gates", 2, gate, gated)
            mla(core, layer_in, k, lat, yT[0])
            mlstm(core, k, qk, (gi, gf), vx, og[:, :, :], yT[1], fv)
        with ExitStack() as inner:
            m = core.sb(inner, "merged", [P, TT, DM])
            tmp = core.sb(inner, "merge_tmp", [P, TT, 512])
            mT = core.sb(inner, "mergedT", [P, KD, SEQ])
            br = core.sb(inner, "br", [P, TT, 2 * DM])

            def gate_out(j, t, bank, eng, order):
                return nc.scalar.activation(br[:, t, j * 512:(j + 1) * 512], bank, ACT.Sigmoid)
            linear(core, "branch_gates", hT, layer_in("w_in"),
                   [(BR_AT + 512 * j, 512, both) for j in range(4)], gate_out, lambda i: True)
            for b, name in enumerate(("w_br_mla", "w_br_mlstm")):
                def out(j, t, bank, eng, order, b=b):
                    dst = m[:, t, j * 512:(j + 1) * 512]
                    gate = br[:, t, b * DM + j * 512:b * DM + (j + 1) * 512]
                    if b == 0:
                        return nc.vector.tensor_tensor(dst, bank, gate, ALU.mult)
                    order(nc.vector.tensor_tensor(tmp[:, t, :], bank, gate, ALU.mult))
                    return nc.vector.tensor_tensor(dst, dst, tmp[:, t, :], ALU.add)
                linear(core, f"branch{b}", yT[b], layer_in(name),
                       [(0, 512, both), (512, 512, both)], out)
            turn_features(core, "merge_turn", k["ident"], m, KD, mT)
            residual(core, "w_out", mT, layer_in("w_out"), g_row, tmp, x)


def residual(core, what, yT, w, g_row, tmp, x):
    nc = core.nc

    def out(j, t, bank, eng, order):
        dst = x[:, t, j * 512:(j + 1) * 512]
        order(nc.vector.tensor_tensor(tmp[:, t, :], bank, g_row[:, j * 512:(j + 1) * 512], ALU.mult))
        return nc.vector.tensor_tensor(dst, dst, tmp[:, t, :], ALU.add)
    linear(core, what, yT, w, [(0, 512, range(TT)), (512, 512, range(TT))], out)


def ffn(core, layer_in, k, fv, hT, g_row, x):
    nc = core.nc
    pairs = 2
    n_chunks = FF_TILES // pairs
    width = 2 * pairs * P
    kh = KD // 2
    w = layer_in("ffn_w_up").rearrange("(k p) n -> p k n", p=P)
    with ExitStack() as mem:
        hid = [core.sb(mem, f"hid_{n}", [P, FF_TILES, SEQ], F32R) for n in ("high", "low")]
        with ExitStack() as inner:
            xs = [core.sb(inner, f"up_x{n}", [P, KD, SEQ], F32R) for n in ("high", "low")]
            raw = core.sb(inner, "up_w", [P, STAGES, KD, width])
            parts = [core.sb(inner, f"up_w{n}", [P, STAGES, KD, width], F32R) for n in ("high", "low")]
            u = core.sb(inner, "u", [P, 4, 2 + SEQ])
            cv = core.sb(inner, "cv", [P, 4, SEQ])

            with core.stage("up_pad", "up_multiplied", "up_copied", "up_conv", "up_gelu", "up_order", "up_product",
                            "up_hid_high", "up_hid", "up_x_high", "up_x_low", "up_high", "up_low",
                            *[f"up_landed{s}" for s in range(STAGES)]) as (
                    block, padded, multiplied, copied, convolved, gelued, own, product_done, hid_high, hid_done,
                    x_high, x_low, high, low, *landed):
                @block.sync
                def _(sp):
                    for j in range(n_chunks):
                        if j >= STAGES:
                            sp.wait_ge(low, 2 * (j - STAGES + 1))
                        for s in range(2):
                            c0 = s * D_FF + j * pairs * P
                            sp.dma_start(raw[:, j % STAGES, :, s * pairs * P:(s + 1) * pairs * P],
                                         w[:, :, c0:c0 + pairs * P]).then_inc(landed[j % STAGES], 16)

                @block.gpsimd
                def _(pool):
                    nc.gpsimd.memset(u[:, :, 0:2], 0.0).then_inc(padded, 1)

                @block.tensor
                def _(pe):
                    pe.wait_ge(x_low, 1)
                    for n in range(2 * FF_TILES):
                        tile, side = divmod(n, 2)
                        j, i = divmod(tile, pairs)
                        if n >= 8:
                            pe.wait_ge(copied, n - 7)
                        col = side * pairs * P + i * P
                        for kt in range(KD):
                            if n % (2 * pairs) == 0 and kt in (0, kh):
                                pe.wait_ge(low, 2 * j + 1 + (kt > 0))
                            mm = split_product(nc, core.ps[:, n % 8, 0:SEQ],
                                               [a[:, j % STAGES, kt, col:col + P] for a in parts],
                                               [a[:, kt, :] for a in xs], kt == 0, kt == KD - 1)
                        mm.then_inc(multiplied, 1)

                @block.scalar
                def _(act):
                    def split(j):
                        act.wait_ge(landed[j % STAGES], 32 * (j // STAGES + 1))
                        if j >= STAGES:
                            act.wait_ge(multiplied, 2 * pairs * (j - STAGES + 1))
                        for ks in (slice(0, kh), slice(kh, KD)):
                            split_high(nc, parts[0][:, j % STAGES, ks, :], raw[:, j % STAGES, ks, :])\
                                .then_inc(high, 1)

                    def gelu(tile):
                        act.wait_ge(convolved, 2 * tile + 1)
                        nc.scalar.activation(cv[:, (2 * tile) % 4, :], cv[:, (2 * tile) % 4, :],
                                             ACT.Gelu_apprx_tanh).then_inc(gelued, 1)

                    def hidden(tile):
                        act.wait_ge(product_done, tile + 1)
                        split_high(nc, hid[0][:, tile, :], cv[:, (2 * tile) % 4, :]).then_inc(hid_high, 1)

                    split_high(nc, xs[0][:, :, :], hT).then_inc(x_high, 1)
                    act.wait_ge(padded, 1)
                    for j in range(STAGES):
                        split(j)
                    for n in range(2 * FF_TILES):
                        act.wait_ge(multiplied, n + 1)
                        if n >= 4:
                            act.wait_ge(convolved, n - 3)
                        nc.scalar.activation(u[:, n % 4, 2:], core.ps[:, n % 8, 0:SEQ], ACT.Copy).then_inc(copied, 1)
                        if n % 2 and n >= 3:
                            gelu(n // 2 - 1)
                            hidden(n // 2 - 1)
                        if n % (2 * pairs) == 2 * pairs - 1 and n // (2 * pairs) + STAGES < n_chunks:
                            split(n // (2 * pairs) + STAGES)
                    gelu(FF_TILES - 1)
                    hidden(FF_TILES - 1)

                @block.vector
                def _(dve):
                    order = Order(dve, own)

                    def split(j):
                        for n, ks in enumerate((slice(0, kh), slice(kh, KD))):
                            dve.wait_ge(high, 2 * j + n + 1)
                            split_low(nc, parts[1][:, j % STAGES, ks, :], raw[:, j % STAGES, ks, :],
                                      parts[0][:, j % STAGES, ks, :]).then_inc(low, 1)

                    def product(tile):
                        a = cv[:, (2 * tile) % 4, :]
                        dve.wait_ge(gelued, tile + 1)
                        nc.vector.tensor_tensor(a, a, cv[:, (2 * tile + 1) % 4, :], ALU.mult)\
                            .then_inc(product_done, 1)

                    def hidden(tile):
                        dve.wait_ge(hid_high, tile + 1)
                        split_low(nc, hid[1][:, tile, :], cv[:, (2 * tile) % 4, :], hid[0][:, tile, :])\
                            .then_inc(hid_done, 1)

                    dve.wait_ge(x_high, 1)
                    split_low(nc, xs[1][:, :, :], hT, xs[0][:, :, :]).then_inc(x_low, 1)
                    for j in range(STAGES):
                        split(j)
                    cw, cb = fv["ffn_conv_w"], fv["ffn_conv_b"]
                    for n in range(2 * FF_TILES):
                        tile, side = divmod(n, 2)
                        f = side * FF_TILES + tile
                        dve.wait_ge(copied, n + 1)
                        if n >= 4 and side == 0:
                            hidden(tile - 2)
                            dve.wait_ge(hid_done, tile - 1)
                        order(nc.vector.tensor_scalar(cv[:, n % 4, :], u[:, n % 4, 0:SEQ], cw[:, f:f + 1],
                                                      cb[:, f:f + 1], ALU.mult, ALU.add))
                        for i in (1, 2):
                            col = i * 2 * FF_TILES + f
                            ins = nc.vector.scalar_tensor_tensor(out=cv[:, n % 4, :], in0=u[:, n % 4, i:i + SEQ],
                                                                 scalar=cw[:, col:col + 1], in1=cv[:, n % 4, :],
                                                                 op0=ALU.mult, op1=ALU.add)
                            if i == 1:
                                order(ins)
                        ins.then_inc(convolved, 1)
                        if side == 1:
                            dve.wait_ge(convolved, n + 1)
                            if tile >= 1:
                                product(tile - 1)
                        if n % (2 * pairs) == 2 * pairs - 1 and n // (2 * pairs) + STAGES < n_chunks:
                            split(n // (2 * pairs) + STAGES)
                    product(FF_TILES - 1)
                    hidden(FF_TILES - 2)
                    hidden(FF_TILES - 1)
        with ExitStack() as inner:
            tmp = core.sb(inner, "down_tmp", [P, 512])
            half = DM // 2
            wd = layer_in("ffn_w_down").rearrange("(k p) n -> p k n", p=P)
            kts = 8
            raw = core.sb(inner, "down_w", [P, STAGES, kts, half])
            parts = [core.sb(inner, f"down_w{n}", [P, STAGES, kts, half], F32R) for n in ("high", "low")]
            chunks = [(c, k0, min(kts, FF_TILES - k0)) for c in range(2) for k0 in range(0, FF_TILES, kts)]

            with core.stage("down_multiplied", "down_chunk", "down_order", "down_high", "down_low",
                            *[f"down_landed{n}" for n in range(STAGES)]) as (
                    block, multiplied, chunk_done, own, high, low, *landed):
                @block.sync
                def _(sp):
                    for n, (c, k0, kn) in enumerate(chunks):
                        if n >= STAGES:
                            sp.wait_ge(low, n - STAGES + 1)
                        sp.dma_start(raw[:, n % STAGES, 0:kn], wd[:, k0:k0 + kn, c * half:(c + 1) * half])\
                            .then_inc(landed[n % STAGES], 16)

                @block.scalar
                def _(act):
                    for n, (c, k0, kn) in enumerate(chunks):
                        act.wait_ge(landed[n % STAGES], 16 * (n // STAGES + 1))
                        if n >= STAGES:
                            act.wait_ge(chunk_done, n - STAGES + 1)
                        split_high(nc, parts[0][:, n % STAGES, 0:kn], raw[:, n % STAGES, 0:kn]).then_inc(high, 1)

                @block.tensor
                def _(pe):
                    for n, (c, k0, kn) in enumerate(chunks):
                        pe.wait_ge(low, n + 1)
                        for t in range(TT):
                            for i in range(kn):
                                mm = split_product(nc, core.ps[:, 2 * c + t, :],
                                                   [a[:, k0 + i, t * P:(t + 1) * P] for a in hid],
                                                   [a[:, n % STAGES, i, :] for a in parts], k0 + i == 0,
                                                   k0 + i == FF_TILES - 1)
                            if k0 + kn == FF_TILES and t == 0:
                                mm.then_inc(multiplied, 1)
                        mm.then_inc(chunk_done, 1)

                @block.vector
                def _(dve):
                    order = Order(dve, own)
                    for n, (c, k0, kn) in enumerate(chunks):
                        dve.wait_ge(high, n + 1)
                        split_low(nc, parts[1][:, n % STAGES, 0:kn], raw[:, n % STAGES, 0:kn],
                                  parts[0][:, n % STAGES, 0:kn]).then_inc(low, 1)
                        if k0 + kn == FF_TILES:
                            for t in range(TT):
                                dst = x[:, t, c * half:(c + 1) * half]
                                if t == 0:
                                    dve.wait_ge(multiplied, c + 1)
                                else:
                                    dve.wait_ge(chunk_done, n + 1)
                                order(nc.vector.tensor_tensor(tmp[:, :], core.ps[:, 2 * c + t, :],
                                                              g_row[:, c * half:(c + 1) * half], ALU.mult))
                                order(nc.vector.tensor_tensor(dst, dst, tmp[:, :], ALU.add))


def first_block(core, I, k, x):
    nc = core.nc
    L_OFF, n_cols = offsets(L_COLS)
    with ExitStack() as mem:
        fvt = core.sb(mem, "layer_vectors", [P, n_cols])
        fv = {n: fvt[:, a:b] for n, (a, b) in L_OFF.items()}
        core.settle()
        with nc.Fori(0, DEPTH, 1) as layer:
            def layer_in(name):
                return I[name][layer]
            load(core, "layer_vectors", [(fvt[:, :], I["layer_vectors"][layer])])
            mod = core.sb(mem, "mod", [P, 48, 1])
            gain = core.sb(mem, "gain", [P, KD])
            g_row = core.sb(mem, "g_row", [P, DM])
            hT = core.sb(mem, "hT", [P, KD, SEQ])
            kk = dict(k, lat_gain=fvt[:, L_OFF["q_norm"][0]:L_OFF["kv_norm"][1]])
            modulation(core, "ada", layer_in("ada_w"), fv["c"].unsqueeze(1), fv["ada_b"], mod[:, :, :],
                       k["ones"], [6 * DM])
            for part in range(2):
                with ExitStack() as inner:
                    rstd = core.sb(inner, "rstd", [P, TT])
                    xn = core.sb(inner, "xn", [P, TT, DM])
                    gains(core, f"gain{part}", mod, 0, fv[("norm_mix", "norm_ffn")[part]], gain[:, :],
                          (3 * part + 1) * KD)
                    norm_transposed(core, f"norm{part}", k["ident"], x, hT, 0, gain,
                                    mod[:, 3 * part * KD:(3 * part + 1) * KD, 0], (rstd, xn))
                    spread_rows(core, f"gate{part}", k["ident"], k["ones"],
                                mod[:, (3 * part + 2) * KD:(3 * part + 3) * KD, 0],
                                xn[:, 0, :].rearrange("p (k f) -> p k f", k=KD), g_row)
                (mixer, ffn)[part](core, layer_in, kk, fv, hT[:, :, :], g_row, x)
            core.settle()
        with ExitStack() as inner:
            rstd = core.sb(inner, "rstd", [P, TT])
            junk = core.sb(inner, "junk", [P, DM])
            inverse_rms(core, "final_rms", [x[:, t, :] for t in range(TT)], rstd, junk, DM)
            with core.stage("final") as (block, own):
                @block.vector
                def _(dve):
                    for t in range(TT):
                        nc.vector.scalar_tensor_tensor(out=x[:, t, :], in0=x[:, t, :], scalar=rstd[:, t:t + 1],
                                                       in1=k["final"], op0=ALU.mult, op1=ALU.mult).then_inc(own, 1)


SPACE = 24 * 1024


class Carver:

    def __init__(self, space, at=0):
        self.space, self.at = space, at

    def __call__(self, *shape):
        n = int(np.prod(shape))
        assert self.at + n <= self.space.shape[1], (self.at, shape)
        part = self.space[:, self.at:self.at + n]
        self.at += n
        names = "abcde"[:len(shape)]
        if len(shape) == 1:
            return part
        return part.rearrange(f"p ({' '.join(names)}) -> p {' '.join(names)}", **dict(zip(names[1:], shape[1:])))


LAT = slice(SEQ, NTOK)


def flat(a):
    names = "abcde"[:len(a.shape) - 1]
    return a.rearrange(f"p {' '.join(names)} -> p ({' '.join(names)})")


def rows_of(head):
    return slice(HD * (head % 2), HD * (head % 2) + HD)


def hgrn(core, I, k, fv, masks, hT, ycat):
    nc, ident = core.nc, k["ident"]
    with ExitStack() as mem:
        f = core.sb(mem, "hg_f", [P, 6, NTOK])
        v = core.sb(mem, "hg_v", [P, NT4, A_W])
        g = core.sb(mem, "hg_g", [P, TT, A_W])
        lb = core.sb(mem, "hg_lb", [P, 4, 4])
        spans = [(0, 512, None), (512, 256, None), (3 * A_W, A_W, range(NT4)), (4 * A_W, A_W, (2, 3))]

        def out(j, t, bank, eng, order):
            if j < 2:
                return copy(nc, eng, f[:, 4 * j + t, :], bank)
            if j == 2:
                return copy(nc, eng, v[:, t, :], bank[:, 0:A_W])
            return copy(nc, eng, g[:, t - 2, :], bank[:, 0:A_W])
        linear(core, "hg_proj", hT, I["w_in_2"], spans, out, odd)
        carve = Carver(core.sb(mem, "hg_space", [P, SPACE])[:, :])
        inc, exc, kd = (carve(2, 2, NTOK) for _ in range(3))
        sg, sn = (carve(2, 2, NTOK) for _ in range(2))
        qs, ks = (carve(2, 2, SEQ) for _ in range(2))
        near = carve(TT, 2, 2, P)
        cross = carve(2, 2, 2, P)
        far = carve(TT, 2, 2, SEQ)
        tmp = carve(TT, 2, 2, P)
        sq = carve(TT, A_HEADS, HD)
        o = carve(TT, A_HEADS, HD)
        rs = carve(TT, A_HEADS)

        with core.stage("lb_order", "lb_exp") as (block, own, exped):
            @block.vector
            def _(dve):
                order = Order(dve, own)
                order(nc.vector.tensor_tensor(lb[:, 0, :], fv["lb"], fv["lb"], ALU.subtract))
                dve.wait_ge(exped, 1)
                order(nc.vector.reciprocal(lb[:, 2, :], lb[:, 1, :]))
                order(nc.vector.tensor_tensor(lb[:, 1, :], lb[:, 1, :], lb[:, 2, :], ALU.mult))
                order(nc.vector.tensor_tensor(lb[:, 0, :], lb[:, 1, :], lb[:, 1, :], ALU.subtract))
                order(nc.vector.tensor_scalar(lb[:, 3, :], lb[:, 0, :], -1.0, 1.0, ALU.mult, ALU.add))

            @block.scalar
            def _(act):
                act.wait_ge(own, 1)
                nc.scalar.activation(lb[:, 1, :], lb[:, 0, :], ACT.Exp).then_inc(exped, 1)

        with core.stage("fg_order", "fg_sigmoid", "fg_bounded", "fg_order_s", "fg_logged", "fg_silu") as (
                block, own, sigmoid, bounded, own_s, logged, silu):
            @block.scalar
            def _(act):
                order = Order(act, own_s)
                for d in range(2):
                    nc.scalar.activation(sg[:, d], f[:, 2 + 2 * d:4 + 2 * d, :], ACT.Sigmoid).then_inc(sigmoid, 1)
                    nc.scalar.activation(sn[:, d], f[:, 2 + 2 * d:4 + 2 * d, :], ACT.Sigmoid, scale=-1.0)\
                        .then_inc(sigmoid, 1)
                nc.scalar.activation(g[:, :, :], g[:, :, :], ACT.Silu).then_inc(silu, 1)
                act.wait_ge(bounded, 4)
                order(nc.scalar.activation(flat(sg), flat(sg), ACT.Sqrt))
                nc.scalar.activation(flat(inc), flat(sg), ACT.Ln).then_inc(logged, 1)

            @block.vector
            def _(dve):
                order = Order(dve, own)
                for d in range(2):
                    dve.wait_ge(sigmoid, 2 * d + 2)
                    for i in range(2):
                        c = 2 * d + i
                        order(nc.vector.tensor_scalar(kd[:, d, i], sn[:, d, i], lb[:, 3, c:c + 1], None, ALU.mult))
                        order(nc.vector.tensor_scalar(sg[:, d, i], sg[:, d, i], lb[:, 3, c:c + 1], lb[:, 0, c:c + 1],
                                                      ALU.mult, ALU.add))
                        nc.vector.tensor_scalar(sg[:, d, i], sg[:, d, i], 1e-20, None, ALU.max).then_inc(bounded, 1)
                order(nc.vector.memset(flat(exc), 0.0))
                order(nc.vector.memset(flat(near), 0.0))
                dve.wait_ge(logged, 1)
                order(nc.vector.tensor_scalar(flat(inc), flat(inc), 2.0, None, ALU.mult))

        def decayed(order, dve, exped, n, q_cols, k_cols, b):
            for d in range(2):
                if b:
                    dve.wait_ge(exped, n + 2 * d + 2)
                    order(nc.vector.tensor_tensor(qs[:, d], qs[:, d], f[:, 0:2, q_cols], ALU.mult))
                    ins = nc.vector.tensor_tensor(ks[:, d], ks[:, d], kd[:, d, :, k_cols], ALU.mult)
                else:
                    order(nc.vector.tensor_copy(qs[:, d], f[:, 0:2, q_cols]))
                    ins = nc.vector.tensor_copy(ks[:, d], kd[:, d, :, k_cols])
                yield ins

        def double(order, b):
            for d in range(2):
                a, z, edge = ((0, 1, b - 1), (1, 0, 0))[d]
                i_ = inc[:, d].rearrange("p h t -> p (h t)").rearrange("p (n s b) -> p n s b", s=2, b=b)
                e_ = exc[:, d].rearrange("p h t -> p (h t)").rearrange("p (n s b) -> p n s b", s=2, b=b)
                shape = [P, 2 * NTOK // (2 * b), b]
                order(nc.vector.tensor_tensor(e_[:, :, a, :], e_[:, :, a, :],
                                              i_[:, :, z, edge:edge + 1].to_broadcast(shape), ALU.add))
                order(nc.vector.tensor_tensor(i_[:, :, z, :], i_[:, :, z, :],
                                              i_[:, :, a, edge:edge + 1].to_broadcast(shape), ALU.add))

        for b in (0,) + LEVELS:
            with core.stage(f"hg{b}_exp", f"hg{b}_decayed", f"hg{b}_multiplied", f"hg{b}_order") as (
                    block, exped, decays, multiplied, own):
                @block.scalar
                def _(act):
                    if b:
                        for d in range(2):
                            nc.scalar.activation(qs[:, d], inc[:, d, :, LAT], ACT.Exp).then_inc(exped, 1)
                            nc.scalar.activation(ks[:, d], exc[:, d, :, LAT], ACT.Exp).then_inc(exped, 1)

                @block.tensor
                def _(pe):
                    for d in range(2):
                        pe.wait_ge(decays, d + 1)
                        for t in range(TT):
                            cols = slice(t * P, (t + 1) * P)
                            for par in range(2):
                                for hp in range(2):
                                    r = rows_of(par)
                                    mm = nc.tensor.matmul(core.ps[:, 4 * d + 2 * t + par, hp * P:(hp + 1) * P],
                                                          ks[r, d, hp, cols], qs[r, d, hp, cols],
                                                          start=True, stop=True)
                        mm.then_inc(multiplied, 1)

                @block.vector
                def _(dve):
                    order = Order(dve, own)
                    for ins in decayed(order, dve, exped, 0, LAT, LAT, b):
                        ins.then_inc(decays, 1)
                    if b:
                        dve.wait_ge(exped, 4)
                        double(order, b)
                    for d in range(2):
                        dve.wait_ge(multiplied, d + 1)
                        at = M_OFF["ident"][0] if b == 0 else M_OFF["lv"][0] + LEVELS.index(b) * P
                        mask = masks[:, d, at:at + P]
                        order(nc.vector.tensor_tensor(
                            tmp.rearrange("p a b c t -> p (a b) c t"),
                            core.ps[:, 4 * d:4 * d + 4, 0:2 * P].rearrange("p b (c t) -> p b c t", c=2),
                            mask.unsqueeze(1).unsqueeze(1).to_broadcast([P, 4, 2, P]), ALU.mult))
                        order(nc.vector.tensor_tensor(flat(near), flat(near), flat(tmp), ALU.add))

        with core.stage("hgx_exp", "hgx_decayed", "hgx_multiplied", "hgx_order", "hgx_doubled", "hgx_read") as (
                block, exped, decays, multiplied, own, doubled, read):
            @block.scalar
            def _(act):
                for stage in range(2):
                    if stage:
                        act.wait_ge(doubled, 1)
                        act.wait_ge(multiplied, 1)
                    for d in range(2):
                        nc.scalar.activation(qs[:, d], inc[:, d, :, LAT], ACT.Exp).then_inc(exped, 1)
                        nc.scalar.activation(ks[:, d], exc[:, d, :, (LAT, slice(0, SEQ))[stage]], ACT.Exp)\
                            .then_inc(exped, 1)

            @block.tensor
            def _(pe):
                pe.wait_ge(decays, 2)
                for d in range(2):
                    t, s = (1, 0) if d == 0 else (0, 1)
                    for par in range(2):
                        for hp in range(2):
                            r = rows_of(par)
                            mm = nc.tensor.matmul(core.ps[:, 2 * d + par, hp * P:(hp + 1) * P],
                                                  ks[r, d, hp, s * P:(s + 1) * P], qs[r, d, hp, t * P:(t + 1) * P],
                                                  start=True, stop=True)
                mm.then_inc(multiplied, 1)
                pe.wait_ge(decays, 4)
                for s in range(TT):
                    for par in range(2):
                        for hp in range(2):
                            r = rows_of(par)
                            for d in range(2):
                                mm = nc.tensor.matmul(core.ps[:, 4 + 2 * s + par, hp * SEQ:(hp + 1) * SEQ],
                                                      ks[r, d, hp, s * P:(s + 1) * P], qs[r, d, hp, :],
                                                      start=(d == 0), stop=(d == 1))
                mm.then_inc(multiplied, 1)

            @block.vector
            def _(dve):
                order = Order(dve, own)
                for ins in decayed(order, dve, exped, 0, LAT, LAT, 128):
                    ins.then_inc(decays, 1)
                dve.wait_ge(exped, 4)
                double(order, P)
                nc.vector.tensor_copy(tmp[:, 0, 0, 0, 0:1], tmp[:, 0, 0, 0, 0:1]).then_inc(doubled, 1)
                dve.wait_ge(multiplied, 1)
                order(nc.vector.tensor_copy(cross.rearrange("p a b c t -> p (a b) (c t)"), core.ps[:, 0:4, 0:2 * P]))
                for ins in decayed(order, dve, exped, 4, LAT, slice(0, SEQ), 256):
                    ins.then_inc(decays, 1)
                dve.wait_ge(multiplied, 2)
                nc.vector.tensor_copy(far.rearrange("p a b c t -> p (a b) (c t)"), core.ps[:, 4:8, :]).then_inc(read, 1)

        def weigh(t, bank):
            for h in range(A_HEADS):
                hp, par = divmod(h, 2)
                cols = slice(t * P, (t + 1) * P)
                lefts = [far[:, 0, par, hp, cols], far[:, 1, par, hp, cols], near[:, t, par, hp, :],
                         cross[:, 1 - t, par, hp, :]]
                for j, (left, tile) in enumerate(zip(lefts, (0, 1, 2 + t, 3 - t))):
                    mm = nc.tensor.matmul(bank[:, h * HD:(h + 1) * HD], left, v[:, tile, h * HD:(h + 1) * HD],
                                          start=(j == 0), stop=(j == 3))
            return mm

        def weighed(t, bank, eng, order):
            return copy(nc, eng, o[:, t], bank[:, 0:A_W].rearrange("p (h d) -> p h d", d=HD))
        products(core, "hg_weigh", TT, weigh, weighed, odd)
        head_inverse_rms(core, "hg_rms", o, sq, rs, TT, A_HEADS)
        with core.stage("hg_out") as (block, own):
            @block.vector
            def _(dve):
                order = Order(dve, own)
                for t in range(TT):
                    order(nc.vector.tensor_tensor(o[:, t], o[:, t],
                                                  rs[:, t, :].unsqueeze(2).to_broadcast([P, A_HEADS, HD]), ALU.mult))
                    order(nc.vector.tensor_tensor(ycat[:, t, 0:A_W], o[:, t].rearrange("p h d -> p (h d)"),
                                                  g[:, t, :], ALU.mult))


def rwkv(core, I, k, fv, masks, consts, hT, ycat):
    nc, ident = core.nc, k["ident"]
    with ExitStack() as mem:
        raw_space = core.sb(mem, "rw_raw", [P, B_TILES * 2 * (SEQ + 2)])
        raw = raw_space[:, :].rearrange("p (j s n) -> p j s n", j=B_TILES, s=2)
        with core.stage("rw_pad") as (block, pad):
            @block.vector
            def _(dve):
                nc.vector.memset(raw[:, :, :, 0:1], 0.0).then_inc(pad, 1)
                nc.vector.memset(raw[:, :, :, SEQ + 1:SEQ + 2], 0.0).then_inc(pad, 1)

        def out(j, t, bank, eng, order):
            return copy(nc, eng, raw[:, 4 * j + t, :, 1:SEQ + 1], bank.rearrange("p (s n) -> p s n", s=2))
        linear(core, "rw_proj", hT, I["w_in_2"],
               [(B_AT, 512, None), (B_AT + 512, 512, None), (B_AT + 1024, P, None)], out, odd)

        X = core.sb(mem, "rw_x", [P, B_TILES, NTOK])
        up = core.sb(mem, "rw_up", [P, 3 * A_W])
        vt = core.sb(mem, "rw_v", [P, NT4, A_W])
        gt = core.sb(mem, "rw_g", [P, TT, A_W])
        bon = core.sb(mem, "rw_bonus", [P, TT, B_HEADS])
        S = core.sb(mem, "rw_state", [P, 2, 2, HD])
        tot = core.sb(mem, "rw_total", [P, 2, 2, 8])
        y = core.sb(mem, "rw_y", [P, 2, TT, A_W])
        space = core.sb(mem, "rw_space", [P, SPACE])[:, :]
        freed = Carver(raw_space[:, :])
        k2t, a2t = (freed(2, NT4, A_W) for _ in range(2))
        load(core, "rw_up", [(up[:, :], I["rwkv_up"])])
        with core.stage("mix_order", "mix_done", "mix_act") as (block, own, mixed, acted):
            @block.vector
            def _(dve):
                order = Order(dve, own)
                for j in (6, 8, 7, 0, 1, 2, 3, 4, 5):
                    xj = X[:, j, :].rearrange("p (s n) -> p s n", s=2)
                    mid = raw[:, j, :, 1:SEQ + 1]
                    order(nc.vector.tensor_tensor(xj, raw[:, j, :, 0:SEQ], raw[:, j, :, 2:SEQ + 2], ALU.add))
                    order(nc.vector.scalar_tensor_tensor(out=xj, in0=xj, scalar=0.5, in1=mid, op0=ALU.mult,
                                                         op1=ALU.subtract))
                    nc.vector.scalar_tensor_tensor(out=xj, in0=xj, scalar=fv["mu"][:, j:j + 1], in1=mid,
                                                   op0=ALU.mult, op1=ALU.add).then_inc(mixed, 1)

            @block.scalar
            def _(act):
                act.wait_ge(mixed, 1)
                nc.scalar.activation(X[:, 6, :], X[:, 6, :], ACT.Tanh).then_inc(acted, 1)
                act.wait_ge(mixed, 2)
                nc.scalar.activation(X[:, 8, :], X[:, 8, :], ACT.Sigmoid).then_inc(acted, 1)

        carve = Carver(space)
        sw, sa = (carve(2, 2, NTOK) for _ in range(2))
        kk, kn = (carve(2, NTOK) for _ in range(2))
        kt, rt, kh, ah, k2, a2 = (carve(2, 2, NTOK) for _ in range(6))
        pi = carve(2, 2, NTOK)
        def low_rank(i, bank):
            which, d, hp = i // 4, (i // 2) % 2, i % 2
            r = rows_of(d)
            return nc.tensor.matmul(bank, up[r, which * A_W + hp * P:which * A_W + (hp + 1) * P],
                                    X[r, 6 + which, :], start=True, stop=True)

        def low_rank_out(i, bank, eng, order):
            which, d, hp = i // 4, (i // 2) % 2, i % 2
            return nc.scalar.activation((sw, sa)[which][:, d, hp], bank, ACT.Sigmoid,
                                        bias=fv[("w0", "a0")[which]][:, 2 * d + hp:2 * d + hp + 1])
        products(core, "rw_low", 8, low_rank, low_rank_out, lambda i: True)

        def gate(t, bank):
            return nc.tensor.matmul(bank[:, 0:A_W], X[:, 8, (2 + t) * P:(3 + t) * P], up[:, 2 * A_W:], start=True,
                                    stop=True)

        def gated(t, bank, eng, order):
            return copy(nc, eng, gt[:, t, :], bank[:, 0:A_W])
        products(core, "rw_gate", TT, gate, gated, odd)

        with core.stage("kk_order") as (block, own):
            @block.vector
            def _(dve):
                order = Order(dve, own)
                for hp in range(2):
                    order(nc.vector.tensor_scalar(kk[:, hp], X[:, 2 + hp, :], fv["kk_scale"][:, hp:hp + 1], None,
                                                  ALU.mult))
                    order(nc.vector.tensor_tensor(kn[:, hp], kk[:, hp], kk[:, hp], ALU.mult))

        def norm(hp, bank):
            return nc.tensor.matmul(bank, consts["head_ones"], kn[:, hp], start=True, stop=True)

        def normed(hp, bank, eng, order):
            return nc.scalar.activation(kn[:, hp], bank, ACT.Sqrt)
        products(core, "kk_norm", 2, norm, normed, lambda i: True)
        with core.stage("prep_order", "prep_ready", "prep_exp") as (block, own, ready, exped):
            @block.vector
            def _(dve):
                order = Order(dve, own)
                order(nc.vector.tensor_scalar(kn, kn, 1e-12, None, ALU.max))
                order(nc.vector.reciprocal(kn, kn))
                order(nc.vector.tensor_tensor(kk, kk, kn, ALU.mult))
                order(nc.vector.tensor_scalar(flat(sw), flat(sw), -float(np.exp(np.float32(-0.5))), None, ALU.mult))
                for d in range(2):
                    for hp in range(2):
                        order(nc.vector.tensor_tensor_scan(pi[:, d, hp], consts["chunk_start"], sw[:, d, hp], 0.0,
                                                           ALU.mult, ALU.add))
                for d in range(2):
                    c = [a[:, d].rearrange("p h t -> p (h t)").rearrange("p (c n) -> p c n", n=RW_CHUNK)
                         for a in (pi, sw, kt, k2, rt)]
                    p_, l_, before, after, here = c
                    last = p_[:, :, RW_CHUNK - 1:RW_CHUNK]
                    if d == 1:
                        before, after = after, before
                    order(nc.vector.tensor_tensor(before, p_, l_, ALU.subtract))
                    order(nc.vector.tensor_tensor(after, last.to_broadcast([P, 16, RW_CHUNK]), p_, ALU.subtract))
                    order(nc.vector.tensor_copy(tot[:, d].rearrange("p h c -> p (h c)"), last.squeeze(2)))
                    if d == 0:
                        ins = nc.vector.tensor_copy(here, p_)
                    else:
                        ins = nc.vector.tensor_tensor(here, after, l_, ALU.add)
                    ins.then_inc(ready, 1)
                for d in range(2):
                    for hp in range(2):
                        order(nc.vector.tensor_tensor(a2[:, d, hp], sa[:, d, hp], kk[:, hp], ALU.mult))
                        order(nc.vector.tensor_scalar(sa[:, d, hp], sa[:, d, hp], 1.0, fv["k_a"][:, hp:hp + 1],
                                                      ALU.subtract, ALU.mult))
                        order(nc.vector.scalar_tensor_tensor(out=sa[:, d, hp], in0=sa[:, d, hp], scalar=1.0,
                                                             in1=X[:, 2 + hp, :], op0=ALU.add, op1=ALU.mult))
                dve.wait_ge(exped, 10)
                for d in range(2):
                    order(nc.vector.tensor_tensor(kh[:, d], ah[:, d], sa[:, d], ALU.mult))
                    order(nc.vector.tensor_tensor(ah[:, d], ah[:, d], a2[:, d], ALU.mult))
                    order(nc.vector.tensor_tensor(kt[:, d], kt[:, d], kk, ALU.mult))
                    order(nc.vector.tensor_tensor(rt[:, d], rt[:, d], X[:, 0:2, :], ALU.mult))
                    order(nc.vector.tensor_tensor(a2[:, d], a2[:, d], k2[:, d], ALU.mult))
                    order(nc.vector.tensor_tensor(k2[:, d], k2[:, d], sa[:, d], ALU.mult))
                order(nc.vector.tensor_tensor(kn[:, :, LAT], sa[:, 0, :, LAT], sa[:, 1, :, LAT], ALU.add))
                order(nc.vector.tensor_tensor(kn[:, :, LAT], kn[:, :, LAT], X[:, 0:2, LAT], ALU.mult))
                for hp in range(2):
                    order(nc.vector.tensor_scalar(kn[:, hp, LAT], kn[:, hp, LAT], fv["r_k"][:, hp:hp + 1], None,
                                                  ALU.mult))
                order(nc.vector.memset(S[:, :, :, :], 0.0))

            @block.scalar
            def _(act):
                for d in range(2):
                    act.wait_ge(ready, d + 1)
                    nc.scalar.activation(ah[:, d], rt[:, d], ACT.Exp, scale=-1.0).then_inc(exped, 1)
                    act.wait_ge(exped, 5 * d + 1)
                    for a in (kt, k2, rt):
                        nc.scalar.activation(a[:, d], a[:, d], ACT.Exp).then_inc(exped, 1)
                    nc.scalar.activation(tot[:, d], tot[:, d], ACT.Exp).then_inc(exped, 1)

        def bonus(t, bank):
            for hp in range(2):
                mm = nc.tensor.matmul(bank[:, 2 * hp:2 * hp + 2], kn[:, hp, (2 + t) * P:(3 + t) * P],
                                      consts["head_pick"], start=True, stop=True)
            return mm

        def bonus_out(t, bank, eng, order):
            return copy(nc, eng, bon[:, t, :], bank[:, 0:B_HEADS])
        products(core, "rw_bonus", TT, bonus, bonus_out, odd)

        sources = [(X[:, 4:6, :], vt), (k2[:, 0], k2t[:, 0]), (a2[:, 0], a2t[:, 0]), (k2[:, 1], k2t[:, 1]),
                   (a2[:, 1], a2t[:, 1])]

        def turn(i, bank):
            src, t = sources[i // NT4][0], i % NT4
            for hp in range(2):
                ins = nc.tensor.transpose(bank[:, hp * P:(hp + 1) * P], src[:, hp, t * P:(t + 1) * P], ident)
            return ins

        def turned(i, bank, eng, order):
            return copy(nc, eng, sources[i // NT4][1][:, i % NT4, :], bank[:, 0:A_W])
        products(core, "rw_turn", 5 * NT4, turn, turned, odd)

        low = Carver(space)
        M1 = low(2, NT4, 4, P)
        N_ = [low(NT4, 4, P)]
        low.at = (8 + 4 + 8) * NTOK
        T_ = low(2, NT4, 4, P)
        Rk, Ra = (low(2, TT, 4, P) for _ in range(2))
        P_ = low(2, NT4, 4, P)
        N_.append(low(NT4, 4, P))
        G = Carver(flat(X[:, :, :]))(2, NT4, 4, P)
        NM = Carver(flat(hT))(2, NT4, 4, P)
        kinds = [(d, t, kind, par) for d in range(2) for t in range(NT4) for kind in range(4) for par in range(2)
                 if kind < 2 or t >= 2]

        def matrix(i, bank):
            d, t, kind, par = kinds[i]
            left = (ah, kh, kh, ah)[kind]
            right = (kt, kt, rt, rt)[kind]
            r, cols = rows_of(par), slice(t * P, (t + 1) * P)
            for hp in range(2):
                mm = nc.tensor.matmul(bank[:, hp * P:(hp + 1) * P], left[r, d, hp, cols], right[r, d, hp, cols],
                                      start=True, stop=True)
            return mm

        def matrix_out(i, bank, eng, order):
            d, t, kind, par = kinds[i]
            dst = (N_[d], M1[:, d], Rk[:, d], Ra[:, d])[kind][:, t if kind < 2 else t - 2]
            a, b = M_OFF["strict" if kind < 2 else "incl"]
            dst = dst.rearrange("p (hp par) t -> p par hp t", par=2)[:, par]
            return nc.vector.tensor_tensor(dst, bank[:, 0:2 * P].rearrange("p (h t) -> p h t", h=2),
                                           masks[:, d, a:b].unsqueeze(1).to_broadcast([P, 2, P]), ALU.mult)
        products(core, "rw_matrix", len(kinds), matrix, matrix_out)

        with core.stage("unit") as (block, unit):
            @block.vector
            def _(dve):
                for a in (G, T_):
                    nc.vector.tensor_copy(a.rearrange("p d t h c -> p (d t h) c"),
                                          ident.unsqueeze(1).to_broadcast([P, 32, P])).then_inc(unit, 1)
        for b in LEVELS[:-1]:
            with core.stage(f"nm{b}_order") as (block, own):
                @block.vector
                def _(dve):
                    at = M_OFF["lv"][0] + LEVELS.index(b) * P
                    for d in range(2):
                        nc.vector.tensor_tensor(NM[:, d].rearrange("p t h c -> p (t h) c"),
                                                N_[d].rearrange("p t h c -> p (t h) c"),
                                                masks[:, d, at:at + P].unsqueeze(1).to_broadcast([P, 16, P]),
                                                ALU.mult).then_inc(own, 1)

            def first(i, bank):
                d, t = divmod(i, NT4)
                for h in range(B_HEADS):
                    mm = nc.tensor.matmul(bank[:, h * P:(h + 1) * P], NM[:, d, t, h], T_[:, d, t, h], start=True,
                                          stop=True)
                return mm

            def first_out(i, bank, eng, order):
                d, t = divmod(i, NT4)
                return copy(nc, eng, P_[:, d, t].rearrange("p h c -> p (h c)"), bank)
            products(core, f"inv{b}_first", 8, first, first_out, odd)
            last = b == LEVELS[-2]
            units = [(d, t, x) for d in range(2) for t in range(NT4) for x in range(2) if x or not last]

            def second(i, bank):
                d, t, x = units[i]
                for h in range(B_HEADS):
                    left, right = ((G, P_), (P_, G))[x]
                    mm = nc.tensor.matmul(bank[:, h * P:(h + 1) * P], left[:, d, t, h], right[:, d, t, h],
                                          start=True, stop=True)
                return mm

            def second_out(i, bank, eng, order):
                d, t, x = units[i]
                dst = (T_, G)[x][:, d, t].rearrange("p h c -> p (h c)")
                return nc.vector.tensor_tensor(dst, dst, bank, ALU.subtract)
            products(core, f"inv{b}_second", len(units), second, second_out)
        low = Carver(flat(P_))
        rw_sequence(core, S, kt, rt, M1, G, Rk, Ra, vt, k2t, a2t, tot, y,
                    low(2, 2, 2, HD),
                    low(2, A_W))
        with ExitStack() as inner:
            st = core.sb(inner, "rw_stat", [P, 2, TT, B_HEADS])
            yy = y[:, 0].rearrange("p t (h d) -> p t h d", d=HD)
            y1 = y[:, 1].rearrange("p t (h d) -> p t h d", d=HD)

            def wide(a, t):
                return a[:, t, :].unsqueeze(2).to_broadcast([P, B_HEADS, HD])
            with core.stage("ln_order", "ln_rooted", "ln_meaned") as (block, own, rooted, meaned):
                @block.vector
                def _(dve):
                    order = Order(dve, own)
                    order(nc.vector.tensor_tensor(y[:, 0], y[:, 0], y[:, 1], ALU.add))
                    for t in range(TT):
                        order(nc.vector.tensor_reduce(st[:, 0, t, :], yy[:, t], AX_X, ALU.add))
                    order(nc.vector.tensor_scalar(st[:, 0], st[:, 0], 1.0 / HD, None, ALU.mult))
                    for t in range(TT):
                        order(nc.vector.tensor_tensor(yy[:, t], yy[:, t], wide(st[:, 0], t), ALU.subtract))
                        order(nc.vector.tensor_tensor(y1[:, t], yy[:, t], yy[:, t], ALU.mult))
                        order(nc.vector.tensor_reduce(st[:, 1, t, :], y1[:, t], AX_X, ALU.add))
                    nc.vector.tensor_scalar(st[:, 1], st[:, 1], 1.0 / HD, 64e-5, ALU.mult, ALU.add)\
                        .then_inc(meaned, 1)
                    dve.wait_ge(rooted, 1)
                    order(nc.vector.reciprocal(st[:, 1], st[:, 1]))
                    for t in range(TT):
                        order(nc.vector.tensor_tensor(yy[:, t], yy[:, t], wide(st[:, 1], t), ALU.mult))
                        order(nc.vector.tensor_tensor(y[:, 0, t], y[:, 0, t], k["ln_gain"], ALU.mult))
                        order(nc.vector.tensor_tensor(y[:, 0, t], y[:, 0, t], k["ln_bias"], ALU.add))
                        order(nc.vector.tensor_tensor(y1[:, t],
                                                      vt[:, 2 + t, :].rearrange("p (h d) -> p h d", d=HD),
                                                      wide(bon, t), ALU.mult))
                        order(nc.vector.tensor_tensor(y[:, 0, t], y[:, 0, t], y[:, 1, t], ALU.add))
                        order(nc.vector.tensor_tensor(ycat[:, t, A_W:2 * A_W], y[:, 0, t], gt[:, t, :], ALU.mult))

                @block.scalar
                def _(act):
                    act.wait_ge(meaned, 1)
                    nc.scalar.activation(st[:, 1], st[:, 1], ACT.Sqrt).then_inc(rooted, 1)


def rw_sequence(core, S, kt, rt, M1, G, Rk, Ra, vt, k2t, a2t, tot, y, rhs, nu):
    nc = core.nc
    chunks = [[0, 1, 2, 3, 4, 5, 6, 7], [3, 2, 1, 0, 7, 6, 5, 4]]
    steps = 8
    with ExitStack() as mem:
        names = ("rhs_ready", "rhs_copied", "u_ready", "u_copied", "state_added", "state_ready", "y_ready", "y_copied")
        with core.stage(*[f"{n}{d}" for d in range(2) for n in names]) as (block, *sems):
            (rhs_ready, rhs_copied, u_ready, u_copied, state_added, state_ready, y_ready, y_copied) = [
                (sems[i], sems[8 + i]) for i in range(8)]

            def place(n, d):
                c = chunks[d][n]
                return c, c // 2, slice(HD * (c % 2), HD * (c % 2) + HD)

            @block.tensor
            def _(pe):
                for n in range(steps):
                    for d in range(2):
                        c, tile, half = place(n, d)
                        cols = slice(tile * P, (tile + 1) * P)
                        if n:
                            pe.wait_ge(state_ready[d], 4 * n)
                        if n > 4:
                            pe.wait_ge(y_copied[d], n - 4)
                        for par in range(2):
                            r = rows_of(par)
                            for hp in range(2):
                                o = core.ps[:, 4 * d + par, hp * HD:(hp + 1) * HD]
                                h = 2 * hp + par
                                nc.tensor.matmul(o, kt[r, d, hp, cols], S[r, d, hp, :], start=True, stop=False)
                                mm = nc.tensor.matmul(o, M1[:, d, tile, h], vt[:, tile, h * HD:(h + 1) * HD],
                                                      start=False, stop=True)
                        mm.then_inc(rhs_ready[d], 1)
                    for d in range(2):
                        c, tile, half = place(n, d)
                        pe.wait_ge(rhs_copied[d], n + 1)
                        for h in range(B_HEADS):
                            mm = nc.tensor.matmul(core.ps[:, 4 * d + 2, h * HD:(h + 1) * HD], G[:, d, tile, h],
                                                  rhs[:, d, h % 2, h // 2, :], start=True, stop=True)
                        mm.then_inc(u_ready[d], 1)
                    for d in range(2):
                        c, tile, half = place(n, d)
                        pe.wait_ge(u_copied[d], n + 1)
                        for hp in range(2):
                            o = core.ps[:, 4 * d + 3, hp * P:(hp + 1) * P]
                            cols = slice(hp * P, (hp + 1) * P)
                            nc.tensor.matmul(o, k2t[half, d, tile, cols], vt[half, tile, cols], start=True, stop=False)
                            mm = nc.tensor.matmul(o, a2t[half, d, tile, cols], nu[half, d, cols], start=False,
                                                  stop=True)
                        mm.then_inc(state_added[d], 1)
                        if n < 4:
                            continue
                        for par in range(2):
                            r = rows_of(par)
                            for hp in range(2):
                                h = 2 * hp + par
                                o = core.ps[:, 4 * d + par, 2 * P + hp * HD:2 * P + (hp + 1) * HD]
                                nc.tensor.matmul(o, rt[r, d, hp, tile * P:(tile + 1) * P], S[r, d, hp, :], start=True,
                                                 stop=False)
                                nc.tensor.matmul(o, Rk[:, d, tile - 2, h], vt[:, tile, h * HD:(h + 1) * HD],
                                                 start=False, stop=False)
                                mm = nc.tensor.matmul(o, Ra[:, d, tile - 2, h], nu[:, d, h * HD:(h + 1) * HD],
                                                      start=False, stop=True)
                        mm.then_inc(y_ready[d], 1)

            @block.scalar
            def _(act):
                for n in range(steps):
                    for d in range(2):
                        act.wait_ge(rhs_ready[d], n + 1)
                        nc.scalar.activation(rhs[:, d].rearrange("p a b v -> p a (b v)"),
                                             core.ps[:, 4 * d:4 * d + 2, 0:P], ACT.Copy).then_inc(rhs_copied[d], 1)
                    for d in range(2):
                        act.wait_ge(u_ready[d], n + 1)
                        if n > 4:
                            act.wait_ge(y_ready[d], n - 4)
                        nc.scalar.activation(nu[:, d, :], core.ps[:, 4 * d + 2, 0:A_W], ACT.Copy, scale=-1.0)\
                            .then_inc(u_copied[d], 1)

            @block.vector
            def _(dve):
                for n in range(steps):
                    for d in range(2):
                        c, tile, half = place(n, d)
                        dve.wait_ge(state_added[d], n + 1)
                        if n >= 4:
                            dve.wait_ge(y_ready[d], n - 3)
                        for par in range(2):
                            r = rows_of(par)
                            for hp in range(2):
                                nc.vector.scalar_tensor_tensor(
                                    out=S[r, d, hp, :], in0=S[r, d, hp, :], scalar=tot[r, d, hp, c:c + 1],
                                    in1=core.ps[r, 4 * d + 3, hp * P + par * HD:hp * P + (par + 1) * HD],
                                    op0=ALU.mult, op1=ALU.add).then_inc(state_ready[d], 1)
                        if n >= 4:
                            dst = y[half, d, tile - 2, :].rearrange("p (hp par v) -> p par hp v", par=2, v=HD)
                            for par in range(2):
                                ins = nc.vector.tensor_copy(
                                    dst[:, par], core.ps[half, 4 * d + par, 2 * P:3 * P]
                                    .rearrange("p (hp v) -> p hp v", v=HD))
                            ins.then_inc(y_copied[d], 1)


def neighbourhood(core, I, k, consts, hT, ycat):
    nc, ident = core.nc, k["ident"]
    with ExitStack() as mem:
        q = core.sb(mem, "na_q", [P, TT, C_W])
        kx = core.sb(mem, "na_k", [P, NT4, C_W])
        v = core.sb(mem, "na_v", [P, NT4, C_W])
        spans = [(C_AT, 512, (2, 3)), (C_AT + 512, 512, range(NT4)), (C_AT + 1024, 512, range(NT4))]

        def out(j, t, bank, eng, order):
            return copy(nc, eng, (q[:, t - 2] if j == 0 else (kx, v)[j - 1][:, t]), bank)
        linear(core, "na_proj", hT, I["w_in_2"], spans, out, odd)
        kT = core.sb(mem, "na_kT", [P, 4, NTOK])
        qT = core.sb(mem, "na_qT", [P, 4, SEQ])
        rs = core.sb(mem, "na_rs", [P, TT + NT4, C_HEADS])
        carve = Carver(core.sb(mem, "na_space", [P, SPACE])[:, :])
        s, pT = carve(2 * C_HEADS * NTOK), carve(2 * C_HEADS * NTOK)
        bias = carve(TT, C_HEADS, SEQ)
        tmp = carve(3, C_HEADS, HD // 2)
        sq = s[:, 0:NT4 * C_W].rearrange("p (t h d) -> p t h d", t=NT4, h=C_HEADS)
        load(core, "na_bias", [(bias[:, t], I["bias"][t]) for t in range(TT)])
        qh = q[:, :, :].rearrange("p t (h d) -> p t h d", d=HD)
        kh = kx[:, :, :].rearrange("p t (h d) -> p t h d", d=HD)
        head_inverse_rms(core, "naq_rms", qh, sq, rs[:, 0:TT, :], TT, C_HEADS)
        head_inverse_rms(core, "nak_rms", kh, sq, rs[:, TT:, :], NT4, C_HEADS)
        with core.stage("na_order") as (block, own):
            @block.vector
            def _(dve):
                order = Order(dve, own)
                for x, tiles, at, gain in ((qh, TT, 0, k["q_gain"]), (kh, NT4, TT, k["k_gain"])):
                    for t in range(tiles):
                        order(nc.vector.tensor_tensor(
                            x[:, t], x[:, t], rs[:, at + t, :].unsqueeze(2).to_broadcast([P, C_HEADS, HD]), ALU.mult))
                        order(nc.vector.tensor_tensor(x[:, t], x[:, t],
                                                      gain.unsqueeze(1).to_broadcast([P, C_HEADS, HD]), ALU.mult))
                    for t in range(TT):
                        xl = x[:, tiles - 2 + t]
                        cos, sin = (consts[n][:, 32 * t:32 * t + 32].unsqueeze(1).to_broadcast([P, C_HEADS, 32])
                                    for n in ("na_cos", "na_sin"))
                        rotate(nc, order, xl[:, :, 0:32], xl[:, :, 32:64], cos, sin, [tmp[:, i] for i in range(3)])

        key_tiles = (2, 3, 0, 1)

        def turn(i, bank):
            src, tiles = (q, (0, 1)) if i < 4 else (kx, key_tiles)
            for j, t in enumerate(tiles):
                ins = nc.tensor.transpose(bank[:, j * P:(j + 1) * P], src[:, t, (i % 4) * P:(i % 4 + 1) * P], ident)
            return ins

        def turned(i, bank, eng, order):
            return copy(nc, eng, qT[:, i, :] if i < 4 else kT[:, i - 4, :], bank[:, 0:SEQ if i < 4 else NTOK])
        products(core, "na_turn", 8, turn, turned, odd)
        attention(core, "na", mem, ident, C_HEADS, NTOK, HD,
                  lambda h, t: qT[rows_of(h), h // 2, t * P:(t + 1) * P], lambda h: kT[rows_of(h), h // 2, :],
                  HD ** -0.5, lambda h, t: bias[:, t, h, :], SEQ,
                  lambda h, j: v[:, key_tiles[j], h * HD:(h + 1) * HD],
                  lambda t: ycat[:, t, 2 * A_W:].rearrange("p (h d) -> p h d", d=HD), (s, pT))


def router(core, I, k, hT, comb_d):
    nc = core.nc
    n = GROUPS + EXPERTS
    with ExitStack() as mem:
        w = core.sb(mem, "rt_w", [P, KD, n])
        lg = core.sb(mem, "rt_logits", [P, TT, n])
        place = core.sb(mem, "rt_place", [P, PER_GROUP])
        a, b, c, e, pr = (core.sb(mem, f"rt_{i}", [P, TT, PER_GROUP]) for i in "abcde")
        pick = [core.sb(mem, f"rt_pick{i}", [P, TT, PER_GROUP]) for i in range(2)]
        group = core.sb(mem, "rt_group", [P, TT, GROUPS])
        col = core.sb(mem, "rt_col", [P, 8, TT])
        comb = core.sb(mem, "rt_comb", [P, GROUPS, PER_GROUP, TT])
        load(core, "router", [(w[:, :, :], I["router"].rearrange("(k p) n -> p k n", p=P))])

        def logit(t, bank):
            for kt in range(KD):
                mm = nc.tensor.matmul(bank[:, 0:n], hT[:, kt, t * P:(t + 1) * P], w[:, kt, :], start=(kt == 0),
                                      stop=(kt == KD - 1))
            return mm

        def logit_out(t, bank, eng, order):
            return nc.vector.tensor_tensor(lg[:, t, :], bank[:, 0:n], k["b_r"], ALU.add)
        products(core, "rt_logit", TT, logit, logit_out)

        def wide(x, m):
            return x.unsqueeze(2).to_broadcast([P, TT, m])

        def first_of_max(order, x, top, out, m, s1, s2):
            order(nc.vector.tensor_tensor(s1, x, wide(top, m), ALU.is_equal))
            order(nc.vector.tensor_scalar(s1, s1, -64.0, 64.0, ALU.mult, ALU.add))
            order(nc.vector.tensor_tensor(s1, s1, place[:, 0:m].unsqueeze(1).to_broadcast([P, TT, m]), ALU.add))
            order(nc.vector.tensor_reduce(s2, s1, AX_X, ALU.min))
            order(nc.vector.tensor_tensor(out, s1, wide(s2, m), ALU.is_equal))

        with core.stage("rt_order", "rt_shift", "rt_exp", "rt_place", "rt_comb", "rt_stored") as (
                block, own, shifted, exped, placed, combed, stored):
            @block.gpsimd
            def _(pool):
                for i in range(PER_GROUP):
                    nc.gpsimd.memset(place[:, i:i + 1], float(i)).then_inc(placed, 1)
                pool.wait_ge(placed, PER_GROUP)

            @block.scalar
            def _(act):
                act.wait_ge(shifted, 1)
                nc.scalar.activation(a[:, :, 0:GROUPS], a[:, :, 0:GROUPS], ACT.Exp).then_inc(exped, 1)
                act.wait_ge(shifted, 2)
                nc.scalar.activation(pr[:, :, :], pr[:, :, :], ACT.Exp).then_inc(exped, 1)

            @block.vector
            def _(dve):
                order = Order(dve, own)
                V = nc.vector
                g = lg[:, :, 0:GROUPS]
                dve.wait_ge(placed, PER_GROUP)
                order(V.tensor_reduce(col[:, 0], g, AX_X, ALU.max))
                V.tensor_tensor(a[:, :, 0:GROUPS], g, wide(col[:, 0], GROUPS), ALU.subtract).then_inc(shifted, 1)
                first_of_max(order, g, col[:, 0], group[:, :, :], GROUPS, b[:, :, 0:GROUPS], col[:, 1])
                dve.wait_ge(exped, 1)
                order(V.tensor_reduce(col[:, 2], a[:, :, 0:GROUPS], AX_X, ALU.add))
                order(V.reciprocal(col[:, 2], col[:, 2]))
                order(V.tensor_tensor(a[:, :, 0:GROUPS], a[:, :, 0:GROUPS], group[:, :, :], ALU.mult))
                order(V.tensor_reduce(col[:, 3], a[:, :, 0:GROUPS], AX_X, ALU.add))
                order(V.tensor_tensor(col[:, 2], col[:, 2], col[:, 3], ALU.mult))
                for gi in range(GROUPS):
                    src = lg[:, :, GROUPS + gi * PER_GROUP:GROUPS + (gi + 1) * PER_GROUP]
                    weight = group[:, :, gi:gi + 1].to_broadcast([P, TT, PER_GROUP])
                    order(V.tensor_tensor(c[:, :, :], src, weight, ALU.mult))
                    if gi == 0:
                        order(V.tensor_copy(e[:, :, :], c[:, :, :]))
                    else:
                        order(V.tensor_tensor(e[:, :, :], e[:, :, :], c[:, :, :], ALU.add))
                order(V.tensor_reduce(col[:, 4], e[:, :, :], AX_X, ALU.max))
                V.tensor_tensor(pr[:, :, :], e[:, :, :], wide(col[:, 4], PER_GROUP), ALU.subtract).then_inc(shifted, 1)
                dve.wait_ge(exped, 2)
                order(V.tensor_reduce(col[:, 5], pr[:, :, :], AX_X, ALU.add))
                order(V.reciprocal(col[:, 5], col[:, 5]))
                order(V.tensor_tensor(pr[:, :, :], pr[:, :, :], wide(col[:, 5], PER_GROUP), ALU.mult))
                order(V.tensor_copy(e[:, :, :], pr[:, :, :]))
                for i in range(2):
                    order(V.tensor_reduce(col[:, 4], e[:, :, :], AX_X, ALU.max))
                    first_of_max(order, e[:, :, :], col[:, 4], pick[i][:, :, :], PER_GROUP, b[:, :, :], col[:, 1])
                    order(V.scalar_tensor_tensor(out=e[:, :, :], in0=pick[i][:, :, :], scalar=-4.0, in1=e[:, :, :],
                                                 op0=ALU.mult, op1=ALU.add))
                order(V.tensor_tensor(b[:, :, :], pick[0][:, :, :], pick[1][:, :, :], ALU.add))
                order(V.tensor_tensor(pr[:, :, :], pr[:, :, :], b[:, :, :], ALU.mult))
                order(V.tensor_reduce(col[:, 5], pr[:, :, :], AX_X, ALU.add))
                order(V.reciprocal(col[:, 5], col[:, 5]))
                order(V.tensor_tensor(pr[:, :, :], pr[:, :, :], wide(col[:, 5], PER_GROUP), ALU.mult))
                order(V.tensor_tensor(pr[:, :, :], pr[:, :, :], wide(col[:, 2], PER_GROUP), ALU.mult))
                for gi in range(GROUPS):
                    V.tensor_tensor(comb[:, gi].rearrange("p e t -> p t e"), pr[:, :, :],
                                    group[:, :, gi:gi + 1].to_broadcast([P, TT, PER_GROUP]), ALU.mult)\
                        .then_inc(combed, 1)

            @block.sync
            def _(sp):
                sp.wait_ge(combed, GROUPS)
                sp.dma_start(comb_d.rearrange("e p t -> p e t"), comb[:, :, :, :].rearrange("p g e t -> p (g e) t"))\
                    .then_inc(stored, 16)
                sp.wait_ge(stored, 16)


TURN = 4
RAW = 4
PARTS = 4


def experts(core, I, hT, comb_d, y):
    nc = core.nc
    wg, wu, wd = (I[f"w_exp_{n}_2"].rearrange("(g e) a b -> g e a b", e=TURN) for n in ("gate", "up", "down"))
    FT = D_EXP // P
    HALF = SLOT // 2
    plan = []
    for e in range(TURN):
        plan += [("rise0", e)] + ([("fall", e - 1)] if e else []) + [("rise1", e)]
    plan.append(("fall", TURN - 1))
    halves = [(u, h) for u in range(len(plan)) for h in range(2)]
    risen = {}
    fallen = {}
    for u, h in halves:
        kind, e = plan[u]
        if kind == "fall":
            fallen[e, h] = len(fallen)
        else:
            risen[e, 2 * int(kind[-1]) + h] = len(risen)
    assert len(plan) % RAW == 0 and len(halves) % PARTS == 0
    with ExitStack() as mem:
        xs = [core.sb(mem, f"me_x{n}", [P, KD, SEQ], F32R) for n in ("high", "low")]
        raw = core.sb(mem, "me_w", [P, RAW, SLOT])
        parts = [core.sb(mem, f"me_w{n}", [P, PARTS, HALF], F32R) for n in ("high", "low")]
        hid = [core.sb(mem, f"me_hid{n}", [P, 2, FT, SEQ], F32R) for n in ("high", "low")]
        gate = core.sb(mem, "me_gate", [P, 2, SEQ])
        cw = core.sb(mem, "me_comb", [P, TURN, TT])
        landed = [mem.enter_context(nc.semaphore(f"expert_landed{i}")) for i in range(RAW)]

        def fetch(sp, u, base):
            kind, e = plan[u % len(plan)]
            group, s = base + u // len(plan), u % RAW
            if kind == "fall":
                sp.dma_start(raw[:, s].rearrange("p (k n) -> p k n", k=FT),
                             wd[group, e].rearrange("(k p) n -> p k n", p=P)).then_inc(landed[s], 32)
                return
            cols = slice(256 * int(kind[-1]), 256 * int(kind[-1]) + 256)
            for i, w in enumerate((wg, wu)):
                sp.dma_start(raw[:, s, i * HALF:(i + 1) * HALF].rearrange("p (k f) -> p k f", k=KD),
                             w[group, e].rearrange("(k p) f -> p k f", p=P)[:, :, cols]).then_inc(landed[s], 16)

        def halved(u, h, which):
            n = (2 * u + h) % PARTS
            if plan[u][0] == "fall":
                return (raw[:, u % RAW].rearrange("p (k n) -> p k n", k=FT)[:, :, 512 * h:512 * (h + 1)],
                        parts[which][:, n].rearrange("p (k n) -> p k n", k=FT))
            return (raw[:, u % RAW].rearrange("p (w k f) -> p (w k) f", w=2, k=KD)[:, :, P * h:P * (h + 1)],
                    parts[which][:, n].rearrange("p (k f) -> p k f", k=2 * KD))

        with core.stage("me_zero", "me_x_high", "me_x_low") as (block, zeroed, x_high, x_low):
            @block.vector
            def _(dve):
                nc.vector.memset(y, 0.0).then_inc(zeroed, 1)
                dve.wait_ge(x_high, 1)
                split_low(nc, xs[1][:, :, :], hT[:, :, :], xs[0][:, :, :]).then_inc(x_low, 1)

            @block.scalar
            def _(act):
                split_high(nc, xs[0][:, :, :], hT[:, :, :]).then_inc(x_high, 1)

            @block.sync
            def _(sp):
                for u in range(RAW):
                    sp.sem_clear(landed[u])
                    fetch(sp, u, 0)
        core.settle()

        def turn(base, ahead):
            with core.stage("me_high", "me_low", "me_multiplied", "me_half", "me_silu", "me_hidden", "me_hid_high",
                            "me_hid_low", "me_down", "me_added", "me_comb") as (
                    block, high, low, multiplied, half_done, silu, hidden, hid_high, hid_low, down, added,
                    comb_here):
                @block.sync
                def _(sp):
                    sp.dma_start(cw[:, :, :], comb_d.rearrange("(g e) p t -> g p e t", e=TURN)[base])\
                        .then_inc(comb_here, 16)
                    for u in range(RAW, len(plan) + (RAW if ahead else 0)):
                        sp.wait_ge(low, 2 * (u - RAW) + 2)
                        if u >= len(plan):
                            sp.sem_clear(landed[u % RAW])
                        fetch(sp, u, base)

                @block.tensor
                def _(pe):
                    for i, (u, h) in enumerate(halves):
                        kind, e = plan[u]
                        pe.wait_ge(low, i + 1)
                        w = [halved(u, h, which)[1] for which in range(2)]
                        if kind == "fall":
                            pe.wait_ge(hid_low, FT * (e + 1))
                            n = fallen[e, h]
                            for t in range(TT):
                                if n >= 2:
                                    pe.wait_ge(added, 2 * (n - 2) + t + 1)
                                for f in range(FT):
                                    mm = split_product(nc, core.ps[:, 4 + 2 * (n % 2) + t, :],
                                                       [a[:, e % 2, f, t * P:(t + 1) * P] for a in hid],
                                                       [a[:, f, :] for a in w], f == 0, f == FT - 1)
                                if t == 0:
                                    mm.then_inc(down, 1)
                        else:
                            n = risen[e, 2 * int(kind[-1]) + h]
                            if n >= 4:
                                pe.wait_ge(hidden, n - 3)
                            for side in range(2):
                                for kt in range(KD):
                                    mm = split_product(nc, core.ps[:, n % 4, side * SEQ:(side + 1) * SEQ],
                                                       [a[:, side * KD + kt, :] for a in w],
                                                       [a[:, kt, :] for a in xs], kt == 0, kt == KD - 1)
                        mm.then_inc(half_done, 1)

                def waits_for(n):
                    e, f = divmod(n, FT)
                    return 1 + max(i for i, (u, h) in enumerate(halves)
                                   if plan[u] == (f"rise{f // 2}", e) and h == f % 2)

                def fall_at(e, h):
                    return 1 + max(i for i, (u, hh) in enumerate(halves) if plan[u] == ("fall", e) and hh == h)

                AHEAD = 2

                @block.scalar
                def _(act):
                    def split(i):
                        u, h = halves[i]
                        if h == 0:
                            act.wait_ge(landed[u % RAW], 32 * (u // RAW + 1))
                        if i >= PARTS:
                            act.wait_ge(half_done, i - PARTS + 1)
                        src, dst = halved(u, h, 0)
                        split_high(nc, dst, src).then_inc(high, 1)

                    def raise_(n):
                        e, f = divmod(n, FT)
                        act.wait_ge(half_done, waits_for(n))
                        if n >= 2:
                            act.wait_ge(hid_low, n - 1)
                        nc.scalar.activation(gate[:, n % 2, :], core.ps[:, n % 4, 0:SEQ], ACT.Silu).then_inc(silu, 1)
                        act.wait_ge(hidden, n + 1)
                        if e >= 2:
                            act.wait_ge(half_done, fall_at(e - 2, 1))
                        split_high(nc, hid[0][:, e % 2, f, :], gate[:, n % 2, :]).then_inc(hid_high, 1)

                    for i in range(AHEAD):
                        split(i)
                    for i, (u, h) in enumerate(halves):
                        if i + AHEAD < len(halves):
                            split(i + AHEAD)
                        if plan[u][0] != "fall":
                            raise_(risen[plan[u][1], 2 * int(plan[u][0][-1]) + h])

                @block.vector
                def _(dve):
                    def split(i):
                        u, h = halves[i]
                        dve.wait_ge(high, i + 1)
                        src, dst = halved(u, h, 1)
                        split_low(nc, dst, src, halved(u, h, 0)[1]).then_inc(low, 1)

                    def raise_(n):
                        e, f = divmod(n, FT)
                        dve.wait_ge(silu, n + 1)
                        nc.vector.tensor_tensor(gate[:, n % 2, :], gate[:, n % 2, :], core.ps[:, n % 4, SEQ:],
                                                ALU.mult).then_inc(hidden, 1)
                        dve.wait_ge(hid_high, n + 1)
                        split_low(nc, hid[1][:, e % 2, f, :], gate[:, n % 2, :], hid[0][:, e % 2, f, :])\
                            .then_inc(hid_low, 1)

                    def add(e, h):
                        n = fallen[e, h]
                        for t in range(TT):
                            if t == 0:
                                dve.wait_ge(down, n + 1)
                            else:
                                dve.wait_ge(half_done, fall_at(e, h))
                            dst = y[:, t, h * 512:(h + 1) * 512]
                            if n >= 2:
                                dve.wait_ge(added, 2 * (n - 2) + t + 1)
                            nc.vector.scalar_tensor_tensor(out=dst, in0=core.ps[:, 4 + 2 * (n % 2) + t, :],
                                                           scalar=cw[:, e, t:t + 1], in1=dst, op0=ALU.mult,
                                                           op1=ALU.add).then_inc(added, 1)

                    for i in range(AHEAD):
                        split(i)
                    dve.wait_ge(comb_here, 16)
                    for i, (u, h) in enumerate(halves):
                        if i + AHEAD < len(halves):
                            split(i + AHEAD)
                        if plan[u][0] != "fall":
                            raise_(risen[plan[u][1], 2 * int(plan[u][0][-1]) + h])
                        else:
                            add(plan[u][1], h)

        with nc.Fori(0, EXPERTS // TURN - 1, 1) as base:
            turn(base, True)
            core.settle()
        turn(EXPERTS // TURN - 1, False)


def second_block(core, I, k, x):
    nc = core.nc
    S_OFF, n_cols = offsets(S_COLS)
    with ExitStack() as mem:
        fvt = core.sb(mem, "second_vectors", [P, n_cols])
        fv = {n: fvt[:, a:b] for n, (a, b) in S_OFF.items()}
        mod = core.sb(mem, "mod2", [P, 48, 2])
        gain = core.sb(mem, "gain2", [P, KD])
        g_row = core.sb(mem, "g_row2", [P, DM])
        rstd = core.sb(mem, "rstd2", [P, TT])
        k = dict(k)
        comb_d = nc.dram_tensor("comb", [EXPERTS, P, TT], F32).ap()
        load(core, "second", [(fvt[:, :], I["second_vectors"])])
        modulation(core, "ada2", I["w_ada_2"], fv["c"].rearrange("p (v k) -> p v k", v=2), fv["ada_b"],
                   mod[:, :, :], k["ones"], [6 * DM, 2 * DM])
        with ExitStack() as mix:
            ycat = core.sb(mix, "ycat", [P, TT, DM])
            with ExitStack() as inner:
                hT = core.sb(inner, "hT2", [P, KD, NTOK])
                masks = core.sb(inner, "masks", [P, 2, M_WIDTH])
                c_off, n_consts = offsets(C_COLS)
                names = ("head_ones", "head_pick", "na_cos", "na_sin", "chunk_start")
                widths = [c_off[n][1] - c_off[n][0] for n in names]
                ct = core.sb(inner, "consts2", [P, sum(widths)])
                consts = {n: ct[:, sum(widths[:i]):sum(widths[:i + 1])] for i, n in enumerate(names)}
                norms = inner.enter_context(ExitStack())
                xc, xn = (core.sb(norms, n, [P, TT, DM]) for n in ("xc", "xn"))
                load(core, "masks", [(masks[:, d, :], I["masks"][d]) for d in range(2)]
                     + [(consts[n], I["consts"][:, c_off[n][0]:c_off[n][1]]) for n in names]
                     + [(xc[:, :, :], I["ctx"].rearrange("b (t p) d -> p (b t) d", p=P))])
                for v, src in ((1, xc), (0, x)):
                    gains(core, f"gain_v{v}", mod, v, fv["norm1"], gain[:, :], KD)
                    norm_transposed(core, f"norm_v{v}", k["ident"], src, hT, SEQ * (1 - v), gain, mod[:, 0:KD, v],
                                    (rstd, xn))
                norms.close()
                hgrn(core, I, k, fv, masks, hT[:, :, :], ycat)
                neighbourhood(core, I, k, consts, hT[:, :, :], ycat)
                rwkv(core, I, k, fv, masks, consts, hT[:, :, :], ycat)
            with ExitStack() as inner:
                yT = core.sb(inner, "yT2", [P, KD, SEQ])
                tmp = core.sb(inner, "res_tmp", [P, TT, 512])
                diag = core.sb(inner, "diag2", [P, KD, P])
                spread_rows(core, "g1", k["ident"], k["ones"], mod[:, 2 * KD:3 * KD, 0], diag[:, :, :], g_row)
                turn_features(core, "ycat_turn", k["ident"], ycat, KD, yT, fv["out_gain"])
                residual(core, "w_out2", yT, I["w_out_2"], g_row, tmp, x)
        hT = core.sb(mem, "h2T", [P, KD, SEQ])
        y = core.sb(mem, "moe_y", [P, TT, DM])
        gains(core, "gain_ffn", mod, 0, fv["norm2"], gain[:, :], 4 * KD)
        norm_transposed(core, "norm_ffn", k["ident"], x, hT, 0, gain, mod[:, 3 * KD:4 * KD, 0], (rstd, y))
        spread_rows(core, "g2", k["ident"], k["ones"], mod[:, 5 * KD:6 * KD, 0],
                    y[:, 0, :].rearrange("p (k f) -> p k f", k=KD), g_row)
        router(core, I, k, hT, comb_d)
        experts(core, I, hT, comb_d, y[:, :, :])
        with core.stage("last_order") as (block, own):
            @block.vector
            def _(dve):
                order = Order(dve, own)
                for t in range(TT):
                    order(nc.vector.tensor_tensor(y[:, t, :], y[:, t, :], g_row[:, :], ALU.mult))
                    order(nc.vector.tensor_tensor(x[:, t, :], x[:, t, :], y[:, t, :], ALU.add))


M_OFF, M_WIDTH = offsets(M_COLS)


def build(nc, I, out, second=True):
    with ExitStack() as ctx:
        core = Core(nc, ctx)
        x = core.sb(ctx, "x", [P, TT, DM])
        C_OFF, n_consts = offsets(C_COLS)
        R_OFF, n_rows = offsets(R_COLS)
        rows = core.sb(ctx, "rows", [P, n_rows])
        ones = core.sb(ctx, "ones", [P, P])
        ident = core.sb(ctx, "ident", [P, P])
        cv = I["consts"]
        pairs = [(x[:, :, :], I["x"].rearrange("b (t p) d -> p (b t) d", p=P)),
                 (rows[:, :], I["rows"].to_broadcast([P, n_rows])), (ident[:, :], cv[:, 0:P])]
        with ExitStack() as first:
            consts = core.sb(first, "consts", [P, n_consts])
            pos = core.sb(first, "pos", [P, TT], I32)
            k = {n: consts[:, a:b] for n, (a, b) in C_OFF.items()}
            k["ones"] = ones[:, :]
            k["ident"] = ident[:, :]
            k["final"] = rows[:, R_OFF["final"][0]:R_OFF["final"][1]]
            k["cos"] = core.sb(first, "cos", [P, TT, ROPE // 2])
            k["sin"] = core.sb(first, "sin", [P, TT, ROPE // 2])
            load(core, "inputs", pairs + [(consts[:, :], cv[:, 0:n_consts]),
                                          (pos[:, :], I["positions"])])
            with core.stage("ones_set") as (block, ones_set):
                @block.gpsimd
                def _(pool):
                    nc.gpsimd.memset(ones[:, :], 1.0).then_inc(ones_set, 1)
                    pool.wait_ge(ones_set, 1)
            with ExitStack() as mem:
                rotary_tables(core, mem, pos[:, :], k["inv_freq"], k["cos"][:, :, :], k["sin"][:, :, :])
            first_block(core, I, k, x)
        if second:
            second_block(core, I, dict(ident=ident[:, :], ones=ones[:, :],
                                       b_r=rows[:, R_OFF["b_rg"][0]:R_OFF["b_re"][1]],
                                       **{n: rows[:, a:b] for n, (a, b) in R_OFF.items()}), x)
        with core.stage("stored") as (block, stored):
            @block.sync
            def _(sp):
                sp.dma_start(out.rearrange("b (t p) d -> p (b t) d", p=P), x[:, :, :]).then_inc(stored, 16)
                sp.wait_ge(stored, 16)
        core.settle()


def columns(n, *arrays):
    return np.concatenate([a.reshape(-1, P).T for a in arrays], axis=1)


def head_rows(a):
    out = np.zeros((P, a.shape[1]), np.float32)
    out[:a.shape[0]] = a
    return out


def constants():
    p, q = np.arange(P)[:, None], np.arange(P)[None, :]
    ident = (p == q).astype(np.float32)
    sel = np.zeros((P, HEADS, P), np.float32)
    for h in range(HEADS):
        sel[h, h] = 1.0
    diag = np.where(p <= q, 0.0, MASKED)
    mla = np.zeros((P, TT, SEQ))
    for t in range(TT):
        mla[:, t] = np.where(np.arange(SEQ)[None, :] // 64 <= (t * P + p) // 64, 0.0, MASKED)
    quarter = HD // 4
    inv = (10000.0 ** (-np.arange(quarter, dtype=np.float32) / quarter)).astype(np.float32)
    pos = np.arange(SEQ)
    ang = np.concatenate([(pos // GRID_W).astype(np.float32)[:, None] * inv,
                          (pos % GRID_W).astype(np.float32)[:, None] * inv], axis=1)
    turn = lambda a: a.reshape(TT, P, 32).transpose(1, 0, 2).reshape(P, -1)
    half = ROPE // 2
    inv_freq = np.float32(10000.0) ** (-np.arange(half, dtype=np.float32) / np.float32(half))
    start = np.tile((np.arange(NTOK) % RW_CHUNK != 0).astype(np.float32), (P, 1))
    parts = dict(ident=ident, head_ones=(p // HD == q // HD), head_pick=(p // HD == np.arange(2)[None, :]),
                 inv_freq=np.tile(inv_freq, (P, 1)), sel=sel.reshape(P, -1),
                 ml_mask=np.concatenate([diag, 0 * diag], axis=1), mla_mask=mla.reshape(P, -1),
                 na_cos=turn(np.cos(ang)), na_sin=turn(np.sin(ang)), chunk_start=start,
                 ones_row=np.ones((P, SEQ)))
    consts = np.concatenate([parts[n].astype(np.float32) for n in C_COLS], axis=1)
    levels = [(q // b == p // b + 1) & ((q // b) % 2 == 1) for b in LEVELS]
    chunk = p // RW_CHUNK == q // RW_CHUNK
    masks = []
    for forward in (True, False):
        cols = [ident] + levels + [chunk & (p < q), chunk & (p <= q)]
        masks.append(np.concatenate([(m if forward else m.T).astype(np.float32) for m in cols], axis=1))
    return consts, np.stack(masks)


def window_bias(rpb):
    q = np.arange(SEQ)
    qr, qc = q[:, None] // GRID_W, q[:, None] % GRID_W
    kr, kc = q[None, :] // GRID_W, q[None, :] % GRID_W
    start = np.clip(qc - 8, 0, GRID_W - 16)
    inside = (kc >= start) & (kc < start + 16)
    cols = np.clip(kc - qc + 15, 0, 30)
    b = np.where(inside[None], rpb[:, kr - qr + 7, cols], np.float32(MASKED))
    return np.ascontiguousarray(b.reshape(C_HEADS, TT, P, SEQ).transpose(1, 2, 0, 3))


def layouts(a):
    d = {n: a[n] for n in ("x", "positions", "ada_w", "w_in", "w_uq", "w_ukv", "w_br_mla", "w_br_mlstm", "w_out",
                           "ffn_w_up", "ffn_w_down")}
    d["positions"] = a["positions"].reshape(TT, P).T
    layers = []
    for l in range(DEPTH):
        parts = dict(c=columns(8, a["c"][0]), ada_b=columns(48, a["ada_b"][l]), norm_mix=columns(8, a["norm_mix_w"][l]),
                     q_norm=columns(3, a["q_norm_w"][l]), kv_norm=columns(2, a["kv_norm_w"][l]),
                     conv_w=columns(32, *a["mlstm_conv_w"][l]), conv_b=columns(8, a["mlstm_conv_b"][l]),
                     head_norm=columns(4, a["mlstm_head_norm_w"][l]), norm_ffn=columns(8, a["norm_ffn_w"][l]),
                     ffn_conv_w=columns(3, *a["ffn_conv_w"][l]), ffn_conv_b=columns(44, a["ffn_conv_b"][l]),
                     gate_b=head_rows(a["mlstm_gate_b"][l].reshape(2, HEADS).T))
        layers.append(np.concatenate([parts[n] for n in L_COLS], axis=1))
    d["layer_vectors"] = np.stack(layers)
    s = {n[:-2]: v[0] for n, v in a.items() if n.endswith("_2") and n != "c_ctx_2"}
    gn = np.concatenate([s["hgrn_gn_gain"].reshape(-1), np.ones(DM - A_W, np.float32)])
    parts = dict(c=np.stack([columns(8, s["c"]), columns(8, a["c_ctx_2"])], axis=1).reshape(P, -1),
                 ada_b=columns(48, s["b_ada"]), norm1=columns(8, s["norm1_gain"]), norm2=columns(8, s["norm2_gain"]),
                 lb=columns(4, a["hgrn_lb_logits_2"][:, 0]), out_gain=columns(8, gn), mu=columns(9, s["rwkv_mu"]),
                 w0=columns(4, s["rwkv_w0"]), a0=columns(4, s["rwkv_a0"]), kk_scale=columns(2, s["rwkv_kk_scale"]),
                 k_a=columns(2, s["rwkv_k_a"]), r_k=columns(2, s["rwkv_r_k"]))
    d["second_vectors"] = np.concatenate([parts[n] for n in S_COLS], axis=1)
    rows = dict(final=a["final_norm_w"], ln_gain=s["rwkv_ln_gain"], ln_bias=s["rwkv_ln_bias"], q_gain=s["na_q_gain"],
                k_gain=s["na_k_gain"], b_rg=s["b_router_group"], b_re=s["b_router_expert"])
    d["rows"] = np.concatenate([rows[n] for n in R_COLS])[None, :]
    d["ctx"] = s["ctx"][None]
    for n in ("w_ada", "w_in", "w_out", "w_exp_gate", "w_exp_up", "w_exp_down"):
        d[n + "_2"] = s[n].reshape((EXPERTS,) + s[n].shape[2:]) if s[n].ndim == 4 else s[n]
    d["rwkv_up"] = np.concatenate([s["rwkv_w_up"].reshape(P, A_W), s["rwkv_a_up"].reshape(P, A_W),
                                   s["rwkv_g_up"]], axis=1)
    d["router"] = np.concatenate([s["w_router_group"], s["w_router_expert"]], axis=1)
    d["bias"] = window_bias(s["na_rpb"])
    d["consts"], d["masks"] = constants()
    return {n: np.ascontiguousarray(v) for n, v in d.items()}


def kernel(**inputs):
    import concourse.bacc as bacc
    from concourse.bass_utils import run_bass_kernel_spmd

    nc = bacc.Bacc("TRN2", target_bir_lowering=False, num_devices=1)
    arrays = layouts({n: np.asarray(v) for n, v in inputs.items()})
    I = {n: nc.dram_tensor(n, v.shape, mybir.dt.from_np(v.dtype), kind="ExternalInput").ap()
         for n, v in arrays.items()}
    out = nc.dram_tensor("out", (1, SEQ, DM), F32, kind="ExternalOutput").ap()
    build(nc, I, out)
    r = run_bass_kernel_spmd(nc, [arrays], core_ids=[0])
    return r.results[0]["out"]
```

```python
from contextlib import ExitStack, contextmanager

import numpy as np

import concourse.bass as bass
from concourse import mybir

F32 = mybir.dt.float32
F32R = mybir.dt.float32r
I32 = mybir.dt.int32
ALU = mybir.AluOpType
ACT = mybir.ActivationFunctionType
AX_X = mybir.AxisListType.X

P = 128
DM = 1024
KD = DM // P
SEQ = 256
TT = SEQ // P
DEPTH = 2
EPS = 1e-6
MASKED = -1e30

Q_LORA, KV_LORA, ROPE = 384, 256, 32
NOPE, VH = 64, 64
HEADS = 8
QK = NOPE + ROPE
ML_W = 512
LATENT = Q_LORA + KV_LORA + ROPE
ML_AT = LATENT
GATE_AT = ML_AT + 4 * ML_W
BR_AT = GATE_AT + 2 * HEADS
D_FF = 2816
FF_TILES = D_FF // P

GRID_W = 64
A_HEADS = B_HEADS = 4
HD = 64
A_W = A_HEADS * HD
B_AT = 5 * A_W
B_PROJ = 3 * A_W + 4 * 64 + 128
B_TILES = B_PROJ // P
C_AT = B_AT + B_PROJ
C_HEADS = 8
C_W = C_HEADS * HD
GROUPS, PER_GROUP = 4, 8
EXPERTS = GROUPS * PER_GROUP
D_EXP = 512
RW_CHUNK = 64
NTOK = 2 * SEQ
NT4 = NTOK // P

L_COLS = dict(c=8, ada_b=48, norm_mix=8, q_norm=3, kv_norm=2, conv_w=32, conv_b=8, head_norm=4,
              norm_ffn=8, ffn_conv_w=3 * 2 * FF_TILES, ffn_conv_b=2 * FF_TILES, gate_b=2)
S_COLS = dict(c=16, ada_b=48, norm1=8, norm2=8, lb=4, out_gain=8, mu=B_TILES, w0=4, a0=4,
              kk_scale=2, k_a=2, r_k=2)
R_COLS = dict(final=DM, ln_gain=A_W, ln_bias=A_W, q_gain=HD, k_gain=HD, b_rg=GROUPS, b_re=EXPERTS)
LEVELS = (1, 2, 4, 8, 16, 32, 64)
C_COLS = dict(ident=P, head_ones=P, head_pick=2, inv_freq=ROPE // 2, sel=HEADS * P, ml_mask=2 * P,
              mla_mask=2 * SEQ, na_cos=2 * 32, na_sin=2 * 32, chunk_start=NTOK, ones_row=SEQ)
M_COLS = dict(ident=P, lv=len(LEVELS) * P, strict=P, incl=P)


def offsets(cols):
    out, at = {}, 0
    for name, n in cols.items():
        out[name] = (at, at + n)
        at += n
    return out, at


class Order:

    def __init__(self, eng, sem):
        self.eng, self.sem, self.n = eng, sem, 0

    def __call__(self, ins):
        self.n += 1
        ins.then_inc(self.sem, 1)
        self.eng.wait_ge(self.sem, self.n)


class Core:

    def __init__(self, nc, ctx):
        self.nc, self.ctx = nc, ctx
        self.spent, self.number, self.tensors = [], 0, 0
        self.ps = ctx.enter_context(nc.psum_tensor("ps", [P, 8, 512], F32))

    def sb(self, mem, name, shape, dt=F32):
        self.tensors += 1
        return mem.enter_context(self.nc.sbuf_tensor(f"{name}_{self.tensors}", shape, dt))

    def clear_spent(self):
        for s in self.spent:
            self.nc.gpsimd.sem_clear(s)

    @contextmanager
    def stage(self, *names):
        before = self.spent
        self.clear_spent()
        self.number += 1
        sems = [self.nc.alloc_semaphore(f"{n}_{self.number}") for n in names]
        with self.nc.Block(no_gpsimd_drain=True) as block:
            yield (block, *sems)
        self.nc.extend_free_semaphores([s.num for s in before])
        self.spent = sems

    def settle(self):
        with self.stage():
            pass


def products(core, what, n, multiply, evacuate, on_scalar=None, banks=8):
    nc = core.nc
    on_scalar = on_scalar or (lambda i: False)
    by_scalar = [on_scalar(i) for i in range(n)]
    with core.stage(f"{what}_multiplied", f"{what}_read_v", f"{what}_read_s", f"{what}_order_v",
                    f"{what}_order_s") as (block, multiplied, read_v, read_s, order_v, order_s):
        def bank(i):
            return core.ps[:, i % banks, :]

        @block.tensor
        def _(pe):
            for i in range(n):
                if i >= banks:
                    j = i - banks
                    if by_scalar[j]:
                        pe.wait_ge(read_s, sum(by_scalar[:j + 1]))
                    else:
                        pe.wait_ge(read_v, j + 1 - sum(by_scalar[:j + 1]))
                multiply(i, bank(i)).then_inc(multiplied, 1)

        @block.vector
        def _(dve):
            order = Order(dve, order_v)
            for i in range(n):
                if not by_scalar[i]:
                    dve.wait_ge(multiplied, i + 1)
                    evacuate(i, bank(i), nc.vector, order).then_inc(read_v, 1)

        @block.scalar
        def _(act):
            order = Order(act, order_s)
            for i in range(n):
                if by_scalar[i]:
                    act.wait_ge(multiplied, i + 1)
                    evacuate(i, bank(i), nc.scalar, order).then_inc(read_s, 1)


def odd(i):
    return i % 2 == 1


def copy(nc, eng, out, in_, scale=None, bias=None):
    if eng is nc.scalar:
        return eng.activation(out, in_, ACT.Identity if bias is not None else ACT.Copy,
                              bias=0.0 if bias is None else bias, scale=1.0 if scale is None else scale)
    if scale is None:
        return eng.tensor_copy(out, in_)
    if bias is None:
        return eng.tensor_scalar(out, in_, scale, None, ALU.mult)
    return eng.tensor_scalar(out, in_, scale, bias, ALU.mult, ALU.add)


SLOT = KD * 512
STAGES = 2


def split_high(nc, high, x):
    return nc.scalar.activation(high, x, ACT.Copy)


def split_low(nc, low, x, high):
    return nc.vector.tensor_tensor(low, x, high.bitcast(F32), ALU.subtract)


def split_product(nc, out, left, right, start, stop):
    (lh, ll), (rh, rl) = left, right
    nc.tensor.matmul(out, lh, rh, start=start, stop=False)
    nc.tensor.matmul(out, lh, rl, start=False, stop=False)
    return nc.tensor.matmul(out, ll, rh, start=False, stop=stop)


def linear(core, what, xT, w, chunks, evacuate, on_scalar=None, banks=8):
    nc = core.nc
    xT = xT[:, :, :]
    kt = w.shape[0] // P
    tokens = xT.shape[2]

    def pieces(j):
        n = -(-kt // (4 if j == 0 else 2))
        return [(k, min(k + n, kt)) for k in range(0, kt, n)]

    before = [sum(len(pieces(i)) for i in range(j)) for j in range(len(chunks) + 1)]
    wv = w.rearrange("(k p) n -> p k n", p=P)
    units = []
    for j, (c0, width, tiles) in enumerate(chunks):
        units += [(j, t) for t in (range(width // P) if tiles is None else tiles)]
    last_unit = [max(i for i, u in enumerate(units) if u[0] == j) for j in range(len(chunks))]
    by_scalar = [bool(on_scalar and on_scalar(i)) for i in range(len(units))]
    size = kt * max(width for _, width, _ in chunks)

    def bank(i):
        return core.ps[:, i % banks, :]

    with ExitStack() as mem:
        xs = [core.sb(mem, f"{what}_x{n}", [P, kt, tokens], F32R) for n in ("high", "low")]
        raw = core.sb(mem, f"{what}_w", [P, STAGES, size])
        parts = [core.sb(mem, f"{what}_w{n}", [P, STAGES, size], F32R) for n in ("high", "low")]

        def slot(buffer, j):
            return buffer[:, j % STAGES, 0:kt * chunks[j][1]].rearrange("p (k n) -> p k n", k=kt)

        with core.stage(f"{what}_multiplied", f"{what}_read_v", f"{what}_read_s", f"{what}_order_v",
                        f"{what}_order_s", f"{what}_x_high", f"{what}_x_low", f"{what}_high", f"{what}_low",
                        *[f"{what}_landed{s}" for s in range(STAGES)],
                        *[f"{what}_first{s}" for s in range(len(pieces(0)))]) as (
                block, multiplied, read_v, read_s, order_v, order_s, x_high, x_low, high, low, *arrived):
            landed, first = arrived[:STAGES], arrived[STAGES:]

            @block.sync
            def _(sp):
                for n, (a, b) in enumerate(pieces(0)):
                    sp.dma_start(slot(raw, 0)[:, a:b, :], wv[:, a:b, chunks[0][0]:chunks[0][0] + chunks[0][1]])\
                        .then_inc(first[n], 16)
                for j in range(1, len(chunks)):
                    c0, width, _ = chunks[j]
                    if j >= STAGES:
                        sp.wait_ge(low, before[j - STAGES + 1])
                    sp.dma_start(slot(raw, j), wv[:, :, c0:c0 + width]).then_inc(landed[j % STAGES], 16)

            @block.tensor
            def _(pe):
                pe.wait_ge(x_low, 1)
                for i, (j, t) in enumerate(units):
                    fresh = i == 0 or units[i - 1][0] != j
                    if i >= banks:
                        r = i - banks
                        if by_scalar[r]:
                            pe.wait_ge(read_s, sum(by_scalar[:r + 1]))
                        else:
                            pe.wait_ge(read_v, r + 1 - sum(by_scalar[:r + 1]))
                    _, width, tiles = chunks[j]
                    for k in range(kt):
                        starts = [a for a, b in pieces(j)]
                        if fresh and k in starts:
                            pe.wait_ge(low, before[j] + 1 + starts.index(k))
                        if tiles is None:
                            mm = split_product(nc, bank(i)[:, 0:tokens],
                                               [slot(a, j)[:, k, t * P:(t + 1) * P] for a in parts],
                                               [a[:, k, :] for a in xs], k == 0, k == kt - 1)
                        else:
                            mm = split_product(nc, bank(i)[:, 0:width], [a[:, k, t * P:(t + 1) * P] for a in xs],
                                               [slot(a, j)[:, k, :] for a in parts], k == 0, k == kt - 1)
                    mm.then_inc(multiplied, 1)

            @block.vector
            def _(dve):
                order = Order(dve, order_v)
                dve.wait_ge(x_high, 1)
                split_low(nc, xs[1][:, :, :], xT, xs[0][:, :, :]).then_inc(x_low, 1)

                def split(j):
                    for n, (a, b) in enumerate(pieces(j)):
                        dve.wait_ge(high, before[j] + n + 1)
                        if j >= STAGES and n == 0:
                            dve.wait_ge(multiplied, last_unit[j - STAGES] + 1)
                        split_low(nc, slot(parts[1], j)[:, a:b, :], slot(raw, j)[:, a:b, :],
                                  slot(parts[0], j)[:, a:b, :]).then_inc(low, 1)

                def read(j):
                    for i, (jj, t) in enumerate(units):
                        if jj == j and not by_scalar[i]:
                            dve.wait_ge(multiplied, i + 1)
                            evacuate(j, t, bank(i), nc.vector, order).then_inc(read_v, 1)

                for j in range(len(chunks)):
                    if j >= STAGES:
                        read(j - STAGES)
                    split(j)
                for j in range(max(0, len(chunks) - STAGES), len(chunks)):
                    read(j)

            @block.scalar
            def _(act):
                order = Order(act, order_s)
                split_high(nc, xs[0][:, :, :], xT).then_inc(x_high, 1)

                def split(j):
                    for n, (a, b) in enumerate(pieces(j)):
                        if j == 0:
                            act.wait_ge(first[n], 16)
                        elif n == 0:
                            act.wait_ge(landed[j % STAGES], 16 * (j // STAGES + (j % STAGES > 0)))
                        if j >= STAGES and n == 0:
                            act.wait_ge(multiplied, last_unit[j - STAGES] + 1)
                        split_high(nc, slot(parts[0], j)[:, a:b, :], slot(raw, j)[:, a:b, :]).then_inc(high, 1)

                def read(j):
                    for i, (jj, t) in enumerate(units):
                        if jj == j and by_scalar[i]:
                            act.wait_ge(multiplied, i + 1)
                            evacuate(j, t, bank(i), nc.scalar, order).then_inc(read_s, 1)

                for j in range(len(chunks)):
                    if j >= STAGES:
                        read(j - STAGES)
                    split(j)
                for j in range(max(0, len(chunks) - STAGES), len(chunks)):
                    read(j)


def load(core, what, pairs):
    with core.stage(f"{what}_landed") as (block, landed):
        @block.sync
        def _(sp):
            for dst, src in pairs:
                sp.dma_start(dst, src).then_inc(landed, 16)
            sp.wait_ge(landed, 16 * len(pairs))


def inverse_rms(core, what, parts, out, junk, width, eps=EPS):
    nc = core.nc
    n = len(parts)
    with core.stage(f"{what}_squared", f"{what}_meaned", f"{what}_rooted", f"{what}_done") as (
            block, squared, meaned, rooted, done):
        @block.scalar
        def _(act):
            order = Order(act, squared)
            for i, part in enumerate(parts):
                order(nc.scalar.activation(junk[:, 0:width], part, ACT.Square, accum_out=out[:, i:i + 1]))
            act.wait_ge(meaned, 1)
            nc.scalar.activation(out[:, 0:n], out[:, 0:n], ACT.Sqrt).then_inc(rooted, 1)

        @block.vector
        def _(dve):
            dve.wait_ge(squared, n)
            nc.vector.tensor_scalar(out[:, 0:n], out[:, 0:n], 1.0 / width, eps, ALU.mult, ALU.add)\
                .then_inc(meaned, 1)
            dve.wait_ge(rooted, 1)
            nc.vector.reciprocal(out[:, 0:n], out[:, 0:n]).then_inc(done, 1)


def head_inverse_rms(core, what, x, sq, out, tiles, heads, eps=EPS):
    nc = core.nc
    flat = out.rearrange("p t h -> p (t h)")
    with core.stage(f"{what}_order", f"{what}_meaned", f"{what}_rooted") as (block, own, meaned, rooted):
        @block.vector
        def _(dve):
            order = Order(dve, own)
            for t in range(tiles):
                order(nc.vector.tensor_tensor(sq[:, t], x[:, t], x[:, t], ALU.mult))
                order(nc.vector.tensor_reduce(out[:, t, :], sq[:, t], AX_X, ALU.add))
            nc.vector.tensor_scalar(flat, flat, 1.0 / HD, eps, ALU.mult, ALU.add).then_inc(meaned, 1)
            dve.wait_ge(rooted, 1)
            order(nc.vector.reciprocal(flat, flat))

        @block.scalar
        def _(act):
            act.wait_ge(meaned, 1)
            nc.scalar.activation(flat, flat, ACT.Sqrt).then_inc(rooted, 1)


def norm_transposed(core, what, ident, x, hT, at, gain, shift, mem_junk):
    nc = core.nc
    rstd, xn = mem_junk
    inverse_rms(core, f"{what}_rms", [x[:, t, :] for t in range(TT)], rstd, xn[:, 0, :], DM)
    with core.stage(f"{what}_scaled") as (block, scaled):
        @block.vector
        def _(dve):
            nc.vector.tensor_scalar(xn[:, 0, :], x[:, 0, :], rstd[:, 0:1], None, ALU.mult).then_inc(scaled, 1)

        @block.scalar
        def _(act):
            nc.scalar.activation(xn[:, 1, :], x[:, 1, :], ACT.Copy, scale=rstd[:, 1:2]).then_inc(scaled, 1)

    def turn(i, bank):
        for t in range(TT):
            ins = nc.tensor.transpose(bank[:, t * P:(t + 1) * P], xn[:, t, i * P:(i + 1) * P], ident)
        return ins

    def out(i, bank, eng, order):
        return copy(nc, eng, hT[:, i, at:at + SEQ], bank[:, 0:SEQ], gain[:, i:i + 1], shift[:, i:i + 1])

    products(core, f"{what}_turn", KD, turn, out, odd)


def modulation(core, what, w, c, bias, mod, ones, widths):
    nc = core.nc
    n = 6 * DM // 512
    slots = 4
    wv = w.rearrange("(k p) n -> p k n", p=P)
    jobs = [(j, v) for j in range(n) for v in range(len(widths)) if 512 * j < widths[v]]
    with ExitStack() as mem:
        raw = core.sb(mem, f"{what}_w", [P, slots, KD, 512])
        acc = core.sb(mem, f"{what}_acc", [P, len(widths), 6 * DM])
        with core.stage(f"{what}_silu", f"{what}_order", f"{what}_summed", f"{what}_multiplied", f"{what}_added",
                        *[f"{what}_landed{s}" for s in range(slots)]) as (
                block, silu, own, summed, multiplied, added, *landed):
            @block.scalar
            def _(act):
                nc.scalar.activation(c, c, ACT.Silu).then_inc(silu, 1)

            @block.sync
            def _(sp):
                for j in range(n):
                    if j >= slots:
                        sp.wait_ge(summed, 1 + max(i for i, job in enumerate(jobs) if job[0] == j - slots))
                    sp.dma_start(raw[:, j % slots], wv[:, :, j * 512:(j + 1) * 512]).then_inc(landed[j % slots], 16)

            @block.vector
            def _(dve):
                order = Order(dve, own)
                dve.wait_ge(silu, 1)
                for j, v in jobs:
                    dve.wait_ge(landed[j % slots], 16 * (j // slots + 1))
                    a = acc[:, v, j * 512:(j + 1) * 512]
                    order(nc.vector.tensor_scalar(a, raw[:, j % slots, 0, :], c[:, v, 0:1], None, ALU.mult))
                    for k in range(1, KD):
                        ins = nc.vector.scalar_tensor_tensor(out=a, in0=raw[:, j % slots, k, :],
                                                             scalar=c[:, v, k:k + 1], in1=a, op0=ALU.mult,
                                                             op1=ALU.add)
                        if k < KD - 1:
                            order(ins)
                    ins.then_inc(summed, 1)
                dve.wait_ge(multiplied, len(jobs))
                for v, width in enumerate(widths):
                    m = width // P
                    nc.vector.tensor_tensor(mod[:, 0:m, v], core.ps[:, v, 0:m], bias[:, 0:m], ALU.add)\
                        .then_inc(added, 1)

            @block.tensor
            def _(pe):
                for i, (j, v) in enumerate(jobs):
                    pe.wait_ge(summed, i + 1)
                    for m in range(4 * j, 4 * j + 4):
                        mm = nc.tensor.matmul(core.ps[:, v, m:m + 1], acc[:, v, m * P:(m + 1) * P], ones[:, 0:1],
                                              start=True, stop=True)
                    mm.then_inc(multiplied, 1)


def spread_rows(core, what, ident, ones, cols, diag, out):
    nc = core.nc
    with core.stage(f"{what}_diag") as (block, made):
        @block.vector
        def _(dve):
            nc.vector.tensor_tensor(diag, ident.unsqueeze(1).to_broadcast([P, KD, P]),
                                    cols.unsqueeze(2).to_broadcast([P, KD, P]), ALU.mult).then_inc(made, 1)

    def mult(i, bank):
        for k in range(4):
            mm = nc.tensor.matmul(bank[:, k * P:(k + 1) * P], ones, diag[:, 4 * i + k, :], start=True, stop=True)
        return mm

    def out_(i, bank, eng, order):
        return copy(nc, eng, out[:, i * 512:(i + 1) * 512], bank)

    products(core, f"{what}_spread", 2, mult, out_, odd)


def gains(core, what, mod, v, norm, out, at_scale):
    nc = core.nc
    with core.stage(f"{what}_made") as (block, made):
        @block.vector
        def _(dve):
            nc.vector.scalar_tensor_tensor(out=out, in0=mod[:, at_scale:at_scale + KD, v], scalar=1.0, in1=norm,
                                           op0=ALU.add, op1=ALU.mult).then_inc(made, 1)


def attention(core, what, mem, ident, heads, keys, d, qT, kT, scale, mask, masked_keys, value, out, scratch):
    nc = core.nc
    n = heads * TT
    kt = keys // P
    s, pT = (a.rearrange("p (n k) -> p n k", n=n) for a in scratch)
    top = core.sb(mem, f"{what}_top", [P, n])
    total = core.sb(mem, f"{what}_total", [P, n])

    def score(i, bank):
        t, h = divmod(i, heads)
        return nc.tensor.matmul(bank[:, 0:keys], qT(h, t), kT(h), start=True, stop=True)

    def masked(i, bank, eng, order):
        t, h = divmod(i, heads)
        ins = nc.vector.scalar_tensor_tensor(out=s[:, i, 0:masked_keys], in0=bank[:, 0:masked_keys], scalar=scale,
                                             in1=mask(h, t), op0=ALU.mult, op1=ALU.add)
        if masked_keys < keys:
            order(ins)
            ins = nc.vector.tensor_scalar(s[:, i, masked_keys:keys], bank[:, masked_keys:keys], scale, None, ALU.mult)
        return ins

    products(core, f"{what}_score", n, score, masked)

    with core.stage(f"{what}_topped", f"{what}_exped", f"{what}_summed") as (block, topped, exped, summed):
        @block.vector
        def _(dve):
            for i in range(n):
                nc.vector.tensor_reduce(top[:, i:i + 1], s[:, i, :], AX_X, ALU.max, negate=True).then_inc(topped, 1)
            dve.wait_ge(exped, n)
            nc.vector.reciprocal(total[:, :], total[:, :]).then_inc(summed, 1)

        @block.scalar
        def _(act):
            for i in range(n):
                act.wait_ge(topped, i + 1)
                nc.scalar.activation(s[:, i, :], s[:, i, :], ACT.Exp, bias=top[:, i:i + 1],
                                     accum_out=total[:, i:i + 1]).then_inc(exped, 1)

    def turn(i, bank):
        for k in range(kt):
            ins = nc.tensor.transpose(bank[:, k * P:(k + 1) * P], s[:, i, k * P:(k + 1) * P], ident)
        return ins

    def turned(i, bank, eng, order):
        return copy(nc, eng, pT[:, i, :], bank[:, 0:keys])

    products(core, f"{what}_turn", n, turn, turned, odd)

    def weigh(i, bank):
        for h in range(heads):
            for k in range(kt):
                mm = nc.tensor.matmul(bank[:, h * HD:(h + 1) * HD], pT[:, i * heads + h, k * P:(k + 1) * P],
                                      value(h, k), start=(k == 0), stop=(k == kt - 1))
        return mm

    def normed(i, bank, eng, order):
        return nc.vector.tensor_tensor(out(i), bank.rearrange("p (h d) -> p h d", d=HD),
                                       total[:, i * heads:(i + 1) * heads].unsqueeze(2)
                                       .to_broadcast([P, heads, HD]), ALU.mult)

    products(core, f"{what}_weigh", TT, weigh, normed)


def turn_features(core, what, ident, src, tiles, yT, scale=None):
    nc = core.nc

    def turn(i, bank):
        for t in range(TT):
            ins = nc.tensor.transpose(bank[:, t * P:(t + 1) * P], src[:, t, i * P:(i + 1) * P], ident)
        return ins

    def out(i, bank, eng, order):
        return copy(nc, eng, yT[:, i, :], bank[:, 0:SEQ], None if scale is None else scale[:, i:i + 1])

    products(core, what, tiles, turn, out, odd)


def rotary_tables(core, mem, pos, inv, cos, sin):
    nc = core.nc
    n = ROPE // 2
    posf = core.sb(mem, "posf", [P, TT])
    ang = core.sb(mem, "ang", [P, TT, n])
    turns = core.sb(mem, "turns", [P, TT, n])
    over = core.sb(mem, "over", [P, TT, n])
    two_pi = 2 * np.pi
    c1 = 6.28125
    c2 = float(np.float32(np.round((two_pi - c1) * 2 ** 21) / 2 ** 21))
    c3 = float(two_pi - c1 - c2)
    pi = 3.1415925
    magic = 12582912.0
    with core.stage("rotary_order", "rotary_reduced", "rotary_done") as (block, own, reduced, done):
        @block.vector
        def _(dve):
            order = Order(dve, own)
            order(nc.vector.tensor_copy(posf[:, :], pos))
            order(nc.vector.tensor_tensor(ang[:, :, :], posf[:, :].unsqueeze(2).to_broadcast([P, TT, n]),
                                          inv.unsqueeze(1).to_broadcast([P, TT, n]), ALU.mult))
            order(nc.vector.tensor_scalar(turns[:, :, :], ang[:, :, :], 1.0 / two_pi, None, ALU.mult))
            order(nc.vector.tensor_scalar(turns[:, :, :], turns[:, :, :], magic, None, ALU.add))
            order(nc.vector.tensor_scalar(turns[:, :, :], turns[:, :, :], magic, None, ALU.subtract))
            for c in (c1, c2, c3):
                order(nc.vector.scalar_tensor_tensor(out=ang[:, :, :], in0=turns[:, :, :], scalar=-c,
                                                     in1=ang[:, :, :], op0=ALU.mult, op1=ALU.add))
            order(nc.vector.tensor_scalar(sin, ang[:, :, :], pi, -pi, ALU.min, ALU.max))
            order(nc.vector.tensor_scalar(ang[:, :, :], ang[:, :, :], np.pi / 2, None, ALU.add))
            order(nc.vector.tensor_scalar(over[:, :, :], ang[:, :, :], np.pi, two_pi, ALU.is_gt, ALU.mult))
            order(nc.vector.tensor_tensor(ang[:, :, :], ang[:, :, :], over[:, :, :], ALU.subtract))
            nc.vector.tensor_scalar(cos, ang[:, :, :], pi, -pi, ALU.min, ALU.max).then_inc(reduced, 1)

        @block.scalar
        def _(act):
            act.wait_ge(reduced, 1)
            nc.scalar.activation(sin, sin, ACT.Sin).then_inc(done, 1)
            nc.scalar.activation(cos, cos, ACT.Sin).then_inc(done, 1)


def rotate(nc, order, x1, x2, cos, sin, tmp):
    a, b, c = tmp
    order(nc.vector.tensor_tensor(a, x2, sin, ALU.mult))
    order(nc.vector.tensor_tensor(b, x1, sin, ALU.mult))
    order(nc.vector.tensor_tensor(c, x1, cos, ALU.mult))
    order(nc.vector.tensor_tensor(x1, c, a, ALU.subtract))
    order(nc.vector.tensor_tensor(c, x2, cos, ALU.mult))
    order(nc.vector.tensor_tensor(x2, c, b, ALU.add))


def mla(core, layer_in, k, lat, yT):
    nc, ident = core.nc, k["ident"]
    with ExitStack() as mem:
        rs = core.sb(mem, "lat_rs", [P, 4])
        latT = core.sb(mem, "latT", [P, 5, SEQ])
        q_space = core.sb(mem, "q", [P, TT * HEADS * QK])
        q = q_space[:, :].rearrange("p (t h d) -> p t h d", t=TT, h=HEADS)
        kk = core.sb(mem, "kk", [P, TT, HEADS, QK])
        v = core.sb(mem, "v", [P, TT, HEADS, VH])
        qkT = core.sb(mem, "qkT", [QK, HEADS, 4 * P])
        tmp = core.sb(mem, "rot", [P, 3, HEADS, ROPE // 2])
        junk = q_space[:, 0:Q_LORA]
        y = q_space[:, 0:TT * HEADS * VH].rearrange("p (t h d) -> p t h d", t=TT, h=HEADS)
        inverse_rms(core, "cq_rms", [lat[:, t, 0:Q_LORA] for t in range(TT)], rs[:, 0:2], junk, Q_LORA)
        inverse_rms(core, "ckv_rms", [lat[:, t, Q_LORA:Q_LORA + KV_LORA] for t in range(TT)], rs[:, 2:4],
                    junk, KV_LORA)
        with core.stage("lat_scaled") as (block, scaled):
            @block.vector
            def _(dve):
                for t in range(TT):
                    for j, (a, b) in enumerate(((0, Q_LORA), (Q_LORA, Q_LORA + KV_LORA))):
                        nc.vector.tensor_scalar(lat[:, t, a:b], lat[:, t, a:b], rs[:, 2 * j + t:2 * j + t + 1],
                                                None, ALU.mult).then_inc(scaled, 1)
        turn_features(core, "lat_turn", ident, lat, 5, latT, k["lat_gain"])

        def q_out(j, t, bank, eng, order):
            return copy(nc, eng, q[:, t, 4 * j:4 * j + 4, :], bank[:, 0:4 * QK].rearrange("p (h d) -> p h d", d=QK))
        linear(core, "uq", latT[:, 0:3, :], layer_in("w_uq"),
               [(0, 4 * QK, range(TT)), (4 * QK, 4 * QK, range(TT))], q_out, odd)

        def kv_out(j, t, bank, eng, order):
            kv = bank.rearrange("p (h d) -> p h d", d=NOPE + VH)
            order(copy(nc, eng, kk[:, t, 4 * j:4 * j + 4, 0:NOPE], kv[:, :, 0:NOPE]))
            return copy(nc, eng, v[:, t, 4 * j:4 * j + 4, :], kv[:, :, NOPE:])
        linear(core, "ukv", latT[:, 3:5, :], layer_in("w_ukv"),
               [(0, 512, range(TT)), (512, 512, range(TT))], kv_out, odd)

        with core.stage("rope_order") as (block, own):
            @block.vector
            def _(dve):
                order = Order(dve, own)
                half = ROPE // 2
                for t in range(TT):
                    cos = k["cos"][:, t, :].unsqueeze(1).to_broadcast([P, HEADS, half])
                    sin = k["sin"][:, t, :].unsqueeze(1).to_broadcast([P, HEADS, half])
                    rotate(nc, order, q[:, t, :, NOPE:NOPE + half], q[:, t, :, NOPE + half:QK], cos, sin,
                           [tmp[:, i] for i in range(3)])
                    kr = lat[:, t, Q_LORA + KV_LORA:LATENT]
                    rotate(nc, order, kr[:, 0:half], kr[:, half:ROPE], k["cos"][:, t, :], k["sin"][:, t, :],
                           [tmp[:, i, 0] for i in range(3)])
                    order(nc.vector.tensor_copy(kk[:, t, :, NOPE:QK],
                                                kr.unsqueeze(1).to_broadcast([P, HEADS, ROPE])))

        def turn(h, bank):
            for t in range(TT):
                nc.tensor.transpose(bank[0:QK, t * P:(t + 1) * P], q[:, t, h, :], ident)
                ins = nc.tensor.transpose(bank[0:QK, (2 + t) * P:(3 + t) * P], kk[:, t, h, :], ident)
            return ins

        def turned(h, bank, eng, order):
            return copy(nc, eng, qkT[:, h, :], bank[0:QK, :])
        products(core, "qk_turn", HEADS, turn, turned, odd)

        attention(core, "mla", mem, ident, HEADS, SEQ, QK,
                  lambda h, t: qkT[:, h, t * P:(t + 1) * P], lambda h: qkT[:, h, SEQ:2 * SEQ], QK ** -0.5,
                  lambda h, t: k["mla_mask"][:, t * SEQ:(t + 1) * SEQ], SEQ,
                  lambda h, j: v[:, j, h, :], lambda t: y[:, t],
                  [core.sb(mem, n, [P, HEADS * TT * SEQ])[:, :] for n in ("mla_s", "mla_pT")])
        turn_features(core, "mla_y_turn", ident, y.rearrange("p t h d -> p t (h d)"), 4, yT)


def mlstm(core, k, qk, gates, vx, og, yT, fv):
    nc, ident = core.nc, k["ident"]
    with ExitStack() as mem:
        conv = core.sb(mem, "conv", [P, KD, SEQ])
        g = [core.sb(mem, f"gate{i}", [HEADS, SEQ]) for i in range(5)]
        aT = core.sb(mem, "aT", [P, TT, HEADS])
        floor = core.sb(mem, "floor", [P, TT, HEADS])
        wT = core.sb(mem, "wT", [P, 2, 384])
        pT = core.sb(mem, "pT", [P, HEADS, 384])
        hn = core.sb(mem, "hn", [P, TT, HEADS, HD + 1])
        den = core.sb(mem, "den", [P, TT, HEADS])
        h = core.sb(mem, "h", [P, TT, HEADS, HD])
        sq = conv[:, 0:4, :].rearrange("p a b -> p (a b)").rearrange("p (t h d) -> p t h d", t=TT, h=HEADS)
        rs = core.sb(mem, "h_rs", [P, TT, HEADS])
        with core.stage("conv_order", "conv_tile", "conv_silu") as (block, own, tile_done, silu):
            @block.vector
            def _(dve):
                order = Order(dve, own)
                for j in range(KD):
                    w = fv["conv_w"]
                    order(nc.vector.tensor_scalar(conv[:, j, :], qk[:, j, 0:SEQ], w[:, j:j + 1],
                                                  fv["conv_b"][:, j:j + 1], ALU.mult, ALU.add))
                    for i in range(1, 4):
                        ins = nc.vector.scalar_tensor_tensor(out=conv[:, j, :], in0=qk[:, j, i:i + SEQ],
                                                             scalar=w[:, 8 * i + j:8 * i + j + 1],
                                                             in1=conv[:, j, :], op0=ALU.mult, op1=ALU.add)
                        if i < 3:
                            order(ins)
                    ins.then_inc(tile_done, 1)

            @block.scalar
            def _(act):
                for j in range(KD):
                    act.wait_ge(tile_done, j + 1)
                    nc.scalar.activation(conv[:, j, :], conv[:, j, :], ACT.Silu).then_inc(silu, 1)
        i_, f_ = gates
        with core.stage("gate_order", "gate_abs", "gate_ln", "gate_exp") as (block, own, absed, lned, exped):
            @block.vector
            def _(dve):
                order = Order(dve, own)
                order(nc.vector.tensor_scalar(i_[:, :], i_[:, :], fv["gate_b"][0:HEADS, 0:1], None, ALU.add))
                order(nc.vector.tensor_scalar(f_[:, :], f_[:, :], fv["gate_b"][0:HEADS, 1:2], None, ALU.add))
                order(nc.vector.tensor_scalar(g[0][:, :], f_[:, :], -1.0, None, ALU.mult))
                nc.vector.tensor_tensor(g[0][:, :], g[0][:, :], f_[:, :], ALU.min).then_inc(absed, 1)
                dve.wait_ge(lned, 2)
                order(nc.vector.scalar_tensor_tensor(out=g[1][:, :], in0=f_[:, :], scalar=0.0, in1=g[0][:, :],
                                                     op0=ALU.min, op1=ALU.subtract))
                F, M = g[2], g[4]
                order(nc.vector.tensor_tensor_scan(F[:, :], k["ones_row"][0:HEADS, :], g[1][:, :], 0.0,
                                                   ALU.mult, ALU.add))
                order(nc.vector.tensor_tensor(g[3][:, :], i_[:, :], F[:, :], ALU.subtract))
                order(nc.vector.tensor_tensor_scan(M[:, :], k["ones_row"][0:HEADS, :], g[3][:, :], 0.0,
                                                   ALU.mult, ALU.max))
                order(nc.vector.tensor_tensor(F[:, :], F[:, :], M[:, :], ALU.add))
                order(nc.vector.tensor_scalar(F[:, :], F[:, :], -1.0, 88.0, ALU.mult, ALU.min))
                order(nc.vector.tensor_scalar(M[:, :], M[:, :], -1.0, None, ALU.mult))
                ins = nc.vector.tensor_copy(g[0][:, :], F[:, :])
                ins.then_inc(absed, 1)

            @block.scalar
            def _(act):
                act.wait_ge(absed, 1)
                nc.scalar.activation(g[0][:, :], g[0][:, :], ACT.Exp).then_inc(lned, 1)
                act.wait_ge(lned, 1)
                nc.scalar.activation(g[0][:, :], g[0][:, :], ACT.Ln, bias=k["ones"][0:HEADS, 0:1]).then_inc(lned, 1)
                act.wait_ge(absed, 2)
                nc.scalar.activation(g[0][:, :], g[0][:, :], ACT.Exp).then_inc(exped, 1)
        a, minus_m = g[3], g[4]

        def turn(i, bank):
            src = (a, g[0])[i]
            for t in range(TT):
                ins = nc.tensor.transpose(bank[:, t * HEADS:(t + 1) * HEADS], src[:, t * P:(t + 1) * P],
                                          ident[0:HEADS, 0:HEADS])
            return ins

        def turned(i, bank, eng, order):
            return copy(nc, eng, (aT, floor)[i][:, :, :], bank[:, 0:2 * HEADS].rearrange("p (t h) -> p t h", t=TT))
        products(core, "gate_turn", 2, turn, turned)

        with core.stage("mw_spread", "mw_masked", "mw_exped", "mw_scored", "mw_weighed") as (
                block, spread, maskd, exped, scored, weighed):
            @block.tensor
            def _(pe):
                for hh in range(HEADS):
                    rows = slice(64 * (hh % 2), 64 * (hh % 2) + 64)
                    if hh >= 2:
                        pe.wait_ge(weighed, hh - 1)
                    nc.tensor.matmul(core.ps[:, hh % 2, 0:SEQ], k["sel"][0:HEADS, hh * P:(hh + 1) * P],
                                     minus_m[:, :], start=True, stop=True).then_inc(spread, 1)
                    q_, k_ = conv[rows, hh // 2, :], conv[rows, 4 + hh // 2, :]
                    nc.tensor.matmul(core.ps[:, 2 + hh % 2, 0:256], k_[:, 0:P], q_, start=True, stop=True)
                    nc.tensor.matmul(core.ps[:, 2 + hh % 2, 256:384], k_[:, P:SEQ], q_[:, P:SEQ],
                                     start=True, stop=True).then_inc(scored, 1)

            @block.vector
            def _(dve):
                def weigh(hh):
                    dve.wait_ge(exped, 2 * hh + 2)
                    dve.wait_ge(scored, hh + 1)
                    nc.vector.scalar_tensor_tensor(out=pT[:, hh, :], in0=core.ps[:, 2 + hh % 2, 0:384],
                                                   scalar=HD ** -0.5, in1=wT[:, hh % 2, :],
                                                   op0=ALU.mult, op1=ALU.mult).then_inc(weighed, 1)
                for hh in range(HEADS):
                    dve.wait_ge(spread, hh + 1)
                    if hh >= 2:
                        dve.wait_ge(weighed, hh - 1)
                    b = core.ps[:, hh % 2, :]
                    nc.vector.tensor_tensor(wT[:, hh % 2, 0:256], b[:, 0:256], k["ml_mask"], ALU.add)\
                        .then_inc(maskd, 1)
                    nc.vector.tensor_tensor(wT[:, hh % 2, 256:384], b[:, P:SEQ], k["ml_mask"][:, 0:P], ALU.add)\
                        .then_inc(maskd, 1)
                    if hh >= 1:
                        weigh(hh - 1)
                weigh(HEADS - 1)

            @block.scalar
            def _(act):
                for hh in range(HEADS):
                    act.wait_ge(maskd, 2 * hh + 2)
                    for t, (c0, c1) in enumerate(((0, 256), (256, 384))):
                        nc.scalar.activation(wT[:, hh % 2, c0:c1], wT[:, hh % 2, c0:c1], ACT.Exp,
                                             bias=aT[:, t, hh:hh + 1]).then_inc(exped, 1)

        def total(i, bank):
            t, half = divmod(i, 2)
            for j in range(4):
                hh = 4 * half + j
                o = bank[:, j * (HD + 1):(j + 1) * (HD + 1)]
                if t == 0:
                    mm = nc.tensor.matmul(o, pT[:, hh, 0:P], vx[:, 0, hh, :], start=True, stop=True)
                else:
                    nc.tensor.matmul(o, pT[:, hh, P:2 * P], vx[:, 0, hh, :], start=True, stop=False)
                    mm = nc.tensor.matmul(o, pT[:, hh, 2 * P:3 * P], vx[:, 1, hh, :], start=False, stop=True)
            return mm

        def totalled(i, bank, eng, order):
            t, half = divmod(i, 2)
            return copy(nc, eng, hn[:, t, 4 * half:4 * half + 4, :],
                        bank[:, 0:4 * (HD + 1)].rearrange("p (h d) -> p h d", d=HD + 1))
        products(core, "ml_total", 4, total, totalled, odd)

        with core.stage("hdiv_order", "og_done") as (block, own, og_done):
            @block.vector
            def _(dve):
                order = Order(dve, own)
                order(nc.vector.tensor_scalar(den[:, :, :], hn[:, :, :, HD], -1.0, None, ALU.mult))
                order(nc.vector.tensor_tensor(den[:, :, :], den[:, :, :], hn[:, :, :, HD], ALU.max))
                order(nc.vector.tensor_tensor(den[:, :, :], den[:, :, :], floor[:, :, :], ALU.max))
                order(nc.vector.reciprocal(den[:, :, :], den[:, :, :]))
                for t in range(TT):
                    order(nc.vector.tensor_tensor(h[:, t], hn[:, t, :, 0:HD],
                                                  den[:, t, :].unsqueeze(2).to_broadcast([P, HEADS, HD]), ALU.mult))

            @block.scalar
            def _(act):
                nc.scalar.activation(og, og, ACT.Sigmoid).then_inc(og_done, 1)
        head_inverse_rms(core, "h_rms", h, sq, rs[:, :, :], TT, HEADS)
        with core.stage("hnorm_order") as (block, own):
            @block.vector
            def _(dve):
                order = Order(dve, own)
                for t in range(TT):
                    order(nc.vector.tensor_tensor(h[:, t], h[:, t],
                                                  rs[:, t, :].unsqueeze(2).to_broadcast([P, HEADS, HD]), ALU.mult))
                    order(nc.vector.tensor_tensor(h[:, t], h[:, t],
                                                  og[:, t, :].rearrange("p (h d) -> p h d", d=HD), ALU.mult))
        turn_features(core, "ml_y_turn", ident, h[:, :, :, :].rearrange("p t h d -> p t (h d)"), 4, yT,
                      fv["head_norm"])


def mixer(core, layer_in, k, fv, hT, g_row, x):
    nc = core.nc
    with ExitStack() as mem:
        og = core.sb(mem, "og", [P, TT, ML_W])
        yT = [core.sb(mem, f"yT{i}", [P, 4, SEQ]) for i in range(2)]
        with ExitStack() as inner:
            lat = core.sb(inner, "lat", [P, TT, LATENT])
            qk = core.sb(inner, "qk", [P, KD, SEQ + 3])
            vx = core.sb(inner, "vx", [P, TT, HEADS, HD + 1])
            gi, gf = (core.sb(inner, n, [HEADS, SEQ]) for n in ("gi", "gf"))
            wg = core.sb(inner, "wg", [P, KD, 2 * HEADS])
            with core.stage("pad_set", "gate_w") as (block, pad_set, gate_w):
                @block.gpsimd
                def _(pool):
                    nc.gpsimd.memset(qk[:, :, 0:3], 0.0).then_inc(pad_set, 1)
                    nc.gpsimd.memset(vx[:, :, :, HD:HD + 1], 1.0).then_inc(pad_set, 1)
                    pool.wait_ge(pad_set, 2)

                @block.sync
                def _(sp):
                    sp.dma_start(wg[:, :, :], layer_in("w_in").rearrange("(k p) n -> p k n", p=P)[
                        :, :, GATE_AT:BR_AT]).then_inc(gate_w, 16)
                    sp.wait_ge(gate_w, 16)
            both = range(TT)
            spans = [(0, 512, both), (512, LATENT - 512, both), (ML_AT, 512, None), (ML_AT + 512, 512, None),
                     (ML_AT + 1024, 512, both), (ML_AT + 1536, 512, both)]

            def out(j, t, bank, eng, order):
                c0, width, _ = spans[j]
                if j < 2:
                    return copy(nc, eng, lat[:, t, c0:c0 + width], bank[:, 0:width])
                if j < 4:
                    return copy(nc, eng, qk[:, 4 * (j - 2) + t, 3:], bank[:, 0:SEQ])
                if j == 4:
                    return copy(nc, eng, vx[:, t, :, 0:HD], bank.rearrange("p (h d) -> p h d", d=HD))
                return copy(nc, eng, og[:, t, :], bank)
            linear(core, "proj", hT, layer_in("w_in"), spans, out, odd)

            def gate(i, bank):
                for kt in range(KD):
                    mm = nc.tensor.matmul(bank[0:HEADS, 0:SEQ], wg[:, kt, i * HEADS:(i + 1) * HEADS], hT[:, kt, :],
                                          start=(kt == 0), stop=(kt == KD - 1))
                return mm

            def gated(i, bank, eng, order):
                return copy(nc, eng, (gi, gf)[i][:, :], bank[0:HEADS, 0:SEQ])
            products(core, "gates", 2, gate, gated)
            mla(core, layer_in, k, lat, yT[0])
            mlstm(core, k, qk, (gi, gf), vx, og[:, :, :], yT[1], fv)
        with ExitStack() as inner:
            m = core.sb(inner, "merged", [P, TT, DM])
            tmp = core.sb(inner, "merge_tmp", [P, TT, 512])
            mT = core.sb(inner, "mergedT", [P, KD, SEQ])
            br = core.sb(inner, "br", [P, TT, 2 * DM])

            def gate_out(j, t, bank, eng, order):
                return nc.scalar.activation(br[:, t, j * 512:(j + 1) * 512], bank, ACT.Sigmoid)
            linear(core, "branch_gates", hT, layer_in("w_in"),
                   [(BR_AT + 512 * j, 512, both) for j in range(4)], gate_out, lambda i: True)
            for b, name in enumerate(("w_br_mla", "w_br_mlstm")):
                def out(j, t, bank, eng, order, b=b):
                    dst = m[:, t, j * 512:(j + 1) * 512]
                    gate = br[:, t, b * DM + j * 512:b * DM + (j + 1) * 512]
                    if b == 0:
                        return nc.vector.tensor_tensor(dst, bank, gate, ALU.mult)
                    order(nc.vector.tensor_tensor(tmp[:, t, :], bank, gate, ALU.mult))
                    return nc.vector.tensor_tensor(dst, dst, tmp[:, t, :], ALU.add)
                linear(core, f"branch{b}", yT[b], layer_in(name),
                       [(0, 512, both), (512, 512, both)], out)
            turn_features(core, "merge_turn", k["ident"], m, KD, mT)
            residual(core, "w_out", mT, layer_in("w_out"), g_row, tmp, x)


def residual(core, what, yT, w, g_row, tmp, x):
    nc = core.nc

    def out(j, t, bank, eng, order):
        dst = x[:, t, j * 512:(j + 1) * 512]
        order(nc.vector.tensor_tensor(tmp[:, t, :], bank, g_row[:, j * 512:(j + 1) * 512], ALU.mult))
        return nc.vector.tensor_tensor(dst, dst, tmp[:, t, :], ALU.add)
    linear(core, what, yT, w, [(0, 512, range(TT)), (512, 512, range(TT))], out)


def ffn(core, layer_in, k, fv, hT, g_row, x):
    nc = core.nc
    pairs = 2
    n_chunks = FF_TILES // pairs
    width = 2 * pairs * P
    kh = KD // 2
    w = layer_in("ffn_w_up").rearrange("(k p) n -> p k n", p=P)
    with ExitStack() as mem:
        hid = [core.sb(mem, f"hid_{n}", [P, FF_TILES, SEQ], F32R) for n in ("high", "low")]
        with ExitStack() as inner:
            xs = [core.sb(inner, f"up_x{n}", [P, KD, SEQ], F32R) for n in ("high", "low")]
            raw = core.sb(inner, "up_w", [P, STAGES, KD, width])
            parts = [core.sb(inner, f"up_w{n}", [P, STAGES, KD, width], F32R) for n in ("high", "low")]
            bufs = 8
            cv = core.sb(inner, "cv", [P, bufs, SEQ])

            def pieces(j):
                n = 2 if j == 0 else kh
                return [(a, a + n) for a in range(0, KD, n)]

            before = [sum(len(pieces(i)) for i in range(j)) for j in range(n_chunks + 1)]
            last_of = [i * 2 * pairs + 2 * pairs - 1 for i in range(n_chunks)]

            with core.stage("up_multiplied", "up_tapped", "up_conv", "up_gelu", "up_order", "up_product",
                            "up_hid_high", "up_hid", "up_x_high", "up_x_low", "up_high", "up_low",
                            *[f"up_landed{s}" for s in range(STAGES)],
                            *[f"up_first{s}" for s in range(len(pieces(0)))]) as (
                    block, multiplied, tapped, convolved, gelued, own, product_done, hid_high, hid_done,
                    x_high, x_low, high, low, *arrived):
                landed, first = arrived[:STAGES], arrived[STAGES:]

                @block.sync
                def _(sp):
                    for j in range(n_chunks):
                        if j >= STAGES:
                            sp.wait_ge(low, before[j - STAGES + 1])
                        for n, (a, b) in enumerate(pieces(0) if j == 0 else [(0, KD)]):
                            for s in range(2):
                                c0 = s * D_FF + j * pairs * P
                                sp.dma_start(raw[:, j % STAGES, a:b, s * pairs * P:(s + 1) * pairs * P],
                                             w[:, a:b, c0:c0 + pairs * P])\
                                    .then_inc(first[n] if j == 0 else landed[j % STAGES], 16)

                @block.tensor
                def _(pe):
                    pe.wait_ge(x_low, 1)
                    for n in range(2 * FF_TILES):
                        tile, side = divmod(n, 2)
                        j, i = divmod(tile, pairs)
                        if n >= 8:
                            pe.wait_ge(convolved, n - 7)
                        col = side * pairs * P + i * P
                        starts = [a for a, b in pieces(j)]
                        for kt in range(KD):
                            if n % (2 * pairs) == 0 and kt in starts:
                                pe.wait_ge(low, before[j] + 1 + starts.index(kt))
                            mm = split_product(nc, core.ps[:, n % 8, 0:SEQ],
                                               [a[:, j % STAGES, kt, col:col + P] for a in parts],
                                               [a[:, kt, :] for a in xs], kt == 0, kt == KD - 1)
                        mm.then_inc(multiplied, 1)

                cw, cb = fv["ffn_conv_w"], fv["ffn_conv_b"]

                @block.scalar
                def _(act):
                    def split(j):
                        for n, (a, b) in enumerate(pieces(j)):
                            if j == 0:
                                act.wait_ge(first[n], 32)
                            elif n == 0:
                                act.wait_ge(landed[j % STAGES], 32 * (j // STAGES + (j % STAGES > 0)))
                            if j >= STAGES and n == 0:
                                act.wait_ge(multiplied, last_of[j - STAGES] + 1)
                            split_high(nc, parts[0][:, j % STAGES, a:b, :], raw[:, j % STAGES, a:b, :])\
                                .then_inc(high, 1)

                    def gelu(tile):
                        act.wait_ge(convolved, 2 * tile + 1)
                        nc.scalar.activation(cv[:, (2 * tile) % bufs, :], cv[:, (2 * tile) % bufs, :],
                                             ACT.Gelu_apprx_tanh).then_inc(gelued, 1)

                    def hidden(tile):
                        act.wait_ge(product_done, tile + 1)
                        split_high(nc, hid[0][:, tile, :], cv[:, (2 * tile) % bufs, :]).then_inc(hid_high, 1)

                    split_high(nc, xs[0][:, :, :], hT).then_inc(x_high, 1)
                    for j in range(STAGES):
                        split(j)
                    for n in range(2 * FF_TILES):
                        tile, side = divmod(n, 2)
                        f = side * FF_TILES + tile
                        act.wait_ge(multiplied, n + 1)
                        if n >= bufs and side == 0:
                            act.wait_ge(hid_done, (n - bufs) // 2 + 1)
                        nc.scalar.activation(cv[:, n % bufs, :], core.ps[:, n % 8, 0:SEQ], ACT.Identity,
                                             bias=cb[:, f:f + 1], scale=cw[:, 4 * FF_TILES + f:4 * FF_TILES + f + 1])\
                            .then_inc(tapped, 1)
                        if side and tile >= 1:
                            gelu(tile - 1)
                        if side and tile >= 2:
                            hidden(tile - 2)
                        if n in last_of and last_of.index(n) + STAGES < n_chunks:
                            split(last_of.index(n) + STAGES)
                    gelu(FF_TILES - 1)
                    hidden(FF_TILES - 2)
                    hidden(FF_TILES - 1)

                @block.vector
                def _(dve):
                    order = Order(dve, own)

                    def split(j):
                        for n, (a, b) in enumerate(pieces(j)):
                            dve.wait_ge(high, before[j] + n + 1)
                            split_low(nc, parts[1][:, j % STAGES, a:b, :], raw[:, j % STAGES, a:b, :],
                                      parts[0][:, j % STAGES, a:b, :]).then_inc(low, 1)

                    def product(tile):
                        a = cv[:, (2 * tile) % bufs, :]
                        dve.wait_ge(convolved, 2 * tile + 2)
                        dve.wait_ge(gelued, tile + 1)
                        nc.vector.tensor_tensor(a, a, cv[:, (2 * tile + 1) % bufs, :], ALU.mult)\
                            .then_inc(product_done, 1)

                    def hidden(tile):
                        dve.wait_ge(hid_high, tile + 1)
                        split_low(nc, hid[1][:, tile, :], cv[:, (2 * tile) % bufs, :], hid[0][:, tile, :])\
                            .then_inc(hid_done, 1)

                    dve.wait_ge(x_high, 1)
                    split_low(nc, xs[1][:, :, :], hT, xs[0][:, :, :]).then_inc(x_low, 1)
                    for j in range(STAGES):
                        split(j)
                    for n in range(2 * FF_TILES):
                        tile, side = divmod(n, 2)
                        f = side * FF_TILES + tile
                        dve.wait_ge(tapped, n + 1)
                        for back in (1, 2):
                            col = (2 - back) * 2 * FF_TILES + f
                            dst = cv[:, n % bufs, back:]
                            ins = nc.vector.scalar_tensor_tensor(out=dst, in0=core.ps[:, n % 8, 0:SEQ - back],
                                                                 scalar=cw[:, col:col + 1], in1=dst, op0=ALU.mult,
                                                                 op1=ALU.add)
                            if back == 1:
                                order(ins)
                        ins.then_inc(convolved, 1)
                        if side and tile >= 1:
                            product(tile - 1)
                        if side and tile >= 2:
                            hidden(tile - 2)
                        if n in last_of and last_of.index(n) + STAGES < n_chunks:
                            split(last_of.index(n) + STAGES)
                    product(FF_TILES - 1)
                    hidden(FF_TILES - 2)
                    hidden(FF_TILES - 1)
        with ExitStack() as inner:
            tmp = core.sb(inner, "down_tmp", [P, 512])
            half = DM // 2
            wd = layer_in("ffn_w_down").rearrange("(k p) n -> p k n", p=P)
            kts = 8
            raw = core.sb(inner, "down_w", [P, STAGES, kts, half])
            parts = [core.sb(inner, f"down_w{n}", [P, STAGES, kts, half], F32R) for n in ("high", "low")]
            cuts = ((0, 3, 8, 15, FF_TILES), (0, 8, 16, FF_TILES))
            chunks = [(c, k0, k1 - k0) for c in range(2) for k0, k1 in zip(cuts[c], cuts[c][1:])]

            with core.stage("down_multiplied", "down_chunk", "down_order", "down_high", "down_low",
                            *[f"down_landed{n}" for n in range(STAGES)]) as (
                    block, multiplied, chunk_done, own, high, low, *landed):
                @block.sync
                def _(sp):
                    for n, (c, k0, kn) in enumerate(chunks):
                        if n >= STAGES:
                            sp.wait_ge(low, n - STAGES + 1)
                        sp.dma_start(raw[:, n % STAGES, 0:kn], wd[:, k0:k0 + kn, c * half:(c + 1) * half])\
                            .then_inc(landed[n % STAGES], 16)

                @block.scalar
                def _(act):
                    for n, (c, k0, kn) in enumerate(chunks):
                        act.wait_ge(landed[n % STAGES], 16 * (n // STAGES + 1))
                        if n >= STAGES:
                            act.wait_ge(chunk_done, n - STAGES + 1)
                        split_high(nc, parts[0][:, n % STAGES, 0:kn], raw[:, n % STAGES, 0:kn]).then_inc(high, 1)

                @block.tensor
                def _(pe):
                    for n, (c, k0, kn) in enumerate(chunks):
                        pe.wait_ge(low, n + 1)
                        for t in range(TT):
                            for i in range(kn):
                                mm = split_product(nc, core.ps[:, 2 * c + t, :],
                                                   [a[:, k0 + i, t * P:(t + 1) * P] for a in hid],
                                                   [a[:, n % STAGES, i, :] for a in parts], k0 + i == 0,
                                                   k0 + i == FF_TILES - 1)
                            if k0 + kn == FF_TILES and t == 0:
                                mm.then_inc(multiplied, 1)
                        mm.then_inc(chunk_done, 1)

                @block.vector
                def _(dve):
                    order = Order(dve, own)

                    def read(n):
                        c = chunks[n][0]
                        for t in range(TT):
                            dst = x[:, t, c * half:(c + 1) * half]
                            if t == 0:
                                dve.wait_ge(multiplied, c + 1)
                            else:
                                dve.wait_ge(chunk_done, n + 1)
                            order(nc.vector.tensor_tensor(tmp[:, :], core.ps[:, 2 * c + t, :],
                                                          g_row[:, c * half:(c + 1) * half], ALU.mult))
                            order(nc.vector.tensor_tensor(dst, dst, tmp[:, :], ALU.add))

                    ends = [n for n, (c, k0, kn) in enumerate(chunks) if k0 + kn == FF_TILES]
                    for n, (c, k0, kn) in enumerate(chunks):
                        dve.wait_ge(high, n + 1)
                        split_low(nc, parts[1][:, n % STAGES, 0:kn], raw[:, n % STAGES, 0:kn],
                                  parts[0][:, n % STAGES, 0:kn]).then_inc(low, 1)
                        if n - 1 in ends:
                            read(n - 1)
                    read(len(chunks) - 1)


def first_block(core, I, k, x):
    nc = core.nc
    L_OFF, n_cols = offsets(L_COLS)
    with ExitStack() as mem:
        fvt = core.sb(mem, "layer_vectors", [P, n_cols])
        fv = {n: fvt[:, a:b] for n, (a, b) in L_OFF.items()}
        core.settle()
        with nc.Fori(0, DEPTH, 1) as layer:
            def layer_in(name):
                return I[name][layer]
            load(core, "layer_vectors", [(fvt[:, :], I["layer_vectors"][layer])])
            mod = core.sb(mem, "mod", [P, 48, 1])
            gain = core.sb(mem, "gain", [P, KD])
            g_row = core.sb(mem, "g_row", [P, DM])
            hT = core.sb(mem, "hT", [P, KD, SEQ])
            kk = dict(k, lat_gain=fvt[:, L_OFF["q_norm"][0]:L_OFF["kv_norm"][1]])
            modulation(core, "ada", layer_in("ada_w"), fv["c"].unsqueeze(1), fv["ada_b"], mod[:, :, :],
                       k["ones"], [6 * DM])
            for part in range(2):
                with ExitStack() as inner:
                    rstd = core.sb(inner, "rstd", [P, TT])
                    xn = core.sb(inner, "xn", [P, TT, DM])
                    gains(core, f"gain{part}", mod, 0, fv[("norm_mix", "norm_ffn")[part]], gain[:, :],
                          (3 * part + 1) * KD)
                    norm_transposed(core, f"norm{part}", k["ident"], x, hT, 0, gain,
                                    mod[:, 3 * part * KD:(3 * part + 1) * KD, 0], (rstd, xn))
                    spread_rows(core, f"gate{part}", k["ident"], k["ones"],
                                mod[:, (3 * part + 2) * KD:(3 * part + 3) * KD, 0],
                                xn[:, 0, :].rearrange("p (k f) -> p k f", k=KD), g_row)
                (mixer, ffn)[part](core, layer_in, kk, fv, hT[:, :, :], g_row, x)
            core.settle()
        with ExitStack() as inner:
            rstd = core.sb(inner, "rstd", [P, TT])
            junk = core.sb(inner, "junk", [P, DM])
            inverse_rms(core, "final_rms", [x[:, t, :] for t in range(TT)], rstd, junk, DM)
            with core.stage("final") as (block, own):
                @block.vector
                def _(dve):
                    for t in range(TT):
                        nc.vector.scalar_tensor_tensor(out=x[:, t, :], in0=x[:, t, :], scalar=rstd[:, t:t + 1],
                                                       in1=k["final"], op0=ALU.mult, op1=ALU.mult).then_inc(own, 1)


SPACE = 24 * 1024


class Carver:

    def __init__(self, space, at=0):
        self.space, self.at = space, at

    def __call__(self, *shape):
        n = int(np.prod(shape))
        assert self.at + n <= self.space.shape[1], (self.at, shape)
        part = self.space[:, self.at:self.at + n]
        self.at += n
        names = "abcde"[:len(shape)]
        if len(shape) == 1:
            return part
        return part.rearrange(f"p ({' '.join(names)}) -> p {' '.join(names)}", **dict(zip(names[1:], shape[1:])))


LAT = slice(SEQ, NTOK)


def flat(a):
    names = "abcde"[:len(a.shape) - 1]
    return a.rearrange(f"p {' '.join(names)} -> p ({' '.join(names)})")


def rows_of(head):
    return slice(HD * (head % 2), HD * (head % 2) + HD)


def hgrn(core, I, k, fv, masks, hT, ycat):
    nc, ident = core.nc, k["ident"]
    with ExitStack() as mem:
        f = core.sb(mem, "hg_f", [P, 6, NTOK])
        v = core.sb(mem, "hg_v", [P, NT4, A_W])
        g = core.sb(mem, "hg_g", [P, TT, A_W])
        lb = core.sb(mem, "hg_lb", [P, 4, 4])
        spans = [(0, 512, None), (512, 256, None), (3 * A_W, A_W, range(NT4)), (4 * A_W, A_W, (2, 3))]

        def out(j, t, bank, eng, order):
            if j < 2:
                return copy(nc, eng, f[:, 4 * j + t, :], bank)
            if j == 2:
                return copy(nc, eng, v[:, t, :], bank[:, 0:A_W])
            return copy(nc, eng, g[:, t - 2, :], bank[:, 0:A_W])
        linear(core, "hg_proj", hT, I["w_in_2"], spans, out, odd)
        carve = Carver(core.sb(mem, "hg_space", [P, SPACE])[:, :])
        inc, exc, kd = (carve(2, 2, NTOK) for _ in range(3))
        sg, sn = (carve(2, 2, NTOK) for _ in range(2))
        qs, ks = (carve(2, 2, SEQ) for _ in range(2))
        near = carve(TT, 2, 2, P)
        cross = carve(2, 2, 2, P)
        far = carve(TT, 2, 2, SEQ)
        tmp = carve(TT, 2, 2, P)
        sq = carve(TT, A_HEADS, HD)
        o = carve(TT, A_HEADS, HD)
        rs = carve(TT, A_HEADS)

        with core.stage("lb_order", "lb_exp") as (block, own, exped):
            @block.vector
            def _(dve):
                order = Order(dve, own)
                order(nc.vector.tensor_tensor(lb[:, 0, :], fv["lb"], fv["lb"], ALU.subtract))
                dve.wait_ge(exped, 1)
                order(nc.vector.reciprocal(lb[:, 2, :], lb[:, 1, :]))
                order(nc.vector.tensor_tensor(lb[:, 1, :], lb[:, 1, :], lb[:, 2, :], ALU.mult))
                order(nc.vector.tensor_tensor(lb[:, 0, :], lb[:, 1, :], lb[:, 1, :], ALU.subtract))
                order(nc.vector.tensor_scalar(lb[:, 3, :], lb[:, 0, :], -1.0, 1.0, ALU.mult, ALU.add))

            @block.scalar
            def _(act):
                act.wait_ge(own, 1)
                nc.scalar.activation(lb[:, 1, :], lb[:, 0, :], ACT.Exp).then_inc(exped, 1)

        with core.stage("fg_order", "fg_sigmoid", "fg_bounded", "fg_order_s", "fg_logged", "fg_silu") as (
                block, own, sigmoid, bounded, own_s, logged, silu):
            @block.scalar
            def _(act):
                order = Order(act, own_s)
                for d in range(2):
                    nc.scalar.activation(sg[:, d], f[:, 2 + 2 * d:4 + 2 * d, :], ACT.Sigmoid).then_inc(sigmoid, 1)
                    nc.scalar.activation(sn[:, d], f[:, 2 + 2 * d:4 + 2 * d, :], ACT.Sigmoid, scale=-1.0)\
                        .then_inc(sigmoid, 1)
                nc.scalar.activation(g[:, :, :], g[:, :, :], ACT.Silu).then_inc(silu, 1)
                act.wait_ge(bounded, 4)
                order(nc.scalar.activation(flat(sg), flat(sg), ACT.Sqrt))
                nc.scalar.activation(flat(inc), flat(sg), ACT.Ln).then_inc(logged, 1)

            @block.vector
            def _(dve):
                order = Order(dve, own)
                for d in range(2):
                    dve.wait_ge(sigmoid, 2 * d + 2)
                    for i in range(2):
                        c = 2 * d + i
                        order(nc.vector.tensor_scalar(kd[:, d, i], sn[:, d, i], lb[:, 3, c:c + 1], None, ALU.mult))
                        order(nc.vector.tensor_scalar(sg[:, d, i], sg[:, d, i], lb[:, 3, c:c + 1], lb[:, 0, c:c + 1],
                                                      ALU.mult, ALU.add))
                        nc.vector.tensor_scalar(sg[:, d, i], sg[:, d, i], 1e-20, None, ALU.max).then_inc(bounded, 1)
                order(nc.vector.memset(flat(exc), 0.0))
                order(nc.vector.memset(flat(near), 0.0))
                dve.wait_ge(logged, 1)
                order(nc.vector.tensor_scalar(flat(inc), flat(inc), 2.0, None, ALU.mult))

        def decayed(order, dve, exped, n, q_cols, k_cols, b):
            for d in range(2):
                if b:
                    dve.wait_ge(exped, n + 2 * d + 2)
                    order(nc.vector.tensor_tensor(qs[:, d], qs[:, d], f[:, 0:2, q_cols], ALU.mult))
                    ins = nc.vector.tensor_tensor(ks[:, d], ks[:, d], kd[:, d, :, k_cols], ALU.mult)
                else:
                    order(nc.vector.tensor_copy(qs[:, d], f[:, 0:2, q_cols]))
                    ins = nc.vector.tensor_copy(ks[:, d], kd[:, d, :, k_cols])
                yield ins

        def double(order, b):
            for d in range(2):
                a, z, edge = ((0, 1, b - 1), (1, 0, 0))[d]
                i_ = inc[:, d].rearrange("p h t -> p (h t)").rearrange("p (n s b) -> p n s b", s=2, b=b)
                e_ = exc[:, d].rearrange("p h t -> p (h t)").rearrange("p (n s b) -> p n s b", s=2, b=b)
                shape = [P, 2 * NTOK // (2 * b), b]
                order(nc.vector.tensor_tensor(e_[:, :, a, :], e_[:, :, a, :],
                                              i_[:, :, z, edge:edge + 1].to_broadcast(shape), ALU.add))
                order(nc.vector.tensor_tensor(i_[:, :, z, :], i_[:, :, z, :],
                                              i_[:, :, a, edge:edge + 1].to_broadcast(shape), ALU.add))

        for b in (0,) + LEVELS:
            with core.stage(f"hg{b}_exp", f"hg{b}_decayed", f"hg{b}_multiplied", f"hg{b}_order") as (
                    block, exped, decays, multiplied, own):
                @block.scalar
                def _(act):
                    if b:
                        for d in range(2):
                            nc.scalar.activation(qs[:, d], inc[:, d, :, LAT], ACT.Exp).then_inc(exped, 1)
                            nc.scalar.activation(ks[:, d], exc[:, d, :, LAT], ACT.Exp).then_inc(exped, 1)

                @block.tensor
                def _(pe):
                    for d in range(2):
                        pe.wait_ge(decays, d + 1)
                        for t in range(TT):
                            cols = slice(t * P, (t + 1) * P)
                            for par in range(2):
                                for hp in range(2):
                                    r = rows_of(par)
                                    mm = nc.tensor.matmul(core.ps[:, 4 * d + 2 * t + par, hp * P:(hp + 1) * P],
                                                          ks[r, d, hp, cols], qs[r, d, hp, cols],
                                                          start=True, stop=True)
                        mm.then_inc(multiplied, 1)

                @block.vector
                def _(dve):
                    order = Order(dve, own)
                    for ins in decayed(order, dve, exped, 0, LAT, LAT, b):
                        ins.then_inc(decays, 1)
                    if b:
                        dve.wait_ge(exped, 4)
                        double(order, b)
                    for d in range(2):
                        dve.wait_ge(multiplied, d + 1)
                        at = M_OFF["ident"][0] if b == 0 else M_OFF["lv"][0] + LEVELS.index(b) * P
                        mask = masks[:, d, at:at + P]
                        order(nc.vector.tensor_tensor(
                            tmp.rearrange("p a b c t -> p (a b) c t"),
                            core.ps[:, 4 * d:4 * d + 4, 0:2 * P].rearrange("p b (c t) -> p b c t", c=2),
                            mask.unsqueeze(1).unsqueeze(1).to_broadcast([P, 4, 2, P]), ALU.mult))
                        order(nc.vector.tensor_tensor(flat(near), flat(near), flat(tmp), ALU.add))

        with core.stage("hgx_exp", "hgx_decayed", "hgx_multiplied", "hgx_order", "hgx_doubled", "hgx_read") as (
                block, exped, decays, multiplied, own, doubled, read):
            @block.scalar
            def _(act):
                for stage in range(2):
                    if stage:
                        act.wait_ge(doubled, 1)
                        act.wait_ge(multiplied, 1)
                    for d in range(2):
                        nc.scalar.activation(qs[:, d], inc[:, d, :, LAT], ACT.Exp).then_inc(exped, 1)
                        nc.scalar.activation(ks[:, d], exc[:, d, :, (LAT, slice(0, SEQ))[stage]], ACT.Exp)\
                            .then_inc(exped, 1)

            @block.tensor
            def _(pe):
                pe.wait_ge(decays, 2)
                for d in range(2):
                    t, s = (1, 0) if d == 0 else (0, 1)
                    for par in range(2):
                        for hp in range(2):
                            r = rows_of(par)
                            mm = nc.tensor.matmul(core.ps[:, 2 * d + par, hp * P:(hp + 1) * P],
                                                  ks[r, d, hp, s * P:(s + 1) * P], qs[r, d, hp, t * P:(t + 1) * P],
                                                  start=True, stop=True)
                mm.then_inc(multiplied, 1)
                pe.wait_ge(decays, 4)
                for s in range(TT):
                    for par in range(2):
                        for hp in range(2):
                            r = rows_of(par)
                            for d in range(2):
                                mm = nc.tensor.matmul(core.ps[:, 4 + 2 * s + par, hp * SEQ:(hp + 1) * SEQ],
                                                      ks[r, d, hp, s * P:(s + 1) * P], qs[r, d, hp, :],
                                                      start=(d == 0), stop=(d == 1))
                mm.then_inc(multiplied, 1)

            @block.vector
            def _(dve):
                order = Order(dve, own)
                for ins in decayed(order, dve, exped, 0, LAT, LAT, 128):
                    ins.then_inc(decays, 1)
                dve.wait_ge(exped, 4)
                double(order, P)
                nc.vector.tensor_copy(tmp[:, 0, 0, 0, 0:1], tmp[:, 0, 0, 0, 0:1]).then_inc(doubled, 1)
                dve.wait_ge(multiplied, 1)
                order(nc.vector.tensor_copy(cross.rearrange("p a b c t -> p (a b) (c t)"), core.ps[:, 0:4, 0:2 * P]))
                for ins in decayed(order, dve, exped, 4, LAT, slice(0, SEQ), 256):
                    ins.then_inc(decays, 1)
                dve.wait_ge(multiplied, 2)
                nc.vector.tensor_copy(far.rearrange("p a b c t -> p (a b) (c t)"), core.ps[:, 4:8, :]).then_inc(read, 1)

        def weigh(t, bank):
            for h in range(A_HEADS):
                hp, par = divmod(h, 2)
                cols = slice(t * P, (t + 1) * P)
                lefts = [far[:, 0, par, hp, cols], far[:, 1, par, hp, cols], near[:, t, par, hp, :],
                         cross[:, 1 - t, par, hp, :]]
                for j, (left, tile) in enumerate(zip(lefts, (0, 1, 2 + t, 3 - t))):
                    mm = nc.tensor.matmul(bank[:, h * HD:(h + 1) * HD], left, v[:, tile, h * HD:(h + 1) * HD],
                                          start=(j == 0), stop=(j == 3))
            return mm

        def weighed(t, bank, eng, order):
            return copy(nc, eng, o[:, t], bank[:, 0:A_W].rearrange("p (h d) -> p h d", d=HD))
        products(core, "hg_weigh", TT, weigh, weighed, odd)
        head_inverse_rms(core, "hg_rms", o, sq, rs, TT, A_HEADS)
        with core.stage("hg_out") as (block, own):
            @block.vector
            def _(dve):
                order = Order(dve, own)
                for t in range(TT):
                    order(nc.vector.tensor_tensor(o[:, t], o[:, t],
                                                  rs[:, t, :].unsqueeze(2).to_broadcast([P, A_HEADS, HD]), ALU.mult))
                    order(nc.vector.tensor_tensor(ycat[:, t, 0:A_W], o[:, t].rearrange("p h d -> p (h d)"),
                                                  g[:, t, :], ALU.mult))


def rwkv(core, I, k, fv, masks, consts, hT, ycat):
    nc, ident = core.nc, k["ident"]
    with ExitStack() as mem:
        raw_space = core.sb(mem, "rw_raw", [P, B_TILES * 2 * (SEQ + 2)])
        raw = raw_space[:, :].rearrange("p (j s n) -> p j s n", j=B_TILES, s=2)
        with core.stage("rw_pad") as (block, pad):
            @block.vector
            def _(dve):
                nc.vector.memset(raw[:, :, :, 0:1], 0.0).then_inc(pad, 1)
                nc.vector.memset(raw[:, :, :, SEQ + 1:SEQ + 2], 0.0).then_inc(pad, 1)

        def out(j, t, bank, eng, order):
            return copy(nc, eng, raw[:, 4 * j + t, :, 1:SEQ + 1], bank.rearrange("p (s n) -> p s n", s=2))
        linear(core, "rw_proj", hT, I["w_in_2"],
               [(B_AT, 512, None), (B_AT + 512, 512, None), (B_AT + 1024, P, None)], out, odd)

        X = core.sb(mem, "rw_x", [P, B_TILES, NTOK])
        up = core.sb(mem, "rw_up", [P, 3 * A_W])
        vt = core.sb(mem, "rw_v", [P, NT4, A_W])
        gt = core.sb(mem, "rw_g", [P, TT, A_W])
        bon = core.sb(mem, "rw_bonus", [P, TT, B_HEADS])
        S = core.sb(mem, "rw_state", [P, 2, 2, HD])
        tot = core.sb(mem, "rw_total", [P, 2, 2, 8])
        y = core.sb(mem, "rw_y", [P, 2, TT, A_W])
        space = core.sb(mem, "rw_space", [P, SPACE])[:, :]
        freed = Carver(raw_space[:, :])
        k2t, a2t = (freed(2, NT4, A_W) for _ in range(2))
        load(core, "rw_up", [(up[:, :], I["rwkv_up"])])
        with core.stage("mix_order", "mix_done", "mix_act") as (block, own, mixed, acted):
            @block.vector
            def _(dve):
                order = Order(dve, own)
                for j in (6, 8, 7, 0, 1, 2, 3, 4, 5):
                    xj = X[:, j, :].rearrange("p (s n) -> p s n", s=2)
                    mid = raw[:, j, :, 1:SEQ + 1]
                    order(nc.vector.tensor_tensor(xj, raw[:, j, :, 0:SEQ], raw[:, j, :, 2:SEQ + 2], ALU.add))
                    order(nc.vector.scalar_tensor_tensor(out=xj, in0=xj, scalar=0.5, in1=mid, op0=ALU.mult,
                                                         op1=ALU.subtract))
                    nc.vector.scalar_tensor_tensor(out=xj, in0=xj, scalar=fv["mu"][:, j:j + 1], in1=mid,
                                                   op0=ALU.mult, op1=ALU.add).then_inc(mixed, 1)

            @block.scalar
            def _(act):
                act.wait_ge(mixed, 1)
                nc.scalar.activation(X[:, 6, :], X[:, 6, :], ACT.Tanh).then_inc(acted, 1)
                act.wait_ge(mixed, 2)
                nc.scalar.activation(X[:, 8, :], X[:, 8, :], ACT.Sigmoid).then_inc(acted, 1)

        carve = Carver(space)
        sw, sa = (carve(2, 2, NTOK) for _ in range(2))
        kk, kn = (carve(2, NTOK) for _ in range(2))
        kt, rt, kh, ah, k2, a2 = (carve(2, 2, NTOK) for _ in range(6))
        pi = carve(2, 2, NTOK)
        def low_rank(i, bank):
            which, d, hp = i // 4, (i // 2) % 2, i % 2
            r = rows_of(d)
            return nc.tensor.matmul(bank, up[r, which * A_W + hp * P:which * A_W + (hp + 1) * P],
                                    X[r, 6 + which, :], start=True, stop=True)

        def low_rank_out(i, bank, eng, order):
            which, d, hp = i // 4, (i // 2) % 2, i % 2
            return nc.scalar.activation((sw, sa)[which][:, d, hp], bank, ACT.Sigmoid,
                                        bias=fv[("w0", "a0")[which]][:, 2 * d + hp:2 * d + hp + 1])
        products(core, "rw_low", 8, low_rank, low_rank_out, lambda i: True)

        def gate(t, bank):
            return nc.tensor.matmul(bank[:, 0:A_W], X[:, 8, (2 + t) * P:(3 + t) * P], up[:, 2 * A_W:], start=True,
                                    stop=True)

        def gated(t, bank, eng, order):
            return copy(nc, eng, gt[:, t, :], bank[:, 0:A_W])
        products(core, "rw_gate", TT, gate, gated, odd)

        with core.stage("kk_order") as (block, own):
            @block.vector
            def _(dve):
                order = Order(dve, own)
                for hp in range(2):
                    order(nc.vector.tensor_scalar(kk[:, hp], X[:, 2 + hp, :], fv["kk_scale"][:, hp:hp + 1], None,
                                                  ALU.mult))
                    order(nc.vector.tensor_tensor(kn[:, hp], kk[:, hp], kk[:, hp], ALU.mult))

        def norm(hp, bank):
            return nc.tensor.matmul(bank, consts["head_ones"], kn[:, hp], start=True, stop=True)

        def normed(hp, bank, eng, order):
            return nc.scalar.activation(kn[:, hp], bank, ACT.Sqrt)
        products(core, "kk_norm", 2, norm, normed, lambda i: True)
        with core.stage("prep_order", "prep_ready", "prep_exp") as (block, own, ready, exped):
            @block.vector
            def _(dve):
                order = Order(dve, own)
                order(nc.vector.tensor_scalar(kn, kn, 1e-12, None, ALU.max))
                order(nc.vector.reciprocal(kn, kn))
                order(nc.vector.tensor_tensor(kk, kk, kn, ALU.mult))
                order(nc.vector.tensor_scalar(flat(sw), flat(sw), -float(np.exp(np.float32(-0.5))), None, ALU.mult))
                for d in range(2):
                    for hp in range(2):
                        order(nc.vector.tensor_tensor_scan(pi[:, d, hp], consts["chunk_start"], sw[:, d, hp], 0.0,
                                                           ALU.mult, ALU.add))
                for d in range(2):
                    c = [a[:, d].rearrange("p h t -> p (h t)").rearrange("p (c n) -> p c n", n=RW_CHUNK)
                         for a in (pi, sw, kt, k2, rt)]
                    p_, l_, before, after, here = c
                    last = p_[:, :, RW_CHUNK - 1:RW_CHUNK]
                    if d == 1:
                        before, after = after, before
                    order(nc.vector.tensor_tensor(before, p_, l_, ALU.subtract))
                    order(nc.vector.tensor_tensor(after, last.to_broadcast([P, 16, RW_CHUNK]), p_, ALU.subtract))
                    order(nc.vector.tensor_copy(tot[:, d].rearrange("p h c -> p (h c)"), last.squeeze(2)))
                    if d == 0:
                        ins = nc.vector.tensor_copy(here, p_)
                    else:
                        ins = nc.vector.tensor_tensor(here, after, l_, ALU.add)
                    ins.then_inc(ready, 1)
                for d in range(2):
                    for hp in range(2):
                        order(nc.vector.tensor_tensor(a2[:, d, hp], sa[:, d, hp], kk[:, hp], ALU.mult))
                        order(nc.vector.tensor_scalar(sa[:, d, hp], sa[:, d, hp], 1.0, fv["k_a"][:, hp:hp + 1],
                                                      ALU.subtract, ALU.mult))
                        order(nc.vector.scalar_tensor_tensor(out=sa[:, d, hp], in0=sa[:, d, hp], scalar=1.0,
                                                             in1=X[:, 2 + hp, :], op0=ALU.add, op1=ALU.mult))
                dve.wait_ge(exped, 10)
                for d in range(2):
                    order(nc.vector.tensor_tensor(kh[:, d], ah[:, d], sa[:, d], ALU.mult))
                    order(nc.vector.tensor_tensor(ah[:, d], ah[:, d], a2[:, d], ALU.mult))
                    order(nc.vector.tensor_tensor(kt[:, d], kt[:, d], kk, ALU.mult))
                    order(nc.vector.tensor_tensor(rt[:, d], rt[:, d], X[:, 0:2, :], ALU.mult))
                    order(nc.vector.tensor_tensor(a2[:, d], a2[:, d], k2[:, d], ALU.mult))
                    order(nc.vector.tensor_tensor(k2[:, d], k2[:, d], sa[:, d], ALU.mult))
                order(nc.vector.tensor_tensor(kn[:, :, LAT], sa[:, 0, :, LAT], sa[:, 1, :, LAT], ALU.add))
                order(nc.vector.tensor_tensor(kn[:, :, LAT], kn[:, :, LAT], X[:, 0:2, LAT], ALU.mult))
                for hp in range(2):
                    order(nc.vector.tensor_scalar(kn[:, hp, LAT], kn[:, hp, LAT], fv["r_k"][:, hp:hp + 1], None,
                                                  ALU.mult))
                order(nc.vector.memset(S[:, :, :, :], 0.0))

            @block.scalar
            def _(act):
                for d in range(2):
                    act.wait_ge(ready, d + 1)
                    nc.scalar.activation(ah[:, d], rt[:, d], ACT.Exp, scale=-1.0).then_inc(exped, 1)
                    act.wait_ge(exped, 5 * d + 1)
                    for a in (kt, k2, rt):
                        nc.scalar.activation(a[:, d], a[:, d], ACT.Exp).then_inc(exped, 1)
                    nc.scalar.activation(tot[:, d], tot[:, d], ACT.Exp).then_inc(exped, 1)

        def bonus(t, bank):
            for hp in range(2):
                mm = nc.tensor.matmul(bank[:, 2 * hp:2 * hp + 2], kn[:, hp, (2 + t) * P:(3 + t) * P],
                                      consts["head_pick"], start=True, stop=True)
            return mm

        def bonus_out(t, bank, eng, order):
            return copy(nc, eng, bon[:, t, :], bank[:, 0:B_HEADS])
        products(core, "rw_bonus", TT, bonus, bonus_out, odd)

        sources = [(X[:, 4:6, :], vt), (k2[:, 0], k2t[:, 0]), (a2[:, 0], a2t[:, 0]), (k2[:, 1], k2t[:, 1]),
                   (a2[:, 1], a2t[:, 1])]

        def turn(i, bank):
            src, t = sources[i // NT4][0], i % NT4
            for hp in range(2):
                ins = nc.tensor.transpose(bank[:, hp * P:(hp + 1) * P], src[:, hp, t * P:(t + 1) * P], ident)
            return ins

        def turned(i, bank, eng, order):
            return copy(nc, eng, sources[i // NT4][1][:, i % NT4, :], bank[:, 0:A_W])
        products(core, "rw_turn", 5 * NT4, turn, turned, odd)

        low = Carver(space)
        M1 = low(2, NT4, 4, P)
        N_ = [low(NT4, 4, P)]
        low.at = (8 + 4 + 8) * NTOK
        T_ = low(2, NT4, 4, P)
        Rk, Ra = (low(2, TT, 4, P) for _ in range(2))
        P_ = low(2, NT4, 4, P)
        N_.append(low(NT4, 4, P))
        G = Carver(flat(X[:, :, :]))(2, NT4, 4, P)
        NM = Carver(flat(hT))(2, NT4, 4, P)
        kinds = [(d, t, kind, par) for d in range(2) for t in range(NT4) for kind in range(4) for par in range(2)
                 if kind < 2 or t >= 2]

        def matrix(i, bank):
            d, t, kind, par = kinds[i]
            left = (ah, kh, kh, ah)[kind]
            right = (kt, kt, rt, rt)[kind]
            r, cols = rows_of(par), slice(t * P, (t + 1) * P)
            for hp in range(2):
                mm = nc.tensor.matmul(bank[:, hp * P:(hp + 1) * P], left[r, d, hp, cols], right[r, d, hp, cols],
                                      start=True, stop=True)
            return mm

        def matrix_out(i, bank, eng, order):
            d, t, kind, par = kinds[i]
            dst = (N_[d], M1[:, d], Rk[:, d], Ra[:, d])[kind][:, t if kind < 2 else t - 2]
            a, b = M_OFF["strict" if kind < 2 else "incl"]
            dst = dst.rearrange("p (hp par) t -> p par hp t", par=2)[:, par]
            return nc.vector.tensor_tensor(dst, bank[:, 0:2 * P].rearrange("p (h t) -> p h t", h=2),
                                           masks[:, d, a:b].unsqueeze(1).to_broadcast([P, 2, P]), ALU.mult)
        products(core, "rw_matrix", len(kinds), matrix, matrix_out)

        with core.stage("unit") as (block, unit):
            @block.vector
            def _(dve):
                for a in (G, T_):
                    nc.vector.tensor_copy(a.rearrange("p d t h c -> p (d t h) c"),
                                          ident.unsqueeze(1).to_broadcast([P, 32, P])).then_inc(unit, 1)

        def masked(order, d, t, level):
            at = M_OFF["lv"][0] + LEVELS.index(level) * P
            order(nc.vector.tensor_tensor(NM[:, d, t], N_[d][:, t],
                                          masks[:, d, at:at + P].unsqueeze(1).to_broadcast([P, B_HEADS, P]),
                                          ALU.mult))
        with core.stage("nm_order") as (block, own):
            @block.vector
            def _(dve):
                order = Order(dve, own)
                for i in range(2 * NT4):
                    masked(order, *divmod(i, NT4), LEVELS[0])
        for b in LEVELS[:-1]:

            def first(i, bank):
                d, t = divmod(i, NT4)
                for h in range(B_HEADS):
                    mm = nc.tensor.matmul(bank[:, h * P:(h + 1) * P], NM[:, d, t, h], T_[:, d, t, h], start=True,
                                          stop=True)
                return mm

            def first_out(i, bank, eng, order):
                d, t = divmod(i, NT4)
                return copy(nc, eng, P_[:, d, t].rearrange("p h c -> p (h c)"), bank)
            if b == 1:
                def first_level(i, bank, eng, order):
                    d, t = divmod(i, NT4)
                    order(nc.vector.tensor_tensor(G[:, d, t], G[:, d, t], NM[:, d, t], ALU.subtract))
                    masked(order, d, t, 2 * b)
                    dst = T_[:, d, t].rearrange("p h c -> p (h c)")
                    return nc.vector.tensor_tensor(dst, dst, bank, ALU.subtract)
                products(core, "inv1", 8, first, first_level)
                continue
            products(core, f"inv{b}_first", 8, first, first_out, odd)
            last = b == LEVELS[-2]
            units = [(d, t, x) for d in range(2) for t in range(NT4) for x in range(2) if x or not last]

            def second(i, bank):
                d, t, x = units[i]
                for h in range(B_HEADS):
                    left, right = ((G, P_), (P_, G))[x]
                    mm = nc.tensor.matmul(bank[:, h * P:(h + 1) * P], left[:, d, t, h], right[:, d, t, h],
                                          start=True, stop=True)
                return mm

            def second_out(i, bank, eng, order):
                if i < 2 * NT4 and not last:
                    masked(order, *divmod(i, NT4), 2 * b)
                d, t, x = units[i]
                dst = (T_, G)[x][:, d, t].rearrange("p h c -> p (h c)")
                return nc.vector.tensor_tensor(dst, dst, bank, ALU.subtract)
            products(core, f"inv{b}_second", len(units), second, second_out)
        low = Carver(flat(P_))
        rw_sequence(core, S, kt, rt, M1, G, Rk, Ra, vt, k2t, a2t, tot, y, low)
        with ExitStack() as inner:
            st = core.sb(inner, "rw_stat", [P, 2, TT, B_HEADS])
            yy = y[:, 0].rearrange("p t (h d) -> p t h d", d=HD)
            y1 = y[:, 1].rearrange("p t (h d) -> p t h d", d=HD)

            def wide(a, t):
                return a[:, t, :].unsqueeze(2).to_broadcast([P, B_HEADS, HD])
            with core.stage("ln_order", "ln_rooted", "ln_meaned") as (block, own, rooted, meaned):
                @block.vector
                def _(dve):
                    order = Order(dve, own)
                    order(nc.vector.tensor_tensor(y[:, 0], y[:, 0], y[:, 1], ALU.add))
                    for t in range(TT):
                        order(nc.vector.tensor_reduce(st[:, 0, t, :], yy[:, t], AX_X, ALU.add))
                    order(nc.vector.tensor_scalar(st[:, 0], st[:, 0], 1.0 / HD, None, ALU.mult))
                    for t in range(TT):
                        order(nc.vector.tensor_tensor(yy[:, t], yy[:, t], wide(st[:, 0], t), ALU.subtract))
                        order(nc.vector.tensor_tensor(y1[:, t], yy[:, t], yy[:, t], ALU.mult))
                        order(nc.vector.tensor_reduce(st[:, 1, t, :], y1[:, t], AX_X, ALU.add))
                    nc.vector.tensor_scalar(st[:, 1], st[:, 1], 1.0 / HD, 64e-5, ALU.mult, ALU.add)\
                        .then_inc(meaned, 1)
                    dve.wait_ge(rooted, 1)
                    order(nc.vector.reciprocal(st[:, 1], st[:, 1]))
                    for t in range(TT):
                        order(nc.vector.tensor_tensor(yy[:, t], yy[:, t], wide(st[:, 1], t), ALU.mult))
                        order(nc.vector.tensor_tensor(y[:, 0, t], y[:, 0, t], k["ln_gain"], ALU.mult))
                        order(nc.vector.tensor_tensor(y[:, 0, t], y[:, 0, t], k["ln_bias"], ALU.add))
                        order(nc.vector.tensor_tensor(y1[:, t],
                                                      vt[:, 2 + t, :].rearrange("p (h d) -> p h d", d=HD),
                                                      wide(bon, t), ALU.mult))
                        order(nc.vector.tensor_tensor(y[:, 0, t], y[:, 0, t], y[:, 1, t], ALU.add))
                        order(nc.vector.tensor_tensor(ycat[:, t, A_W:2 * A_W], y[:, 0, t], gt[:, t, :], ALU.mult))

                @block.scalar
                def _(act):
                    act.wait_ge(meaned, 1)
                    nc.scalar.activation(st[:, 1], st[:, 1], ACT.Sqrt).then_inc(rooted, 1)


def rw_sequence(core, S, kt, rt, M1, G, Rk, Ra, vt, k2t, a2t, tot, y, low):
    nc = core.nc
    chunks = [[0, 1, 2, 3, 4, 5, 6, 7], [3, 2, 1, 0, 7, 6, 5, 4]]
    steps = 8
    rhs = low(2, 2, 2, HD)
    nu = low(2, 2, A_W)
    own_part = low(2, NT4, 2, 2, HD)
    states = (S, low(2, 2, HD))

    def own_values(i, bank):
        d, tile = divmod(i, NT4)
        for h in range(B_HEADS):
            at = (2 * (h % 2) + h // 2) * HD
            mm = nc.tensor.matmul(bank[:, at:at + HD], M1[:, d, tile, h], vt[:, tile, h * HD:(h + 1) * HD],
                                  start=True, stop=True)
        return mm

    def own_out(i, bank, eng, order):
        d, tile = divmod(i, NT4)
        return copy(nc, eng, own_part[:, d, tile].rearrange("p a b v -> p (a b v)"), bank[:, 0:A_W])
    products(core, "rw_own", 2 * NT4, own_values, own_out, odd)

    names = ("rhs_ready", "rhs_made", "u_ready", "u_copied", "state_added", "state_ready", "y_ready", "y_copied")
    with core.stage(*[f"{n}{d}" for d in range(2) for n in names]) as (block, *sems):
        (rhs_ready, rhs_made, u_ready, u_copied, state_added, state_ready, y_ready, y_copied) = [
            (sems[i], sems[8 + i]) for i in range(8)]

        def place(n, d):
            c = chunks[d][n]
            return c, c // 2, slice(HD * (c % 2), HD * (c % 2) + HD)

        @block.tensor
        def _(pe):
            def outputs(n, d):
                tile = place(n, d)[1]
                for h in range(B_HEADS):
                    r, hp = rows_of(h % 2), h // 2
                    o = core.ps[:, 4 * d + h % 2, A_W + hp * HD:A_W + (hp + 1) * HD]
                    nc.tensor.matmul(o, Rk[:, d, tile - 2, h], vt[:, tile, h * HD:(h + 1) * HD], start=True,
                                     stop=False)
                    nc.tensor.matmul(o, rt[r, d, hp, tile * P:(tile + 1) * P], states[n % 2][r, d, hp, :],
                                     start=False, stop=False)
                    mm = nc.tensor.matmul(o, Ra[:, d, tile - 2, h], nu[:, n % 2, d, h * HD:(h + 1) * HD],
                                          start=False, stop=True)
                mm.then_inc(y_ready[d], 1)

            for n in range(steps):
                for d in range(2):
                    tile = place(n, d)[1]
                    if n:
                        pe.wait_ge(state_ready[d], 4 * n)
                    if n > 5:
                        pe.wait_ge(y_copied[d], n - 5)
                    for par in range(2):
                        r = rows_of(par)
                        for hp in range(2):
                            mm = nc.tensor.matmul(core.ps[:, 4 * d + par, hp * HD:(hp + 1) * HD],
                                                  kt[r, d, hp, tile * P:(tile + 1) * P],
                                                  states[n % 2][r, d, hp, :], start=True, stop=True)
                    mm.then_inc(rhs_ready[d], 1)
                for d in range(2):
                    tile = place(n, d)[1]
                    pe.wait_ge(rhs_made[d], n + 1)
                    for h in range(B_HEADS):
                        mm = nc.tensor.matmul(core.ps[:, 4 * d + 2, h * HD:(h + 1) * HD], G[:, d, tile, h],
                                              rhs[:, d, h % 2, h // 2, :], start=True, stop=True)
                    mm.then_inc(u_ready[d], 1)
                if n > 4:
                    for d in range(2):
                        outputs(n - 1, d)
                for d in range(2):
                    c, tile, half = place(n, d)
                    pe.wait_ge(u_copied[d], n + 1)
                    for hp in range(2):
                        o = core.ps[:, 4 * d + 3, hp * P:(hp + 1) * P]
                        cols = slice(hp * P, (hp + 1) * P)
                        nc.tensor.matmul(o, k2t[half, d, tile, cols], vt[half, tile, cols], start=True, stop=False)
                        mm = nc.tensor.matmul(o, a2t[half, d, tile, cols], nu[half, n % 2, d, cols], start=False,
                                              stop=True)
                    mm.then_inc(state_added[d], 1)
            for d in range(2):
                pe.wait_ge(y_copied[d], steps - 5)
                outputs(steps - 1, d)

        @block.scalar
        def _(act):
            for n in range(steps):
                for d in range(2):
                    act.wait_ge(u_ready[d], n + 1)
                    nc.scalar.activation(nu[:, n % 2, d, :], core.ps[:, 4 * d + 2, 0:A_W], ACT.Copy, scale=-1.0)\
                        .then_inc(u_copied[d], 1)

        @block.vector
        def _(dve):
            def outputs(n, d):
                c, tile, half = place(n, d)
                dve.wait_ge(y_ready[d], n - 3)
                dst = y[half, d, tile - 2, :].rearrange("p (hp par v) -> p par hp v", par=2, v=HD)
                for par in range(2):
                    ins = nc.vector.tensor_copy(dst[:, par], core.ps[half, 4 * d + par, A_W:A_W + P]
                                                .rearrange("p (hp v) -> p hp v", v=HD))
                ins.then_inc(y_copied[d], 1)

            for n in range(steps):
                for d in range(2):
                    tile = place(n, d)[1]
                    dve.wait_ge(rhs_ready[d], n + 1)
                    nc.vector.tensor_tensor(rhs[:, d].rearrange("p a b v -> p a (b v)"),
                                            core.ps[:, 4 * d:4 * d + 2, 0:P],
                                            own_part[:, d, tile].rearrange("p a b v -> p a (b v)"), ALU.add)\
                        .then_inc(rhs_made[d], 1)
                if n > 4:
                    for d in range(2):
                        outputs(n - 1, d)
                for d in range(2):
                    c, tile, half = place(n, d)
                    dve.wait_ge(state_added[d], n + 1)
                    for par in range(2):
                        r = rows_of(par)
                        for hp in range(2):
                            nc.vector.scalar_tensor_tensor(
                                out=states[(n + 1) % 2][r, d, hp, :], in0=states[n % 2][r, d, hp, :],
                                scalar=tot[r, d, hp, c:c + 1],
                                in1=core.ps[r, 4 * d + 3, hp * P + par * HD:hp * P + (par + 1) * HD],
                                op0=ALU.mult, op1=ALU.add).then_inc(state_ready[d], 1)
            for d in range(2):
                outputs(steps - 1, d)


def neighbourhood(core, I, k, consts, hT, ycat):
    nc, ident = core.nc, k["ident"]
    with ExitStack() as mem:
        q = core.sb(mem, "na_q", [P, TT, C_W])
        kx = core.sb(mem, "na_k", [P, NT4, C_W])
        v = core.sb(mem, "na_v", [P, NT4, C_W])
        spans = [(C_AT, 512, (2, 3)), (C_AT + 512, 512, range(NT4)), (C_AT + 1024, 512, range(NT4))]

        def out(j, t, bank, eng, order):
            return copy(nc, eng, (q[:, t - 2] if j == 0 else (kx, v)[j - 1][:, t]), bank)
        linear(core, "na_proj", hT, I["w_in_2"], spans, out, odd)
        kT = core.sb(mem, "na_kT", [P, 4, NTOK])
        qT = core.sb(mem, "na_qT", [P, 4, SEQ])
        rs = core.sb(mem, "na_rs", [P, TT + NT4, C_HEADS])
        carve = Carver(core.sb(mem, "na_space", [P, SPACE])[:, :])
        s, pT = carve(2 * C_HEADS * NTOK), carve(2 * C_HEADS * NTOK)
        bias = carve(TT, C_HEADS, SEQ)
        tmp = carve(3, C_HEADS, HD // 2)
        sq = s[:, 0:NT4 * C_W].rearrange("p (t h d) -> p t h d", t=NT4, h=C_HEADS)
        load(core, "na_bias", [(bias[:, t], I["bias"][t]) for t in range(TT)])
        qh = q[:, :, :].rearrange("p t (h d) -> p t h d", d=HD)
        kh = kx[:, :, :].rearrange("p t (h d) -> p t h d", d=HD)
        head_inverse_rms(core, "naq_rms", qh, sq, rs[:, 0:TT, :], TT, C_HEADS)
        head_inverse_rms(core, "nak_rms", kh, sq, rs[:, TT:, :], NT4, C_HEADS)
        with core.stage("na_order") as (block, own):
            @block.vector
            def _(dve):
                order = Order(dve, own)
                for x, tiles, at, gain in ((qh, TT, 0, k["q_gain"]), (kh, NT4, TT, k["k_gain"])):
                    for t in range(tiles):
                        order(nc.vector.tensor_tensor(
                            x[:, t], x[:, t], rs[:, at + t, :].unsqueeze(2).to_broadcast([P, C_HEADS, HD]), ALU.mult))
                        order(nc.vector.tensor_tensor(x[:, t], x[:, t],
                                                      gain.unsqueeze(1).to_broadcast([P, C_HEADS, HD]), ALU.mult))
                    for t in range(TT):
                        xl = x[:, tiles - 2 + t]
                        cos, sin = (consts[n][:, 32 * t:32 * t + 32].unsqueeze(1).to_broadcast([P, C_HEADS, 32])
                                    for n in ("na_cos", "na_sin"))
                        rotate(nc, order, xl[:, :, 0:32], xl[:, :, 32:64], cos, sin, [tmp[:, i] for i in range(3)])

        key_tiles = (2, 3, 0, 1)

        def turn(i, bank):
            src, tiles = (q, (0, 1)) if i < 4 else (kx, key_tiles)
            for j, t in enumerate(tiles):
                ins = nc.tensor.transpose(bank[:, j * P:(j + 1) * P], src[:, t, (i % 4) * P:(i % 4 + 1) * P], ident)
            return ins

        def turned(i, bank, eng, order):
            return copy(nc, eng, qT[:, i, :] if i < 4 else kT[:, i - 4, :], bank[:, 0:SEQ if i < 4 else NTOK])
        products(core, "na_turn", 8, turn, turned, odd)
        attention(core, "na", mem, ident, C_HEADS, NTOK, HD,
                  lambda h, t: qT[rows_of(h), h // 2, t * P:(t + 1) * P], lambda h: kT[rows_of(h), h // 2, :],
                  HD ** -0.5, lambda h, t: bias[:, t, h, :], SEQ,
                  lambda h, j: v[:, key_tiles[j], h * HD:(h + 1) * HD],
                  lambda t: ycat[:, t, 2 * A_W:].rearrange("p (h d) -> p h d", d=HD), (s, pT))


TILES = GROUPS + 1


def router(core, I, k, hT, weights, tile_d, tile_i):
    nc = core.nc
    n = GROUPS + EXPERTS
    with ExitStack() as mem:
        w = core.sb(mem, "rt_w", [P, KD, n])
        lg = core.sb(mem, "rt_logits", [P, TT, n])
        place = core.sb(mem, "rt_place", [P, PER_GROUP])
        before = core.sb(mem, "rt_before", [P, P])
        a, b, c, e = (core.sb(mem, f"rt_{i}", [P, TT, PER_GROUP]) for i in "abce")
        pr = weights
        pick = [core.sb(mem, f"rt_pick{i}", [P, TT, PER_GROUP]) for i in range(2)]
        group = core.sb(mem, "rt_group", [P, TT, GROUPS])
        col = core.sb(mem, "rt_col", [P, 8, TT])
        slot = core.sb(mem, "rt_slot", [P, TILES, TT])
        whole = core.sb(mem, "rt_whole", [P, 8])
        load(core, "router", [(w[:, :, :], I["router"].rearrange("(k p) n -> p k n", p=P)),
                              (before[:, :], I["route"][:, 0:P])])

        def logit(t, bank):
            for kt in range(KD):
                mm = nc.tensor.matmul(bank[:, 0:n], hT[:, kt, t * P:(t + 1) * P], w[:, kt, :], start=(kt == 0),
                                      stop=(kt == KD - 1))
            return mm

        def logit_out(t, bank, eng, order):
            return nc.vector.tensor_tensor(lg[:, t, :], bank[:, 0:n], k["b_r"], ALU.add)
        products(core, "rt_logit", TT, logit, logit_out)

        def wide(x, m):
            return x.unsqueeze(2).to_broadcast([P, TT, m])

        def first_of_max(order, x, top, out, m, s1, s2):
            order(nc.vector.tensor_tensor(s1, x, wide(top, m), ALU.is_equal))
            order(nc.vector.tensor_scalar(s1, s1, -64.0, 64.0, ALU.mult, ALU.add))
            order(nc.vector.tensor_tensor(s1, s1, place[:, 0:m].unsqueeze(1).to_broadcast([P, TT, m]), ALU.add))
            order(nc.vector.tensor_reduce(s2, s1, AX_X, ALU.min))
            order(nc.vector.tensor_tensor(out, s1, wide(s2, m), ALU.is_equal))

        with core.stage("rt_order", "rt_shift", "rt_exp", "rt_place", "rt_grouped", "rt_ranked", "rt_over",
                        "rt_totalled", "rt_slots", "rt_stored") as (
                block, own, shifted, exped, placed, grouped, ranked, over, totalled, slotted, stored):
            @block.gpsimd
            def _(pool):
                for i in range(PER_GROUP):
                    nc.gpsimd.memset(place[:, i:i + 1], float(i)).then_inc(placed, 1)
                pool.wait_ge(placed, PER_GROUP)

            @block.scalar
            def _(act):
                act.wait_ge(shifted, 1)
                nc.scalar.activation(a[:, :, 0:GROUPS], a[:, :, 0:GROUPS], ACT.Exp).then_inc(exped, 1)
                act.wait_ge(shifted, 2)
                nc.scalar.activation(pr[:, :, :], pr[:, :, :], ACT.Exp).then_inc(exped, 1)

            @block.tensor
            def _(pe):
                pe.wait_ge(grouped, 1)
                for t in range(TT):
                    for u in range(t + 1):
                        mm = nc.tensor.matmul(core.ps[:, 0, t * GROUPS:(t + 1) * GROUPS],
                                              before[:, :] if u == t else k["ones"], group[:, u, :],
                                              start=(u == 0), stop=(u == t))
                mm.then_inc(ranked, 1)
                pe.wait_ge(over, 1)
                for t in range(TT):
                    mm = nc.tensor.matmul(core.ps[:, 1, 0:GROUPS], k["ones"], c[:, t, 0:GROUPS], start=(t == 0),
                                          stop=(t == TT - 1))
                mm.then_inc(totalled, 1)

            @block.vector
            def _(dve):
                order = Order(dve, own)
                V = nc.vector
                g = lg[:, :, 0:GROUPS]
                dve.wait_ge(placed, PER_GROUP)
                order(V.tensor_reduce(col[:, 0], g, AX_X, ALU.max))
                V.tensor_tensor(a[:, :, 0:GROUPS], g, wide(col[:, 0], GROUPS), ALU.subtract).then_inc(shifted, 1)
                first_of_max(order, g, col[:, 0], group[:, :, :], GROUPS, b[:, :, 0:GROUPS], col[:, 1])
                V.tensor_copy(place[:, 0:1], place[:, 0:1]).then_inc(grouped, 1)
                dve.wait_ge(exped, 1)
                order(V.tensor_reduce(col[:, 2], a[:, :, 0:GROUPS], AX_X, ALU.add))
                order(V.reciprocal(col[:, 2], col[:, 2]))
                order(V.tensor_tensor(a[:, :, 0:GROUPS], a[:, :, 0:GROUPS], group[:, :, :], ALU.mult))
                order(V.tensor_reduce(col[:, 3], a[:, :, 0:GROUPS], AX_X, ALU.add))
                order(V.tensor_tensor(col[:, 2], col[:, 2], col[:, 3], ALU.mult))
                for gi in range(GROUPS):
                    src = lg[:, :, GROUPS + gi * PER_GROUP:GROUPS + (gi + 1) * PER_GROUP]
                    weight = group[:, :, gi:gi + 1].to_broadcast([P, TT, PER_GROUP])
                    order(V.tensor_tensor(c[:, :, :], src, weight, ALU.mult))
                    if gi == 0:
                        order(V.tensor_copy(e[:, :, :], c[:, :, :]))
                    else:
                        order(V.tensor_tensor(e[:, :, :], e[:, :, :], c[:, :, :], ALU.add))
                order(V.tensor_reduce(col[:, 4], e[:, :, :], AX_X, ALU.max))
                V.tensor_tensor(pr[:, :, :], e[:, :, :], wide(col[:, 4], PER_GROUP), ALU.subtract).then_inc(shifted, 1)
                dve.wait_ge(exped, 2)
                order(V.tensor_reduce(col[:, 5], pr[:, :, :], AX_X, ALU.add))
                order(V.reciprocal(col[:, 5], col[:, 5]))
                order(V.tensor_tensor(pr[:, :, :], pr[:, :, :], wide(col[:, 5], PER_GROUP), ALU.mult))
                order(V.tensor_copy(e[:, :, :], pr[:, :, :]))
                for i in range(2):
                    order(V.tensor_reduce(col[:, 4], e[:, :, :], AX_X, ALU.max))
                    first_of_max(order, e[:, :, :], col[:, 4], pick[i][:, :, :], PER_GROUP, b[:, :, :], col[:, 1])
                    order(V.scalar_tensor_tensor(out=e[:, :, :], in0=pick[i][:, :, :], scalar=-4.0, in1=e[:, :, :],
                                                 op0=ALU.mult, op1=ALU.add))
                order(V.tensor_tensor(b[:, :, :], pick[0][:, :, :], pick[1][:, :, :], ALU.add))
                order(V.tensor_tensor(pr[:, :, :], pr[:, :, :], b[:, :, :], ALU.mult))
                order(V.tensor_reduce(col[:, 5], pr[:, :, :], AX_X, ALU.add))
                order(V.reciprocal(col[:, 5], col[:, 5]))
                order(V.tensor_tensor(pr[:, :, :], pr[:, :, :], wide(col[:, 5], PER_GROUP), ALU.mult))
                order(V.tensor_tensor(pr[:, :, :], pr[:, :, :], wide(col[:, 2], PER_GROUP), ALU.mult))
                rank = core.ps[:, 0, 0:TT * GROUPS].rearrange("p (t g) -> p t g", t=TT)
                dve.wait_ge(ranked, 1)
                order(V.tensor_tensor(a[:, :, 0:GROUPS], rank, group[:, :, :], ALU.mult))
                order(V.tensor_reduce(col[:, 6], a[:, :, 0:GROUPS], AX_X, ALU.add))
                order(V.tensor_scalar(col[:, 7], col[:, 6], float(P), None, ALU.is_ge))
                V.tensor_tensor(c[:, :, 0:GROUPS], group[:, :, :], wide(col[:, 7], GROUPS), ALU.mult).then_inc(over, 1)
                dve.wait_ge(totalled, 1)
                order(V.tensor_scalar(whole[:, 0:GROUPS], core.ps[:, 1, 0:GROUPS], 1.0, None, ALU.min))
                order(V.tensor_scalar(col[:, 5], col[:, 6], 1.0, None, ALU.add))
                for gi in range(GROUPS):
                    order(V.tensor_tensor(slot[:, gi, :], group[:, :, gi], col[:, 5], ALU.mult))
                order(V.tensor_scalar(slot[:, 0:GROUPS], slot[:, 0:GROUPS], -1.0, None, ALU.add))
                V.tensor_scalar(slot[:, GROUPS], col[:, 6], -float(P), None, ALU.add).then_inc(slotted, 1)
                order(V.tensor_tensor(b[:, 0, 0:GROUPS], whole[:, 0:GROUPS], place[:, 0:GROUPS], ALU.mult))
                order(V.tensor_copy(e[:, 0, 0:GROUPS], place[:, 0:GROUPS]))
                order(V.tensor_reduce(e[:, 0, GROUPS:GROUPS + 1], b[:, 0, 0:GROUPS], AX_X, ALU.add))
                order(V.tensor_reduce(e[:, 0, TILES:TILES + 1], whole[:, 0:GROUPS], AX_X, ALU.add))
                order(V.tensor_scalar(e[:, 0, TILES:TILES + 1], e[:, 0, TILES:TILES + 1], float(GROUPS), None,
                                      ALU.add))
                order(V.tensor_copy(tile_i[:, :], e[:, 0, 0:TILES + 1]))

            @block.sync
            def _(sp):
                sp.wait_ge(slotted, 1)
                sp.dma_start(tile_d.rearrange("n p t -> p n t"), slot[:, :, :]).then_inc(stored, 16)
                sp.wait_ge(stored, 16)


RAW = 4
PARTS = 4


def experts(core, I, k, hT, weights, tile_d, tile_i, y):
    nc = core.nc
    wg, wu, wd = (I[f"w_exp_{n}_2"].rearrange("(g e) a b -> g e a b", e=PER_GROUP) for n in ("gate", "up", "down"))
    FT = D_EXP // P
    HALF = SLOT // 2
    KH = KD // 2
    plan = []
    for e in range(PER_GROUP):
        plan += [("gate", e), ("up", e)] + ([("down", e - 1)] if e else [])
    plan.append(("down", PER_GROUP - 1))
    halves = [(u, h) for u in range(len(plan)) for h in range(2)]
    done = {(plan[u], h): i + 1 for i, (u, h) in enumerate(halves)}
    assert len(plan) % RAW == 0 and len(halves) % PARTS == 0
    with ExitStack() as mem:
        h_tok = core.sb(mem, "me_h", [P, TT, DM])
        iota = core.sb(mem, "me_iota", [P, P])
        key = core.sb(mem, "me_key", [P, TT])
        pick = core.sb(mem, "me_pick", [P, TT, P])
        pick_T = core.sb(mem, "me_pick_T", [P, SEQ])
        cw = core.sb(mem, "me_weight", [P, PER_GROUP])
        xs = [core.sb(mem, f"me_x{n}", [P, KD, P], F32R) for n in ("high", "low")]
        raw = core.sb(mem, "me_w", [P, RAW, SLOT])
        parts = [core.sb(mem, f"me_w{n}", [P, PARTS, HALF], F32R) for n in ("high", "low")]
        hidden = core.sb(mem, "me_hidden", [P, D_EXP])
        hid = [core.sb(mem, f"me_hid{n}", [P, FT, P], F32R) for n in ("high", "low")]
        landed = [mem.enter_context(nc.semaphore(f"expert_landed{i}")) for i in range(RAW)]
        load(core, "iota", [(iota[:, :], I["route"][:, P:2 * P])])

        def fetch(sp, u, group):
            kind, e = plan[u % len(plan)]
            w = dict(gate=wg, up=wu, down=wd)[kind]
            kt = FT if kind == "down" else KD
            sp.dma_start(raw[:, u % RAW].rearrange("p (k n) -> p k n", k=kt),
                         w[group, e].rearrange("(k p) n -> p k n", p=P)).then_inc(landed[u % RAW], 16)

        def halved(u, h, which):
            n = (2 * u + h) % PARTS
            if plan[u][0] == "down":
                return (raw[:, u % RAW].rearrange("p (k n) -> p k n", k=FT)[:, :, 512 * h:512 * (h + 1)],
                        parts[which][:, n].rearrange("p (k n) -> p k n", k=FT))
            return (raw[:, u % RAW].rearrange("p (k n) -> p k n", k=KD)[:, KH * h:KH * (h + 1), :],
                    parts[which][:, n].rearrange("p (k n) -> p k n", k=KH))

        with core.stage("me_zero") as (block, zeroed):
            @block.vector
            def _(dve):
                nc.vector.memset(y, 0.0).then_inc(zeroed, 1)

            @block.sync
            def _(sp):
                for u in range(RAW):
                    sp.sem_clear(landed[u])
                    fetch(sp, u, 0)

        def turn(i, bank):
            t, half = divmod(i, 2)
            for n in range(KH):
                ins = nc.tensor.transpose(bank[:, n * P:(n + 1) * P],
                                          hT[:, KH * half + n, t * P:(t + 1) * P], k["ident"])
            return ins

        def turned(i, bank, eng, order):
            t, half = divmod(i, 2)
            return copy(nc, eng, h_tok[:, t, 512 * half:512 * (half + 1)], bank)
        products(core, "me_turn", 2 * TT, turn, turned, odd)
        yg = hT[:, 0:KH, :].rearrange("p k n -> p (k n)")
        core.settle()
        tiles = nc.values_load(tile_i[0:1, TILES:TILES + 1], min_val=GROUPS, max_val=TILES)

        with nc.Fori(0, tiles, 1) as tile:
            with core.stage("mg_key", "mg_picked", "mg_gathered", "mg_high", "mg_low", "mg_copied") as (
                    block, key_here, picked, gathered, high, low, copied):
                @block.sync
                def _(sp):
                    sp.dma_start(key[:, :], tile_d[tile]).then_inc(key_here, 16)

                @block.vector
                def _(dve):
                    dve.wait_ge(key_here, 16)
                    nc.vector.tensor_tensor(pick[:, :, :], iota[:, :].unsqueeze(1).to_broadcast([P, TT, P]),
                                            key[:, :].unsqueeze(2).to_broadcast([P, TT, P]), ALU.is_equal)\
                        .then_inc(picked, 1)
                    for i in range(2):
                        dve.wait_ge(high, i + 1)
                        split_low(nc, xs[1][:, KH * i:KH * (i + 1), :],
                                  core.ps[:, i, :].rearrange("p (k n) -> p k n", k=KH),
                                  xs[0][:, KH * i:KH * (i + 1), :]).then_inc(low, 1)
                    dve.wait_ge(gathered, 4)
                    nc.vector.tensor_copy(cw[:, :], core.ps[:, 3, 0:PER_GROUP]).then_inc(copied, 1)

                @block.tensor
                def _(pe):
                    pe.wait_ge(picked, 1)
                    for i in range(2):
                        for n in range(KH):
                            kt = KH * i + n
                            for t in range(TT):
                                mm = nc.tensor.matmul(core.ps[:, i, n * P:(n + 1) * P],
                                                      h_tok[:, t, kt * P:(kt + 1) * P], pick[:, t, :],
                                                      start=(t == 0), stop=(t == TT - 1))
                        mm.then_inc(gathered, 1)
                    for t in range(TT):
                        mm = nc.tensor.transpose(core.ps[:, 2, t * P:(t + 1) * P], pick[:, t, :], k["ident"])
                    mm.then_inc(gathered, 1)
                    for t in range(TT):
                        mm = nc.tensor.matmul(core.ps[:, 3, 0:PER_GROUP], pick[:, t, :], weights[:, t, :],
                                              start=(t == 0), stop=(t == TT - 1))
                    mm.then_inc(gathered, 1)

                @block.scalar
                def _(act):
                    for i in range(2):
                        act.wait_ge(gathered, i + 1)
                        split_high(nc, xs[0][:, KH * i:KH * (i + 1), :],
                                   core.ps[:, i, :].rearrange("p (k n) -> p k n", k=KH)).then_inc(high, 1)
                    act.wait_ge(gathered, 3)
                    nc.scalar.activation(pick_T[:, :], core.ps[:, 2, 0:SEQ], ACT.Copy).then_inc(copied, 1)

            with core.stage("me_high", "me_low", "me_half", "me_silu", "me_hidden", "me_turned", "me_hid_high",
                            "me_hid_low", "me_summed", "me_back", "me_added") as (
                    block, high, low, half_done, silu, hid_done, hid_turned, hid_high, hid_low, summed, back, added):
                @block.sync
                def _(sp):
                    group = sp.value_load(tile_i[0:1, bass.ds(tile, 1)], min_val=0, max_val=GROUPS - 1)
                    for u in range(RAW, len(plan)):
                        sp.wait_ge(low, 2 * (u - RAW) + 2)
                        fetch(sp, u, group)
                    with sp.If(tile + 1 < tiles):
                        group = sp.value_load(tile_i[0:1, bass.ds(tile + 1, 1)], min_val=0, max_val=GROUPS - 1)
                        for u in range(len(plan), len(plan) + RAW):
                            sp.wait_ge(low, 2 * (u - RAW) + 2)
                            sp.sem_clear(landed[u % RAW])
                            fetch(sp, u, group)
                    sp.end_ifs()

                @block.tensor
                def _(pe):
                    for i, (u, h) in enumerate(halves):
                        kind, e = plan[u]
                        pe.wait_ge(low, i + 1)
                        w = [halved(u, h, which)[1] for which in range(2)]
                        if kind == "down":
                            if h == 0:
                                pe.wait_ge(hid_low, e + 1)
                            for f in range(FT):
                                mm = split_product(nc, core.ps[:, 4 + h, :], [a[:, f, :] for a in hid],
                                                   [a[:, f, :] for a in w], e == 0 and f == 0,
                                                   e == PER_GROUP - 1 and f == FT - 1)
                        else:
                            if h == 0 and e:
                                pe.wait_ge(silu if kind == "gate" else hid_done, e)
                            for n in range(KH):
                                mm = split_product(nc, core.ps[:, int(kind == "up"), :],
                                                   [a[:, KH * h + n, :] for a in xs], [a[:, n, :] for a in w],
                                                   h == 0 and n == 0, h == 1 and n == KH - 1)
                        mm.then_inc(half_done, 1)
                        turns = None
                        if (kind, h) == ("gate", 1) and e:
                            turns = e - 1
                        if (kind, h, e) == ("down", 1, PER_GROUP - 2):
                            turns = PER_GROUP - 1
                        if turns is not None:
                            pe.wait_ge(hid_done, turns + 1)
                            if turns:
                                pe.wait_ge(hid_low, turns)
                            for f in range(FT):
                                mm = nc.tensor.transpose(core.ps[:, 2, f * P:(f + 1) * P],
                                                         hidden[:, f * P:(f + 1) * P], k["ident"])
                            mm.then_inc(hid_turned, 1)
                    for n in range(2):
                        pe.wait_ge(summed, n + 1)
                        for t in range(TT):
                            nc.tensor.matmul(core.ps[:, 2 * n + t, :], pick_T[:, t * P:(t + 1) * P],
                                             yg[:, 512 * n:512 * (n + 1)], start=True, stop=True).then_inc(back, 1)

                AHEAD = 3

                @block.scalar
                def _(act):
                    def split(i):
                        u, h = halves[i]
                        if h == 0:
                            act.wait_ge(landed[u % RAW], 16 * (u // RAW + 1))
                        if i >= PARTS:
                            act.wait_ge(half_done, i - PARTS + 1)
                        src, dst = halved(u, h, 0)
                        split_high(nc, dst, src).then_inc(high, 1)

                    def gated(e):
                        act.wait_ge(half_done, done[("gate", e), 1])
                        if e:
                            act.wait_ge(hid_turned, e)
                        nc.scalar.activation(hidden[:, :], core.ps[:, 0, :], ACT.Silu).then_inc(silu, 1)

                    def turned(e):
                        act.wait_ge(hid_turned, e + 1)
                        if e:
                            act.wait_ge(half_done, done[("down", e - 1), 1])
                        split_high(nc, hid[0][:, :, :], core.ps[:, 2, :].rearrange("p (f n) -> p f n", f=FT))\
                            .then_inc(hid_high, 1)

                    for i in range(AHEAD):
                        split(i)
                    for i, (u, h) in enumerate(halves):
                        if i + AHEAD < len(halves):
                            split(i + AHEAD)
                        kind, e = plan[u]
                        if (kind, h) == ("gate", 1):
                            if e:
                                turned(e - 1)
                            gated(e)
                        if (kind, h, e) == ("down", 1, PER_GROUP - 2):
                            turned(PER_GROUP - 1)
                    act.wait_ge(half_done, done[("down", PER_GROUP - 1), 0])
                    nc.scalar.activation(yg[:, 0:512], core.ps[:, 4, :], ACT.Copy).then_inc(summed, 1)

                @block.vector
                def _(dve):
                    def split(i):
                        u, h = halves[i]
                        dve.wait_ge(high, i + 1)
                        src, dst = halved(u, h, 1)
                        split_low(nc, dst, src, halved(u, h, 0)[1]).then_inc(low, 1)

                    def multiplied(e):
                        dve.wait_ge(half_done, done[("up", e), 1])
                        dve.wait_ge(silu, e + 1)
                        nc.vector.scalar_tensor_tensor(out=hidden[:, :], in0=core.ps[:, 1, :], scalar=cw[:, e:e + 1],
                                                       in1=hidden[:, :], op0=ALU.mult, op1=ALU.mult)\
                            .then_inc(hid_done, 1)

                    def turned(e):
                        dve.wait_ge(hid_high, e + 1)
                        split_low(nc, hid[1][:, :, :], core.ps[:, 2, :].rearrange("p (f n) -> p f n", f=FT),
                                  hid[0][:, :, :]).then_inc(hid_low, 1)

                    for i in range(AHEAD):
                        split(i)
                    for i, (u, h) in enumerate(halves):
                        if i + AHEAD < len(halves):
                            split(i + AHEAD)
                        kind, e = plan[u]
                        if (kind, h) == ("up", 1):
                            multiplied(e)
                        if (kind, h) == ("gate", 1) and e:
                            turned(e - 1)
                        if (kind, h, e) == ("down", 1, PER_GROUP - 2):
                            turned(PER_GROUP - 1)
                    dve.wait_ge(half_done, done[("down", PER_GROUP - 1), 1])
                    dve.wait_ge(summed, 1)
                    nc.vector.tensor_copy(yg[:, 512:], core.ps[:, 5, :]).then_inc(summed, 1)
                    for n in range(2):
                        for t in range(TT):
                            dve.wait_ge(back, 2 * n + t + 1)
                            dst = y[:, t, 512 * n:512 * (n + 1)]
                            nc.vector.tensor_tensor(dst, core.ps[:, 2 * n + t, :], dst, ALU.add).then_inc(added, 1)
            core.settle()


def second_block(core, I, k, x):
    nc = core.nc
    S_OFF, n_cols = offsets(S_COLS)
    with ExitStack() as mem:
        fvt = core.sb(mem, "second_vectors", [P, n_cols])
        fv = {n: fvt[:, a:b] for n, (a, b) in S_OFF.items()}
        mod = core.sb(mem, "mod2", [P, 48, 2])
        gain = core.sb(mem, "gain2", [P, KD])
        g_row = core.sb(mem, "g_row2", [P, DM])
        rstd = core.sb(mem, "rstd2", [P, TT])
        k = dict(k)
        tile_d = nc.dram_tensor("tile_slots", [TILES, P, TT], F32).ap()
        load(core, "second", [(fvt[:, :], I["second_vectors"])])
        modulation(core, "ada2", I["w_ada_2"], fv["c"].rearrange("p (v k) -> p v k", v=2), fv["ada_b"],
                   mod[:, :, :], k["ones"], [6 * DM, 2 * DM])
        with ExitStack() as mix:
            ycat = core.sb(mix, "ycat", [P, TT, DM])
            with ExitStack() as inner:
                hT = core.sb(inner, "hT2", [P, KD, NTOK])
                masks = core.sb(inner, "masks", [P, 2, M_WIDTH])
                c_off, n_consts = offsets(C_COLS)
                names = ("head_ones", "head_pick", "na_cos", "na_sin", "chunk_start")
                widths = [c_off[n][1] - c_off[n][0] for n in names]
                ct = core.sb(inner, "consts2", [P, sum(widths)])
                consts = {n: ct[:, sum(widths[:i]):sum(widths[:i + 1])] for i, n in enumerate(names)}
                norms = inner.enter_context(ExitStack())
                xc, xn = (core.sb(norms, n, [P, TT, DM]) for n in ("xc", "xn"))
                load(core, "masks", [(masks[:, d, :], I["masks"][d]) for d in range(2)]
                     + [(consts[n], I["consts"][:, c_off[n][0]:c_off[n][1]]) for n in names]
                     + [(xc[:, :, :], I["ctx"].rearrange("b (t p) d -> p (b t) d", p=P))])
                for v, src in ((1, xc), (0, x)):
                    gains(core, f"gain_v{v}", mod, v, fv["norm1"], gain[:, :], KD)
                    norm_transposed(core, f"norm_v{v}", k["ident"], src, hT, SEQ * (1 - v), gain, mod[:, 0:KD, v],
                                    (rstd, xn))
                norms.close()
                hgrn(core, I, k, fv, masks, hT[:, :, :], ycat)
                neighbourhood(core, I, k, consts, hT[:, :, :], ycat)
                rwkv(core, I, k, fv, masks, consts, hT[:, :, :], ycat)
            with ExitStack() as inner:
                yT = core.sb(inner, "yT2", [P, KD, SEQ])
                tmp = core.sb(inner, "res_tmp", [P, TT, 512])
                diag = core.sb(inner, "diag2", [P, KD, P])
                spread_rows(core, "g1", k["ident"], k["ones"], mod[:, 2 * KD:3 * KD, 0], diag[:, :, :], g_row)
                turn_features(core, "ycat_turn", k["ident"], ycat, KD, yT, fv["out_gain"])
                residual(core, "w_out2", yT, I["w_out_2"], g_row, tmp, x)
        hT = core.sb(mem, "h2T", [P, KD, SEQ])
        y = core.sb(mem, "moe_y", [P, TT, DM])
        gains(core, "gain_ffn", mod, 0, fv["norm2"], gain[:, :], 4 * KD)
        norm_transposed(core, "norm_ffn", k["ident"], x, hT, 0, gain, mod[:, 3 * KD:4 * KD, 0], (rstd, y))
        spread_rows(core, "g2", k["ident"], k["ones"], mod[:, 5 * KD:6 * KD, 0],
                    y[:, 0, :].rearrange("p (k f) -> p k f", k=KD), g_row)
        weights = core.sb(mem, "moe_weights", [P, TT, PER_GROUP])
        tile_i = core.sb(mem, "moe_tiles", [P, TILES + 1], I32)
        router(core, I, k, hT, weights, tile_d, tile_i)
        experts(core, I, k, hT, weights, tile_d, tile_i, y[:, :, :])
        with core.stage("last_order") as (block, own):
            @block.vector
            def _(dve):
                order = Order(dve, own)
                for t in range(TT):
                    order(nc.vector.tensor_tensor(y[:, t, :], y[:, t, :], g_row[:, :], ALU.mult))
                    order(nc.vector.tensor_tensor(x[:, t, :], x[:, t, :], y[:, t, :], ALU.add))


M_OFF, M_WIDTH = offsets(M_COLS)


def build(nc, I, out, second=True):
    with ExitStack() as ctx:
        core = Core(nc, ctx)
        x = core.sb(ctx, "x", [P, TT, DM])
        C_OFF, n_consts = offsets(C_COLS)
        R_OFF, n_rows = offsets(R_COLS)
        rows = core.sb(ctx, "rows", [P, n_rows])
        ones = core.sb(ctx, "ones", [P, P])
        ident = core.sb(ctx, "ident", [P, P])
        cv = I["consts"]
        pairs = [(x[:, :, :], I["x"].rearrange("b (t p) d -> p (b t) d", p=P)),
                 (rows[:, :], I["rows"].to_broadcast([P, n_rows])), (ident[:, :], cv[:, 0:P])]
        with ExitStack() as first:
            consts = core.sb(first, "consts", [P, n_consts])
            pos = core.sb(first, "pos", [P, TT], I32)
            k = {n: consts[:, a:b] for n, (a, b) in C_OFF.items()}
            k["ones"] = ones[:, :]
            k["ident"] = ident[:, :]
            k["final"] = rows[:, R_OFF["final"][0]:R_OFF["final"][1]]
            k["cos"] = core.sb(first, "cos", [P, TT, ROPE // 2])
            k["sin"] = core.sb(first, "sin", [P, TT, ROPE // 2])
            load(core, "inputs", pairs + [(consts[:, :], cv[:, 0:n_consts]),
                                          (pos[:, :], I["positions"])])
            with core.stage("ones_set") as (block, ones_set):
                @block.gpsimd
                def _(pool):
                    nc.gpsimd.memset(ones[:, :], 1.0).then_inc(ones_set, 1)
                    pool.wait_ge(ones_set, 1)
            with ExitStack() as mem:
                rotary_tables(core, mem, pos[:, :], k["inv_freq"], k["cos"][:, :, :], k["sin"][:, :, :])
            first_block(core, I, k, x)
        if second:
            second_block(core, I, dict(ident=ident[:, :], ones=ones[:, :],
                                       b_r=rows[:, R_OFF["b_rg"][0]:R_OFF["b_re"][1]],
                                       **{n: rows[:, a:b] for n, (a, b) in R_OFF.items()}), x)
        with core.stage("stored") as (block, stored):
            @block.sync
            def _(sp):
                sp.dma_start(out.rearrange("b (t p) d -> p (b t) d", p=P), x[:, :, :]).then_inc(stored, 16)
                sp.wait_ge(stored, 16)
        core.settle()


def columns(n, *arrays):
    return np.concatenate([a.reshape(-1, P).T for a in arrays], axis=1)


def head_rows(a):
    out = np.zeros((P, a.shape[1]), np.float32)
    out[:a.shape[0]] = a
    return out


def constants():
    p, q = np.arange(P)[:, None], np.arange(P)[None, :]
    ident = (p == q).astype(np.float32)
    sel = np.zeros((P, HEADS, P), np.float32)
    for h in range(HEADS):
        sel[h, h] = 1.0
    diag = np.where(p <= q, 0.0, MASKED)
    mla = np.zeros((P, TT, SEQ))
    for t in range(TT):
        mla[:, t] = np.where(np.arange(SEQ)[None, :] // 64 <= (t * P + p) // 64, 0.0, MASKED)
    quarter = HD // 4
    inv = (10000.0 ** (-np.arange(quarter, dtype=np.float32) / quarter)).astype(np.float32)
    pos = np.arange(SEQ)
    ang = np.concatenate([(pos // GRID_W).astype(np.float32)[:, None] * inv,
                          (pos % GRID_W).astype(np.float32)[:, None] * inv], axis=1)
    turn = lambda a: a.reshape(TT, P, 32).transpose(1, 0, 2).reshape(P, -1)
    half = ROPE // 2
    inv_freq = np.float32(10000.0) ** (-np.arange(half, dtype=np.float32) / np.float32(half))
    start = np.tile((np.arange(NTOK) % RW_CHUNK != 0).astype(np.float32), (P, 1))
    parts = dict(ident=ident, head_ones=(p // HD == q // HD), head_pick=(p // HD == np.arange(2)[None, :]),
                 inv_freq=np.tile(inv_freq, (P, 1)), sel=sel.reshape(P, -1),
                 ml_mask=np.concatenate([diag, 0 * diag], axis=1), mla_mask=mla.reshape(P, -1),
                 na_cos=turn(np.cos(ang)), na_sin=turn(np.sin(ang)), chunk_start=start,
                 ones_row=np.ones((P, SEQ)))
    consts = np.concatenate([parts[n].astype(np.float32) for n in C_COLS], axis=1)
    levels = [(q // b == p // b + 1) & ((q // b) % 2 == 1) for b in LEVELS]
    chunk = p // RW_CHUNK == q // RW_CHUNK
    masks = []
    for forward in (True, False):
        cols = [ident] + levels + [chunk & (p < q), chunk & (p <= q)]
        masks.append(np.concatenate([(m if forward else m.T).astype(np.float32) for m in cols], axis=1))
    return consts, np.stack(masks)


def window_bias(rpb):
    q = np.arange(SEQ)
    qr, qc = q[:, None] // GRID_W, q[:, None] % GRID_W
    kr, kc = q[None, :] // GRID_W, q[None, :] % GRID_W
    start = np.clip(qc - 8, 0, GRID_W - 16)
    inside = (kc >= start) & (kc < start + 16)
    cols = np.clip(kc - qc + 15, 0, 30)
    b = np.where(inside[None], rpb[:, kr - qr + 7, cols], np.float32(MASKED))
    return np.ascontiguousarray(b.reshape(C_HEADS, TT, P, SEQ).transpose(1, 2, 0, 3))


def layouts(a):
    d = {n: a[n] for n in ("x", "positions", "ada_w", "w_in", "w_uq", "w_ukv", "w_br_mla", "w_br_mlstm", "w_out",
                           "ffn_w_up", "ffn_w_down")}
    d["positions"] = a["positions"].reshape(TT, P).T
    layers = []
    for l in range(DEPTH):
        parts = dict(c=columns(8, a["c"][0]), ada_b=columns(48, a["ada_b"][l]), norm_mix=columns(8, a["norm_mix_w"][l]),
                     q_norm=columns(3, a["q_norm_w"][l]), kv_norm=columns(2, a["kv_norm_w"][l]),
                     conv_w=columns(32, *a["mlstm_conv_w"][l]), conv_b=columns(8, a["mlstm_conv_b"][l]),
                     head_norm=columns(4, a["mlstm_head_norm_w"][l]), norm_ffn=columns(8, a["norm_ffn_w"][l]),
                     ffn_conv_w=columns(3, *a["ffn_conv_w"][l]), ffn_conv_b=columns(44, a["ffn_conv_b"][l]),
                     gate_b=head_rows(a["mlstm_gate_b"][l].reshape(2, HEADS).T))
        layers.append(np.concatenate([parts[n] for n in L_COLS], axis=1))
    d["layer_vectors"] = np.stack(layers)
    s = {n[:-2]: v[0] for n, v in a.items() if n.endswith("_2") and n != "c_ctx_2"}
    gn = np.concatenate([s["hgrn_gn_gain"].reshape(-1), np.ones(DM - A_W, np.float32)])
    parts = dict(c=np.stack([columns(8, s["c"]), columns(8, a["c_ctx_2"])], axis=1).reshape(P, -1),
                 ada_b=columns(48, s["b_ada"]), norm1=columns(8, s["norm1_gain"]), norm2=columns(8, s["norm2_gain"]),
                 lb=columns(4, a["hgrn_lb_logits_2"][:, 0]), out_gain=columns(8, gn), mu=columns(9, s["rwkv_mu"]),
                 w0=columns(4, s["rwkv_w0"]), a0=columns(4, s["rwkv_a0"]), kk_scale=columns(2, s["rwkv_kk_scale"]),
                 k_a=columns(2, s["rwkv_k_a"]), r_k=columns(2, s["rwkv_r_k"]))
    d["second_vectors"] = np.concatenate([parts[n] for n in S_COLS], axis=1)
    rows = dict(final=a["final_norm_w"], ln_gain=s["rwkv_ln_gain"], ln_bias=s["rwkv_ln_bias"], q_gain=s["na_q_gain"],
                k_gain=s["na_k_gain"], b_rg=s["b_router_group"], b_re=s["b_router_expert"])
    d["rows"] = np.concatenate([rows[n] for n in R_COLS])[None, :]
    d["ctx"] = s["ctx"][None]
    for n in ("w_ada", "w_in", "w_out", "w_exp_gate", "w_exp_up", "w_exp_down"):
        d[n + "_2"] = s[n].reshape((EXPERTS,) + s[n].shape[2:]) if s[n].ndim == 4 else s[n]
    d["rwkv_up"] = np.concatenate([s["rwkv_w_up"].reshape(P, A_W), s["rwkv_a_up"].reshape(P, A_W),
                                   s["rwkv_g_up"]], axis=1)
    d["router"] = np.concatenate([s["w_router_group"], s["w_router_expert"]], axis=1)
    d["bias"] = window_bias(s["na_rpb"])
    d["consts"], d["masks"] = constants()
    place = np.arange(P, dtype=np.float32)
    d["route"] = np.concatenate([(place[:, None] < place).astype(np.float32), np.tile(place, (P, 1))], axis=1)
    return {n: np.ascontiguousarray(v) for n, v in d.items()}


def kernel(**inputs):
    import concourse.bacc as bacc
    from concourse.bass_utils import run_bass_kernel_spmd

    nc = bacc.Bacc("TRN2", target_bir_lowering=False, num_devices=1)
    arrays = layouts({n: np.asarray(v) for n, v in inputs.items()})
    I = {n: nc.dram_tensor(n, v.shape, mybir.dt.from_np(v.dtype), kind="ExternalInput").ap()
         for n, v in arrays.items()}
    out = nc.dram_tensor("out", (1, SEQ, DM), F32, kind="ExternalOutput").ap()
    build(nc, I, out)
    r = run_bass_kernel_spmd(nc, [arrays], core_ids=[0])
    return r.results[0]["out"]
```
